# Optimizing a Trainium2 kernel written in Bass

```python
import jax, jax.numpy as jnp
from jax import lax
import numpy as np

D_MODEL = 2048
BATCH = 1
SEQ = 256
DEPTH = 1

N_MEM = 256
NORM_EPS = 1e-6
NEG_INF = -1e30
A_HEADS = 12
A_KV_HEADS = 4
A_HEAD_DIM = 64
A_WIDTH = A_HEADS * A_HEAD_DIM
A_KV_WIDTH = A_KV_HEADS * A_HEAD_DIM
WINDOW = 128
BLOCK = 128
ROPE_THETA = 10000.0
R_HEADS = 12
R_HEAD_DIM = 64
R_WIDTH = R_HEADS * R_HEAD_DIM
DECAY_LORA = 64
ICLR_LORA = 64
N_DIR = 2
GN_EPS = 64e-5
R_SHIFT_WIDTH = 3 * R_WIDTH + N_DIR * DECAY_LORA + N_DIR * ICLR_LORA
X_HEADS = 4
X_HEAD_DIM = 128
X_WIDTH = X_HEADS * X_HEAD_DIM
N_BRANCH = 3
IN_WIDTH = (2 * A_WIDTH + 2 * A_KV_WIDTH + R_SHIFT_WIDTH + R_WIDTH
            + 2 * X_WIDTH + N_BRANCH * D_MODEL)


def _split(t, sizes):
    idx = np.cumsum(sizes)[:-1].tolist()
    return jnp.split(t, idx, axis=-1)

def rms_norm(t, g, eps=NORM_EPS):
    tf = t.astype(jnp.float32)
    y = tf * lax.rsqrt(jnp.mean(tf * tf, axis=-1, keepdims=True) + eps)
    return (y * g.astype(jnp.float32)).astype(t.dtype)

def rope(t, positions):
    half = t.shape[-1] // 2
    inv = ROPE_THETA ** (-jnp.arange(half, dtype=jnp.float32) / half)
    ang = positions.astype(jnp.float32)[:, None] * inv[None, :]
    cos = jnp.cos(ang)[None, :, None, :]
    sin = jnp.sin(ang)[None, :, None, :]
    t1 = t[..., :half].astype(jnp.float32)
    t2 = t[..., half:].astype(jnp.float32)
    return jnp.concatenate([t1 * cos - t2 * sin, t2 * cos + t1 * sin], axis=-1).astype(t.dtype)

def windowed_gqa(q, k, v, sink):
    B, S, Hq, D = q.shape
    nb = S // BLOCK
    G = Hq // A_KV_HEADS
    qb = q.reshape(B, nb, BLOCK, A_KV_HEADS, G, D)
    pad = ((0, 0), (BLOCK, BLOCK), (0, 0), (0, 0))
    kp = jnp.pad(k, pad).reshape(B, nb + 2, BLOCK, A_KV_HEADS, D)
    vp = jnp.pad(v, pad).reshape(B, nb + 2, BLOCK, A_KV_HEADS, D)
    kb = jnp.concatenate([kp[:, :-2], kp[:, 1:-1], kp[:, 2:]], axis=2)
    vb = jnp.concatenate([vp[:, :-2], vp[:, 1:-1], vp[:, 2:]], axis=2)
    s = jnp.einsum('bnqhgd,bnkhd->bnhgqk', qb, kb).astype(jnp.float32) * (D ** -0.5)
    blk = jnp.arange(nb)[:, None] * BLOCK
    qpos = blk + jnp.arange(BLOCK)[None, :]
    kpos = blk - BLOCK + jnp.arange(3 * BLOCK)[None, :]
    rel = kpos[:, None, :] - qpos[:, :, None]
    valid = (jnp.abs(rel) <= WINDOW) & (kpos[:, None, :] >= 0) & (kpos[:, None, :] < S)
    s = jnp.where(valid[None, :, None, None, :, :], s, NEG_INF)
    sink_l = sink.astype(jnp.float32).reshape(A_KV_HEADS, G)[None, None, :, :, None, None]
    sink_l = jnp.broadcast_to(sink_l, s.shape[:-1] + (1,))
    p = jax.nn.softmax(jnp.concatenate([s, sink_l], axis=-1), axis=-1)[..., :-1]
    o = jnp.einsum('bnhgqk,bnkhd->bnqhgd', p.astype(v.dtype), vb)
    return o.reshape(B, S, Hq * D)

def rwkv7_scan(r, w, k, v, kk, a):
    B, T, H, N = r.shape
    decay = jnp.exp(-jnp.exp(w))
    b = kk * a
    xs = tuple(t.swapaxes(0, 1) for t in (r, decay, k, v, kk, b))

    def step(S, inp):
        r_t, d_t, k_t, v_t, kk_t, b_t = inp
        sa = jnp.einsum('bhij,bhj->bhi', S, -kk_t)
        S = S * d_t[:, :, None, :] + sa[..., None] * b_t[:, :, None, :] + v_t[..., None] * k_t[:, :, None, :]
        return S, jnp.einsum('bhij,bhj->bhi', S, r_t)

    S0 = jnp.zeros((B, H, N, N), jnp.float32)
    _, y = lax.scan(step, S0, xs)
    return y.swapaxes(0, 1)

def rwkv7_branch(p_shift, mu, k_k, k_a, r_k, w0, w2, a0, a2, ln_w, ln_b):
    B, T, _ = p_shift.shape
    p = p_shift.astype(jnp.float32)
    prev = jnp.pad(p, ((0, 0), (1, 0), (0, 0)))[:, :-1]
    nxt = jnp.pad(p, ((0, 0), (0, 1), (0, 0)))[:, 1:]
    p = p + mu.astype(jnp.float32) * (0.5 * (prev + nxt) - p)
    r, k, v, wf, wb, af, ab = _split(p, (R_WIDTH, R_WIDTH, R_WIDTH, DECAY_LORA, DECAY_LORA,
                                         ICLR_LORA, ICLR_LORA))
    hs = (B, T, R_HEADS, R_HEAD_DIM)
    r4 = r.reshape(hs)
    v4 = v.reshape(hs)
    kk = (k * k_k.astype(jnp.float32)).reshape(hs)
    kk = kk / jnp.maximum(jnp.linalg.norm(kk, axis=-1, keepdims=True), 1e-12)
    w_in = (wf, wb)
    a_in = (af, ab)
    y_sum = jnp.zeros(hs, jnp.float32)
    bonus = jnp.zeros(hs, jnp.float32)
    r_k4 = r_k.astype(jnp.float32)[None, None]
    for d in range(N_DIR):
        wd = -jax.nn.softplus(-(w0[d].astype(jnp.float32)
                                + jnp.tanh(w_in[d]) @ w2[d].astype(jnp.float32))) - 0.5
        ad = jax.nn.sigmoid(a0[d].astype(jnp.float32) + a_in[d] @ a2[d].astype(jnp.float32))
        kd = k * (1.0 + (ad - 1.0) * k_a.astype(jnp.float32))
        wd4, ad4, kd4 = wd.reshape(hs), ad.reshape(hs), kd.reshape(hs)
        if d == 0:
            y_sum = y_sum + rwkv7_scan(r4, wd4, kd4, v4, kk, ad4)
        else:
            flip = lambda t: jnp.flip(t, axis=1)
            y_sum = y_sum + flip(rwkv7_scan(flip(r4), flip(wd4), flip(kd4), flip(v4), flip(kk), flip(ad4)))
        bonus = bonus + jnp.sum(r4 * kd4 * r_k4, axis=-1, keepdims=True) * v4
    mean = jnp.mean(y_sum, axis=-1, keepdims=True)
    var = jnp.mean(jnp.square(y_sum - mean), axis=-1, keepdims=True)
    y = ((y_sum - mean) * lax.rsqrt(var + GN_EPS)).reshape(B, T, R_WIDTH)
    y = y * ln_w.astype(jnp.float32) + ln_b.astype(jnp.float32)
    return y + bonus.reshape(B, T, R_WIDTH)

def memory_xattn(q, km, vm):
    s = jnp.einsum('bshd,bmhd->bhsm', q, km).astype(jnp.float32) * (X_HEAD_DIM ** -0.5)
    p = jax.nn.softmax(s, axis=-1)
    o = jnp.einsum('bhsm,bmhd->bshd', p.astype(vm.dtype), vm)
    return o.reshape(q.shape[0], q.shape[1], X_WIDTH)

def hybrid_layer(x, mem, norm_g, mem_norm_g, w_in, gate_b, attn_q_norm_g, attn_k_norm_g,
                 attn_sink, attn_w_o, rwkv_mu, rwkv_k_k, rwkv_k_a, rwkv_r_k, rwkv_w0, rwkv_w2,
                 rwkv_a0, rwkv_a2, rwkv_ln_w, rwkv_ln_b, rwkv_w_o, x_w_kv, x_q_norm_g,
                 x_k_norm_g, x_w_o, w_out):
    B, S, _ = x.shape
    positions = jnp.arange(S)
    h = rms_norm(x, norm_g)
    proj = h @ w_in
    aq, ak, av, ag, rs, rg, xq, xg, mg = _split(
        proj, (A_WIDTH, A_KV_WIDTH, A_KV_WIDTH, A_WIDTH, R_SHIFT_WIDTH, R_WIDTH,
               X_WIDTH, X_WIDTH, N_BRANCH * D_MODEL))

    q = rope(rms_norm(aq.reshape(B, S, A_HEADS, A_HEAD_DIM), attn_q_norm_g), positions)
    k = rope(rms_norm(ak.reshape(B, S, A_KV_HEADS, A_HEAD_DIM), attn_k_norm_g), positions)
    va = av.reshape(B, S, A_KV_HEADS, A_HEAD_DIM)
    y_a = windowed_gqa(q, k, va, attn_sink) * jax.nn.silu(ag)

    y_r = rwkv7_branch(rs, rwkv_mu, rwkv_k_k, rwkv_k_a, rwkv_r_k, rwkv_w0, rwkv_w2,
                       rwkv_a0, rwkv_a2, rwkv_ln_w, rwkv_ln_b)
    y_r = y_r.astype(x.dtype) * jax.nn.silu(rg)

    mkv = rms_norm(mem, mem_norm_g) @ x_w_kv
    km, vm = _split(mkv, (X_WIDTH, X_WIDTH))
    km = rms_norm(km.reshape(B, -1, X_HEADS, X_HEAD_DIM), x_k_norm_g)
    vm = vm.reshape(B, -1, X_HEADS, X_HEAD_DIM)
    qx = rms_norm(xq.reshape(B, S, X_HEADS, X_HEAD_DIM), x_q_norm_g)
    y_x = memory_xattn(qx, km, vm) * jax.nn.silu(xg)

    gates = jax.nn.sigmoid((mg + gate_b).astype(jnp.float32)).reshape(B, S, N_BRANCH, D_MODEL)
    gates = gates.astype(x.dtype)
    merged = (gates[:, :, 0] * (y_a @ attn_w_o)
              + gates[:, :, 1] * (y_r @ rwkv_w_o)
              + gates[:, :, 2] * (y_x @ x_w_o))
    return x + merged @ w_out

def first_inputs(seed: int = 0) -> dict:
    key = jax.random.key(seed)
    ks = jax.random.split(key, 32)
    n = lambda i, shape, s=1.0: jax.random.normal(ks[i], shape, jnp.float32) * s
    L = DEPTH
    return {
        "x": n(0, (BATCH, SEQ, D_MODEL)),
        "mem": n(1, (BATCH, N_MEM, D_MODEL)),
        "norm_g": 1.0 + n(2, (L, D_MODEL), 0.02),
        "mem_norm_g": 1.0 + n(3, (L, D_MODEL), 0.02),
        "w_in": n(4, (L, D_MODEL, IN_WIDTH), D_MODEL ** -0.5),
        "gate_b": n(5, (L, N_BRANCH * D_MODEL), 0.1),
        "attn_q_norm_g": 1.0 + n(6, (L, A_HEAD_DIM), 0.02),
        "attn_k_norm_g": 1.0 + n(7, (L, A_HEAD_DIM), 0.02),
        "attn_sink": n(8, (L, A_HEADS), 0.5),
        "attn_w_o": n(9, (L, A_WIDTH, D_MODEL), A_WIDTH ** -0.5),
        "rwkv_mu": jax.random.uniform(ks[10], (L, R_SHIFT_WIDTH), jnp.float32, 0.0, 1.0),
        "rwkv_k_k": 0.85 + n(11, (L, R_WIDTH), 0.05),
        "rwkv_k_a": 1.0 + n(12, (L, R_WIDTH), 0.05),
        "rwkv_r_k": n(13, (L, R_HEADS, R_HEAD_DIM), 0.1),
        "rwkv_w0": jax.random.uniform(ks[14], (L, N_DIR, R_WIDTH), jnp.float32, -5.0, -1.0),
        "rwkv_w2": n(15, (L, N_DIR, DECAY_LORA, R_WIDTH), 0.1),
        "rwkv_a0": n(16, (L, N_DIR, R_WIDTH), 0.1),
        "rwkv_a2": n(17, (L, N_DIR, ICLR_LORA, R_WIDTH), 0.5 * ICLR_LORA ** -0.5),
        "rwkv_ln_w": 1.0 + n(18, (L, R_WIDTH), 0.02),
        "rwkv_ln_b": n(19, (L, R_WIDTH), 0.02),
        "rwkv_w_o": n(20, (L, R_WIDTH, D_MODEL), R_WIDTH ** -0.5),
        "x_w_kv": n(21, (L, D_MODEL, 2 * X_WIDTH), D_MODEL ** -0.5),
        "x_q_norm_g": 1.0 + n(22, (L, X_HEAD_DIM), 0.02),
        "x_k_norm_g": 1.0 + n(23, (L, X_HEAD_DIM), 0.02),
        "x_w_o": n(24, (L, X_WIDTH, D_MODEL), X_WIDTH ** -0.5),
        "w_out": n(25, (L, D_MODEL, D_MODEL), D_MODEL ** -0.5),
    }

def first_block(x, mem, norm_g, mem_norm_g, w_in, gate_b, attn_q_norm_g, attn_k_norm_g,
              attn_sink, attn_w_o, rwkv_mu, rwkv_k_k, rwkv_k_a, rwkv_r_k, rwkv_w0, rwkv_w2,
              rwkv_a0, rwkv_a2, rwkv_ln_w, rwkv_ln_b, rwkv_w_o, x_w_kv, x_q_norm_g,
              x_k_norm_g, x_w_o, w_out):
    h = x
    for l in range(DEPTH):
        h = hybrid_layer(h, mem, norm_g[l], mem_norm_g[l], w_in[l], gate_b[l],
                         attn_q_norm_g[l], attn_k_norm_g[l], attn_sink[l], attn_w_o[l],
                         rwkv_mu[l], rwkv_k_k[l], rwkv_k_a[l], rwkv_r_k[l], rwkv_w0[l],
                         rwkv_w2[l], rwkv_a0[l], rwkv_a2[l], rwkv_ln_w[l], rwkv_ln_b[l],
                         rwkv_w_o[l], x_w_kv[l], x_q_norm_g[l], x_k_norm_g[l], x_w_o[l],
                         w_out[l])
    return h


_first_inputs = first_inputs


def first_inputs(seed=0):
    import zlib

    import numpy as np

    out = dict(_first_inputs(seed))
    spreads = {}
    factors = {'norm_g': 4.01,
     'mem_norm_g': 8.0,
     'gate_b': 4.493,
     'attn_q_norm_g': 8.0,
     'attn_k_norm_g': 8.0,
     'attn_sink': 8.0,
     'rwkv_k_k': 5.133,
     'rwkv_k_a': 3.361,
     'rwkv_w2': 3.973,
     'rwkv_a0': 4.365,
     'rwkv_ln_w': 8.0,
     'rwkv_ln_b': 8.0,
     'x_q_norm_g': 8.0,
     'x_k_norm_g': 8.0}
    for name, (base, spread) in spreads.items():
        noise = np.random.default_rng([zlib.crc32(name.encode()), seed]).standard_normal(out[name].shape)
        drawn = base * np.exp(spread * noise) if base else spread * noise
        out[name] = __import__('jax').numpy.asarray(drawn.astype(out[name].dtype))
    for name, factor in factors.items():
        out[name] = (out[name] * factor).astype(out[name].dtype)
    return out


_narrow_inputs = first_inputs


def first_inputs(seed=0):

    out = dict(_narrow_inputs(seed))
    wider = {'attn_q_norm_g': 4.29,
     'attn_k_norm_g': 4.37,
     'rwkv_k_k': 12.0,
     'rwkv_ln_w': 12.0,
     'rwkv_ln_b': 12.0}
    for name, times in wider.items():
        mean = out[name].mean()
        out[name] = (mean + times * (out[name] - mean)).astype(out[name].dtype)
    return out


N_META = 16
POOL_WIDTH = D_MODEL
POOL_WINDOWS = (2, 4, 8, 16)
POOL_GROUPS = len(POOL_WINDOWS)
POOL_GROUP_DIM = POOL_WIDTH // POOL_GROUPS
LRU_WIDTH = D_MODEL
LRU_HEAD_DIM = 256
LRU_HEADS = LRU_WIDTH // LRU_HEAD_DIM
CONV_WIDTH = 4
LRU_C = 8.0
D_FF = 4 * D_MODEL
IN_SPLITS = (POOL_WIDTH,
             POOL_WIDTH + LRU_WIDTH,
             POOL_WIDTH + 2 * LRU_WIDTH,
             POOL_WIDTH + 2 * LRU_WIDTH + D_MODEL)
IN_COLS = POOL_WIDTH + 2 * LRU_WIDTH + 2 * D_MODEL


def rmsnorm(x, g):
    xf = x.astype(jnp.float32)
    y = xf * lax.rsqrt(jnp.mean(xf * xf, axis=-1, keepdims=True) + NORM_EPS)
    return (y * g.astype(jnp.float32)).astype(x.dtype)

def causal_window_mean(v, w):
    T = v.shape[1]
    c = lax.cumsum(v, axis=1)
    c_shift = jnp.pad(c, ((0, 0), (w, 0), (0, 0)))[:, :T]
    cnt = jnp.minimum(jnp.arange(1, T + 1), w).astype(jnp.float32)
    return (c - c_shift) / cnt[None, :, None]

def pool_mixer(v, pool_w, pool_scale):
    B, T, _ = v.shape
    vf = v.astype(jnp.float32)
    diffs = []
    for g, w in enumerate(POOL_WINDOWS):
        vg = vf[..., g * POOL_GROUP_DIM:(g + 1) * POOL_GROUP_DIM]
        diffs.append(causal_window_mean(vg, w) - vg)
    d = jnp.stack(diffs, axis=2)
    y = jnp.einsum('btgc,gcd->btgd', d, pool_w.astype(jnp.float32))
    y = y.reshape(B, T, POOL_WIDTH) * pool_scale.astype(jnp.float32)
    return y.astype(v.dtype)

def causal_depthwise_conv(x, w, b):
    y = lax.conv_general_dilated(
        x, w[:, None, :].astype(x.dtype), window_strides=(1,),
        padding=((CONV_WIDTH - 1, 0),),
        dimension_numbers=('NWC', 'WIO', 'NWC'),
        feature_group_count=x.shape[-1])
    return y + b.astype(x.dtype)

def rg_lru(xc, gate_a_w, gate_a_b, gate_x_w, gate_x_b, lam):
    B, T, W = xc.shape
    xf = xc.astype(jnp.float32)
    xh = xf.reshape(B, T, LRU_HEADS, LRU_HEAD_DIM)
    r = jax.nn.sigmoid(jnp.einsum('bthi,hij->bthj', xh, gate_a_w.astype(jnp.float32))
                       + gate_a_b.astype(jnp.float32)).reshape(B, T, W)
    i = jax.nn.sigmoid(jnp.einsum('bthi,hij->bthj', xh, gate_x_w.astype(jnp.float32))
                       + gate_x_b.astype(jnp.float32)).reshape(B, T, W)
    log_a = -LRU_C * r * jax.nn.softplus(-lam.astype(jnp.float32))
    a = jnp.exp(log_a)
    mult = jnp.sqrt(-jnp.expm1(2.0 * log_a))
    bt = mult * (i * xf)

    def combine(left, right):
        a1, b1 = left
        a2, b2 = right
        return a1 * a2, a2 * b1 + b2

    _, h = lax.associative_scan(combine, (a, bt), axis=1)
    return h.astype(xc.dtype)

def second_inputs(seed: int = 0) -> dict:
    key = jax.random.key(seed)
    ks = jax.random.split(key, 20)
    f32 = jnp.float32
    x = jax.random.normal(ks[0], (BATCH, SEQ, D_MODEL), f32)
    meta_tokens = jax.random.normal(ks[1], (N_META, D_MODEL), f32)
    norm1_g = 1.0 + 0.02 * jax.random.normal(ks[2], (DEPTH, D_MODEL), f32)
    w_in = jax.random.normal(ks[3], (DEPTH, D_MODEL, IN_COLS), f32) * D_MODEL ** -0.5
    pool_w = jax.random.normal(ks[4], (DEPTH, POOL_GROUPS, POOL_GROUP_DIM, POOL_GROUP_DIM), f32) * POOL_GROUP_DIM ** -0.5
    pool_scale = 1.0 + 0.02 * jax.random.normal(ks[5], (DEPTH, POOL_WIDTH), f32)
    conv_w = jax.random.normal(ks[6], (DEPTH, CONV_WIDTH, LRU_WIDTH), f32) * CONV_WIDTH ** -0.5
    conv_b = 0.01 * jax.random.normal(ks[7], (DEPTH, LRU_WIDTH), f32)
    gate_a_w = jax.random.normal(ks[8], (DEPTH, LRU_HEADS, LRU_HEAD_DIM, LRU_HEAD_DIM), f32) * LRU_HEAD_DIM ** -0.5
    gate_a_b = 0.01 * jax.random.normal(ks[9], (DEPTH, LRU_HEADS, LRU_HEAD_DIM), f32)
    gate_x_w = jax.random.normal(ks[10], (DEPTH, LRU_HEADS, LRU_HEAD_DIM, LRU_HEAD_DIM), f32) * LRU_HEAD_DIM ** -0.5
    gate_x_b = 0.01 * jax.random.normal(ks[11], (DEPTH, LRU_HEADS, LRU_HEAD_DIM), f32)
    u = jax.random.uniform(ks[12], (DEPTH, LRU_WIDTH), f32, minval=0.9, maxval=0.999)
    s = u ** (1.0 / LRU_C)
    lru_lambda = jnp.log(s) - jnp.log1p(-s)
    w_out = jax.random.normal(ks[13], (DEPTH, D_MODEL, D_MODEL), f32) * D_MODEL ** -0.5
    norm2_g = 1.0 + 0.02 * jax.random.normal(ks[14], (DEPTH, D_MODEL), f32)
    mlp_w1 = jax.random.normal(ks[15], (DEPTH, D_MODEL, D_FF), f32) * D_MODEL ** -0.5
    mlp_w2 = jax.random.normal(ks[16], (DEPTH, D_FF, D_MODEL), f32) * D_FF ** -0.5
    final_g = 1.0 + 0.02 * jax.random.normal(ks[17], (D_MODEL,), f32)
    return {"x": x, "meta_tokens": meta_tokens, "norm1_g": norm1_g, "w_in": w_in,
            "pool_w": pool_w, "pool_scale": pool_scale, "conv_w": conv_w, "conv_b": conv_b,
            "gate_a_w": gate_a_w, "gate_a_b": gate_a_b, "gate_x_w": gate_x_w, "gate_x_b": gate_x_b,
            "lru_lambda": lru_lambda, "w_out": w_out, "norm2_g": norm2_g,
            "mlp_w1": mlp_w1, "mlp_w2": mlp_w2, "final_g": final_g}

def second_block(x, meta_tokens, norm1_g, w_in, pool_w, pool_scale, conv_w, conv_b,
              gate_a_w, gate_a_b, gate_x_w, gate_x_b, lru_lambda, w_out, norm2_g,
              mlp_w1, mlp_w2, final_g):
    B = x.shape[0]
    meta = jnp.broadcast_to(meta_tokens[None].astype(x.dtype), (B, N_META, x.shape[-1]))
    h = jnp.concatenate([meta, x], axis=1)
    for l in range(DEPTH):
        u = rmsnorm(h, norm1_g[l])
        proj = u @ w_in[l]
        v_pool, v_lru, v_gelu, g_pool, g_lru = jnp.split(proj, IN_SPLITS, axis=-1)
        pool_out = pool_mixer(v_pool, pool_w[l], pool_scale[l])
        xc = causal_depthwise_conv(v_lru, conv_w[l], conv_b[l])
        lru_out = rg_lru(xc, gate_a_w[l], gate_a_b[l], gate_x_w[l], gate_x_b[l],
                         lru_lambda[l]) * jax.nn.gelu(v_gelu)
        merged = jax.nn.sigmoid(g_pool) * pool_out + jax.nn.sigmoid(g_lru) * lru_out
        h = h + merged @ w_out[l]
        u2 = rmsnorm(h, norm2_g[l])
        h = h + jnp.square(jax.nn.relu(u2 @ mlp_w1[l])) @ mlp_w2[l]
    out = rmsnorm(h, final_g)
    return out[:, N_META:]


D_CONV = D_MODEL // 2
CONV_GROUPS = 8
CONV_WIDTH_3 = 3
GLA_HEADS = 4
D_GLA_V = D_MODEL // 2
D_GLA_K = D_GLA_V // 2
HEAD_K = D_GLA_K // GLA_HEADS
HEAD_V = D_GLA_V // GLA_HEADS
GATE_RANK = 16
GATE_TAU = 16.0
CHUNK = 64
D_FF_3 = 4 * D_MODEL
LN_EPS = 1e-5
RMS_EPS = 1e-6
DN_ALPHA = (2.0 * DEPTH) ** 0.25
DN_BETA = (8.0 * DEPTH) ** -0.25

PROJ_SIZES = (D_CONV, D_CONV, D_CONV, D_GLA_K, D_GLA_K, D_GLA_V, D_GLA_V, GATE_RANK)
D_IN_PROJ = sum(PROJ_SIZES)
PROJ_SPLITS = tuple(int(s) for s in np.cumsum(PROJ_SIZES)[:-1])


def layer_norm(x, g, b):
    xf = x.astype(jnp.float32)
    mu = jnp.mean(xf, axis=-1, keepdims=True)
    var = jnp.mean(jnp.square(xf - mu), axis=-1, keepdims=True)
    y = (xf - mu) * lax.rsqrt(var + LN_EPS)
    return (y * g.astype(jnp.float32) + b.astype(jnp.float32)).astype(x.dtype)

def group_rms_norm(x, g, groups):
    shp = x.shape
    xf = x.astype(jnp.float32).reshape(shp[:-1] + (groups, shp[-1] // groups))
    xf = xf * lax.rsqrt(jnp.mean(jnp.square(xf), axis=-1, keepdims=True) + RMS_EPS)
    return (xf.reshape(shp) * g.astype(jnp.float32)).astype(x.dtype)

def short_gated_conv(b_gate, c_gate, u, conv_w):
    h = c_gate * u
    y = lax.conv_general_dilated(
        h, conv_w[:, None, :].astype(h.dtype), window_strides=(1,),
        padding=[(CONV_WIDTH_3 - 1, 0)], dimension_numbers=("NWC", "WIO", "NWC"),
        feature_group_count=h.shape[-1])
    return b_gate * y

def gla_chunked(q, k, v, log_a):
    bsz, seq = q.shape[0], q.shape[1]
    n_chunks = seq // CHUNK

    def to_chunks(t):
        return t.reshape(bsz, n_chunks, CHUNK, GLA_HEADS, t.shape[-1]).transpose(0, 3, 1, 2, 4).astype(jnp.float32)

    qc = to_chunks(q) * (HEAD_K ** -0.5)
    kc, vc, gc = to_chunks(k), to_chunks(v), to_chunks(log_a)
    bcum = jnp.cumsum(gc, axis=3)
    b_last = bcum[:, :, :, -1:, :]
    q_dec = qc * jnp.exp(bcum)
    k_inv = kc * jnp.exp(-bcum)
    k_end = kc * jnp.exp(b_last - bcum)

    causal = jnp.tril(jnp.ones((CHUNK, CHUNK), dtype=bool))
    scores = jnp.where(causal, jnp.einsum("bhncd,bhnsd->bhncs", q_dec, k_inv), 0.0)
    o_intra = jnp.einsum("bhncs,bhnse->bhnce", scores, vc)

    delta = jnp.einsum("bhncd,bhnce->bhnde", k_end, vc)
    decay = jnp.exp(b_last[:, :, :, 0, :])

    def step(state, inp):
        dec, dlt = inp
        return dec[..., None] * state + dlt, state

    init = jnp.zeros((bsz, GLA_HEADS, HEAD_K, HEAD_V), jnp.float32)
    _, states = lax.scan(step, init, (jnp.moveaxis(decay, 2, 0), jnp.moveaxis(delta, 2, 0)))
    states = jnp.moveaxis(states, 0, 2)
    o_inter = jnp.einsum("bhncd,bhnde->bhnce", q_dec, states)
    o = o_intra + o_inter
    return o.transpose(0, 2, 3, 1, 4).reshape(bsz, seq, GLA_HEADS * HEAD_V)

def third_inputs(seed: int = 0) -> dict:
    key = jax.random.key(seed)
    ks = jax.random.split(key, 16)
    f32 = jnp.float32
    x = jax.random.normal(ks[0], (BATCH, SEQ, D_MODEL), f32)
    col_scale = jnp.concatenate([
        jnp.full((D_CONV,), 1.0, f32), jnp.full((D_CONV,), 1.0, f32), jnp.full((D_CONV,), DN_BETA, f32),
        jnp.full((D_GLA_K,), 1.0, f32), jnp.full((D_GLA_K,), 1.0, f32), jnp.full((D_GLA_V,), DN_BETA, f32),
        jnp.full((D_GLA_V,), 1.0, f32), jnp.full((GATE_RANK,), 1.0, f32)])
    w_in = jax.random.normal(ks[1], (DEPTH, D_MODEL, D_IN_PROJ), f32) * (D_MODEL ** -0.5) * col_scale
    conv_w = jax.random.normal(ks[2], (DEPTH, CONV_WIDTH_3, D_CONV), f32) * (CONV_WIDTH_3 ** -0.5)
    conv_norm_g = 1.0 + 0.02 * jax.random.normal(ks[3], (DEPTH, D_CONV), f32)
    w_gate_up = jax.random.normal(ks[4], (DEPTH, GATE_RANK, D_GLA_K), f32) * (GATE_RANK ** -0.5)
    gate_bias = 0.1 * jax.random.normal(ks[5], (DEPTH, D_GLA_K), f32)
    gla_norm_g = 1.0 + 0.02 * jax.random.normal(ks[6], (DEPTH, D_GLA_V), f32)
    w_out = jax.random.normal(ks[7], (DEPTH, D_CONV + D_GLA_V, D_MODEL), f32) * ((D_CONV + D_GLA_V) ** -0.5) * DN_BETA
    ln1_g = 1.0 + 0.02 * jax.random.normal(ks[8], (DEPTH, D_MODEL), f32)
    ln1_b = 0.02 * jax.random.normal(ks[9], (DEPTH, D_MODEL), f32)
    w_ff_up = jax.random.normal(ks[10], (DEPTH, D_MODEL, D_FF_3), f32) * (D_MODEL ** -0.5) * DN_BETA
    w_ff_down = jax.random.normal(ks[11], (DEPTH, D_FF_3, D_MODEL), f32) * (D_FF_3 ** -0.5) * DN_BETA
    ln2_g = 1.0 + 0.02 * jax.random.normal(ks[12], (DEPTH, D_MODEL), f32)
    ln2_b = 0.02 * jax.random.normal(ks[13], (DEPTH, D_MODEL), f32)
    return {"x": x, "w_in": w_in, "conv_w": conv_w, "conv_norm_g": conv_norm_g,
            "w_gate_up": w_gate_up, "gate_bias": gate_bias, "gla_norm_g": gla_norm_g,
            "w_out": w_out, "ln1_g": ln1_g, "ln1_b": ln1_b, "w_ff_up": w_ff_up,
            "w_ff_down": w_ff_down, "ln2_g": ln2_g, "ln2_b": ln2_b}

def third_block(x, w_in, conv_w, conv_norm_g, w_gate_up, gate_bias, gla_norm_g, w_out,
              ln1_g, ln1_b, w_ff_up, w_ff_down, ln2_g, ln2_b):
    bsz, seq = x.shape[0], x.shape[1]
    for l in range(DEPTH):
        proj = x @ w_in[l]
        b_gate, c_gate, u, q, k, v, r, z_low = jnp.split(proj, PROJ_SPLITS, axis=-1)

        y_conv = short_gated_conv(b_gate, c_gate, u, conv_w[l])
        y_conv = group_rms_norm(y_conv, conv_norm_g[l], CONV_GROUPS)

        z = (z_low @ w_gate_up[l] + gate_bias[l]).astype(jnp.float32)
        log_a = jax.nn.log_sigmoid(z) / GATE_TAU
        hk = (bsz, seq, GLA_HEADS, HEAD_K)
        o = gla_chunked(q.reshape(hk), k.reshape(hk), v.reshape(bsz, seq, GLA_HEADS, HEAD_V), log_a.reshape(hk))
        o = group_rms_norm(o.astype(x.dtype), gla_norm_g[l], GLA_HEADS)
        y_gla = o * jax.nn.silu(r)

        mix = jnp.concatenate([y_conv, y_gla], axis=-1) @ w_out[l]
        x = layer_norm(DN_ALPHA * x + mix, ln1_g[l], ln1_b[l])

        ff = jnp.square(jax.nn.relu(x @ w_ff_up[l])) @ w_ff_down[l]
        x = layer_norm(DN_ALPHA * x + ff, ln2_g[l], ln2_b[l])
    return x


_first_inputs_3 = third_inputs


def third_inputs(seed=0):
    import zlib

    import numpy as np

    out = dict(_first_inputs_3(seed))
    spreads = {}
    factors = {'conv_norm_g': 27.647,
     'w_gate_up': 2.846,
     'gate_bias': 6.676,
     'gla_norm_g': 42.835,
     'ln1_g': 7.758,
     'ln1_b': 7.534,
     'ln2_g': 8.472,
     'ln2_b': 8.076}
    for name, (base, spread) in spreads.items():
        noise = np.random.default_rng([zlib.crc32(name.encode()), seed]).standard_normal(out[name].shape)
        drawn = base * np.exp(spread * noise) if base else spread * noise
        out[name] = __import__('jax').numpy.asarray(drawn.astype(out[name].dtype))
    for name, factor in factors.items():
        out[name] = (out[name] * factor).astype(out[name].dtype)
    return out


_narrow_inputs_3 = third_inputs


def third_inputs(seed=0):

    out = dict(_narrow_inputs_3(seed))
    wider = {'conv_norm_g': 4.07, 'gla_norm_g': 4.1, 'ln2_g': 3.28, 'ln2_b': 3.28}
    for name, times in wider.items():
        mean = out[name].mean()
        out[name] = (mean + times * (out[name] - mean)).astype(out[name].dtype)
    return out


def setup_inputs(seed=0):
    out = dict(first_inputs(seed))
    for name, value in second_inputs(seed + 1).items():
        if name != "x":
            out[name + "_2"] = value
    for name, value in third_inputs(seed + 2).items():
        if name != "x":
            out[name + "_3"] = value
    return out


def reference(
    x, mem, norm_g, mem_norm_g, w_in, gate_b, attn_q_norm_g, attn_k_norm_g, attn_sink, attn_w_o,
    rwkv_mu, rwkv_k_k, rwkv_k_a, rwkv_r_k, rwkv_w0, rwkv_w2, rwkv_a0, rwkv_a2, rwkv_ln_w,
    rwkv_ln_b, rwkv_w_o, x_w_kv, x_q_norm_g, x_k_norm_g, x_w_o, w_out, meta_tokens_2, norm1_g_2,
    w_in_2, pool_w_2, pool_scale_2, conv_w_2, conv_b_2, gate_a_w_2, gate_a_b_2, gate_x_w_2,
    gate_x_b_2, lru_lambda_2, w_out_2, norm2_g_2, mlp_w1_2, mlp_w2_2, final_g_2, w_in_3,
    conv_w_3, conv_norm_g_3, w_gate_up_3, gate_bias_3, gla_norm_g_3, w_out_3, ln1_g_3, ln1_b_3,
    w_ff_up_3, w_ff_down_3, ln2_g_3, ln2_b_3,
):
    x = first_block(
        x, mem, norm_g, mem_norm_g, w_in, gate_b, attn_q_norm_g, attn_k_norm_g, attn_sink,
        attn_w_o, rwkv_mu, rwkv_k_k, rwkv_k_a, rwkv_r_k, rwkv_w0, rwkv_w2, rwkv_a0, rwkv_a2,
        rwkv_ln_w, rwkv_ln_b, rwkv_w_o, x_w_kv, x_q_norm_g, x_k_norm_g, x_w_o, w_out,
    )
    x = second_block(
        x, meta_tokens_2, norm1_g_2, w_in_2, pool_w_2, pool_scale_2, conv_w_2, conv_b_2,
        gate_a_w_2, gate_a_b_2, gate_x_w_2, gate_x_b_2, lru_lambda_2, w_out_2, norm2_g_2,
        mlp_w1_2, mlp_w2_2, final_g_2,
    )
    return third_block(
        x, w_in_3, conv_w_3, conv_norm_g_3, w_gate_up_3, gate_bias_3, gla_norm_g_3, w_out_3,
        ln1_g_3, ln1_b_3, w_ff_up_3, w_ff_down_3, ln2_g_3, ln2_b_3,
    )


_drawn_inputs = setup_inputs


def setup_inputs(seed=0):
    import zlib

    import numpy as np

    out = dict(_drawn_inputs(seed))
    spreads = {}
    factors = {'meta_tokens_2': 8.0,
     'norm1_g_2': 8.0,
     'w_in_2': 3.139,
     'pool_w_2': 3.396,
     'pool_scale_2': 8.0,
     'conv_w_2': 64.0,
     'conv_b_2': 64.0,
     'gate_a_w_2': 64.0,
     'gate_a_b_2': 64.0,
     'gate_x_w_2': 64.0,
     'gate_x_b_2': 64.0,
     'lru_lambda_2': 64.0,
     'w_out_2': 3.13,
     'norm2_g_2': 64.0,
     'ln1_b_3': 2.698}
    for name, (base, spread) in spreads.items():
        noise = np.random.default_rng([zlib.crc32(name.encode()), seed]).standard_normal(out[name].shape)
        drawn = base * np.exp(spread * noise) if base else spread * noise
        out[name] = __import__('jax').numpy.asarray(drawn.astype(out[name].dtype))
    for name, factor in factors.items():
        out[name] = (out[name] * factor).astype(out[name].dtype)
    return out
```

```python
import numpy as np
import concourse.bass as bass
from concourse import mybir
from contextlib import ExitStack

P = 128
D = 2048
KT = D // P
T = 256
META = 16
TM = META + T
NB = T // P
HALF = KT // 2
UNIT = HALF * P
RING = 4

A_HEADS, A_KV, HD = 12, 4, 64
A_T = A_HEADS * HD // P
KV_T = A_KV * HD // P
R_HEADS = 12
PAIRS = R_HEADS * HD // P
CH = 64
NCH = T // CH
LEVELS = 6
X_HEADS = 4
X_T = X_HEADS
N_BRANCH = 3
WINDOW = 128
POOL_WINDOWS = (2, 4, 8, 16)
POOL_T = D // P // len(POOL_WINDOWS)
CONV2 = 4
LRU_HEADS = 8
FF_GROUPS = 4
CONV3 = 3
C3_T = 8
GLA_H = 4
GLA_VT = 8
HALF_DECAY = 0.5 * float(np.exp(-0.5))
ALPHA3 = 2.0 ** 0.25
EPS = 1e-6
GN_EPS = 64e-5
LN_EPS = 1e-5
GATE_TAU = 16.0
NEG = -1e30

Q_PAIRS = [(0, 3), (1, 4), (2, 5), (6, 9), (7, 10), (8, 11)]

STREAM = [("mem_kv", 8), ("shift", 20), ("silu", 16), ("plain", 14), ("merge1", 64), ("wout1", 16),
          ("gpool", 16), ("gelu", 16), ("pool", 20), ("lru", 20), ("glru", 16), ("wout2", 16),
          ("ff2", 128), ("conv3", 24), ("gla_r", 8), ("gla_p", 17), ("wout3", 16), ("ff3", 128)]
FIRST = {}
N_TILES = 0
for _name, _n in STREAM:
    FIRST[_name] = N_TILES
    N_TILES += _n
COUNT = dict(STREAM)
N_UNITS = 2 * N_TILES

PARAMS = [("mem_norm_g", 16), ("norm_g", 16), ("mu", 20), ("k_k", 6), ("k_a", 6), ("r_k", 6),
          ("w0", 12), ("a0", 12), ("ln_w", 6), ("ln_b", 6), ("gate_b", 48), ("q_g", 1), ("k_g", 1),
          ("xq_g", 1), ("xk_g", 1), ("sink", 24), ("norm1_g", 16), ("pool_scale", 16),
          ("conv_w2", 64), ("conv_b2", 16), ("gate_a_b", 16), ("gate_x_b", 16), ("lam", 16),
          ("norm2_g", 16), ("final_g", 16), ("conv_w3", 24), ("conv_g3", 8), ("gate_bias3", 4),
          ("gla_g3", 8), ("ln1_g", 16), ("ln1_b", 16), ("ln2_g", 16), ("ln2_b", 16)]
PCOL = {}
N_PARAM = 0
for _name, _n in PARAMS:
    PCOL[_name] = N_PARAM
    N_PARAM += _n

CONSTS = [("ident", 128), ("ones", 128), ("bdones", 128), ("rot", 128), ("istack", 64),
          ("cos", 256), ("sin", 256), ("amask", 512), ("strict_up", 128), ("strict_lo", 128),
          ("incl_up", 128), ("incl_lo", 128), ("levels", 768), ("run_up", 256), ("run_lo", 256)]
CCOL = {}
N_CONST = 0
for _name, _n in CONSTS:
    CCOL[_name] = N_CONST
    N_CONST += _n


def constants():
    f = np.float32
    i = np.arange(P)
    head, s = i // CH, i % CH
    same = head[:, None] == head[None, :]
    rot = np.zeros((P, P), f)
    for m in range(P):
        j = m % HD
        if j < HD // 2:
            rot[m + HD // 2, m] = -1.0
        else:
            rot[m - HD // 2, m] = 1.0
    half = HD // 2
    inv = np.float32(10000.0) ** (-np.arange(half, dtype=f) / np.float32(half))
    ang = np.arange(T, dtype=f)[None, :] * inv.astype(f)[:, None]
    cos, sin = (np.tile(fn(ang).astype(f), (4, 1)) for fn in (np.cos, np.sin))
    key = np.arange(T)
    amask = np.stack([np.where(np.abs(key[None, :] - (i[:, None] + b * P)) <= WINDOW, 0.0, NEG)
                      for b in range(NB)], 1)
    up = same & (s[:, None] < s[None, :])
    incl = same & (s[:, None] <= s[None, :])
    levels = [same & (s[:, None] >> (l + 1) == s[None, :] >> (l + 1))
              & (s[:, None] >> l != s[None, :] >> l) for l in range(LEVELS)]
    t = np.arange(T)
    table = {
        "ident": np.eye(P), "ones": np.ones((P, P)), "bdones": same, "rot": rot,
        "istack": (s[:, None] == np.arange(CH)[None, :]), "cos": cos, "sin": sin,
        "amask": amask.reshape(P, NB * T), "strict_up": up, "strict_lo": up.T, "incl_up": incl,
        "incl_lo": incl.T, "levels": np.concatenate(levels, 1),
        "run_up": np.tile(t % CH != 0, (P, 1)), "run_lo": np.tile(t % CH != CH - 1, (P, 1)),
    }
    return np.ascontiguousarray(np.concatenate([table[n].astype(f) for n, _ in CONSTS], 1))


class Steps:

    def __init__(self, sem, names):
        self.sem, self.names = sem, list(names)
        self.place = {n: k for k, n in enumerate(self.names)}
        assert len(self.place) == len(self.names), "a step's name stands twice"
        self.cursor = 0

    def at(self, name, it=None):
        n = self.place[name] + 1
        return n if it is None else it * len(self.names) + n

    def done(self, ins, name):
        assert self.names[self.cursor % len(self.names)] == name, (name, self.names[self.cursor % len(self.names)])
        self.cursor += 1
        ins.then_inc(self.sem, 1)


def need(eng, steps, name, it=None):
    eng.wait_ge(steps.sem, steps.at(name, it))


class Tile:

    def __init__(self, first, t, loops=()):
        self.first, self.t, self.loops = first, t, tuple(loops)

    def sum(self, c, m):
        for reg, per in self.loops:
            c = reg * (per * m) + c
        return c

    def units(self, c):
        return self.sum(2 * (self.first + self.t) + c, 2)

    def local(self, m=1, c=0):
        return self.sum(m * self.t + c, m)

    def next(self):
        return Tile(self.first, self.t + 1, self.loops)

    @property
    def parity(self):
        return (self.first + self.t) % 2

    @property
    def start(self):
        return not self.loops and self.first + self.t < 2


def ruN_TILES(eng, phase, per, body, loops=(), first=None, count=None, peel=True):
    first = FIRST[phase] if first is None else first
    count = COUNT[phase] if count is None else count
    rounds = count // per
    if peel:
        for j in range(per):
            body(Tile(first, j, loops))
    with eng.Fori(1 if peel else 0, rounds) as i:
        for j in range(per):
            body(Tile(first, j, tuple(loops) + ((i, per),)))
    for t in range(rounds * per, count):
        body(Tile(first, t, loops))


def build(nc, stream, consts, params, w2, a2, wgu, memT, xT, metaT, out):
    F, R = mybir.dt.float32, mybir.dt.float32r
    ACT, ALU = mybir.ActivationFunctionType, mybir.AluOpType
    AX = mybir.AxisListType
    ctx = ExitStack()
    with ctx:
        def sem(name):
            return ctx.enter_context(nc.semaphore(name))

        K = 1024
        base = -(-nc.sbuf_base // 64) * 64
        slab = 206 * K
        ctx.enter_context(nc.sbuf_tensor("slab", [P, slab // 4], F, align_bytes=64))

        def at(name, offset, shape, dtype=F):
            size = 4 * int(np.prod(shape[1:]))
            assert offset + size <= slab, (name, offset + size - slab)
            return nc.alloc_sbuf_tensor_at(name, list(shape), dtype, offset=base + offset)

        raw = at("raw", 0, [P, RING, HALF, P])
        w_hi = at("w_hi", 16 * K, [P, RING, HALF, P], R)
        w_lo = at("w_lo", 32 * K, [P, RING, HALF, P], R)
        cst = at("cst", 48 * K, [P, N_CONST])
        par = at("par", 62 * K, [P, N_PARAM])
        w2_sb = at("w2_sb", 64 * K, [P, PAIRS, P])
        a2_sb = at("a2_sb", 67 * K, [P, PAIRS, P])
        wgu_sb = at("wgu_sb", 70 * K, [16, GLA_H, P])
        lam_sb = at("lam_sb", 72 * K, [P, 6, 16])
        hw_sb = at("hw_sb", 72 * K + 384, [P, 24])
        B = 72 * K + 512
        banks = [ctx.enter_context(nc.psum_tensor(f"bank{b}", [P, 512], F)) for b in range(8)]

        def const(name):
            return cst[:, CCOL[name]:CCOL[name] + dict(CONSTS)[name]]

        def col(name, k):
            return par[:, PCOL[name]:PCOL[name] + dict(PARAMS)[name]][:, bass.ds(k, 1)]

        raw_in = [sem(f"raw_in{k}") for k in range(RING)]
        hi_ready, lo_ready, units_used = sem("hi_ready"), sem("lo_ready"), sem("units_used")

        def split_hi(act, tile):
            if not tile.loops and tile.first + tile.t >= N_TILES:
                return
            for k in range(2):
                slot = (2 * tile.parity + k) % RING
                g = tile.first + tile.t
                act.wait_ge(raw_in[slot], tile.sum(16 * (g // 2 + 1), 8))
                if not tile.start:
                    act.wait_ge(units_used, tile.units(k + 1 - RING))
                nc.scalar.activation(w_hi[:, slot], raw[:, slot], ACT.Copy).then_inc(hi_ready, 1)

        def split_lo(v, tile):
            if not tile.loops and tile.first + tile.t >= N_TILES:
                return
            for k in range(2):
                slot = (2 * tile.parity + k) % RING
                v.wait_ge(hi_ready, tile.units(k + 1))
                nc.vector.tensor_tensor(w_lo[:, slot], raw[:, slot], w_hi[:, slot].bitcast(F),
                                        ALU.subtract).then_inc(lo_ready, 1)

        def tile_done(eng, tile):
            eng.wait_ge(units_used, tile.units(2))

        def product(dst, moving, slot, j, kt, first, last, n=T):
            hi, lo = moving[:, kt, 0, TM - n:] if moving.shape[-1] == TM else moving[:, kt, 0], \
                moving[:, kt, 1, TM - n:] if moving.shape[-1] == TM else moving[:, kt, 1]
            nc.tensor.matmul(dst, w_hi[:, slot, j], hi, start=first, stop=False)
            nc.tensor.matmul(dst, w_hi[:, slot, j], lo, start=False, stop=False)
            return nc.tensor.matmul(dst, w_lo[:, slot, j], hi, start=False, stop=last)

        def full_tile(pe, tile, moving, n=T, before=None):
            dst = banks[tile.parity][:, 0:n]
            for k in range(2):
                if before is not None:
                    before(k)
                pe.wait_ge(lo_ready, tile.units(k + 1))
                for j in range(HALF):
                    kt = HALF * k + j
                    last = product(dst, moving, (2 * tile.parity + k) % RING, j, kt,
                                   kt == 0, kt == KT - 1, n)
                last.then_inc(units_used, 1)

        def plain_phase(pe, phase, moving, bank_free, n=T, before=None, entry=None):
            def body(tile):
                if tile.loops or tile.t >= 2:
                    pe.wait_ge(bank_free, tile.local(1, -1))
                elif entry is not None:
                    entry(tile.t)
                first = not tile.loops and tile.t == 0
                full_tile(pe, tile, moving, n, before if first else None)
            ruN_TILES(pe, phase, 2, body)

        in_cst, in_par, in_lora, in_mem, in_x, in_x2, in_meta, stored = (
            sem(n) for n in ("in_cst", "in_par", "in_lora", "in_mem", "in_x", "in_x2", "in_meta", "stored"))

        class Norm:
            def __init__(self, name, src, n, g, dst, scratch, keep=None):
                self.src, self.n, self.g, self.dst, self.keep = src, n, g, dst, keep
                self.sq = at(name + "_sq", scratch, [P, 2, 4, n])
                self.xn = at(name + "_xn", scratch + 32 * n, [P, 2, 4, n])
                self.std = at(name + "_std", scratch + 64 * n, [P, n])
                self.rstd = at(name + "_rstd", scratch + 68 * n, [P, n])
                self.a = Steps(sem(name + "_act"), ["sq0", "sq1", "sq2", "sq3", "std"] + [f"hi{q}" for q in range(4)])
                self.v = Steps(sem(name + "_dve"), ["rstd"] + [s for q in range(4) for s in (f"xn{q}", f"lo{q}")])
                self.p = Steps(sem(name + "_pe"), [f"stat{q}" for q in range(4)])

            def act(self, act):
                for q in range(4):
                    if q >= 2:
                        need(act, self.p, f"stat{q - 2}")
                    self.a.done(nc.scalar.activation(self.sq[:, q % 2], self.src[:, 4 * q:4 * q + 4], ACT.Square), f"sq{q}")
                need(act, self.p, "stat3")
                self.a.done(nc.scalar.activation(self.std[:], banks[2][:, 0:self.n], ACT.Sqrt,
                                                 bias=EPS, scale=1.0 / D), "std")
                for q in range(4):
                    need(act, self.v, f"xn{q}")
                    self.a.done(nc.scalar.activation(self.dst[:, 4 * q:4 * q + 4, 0], self.out(q), ACT.Copy), f"hi{q}")

            def out(self, q):
                return self.xn[:, q % 2] if self.keep is None else self.keep[:, 4 * q:4 * q + 4]

            def pe(self, pe):
                for q in range(4):
                    need(pe, self.a, f"sq{q}")
                    for j in range(4):
                        last = nc.tensor.matmul(banks[2][:, 0:self.n], const("ones"), self.sq[:, q % 2, j],
                                                start=q + j == 0, stop=q + j == 6)
                    self.p.done(last, f"stat{q}")

            def dve(self, v):
                need(v, self.a, "std")
                self.v.done(nc.vector.reciprocal(self.rstd[:], self.std[:]), "rstd")
                need(v, self.v, "rstd")
                for q in range(4):
                    if q >= 2 and self.keep is None:
                        need(v, self.v, f"lo{q - 2}")
                        need(v, self.a, f"hi{q - 2}")
                    for j in range(4):
                        kt = 4 * q + j
                        last = nc.vector.scalar_tensor_tensor(
                            self.out(q)[:, j], self.src[:, kt], col(self.g, kt), self.rstd[:], ALU.mult, ALU.mult)
                    self.v.done(last, f"xn{q}")
                    need(v, self.a, f"hi{q}")
                    self.v.done(nc.vector.tensor_tensor(self.dst[:, 4 * q:4 * q + 4, 1], self.out(q),
                                                        self.dst[:, 4 * q:4 * q + 4, 0].bitcast(F), ALU.subtract), f"lo{q}")

            def ready(self, pe, k):
                need(pe, self.v, f"lo{2 * k + 1}")

        hx = at("hx", B, [P, KT, 2, T], R)
        sg = at("sg", B + 32 * K, [P, KT, T])
        pl = at("pl", B + 48 * K, [P, 14, T])
        rkv = at("rkv", B + 62 * K, [P, 20, T])
        mkv = at("mkv", B + 82 * K, [P, 8, T])
        Z = B + 90 * K
        mem_raw = at("mem_raw", B + 32 * K, [P, KT, T])
        mem_hl = at("mem_hl", B + 48 * K, [P, KT, 2, T], R)
        x_raw = at("x_raw", Z, [P, KT, T])
        mem_norm = Norm("mem_norm", mem_raw, T, "mem_norm_g", mem_hl, Z + 16 * K)
        x_norm = Norm("x_norm", x_raw, T, "norm_g", hx, Z + 16 * K)

        mem_out, plain_out, silu_out = sem("mem_out"), sem("plain_out"), sem("silu_out")

        def act_copy_phase(act, phase, dst, func, out_sem):
            def body(tile):
                split_hi(act, tile.next())
                tile_done(act, tile)
                nc.scalar.activation(dst[:, tile.local()], banks[tile.parity][:, 0:T], func).then_inc(out_sem, 1)
            ruN_TILES(act, phase, 2, body)

        def dve_split_phase(v, phase):
            ruN_TILES(v, phase, 2, lambda tile: split_lo(v, tile.next()), peel=False)

        pad = [at(f"pad{b}", Z + b * 1088, [P, T + 2]) for b in range(2)]
        sh = [at(f"sh{b}", Z + 2176 + b * 1024, [P, T]) for b in range(2)]
        pads_zero, shift_copied, shift_step = sem("pads_zero"), sem("shift_copied"), sem("shift_step")

        def act_shift(act):
            def body(tile):
                split_hi(act, tile.next())
                tile_done(act, tile)
                if tile.loops or tile.t >= 2:
                    act.wait_ge(shift_step, tile.local(3, -3))
                else:
                    act.wait_ge(pads_zero, 2)
                nc.scalar.activation(pad[tile.t % 2][:, 1:T + 1], banks[tile.parity][:, 0:T],
                                     ACT.Copy).then_inc(shift_copied, 1)
            ruN_TILES(act, "shift", 2, body)

        def dve_shift(v):
            for b in range(2):
                nc.vector.memset(pad[b][:], 0.0).then_inc(pads_zero, 1)

            def body(tile):
                split_lo(v, tile.next())
                p, s = pad[tile.t % 2], sh[tile.t % 2]
                v.wait_ge(shift_copied, tile.local(1, 1))
                nc.vector.tensor_tensor(s[:], p[:, 0:T], p[:, 2:T + 2], ALU.add).then_inc(shift_step, 1)
                v.wait_ge(shift_step, tile.local(3, 1))
                nc.vector.scalar_tensor_tensor(s[:], s[:], 0.5, p[:, 1:T + 1], ALU.mult,
                                               ALU.subtract).then_inc(shift_step, 1)
                v.wait_ge(shift_step, tile.local(3, 2))
                nc.vector.scalar_tensor_tensor(rkv[:, tile.local()], s[:], col("mu", tile.local()), p[:, 1:T + 1],
                                               ALU.mult, ALU.add).then_inc(shift_step, 1)
            ruN_TILES(v, "shift", 2, body)

        sq_at = at("sq_at", Z, [P, 16, T])
        rs_at = at("rs_at", Z + 16 * K, [P, 16, T])
        tmp_at = at("tmp_at", Z, [P, 8, T])
        vtok = at("vtok", Z + 32 * K, [P, NB, KV_T * P])
        vmtok = at("vmtok", Z + 34 * K, [P, NB, X_T * P])
        U_ALL = range(A_T + X_T)
        sc = [at(f"sc{b}", Z + 4 * K * b, [P, 4, T]) for b in range(2)]
        pr = [at(f"pr{b}", Z + 8 * K + 4 * K * b, [P, 4, T]) for b in range(2)]
        pt = [at(f"pt{b}", Z + 16 * K + 4 * K * b, [P, 4, T]) for b in range(2)]
        mx = at("mx", Z + 24 * K, [P, 10, 4])
        ngm = at("ngm", Z + 24 * K + 160, [P, 10, 4])
        sm = at("sm", Z + 24 * K + 320, [P, 10, 4])
        es = at("es", Z + 24 * K + 480, [P, 10, 4])
        rd = at("rd", Z + 24 * K + 640, [P, 10, 4])
        at_src = [(pl, k) for k in range(12)] + [(mkv, k) for k in range(4)]
        at_g = ["q_g"] * 6 + ["k_g"] * 2 + ["xq_g"] * 4 + ["xk_g"] * 4
        ua = [f"{s}{u}" for u in U_ALL for s in ("ex", "sk", "pt")]
        at_a = Steps(sem("attn_act"), ["sq0", "sq1", "sq2"] + [f"std{b}" for b in range(8)] + ["vt", "vm0", "vm1"]
                     + [n for n in ua if not (n.startswith("sk") and int(n[2:]) >= A_T)])

        def attn_dve_names():
            names = [f"rstd{b}" for b in range(8)] + ["norm"]
            names += [f"{s}{b}" for b in range(4) for s in ("sin", "cos", "rope")]
            def soft(u):
                return [f"{s}{u}" for s in (("mask", "max", "msk", "neg", "dsk") if u < A_T else ("max", "neg"))]
            names += soft(0)
            for u in U_ALL:
                names += soft(u + 1) if u + 1 < len(U_ALL) else []
                names += ([f"den{u}"] if u < A_T else []) + [f"rd{u}", f"pr{u}", f"y{u}"]
            return names
        at_v = Steps(sem("attn_dve"), attn_dve_names())
        at_p = Steps(sem("attn_pe"), [f"stat{b}" for b in range(8)] + ["vt", "vm0", "vm1"] + [f"rot{b}" for b in range(4)]
                     + ["sc0"] + [n for u in U_ALL for n in (f"sc{u + 1}", f"tr{u}", f"pv{u}") if n != f"sc{len(U_ALL)}"])

        def heads(u):
            return [(HD * h, HD, b) for h in range(2) for b in range(NB)] if u < A_T else [(0, P, b) for b in range(NB)]

        def sc_bank(u, h):
            return banks[h] if u < A_T else banks[u % 2]

        def pt_bank(u, h):
            return banks[2 + h] if u < A_T else banks[2 + u % 2]

        def pv_bank(u):
            return banks[4 + u % 2]

        def act_attn(act):
            need_sem = plain_out
            act.wait_ge(need_sem, COUNT["plain"])
            act.wait_ge(mem_out, COUNT["mem_kv"])
            at_a.done(nc.scalar.activation(sq_at[:, 0:8], pl[:, 0:8], ACT.Square), "sq0")
            at_a.done(nc.scalar.activation(sq_at[:, 8:12], pl[:, 8:12], ACT.Square), "sq1")
            at_a.done(nc.scalar.activation(sq_at[:, 12:16], mkv[:, 0:4], ACT.Square), "sq2")
            for b in range(8):
                need(act, at_p, f"stat{b}")
                dim = HD if b < 4 else P
                at_a.done(nc.scalar.activation(rs_at[:, 2 * b:2 * b + 2], banks[b][:].rearrange("p (a t) -> p a t", a=2),
                                               ACT.Sqrt, bias=EPS, scale=1.0 / dim), f"std{b}")
            need(act, at_p, "vt")
            at_a.done(nc.scalar.activation(vtok[:], banks[4][:].rearrange("p (b c) -> p b c", b=NB), ACT.Copy), "vt")
            for b in range(NB):
                need(act, at_p, f"vm{b}")
                at_a.done(nc.scalar.activation(vmtok[:, b], banks[5 + b][:], ACT.Copy), f"vm{b}")
            for u in list(U_ALL) + [None]:
                if u is not None:
                    blocks = heads(u)
                    need(act, at_v, f"neg{u}")
                    if u >= 2:
                        need(act, at_p, f"tr{u - 2}")
                    for n in range(len(blocks)):
                        src = sc[u % 2][:, n] if u < A_T else sc_bank(u, 0)[:, T * n:T * n + T]
                        last = nc.scalar.activation(pr[u % 2][:, n], src, ACT.Exp, bias=ngm[:, u, n:n + 1],
                                                    scale=1.0 if u < A_T else P ** -0.5, accum_out=sm[:, u, n:n + 1])
                    at_a.done(last, f"ex{u}")
                    if u < A_T:
                        need(act, at_v, f"dsk{u}")
                        at_a.done(nc.scalar.activation(es[:, u], es[:, u], ACT.Exp), f"sk{u}")
                    need(act, at_p, f"tr{u}")
                    for h in range(2 if u < A_T else 1):
                        last = nc.scalar.activation(pt[u % 2][:, 2 * h:2 * h + 2],
                                                    pt_bank(u, h)[:].rearrange("p (b q) -> p b q", b=NB), ACT.Copy)
                    at_a.done(last, f"pt{u}")

        def pe_attn(pe):
            for b in range(8):
                need(pe, at_a, "sq0" if b < 4 else "sq1" if b < 6 else "sq2")
                at_p.done(nc.tensor.matmul(banks[b][:], const("bdones" if b < 4 else "ones"), sq_at[:, 2 * b:2 * b + 2],
                                           start=True, stop=True), f"stat{b}")
            need(pe, at_a, "std4")
            for b in range(NB):
                for c in range(KV_T):
                    o = (b * KV_T + c) * P
                    last = nc.tensor.transpose(banks[4][:, o:o + P], pl[:, 12 + c, b * P:b * P + P], const("ident"))
            at_p.done(last, "vt")
            for b in range(NB):
                need(pe, at_a, f"std{5 + b}")
                for c in range(X_T):
                    last = nc.tensor.transpose(banks[5 + b][:, c * P:c * P + P], mkv[:, 4 + c, b * P:b * P + P], const("ident"))
                at_p.done(last, f"vm{b}")
            need(pe, at_v, "norm")
            for b in range(4):
                at_p.done(nc.tensor.matmul(banks[b][:], const("rot"), pl[:, 2 * b:2 * b + 2], start=True, stop=True), f"rot{b}")
            need(pe, at_v, "rope3")

            def scores(u):
                if u >= 2:
                    w = u - 1 if u < A_T or u == A_T else u - 2
                    if w < A_T:
                        need(pe, at_v, f"mask{w}")
                    else:
                        need(pe, at_a, f"ex{w}")
                elif u == 1:
                    need(pe, at_v, "mask0")
                for r, n, b in heads(u):
                    q = pl[r:r + n, u if u < A_T else 8 + u - A_T, b * P:b * P + P]
                    k = pl[r:r + n, A_T + u // 3, :] if u < A_T else mkv[:, u - A_T, :]
                    last = nc.tensor.matmul(sc_bank(u, r // HD)[:, b * T:b * T + T], q, k, start=True, stop=True)
                at_p.done(last, f"sc{u}")

            def values(u):
                need(pe, at_v, f"pr{u}")
                if u >= 1:
                    need(pe, at_a, f"pt{u - 1}")
                for n, (r, _, b) in enumerate(heads(u)):
                    for kb in range(NB):
                        o = kb * T + b * P
                        last = nc.tensor.transpose(pt_bank(u, r // HD)[:, o:o + P], pr[u % 2][:, n, kb * P:kb * P + P], const("ident"))
                at_p.done(last, f"tr{u}")
                need(pe, at_a, f"pt{u}")
                if u >= 2:
                    need(pe, at_v, f"y{u - 2}")
                for h in range(2 if u < A_T else 1):
                    rows = HD if u < A_T else P
                    for kb in range(NB):
                        c = (2 * (u // 3) + h) * HD if u < A_T else (u - A_T) * P
                        v = (vtok if u < A_T else vmtok)[:, kb, c:c + rows]
                        last = nc.tensor.matmul(pv_bank(u)[h * HD:h * HD + rows, 0:T], v, pt[u % 2][:, 2 * h + kb],
                                                start=kb == 0, stop=kb == NB - 1)
                at_p.done(last, f"pv{u}")

            scores(0)
            for u in U_ALL:
                if u + 1 < len(U_ALL):
                    scores(u + 1)
                values(u)

        def dve_attn(v):
            for b in range(8):
                need(v, at_a, f"std{b}")
                at_v.done(nc.vector.reciprocal(rs_at[:, 2 * b:2 * b + 2], rs_at[:, 2 * b:2 * b + 2]), f"rstd{b}")
            need(v, at_v, "rstd7")
            for k, ((buf, c), g) in enumerate(zip(at_src, at_g)):
                last = nc.vector.scalar_tensor_tensor(buf[:, c], buf[:, c], col(g, 0), rs_at[:, k], ALU.mult, ALU.mult)
            at_v.done(last, "norm")
            need(v, at_v, "norm")
            for b in range(4):
                need(v, at_p, f"rot{b}")
                cos, sin = (const(n).unsqueeze(1).broadcast_to([P, 2, T]) for n in ("cos", "sin"))
                two = pl[:, 2 * b:2 * b + 2]
                t2 = tmp_at[:, 2 * b:2 * b + 2]
                at_v.done(nc.vector.tensor_tensor(t2, banks[b][:].rearrange("p (a t) -> p a t", a=2), sin, ALU.mult), f"sin{b}")
                at_v.done(nc.vector.tensor_tensor(two, two, cos, ALU.mult), f"cos{b}")
                need(v, at_v, f"cos{b}")
                at_v.done(nc.vector.tensor_tensor(two, two, t2, ALU.add), f"rope{b}")

            def soft(u):
                nb = len(heads(u))
                if u < A_T:
                    need(v, at_p, f"sc{u}")
                    if u >= 2:
                        need(v, at_a, f"ex{u - 2}")
                    mask = const("amask").rearrange("p (b k) -> p b k", b=NB)
                    for h in range(2):
                        last = nc.vector.scalar_tensor_tensor(
                            sc[u % 2][:, 2 * h:2 * h + 2], sc_bank(u, h)[:].rearrange("p (b k) -> p b k", b=NB),
                            HD ** -0.5, mask, ALU.mult, ALU.add)
                    at_v.done(last, f"mask{u}")
                    need(v, at_v, f"mask{u}")
                    at_v.done(nc.vector.tensor_reduce(mx[:, u], sc[u % 2][:], AX.X, ALU.max), f"max{u}")
                    need(v, at_v, f"max{u}")
                    sink = par[:, PCOL["sink"] + 4 * u:PCOL["sink"] + 4 * u + 4]
                    at_v.done(nc.vector.tensor_tensor(mx[:, u], mx[:, u], sink, ALU.max), f"msk{u}")
                    need(v, at_v, f"msk{u}")
                    at_v.done(nc.vector.tensor_scalar(ngm[:, u], mx[:, u], -1.0, None, ALU.mult), f"neg{u}")
                    need(v, at_v, f"neg{u}")
                    at_v.done(nc.vector.tensor_tensor(es[:, u], sink, ngm[:, u], ALU.add), f"dsk{u}")
                else:
                    need(v, at_p, f"sc{u}")
                    at_v.done(nc.vector.tensor_reduce(mx[:, u, 0:2], sc_bank(u, 0)[:].rearrange("p (b k) -> p b k", b=NB),
                                                      AX.X, ALU.max), f"max{u}")
                    need(v, at_v, f"max{u}")
                    at_v.done(nc.vector.tensor_scalar(ngm[:, u, 0:2], mx[:, u, 0:2], -(P ** -0.5), None, ALU.mult), f"neg{u}")

            def scale(u):
                nb = len(heads(u))
                if u < A_T:
                    need(v, at_a, f"sk{u}")
                    at_v.done(nc.vector.tensor_tensor(sm[:, u], sm[:, u], es[:, u], ALU.add), f"den{u}")
                    need(v, at_v, f"den{u}")
                else:
                    need(v, at_a, f"ex{u}")
                at_v.done(nc.vector.reciprocal(rd[:, u, 0:nb], sm[:, u, 0:nb]), f"rd{u}")
                need(v, at_v, f"rd{u}")
                for n in range(nb):
                    last = nc.vector.tensor_scalar(pr[u % 2][:, n], pr[u % 2][:, n], rd[:, u, n:n + 1], None, ALU.mult)
                at_v.done(last, f"pr{u}")
                need(v, at_p, f"pv{u}")
                m = u if u < A_T else 12 + u - A_T
                at_v.done(nc.vector.tensor_tensor(sg[:, m], pv_bank(u)[:, 0:T], sg[:, m], ALU.mult), f"y{u}")

            soft(0)
            for u in U_ALL:
                if u + 1 < len(U_ALL):
                    soft(u + 1)
                scale(u)

        kkn = at("kkn", B + 48 * K, [P, PAIRS, T])
        yall = kkn[:].rearrange("p a (c i) -> p a c i", c=NCH)
        v_bd = at("v_bd", B + 54 * K, [P, NCH, P])
        v_tok = at("v_tok", B + 56 * K, [P, NCH, CH])
        w2t = at("w2t", B + 57 * K, [P, P])
        a2t = at("a2t", B + 57 * K + 512, [P, P])
        small = B + 58 * K
        ws = [at(f"ws{d}", small + 256 * d, [P, CH]) for d in range(2)]
        sas = [at(f"sas{d}", small + 512 + 256 * d, [P, CH]) for d in range(2)]
        st = [at(f"st{d}", small + 1024 + 256 * d, [P, CH]) for d in range(2)]
        sts = [at(f"sts{d}", small + 1536 + 256 * d, [P, CH]) for d in range(2)]
        e_end = [at(f"e_end{d}", small + 2048 + 32 * d, [P, NCH]) for d in range(2)]
        ks = at("ks", B + 61 * K, [P, T])
        dirs = []
        for d in range(2):
            o = B + 82 * K + 24 * K * d
            w = {}
            for k, n in enumerate(("abd", "rbd", "bbd", "kbd", "mt", "kat", "tm", "brt", "krt", "ml", "btok", "ktok")):
                w[n] = at(f"{n}{d}", o + 2 * K * k, [P, NCH, P])
            w["u"], w["x"] = w["kbd"], w["bbd"]
            for k, n in enumerate(("s", "sx", "ad", "bb", "kd", "e1", "e2", "e3", "th")):
                w[n] = at(f"{n}_{d}", o + 8 * K + K * k, [P, T])
            dirs.append(w)
        sq_kk = at("sq_kk", B + 82 * K, [P, PAIRS, T])
        nrm_kk = at("nrm_kk", B + 90 * K, [P, PAIRS, T])
        kk_a = Steps(sem("kk_act"), ["sq", "nrm0", "nrm1", "nrm2", "tanh"])
        kk_v = Steps(sem("kk_dve"), ["raw", "half", "max", "inv", "kk"])
        kk_p = Steps(sem("kk_pe"), ["stat0", "stat1", "stat2"])
        zeroed = sem("rwkv_zeroed")

        def act_kk(act):
            need(act, kk_v, "raw")
            kk_a.done(nc.scalar.activation(sq_kk[:], kkn[:], ACT.Square), "sq")
            for b in range(3):
                need(act, kk_p, f"stat{b}")
                kk_a.done(nc.scalar.activation(nrm_kk[:, 2 * b:2 * b + 2], banks[b][:].rearrange("p (a t) -> p a t", a=2),
                                               ACT.Sqrt), f"nrm{b}")
            kk_a.done(nc.scalar.activation(rkv[:, 18], rkv[:, 18], ACT.Tanh), "tanh")

        def dve_kk(v):
            need(v, at_p, f"pv{A_T + X_T - 1}")
            for p in range(PAIRS):
                last = nc.vector.tensor_scalar(kkn[:, p], rkv[:, PAIRS + p], col("k_k", p), None, ALU.mult)
            kk_v.done(last, "raw")
            kk_v.done(nc.vector.tensor_scalar(hw_sb[:], par[:, PCOL["w0"]:PCOL["w0"] + 24], 0.5, None, ALU.mult), "half")
            need(v, kk_a, "nrm2")
            kk_v.done(nc.vector.tensor_scalar(nrm_kk[:], nrm_kk[:], 1e-12, None, ALU.max), "max")
            need(v, kk_v, "max")
            kk_v.done(nc.vector.reciprocal(nrm_kk[:], nrm_kk[:]), "inv")
            need(v, kk_v, "inv")
            kk_v.done(nc.vector.tensor_tensor(kkn[:], kkn[:], nrm_kk[:], ALU.mult), "kk")

        def pe_kk(pe):
            need(pe, kk_a, "sq")
            need(pe, at_v, f"y{A_T + X_T - 1}")
            for b in range(3):
                kk_p.done(nc.tensor.matmul(banks[b][:], const("bdones"), sq_kk[:, 2 * b:2 * b + 2], start=True, stop=True), f"stat{b}")

        def pool_kk(pool):
            pool.wait_ge(kk_v.sem, kk_v.at("kk"))
            nc.gpsimd.memset(v_bd[:], 0.0).then_inc(zeroed, 1)
            for d in range(2):
                for m in (dirs[d]["abd"], dirs[d]["rbd"], dirs[d]["bbd"], dirs[d]["kbd"]):
                    nc.gpsimd.memset(m[:], 0.0).then_inc(zeroed, 1)

        LV = range(1, LEVELS)
        ST = range(NCH)
        D2 = range(2)
        rw_o = Steps(sem("rwkv_pool"), ["w2t", "a2t", "vbd"] + [f"{n}{d}" for d in D2 for n in ("kbd", "rbd")]
                     + [f"{n}{d}" for d in D2 for n in ("t0_", "t1_", "ml1_", "u0_", "u1_")]
                     + [f"ml{l}_{d}" for l in LV if l > 1 for d in D2])
        rw_v = Steps(sem("rwkv_dve"), [f"{n}{d}" for d in D2 for n in ("u", "s", "sx", "ad", "bb", "t", "kd", "abd", "bbd", "end")]
                     + ["ks", "ksr", "q"] + [f"{n}{d}" for d in D2 for n in ("mt", "kat", "m", "brt")]
                     + [f"krt{d}" for d in D2]
                     + [f"{n}{l}_{d}" for l in LV for d in D2 for n in (("T", "U") if l < LEVELS - 1 else ("U",))]
                     + [f"{n}{s}_{d}" for s in ST for n in ("Y", "G", "S") for d in D2
                        if not (n == "S" and s == NCH - 1) and not (n == "G" and (s == 0 or s == NCH - 1))])
        rw_a = Steps(sem("rwkv_act"), [f"{n}{d}" for d in D2 for n in ("thw", "tha")]
                     + [f"{n}{d}" for d in D2 for n in ("e1", "e2", "e3")]
                     + [f"{n}{d}" for d in D2 for n in (("btok", "ktok", "vtok") if d == 0 else ("btok", "ktok"))]
                     + [f"X{l}_{d}" for l in LV for d in D2] + [f"{n}{s}_{d}" for s in ST for n in ("W", "SA") for d in D2])
        rw_p = Steps(sem("rwkv_pe"), [f"{n}{d}" for d in D2 for n in ("zw", "za")]
                     + [f"{n}{d}" for d in D2 for n in ("mt", "kat", "m", "brt")]
                     + [f"{n}{d}" for d in D2 for n in (("krt", "btok", "ktok", "vtok") if d == 0 else ("krt", "btok", "ktok"))]
                     + [s for l in LV for s in [f"X{l}_{d}" for d in D2]
                        + [f"{n}{l}_{d}" for d in D2 for n in (("U", "T") if l < LEVELS - 1 else ("U",))]]
                     + [f"{n}{s}_{d}" for s in ST for n in ("W", "SA", "S", "Y") for d in D2
                        if not (n == "S" and s == NCH - 1)])

        def chunks(ap):
            return ap.rearrange("p (c t) -> p c t", c=NCH)

        def four(ap):
            return ap.unsqueeze(1).broadcast_to([P, NCH, P])

        def blocks(bank):
            return banks[bank][:].rearrange("p (c t) -> p c t", c=NCH)

        def level(l):
            return four(const("levels")[:, P * l:P * l + P])

        def halves():
            return [slice(CH * h, CH * h + CH) for h in range(2)]

        def chunk_of(d, s):
            return s if d == 0 else NCH - 1 - s

        def pool_rwkv(pool):
            pool.wait_ge(zeroed, 9)
            pool.wait_ge(in_lora, 48)
            need(pool, kk_a, "tanh")
            with pool.Fori(0, PAIRS) as p:
                rw_o.done(nc.gpsimd.tensor_copy(w2t[:], w2_sb[:, p]), "w2t")
                rw_o.done(nc.gpsimd.tensor_copy(a2t[:], a2_sb[:, p]), "a2t")
                need(pool, rw_o, "a2t", p)
                for h in halves():
                    last = nc.gpsimd.tensor_copy(v_bd[h, :, h], rkv[h, 2 * PAIRS + p].rearrange("p (c t) -> p c t", c=NCH))
                rw_o.done(last, "vbd")
                for d, w in enumerate(dirs):
                    need(pool, rw_v, f"kd{d}", p)
                    need(pool, rw_a, f"e3{d}", p)
                    for h in halves():
                        last = nc.gpsimd.tensor_tensor(w["kbd"][h, :, h], chunks(w["kd"][h]), chunks(w["e3"][h]), ALU.mult)
                    rw_o.done(last, f"kbd{d}")
                    for h in halves():
                        last = nc.gpsimd.tensor_tensor(w["rbd"][h, :, h], rkv[h, p].rearrange("p (c t) -> p c t", c=NCH),
                                                       chunks(w["e1"][h]), ALU.mult)
                    rw_o.done(last, f"rbd{d}")
                ident = four(const("ident"))
                need(pool, rw_o, "rbd1", p)
                for d, w in enumerate(dirs):
                    need(pool, rw_v, f"m{d}", p)
                    rw_o.done(nc.gpsimd.tensor_tensor(w["tm"][:], w["tm"][:], level(0), ALU.mult), f"t0_{d}")
                    need(pool, rw_o, f"t0_{d}", p)
                    rw_o.done(nc.gpsimd.tensor_tensor(w["tm"][:], w["tm"][:], ident, ALU.add), f"t1_{d}")
                    rw_o.done(nc.gpsimd.tensor_tensor(w["ml"][:], w["mt"][:], level(1), ALU.mult), f"ml1_{d}")
                    need(pool, rw_p, f"ktok{d}", p)
                    rw_o.done(nc.gpsimd.tensor_tensor(w["u"][:], w["mt"][:], level(0), ALU.mult), f"u0_{d}")
                    need(pool, rw_o, f"u0_{d}", p)
                    rw_o.done(nc.gpsimd.tensor_tensor(w["u"][:], w["u"][:], ident, ALU.add), f"u1_{d}")
                for l in LV:
                    if l > 1:
                        for d, w in enumerate(dirs):
                            need(pool, rw_p, f"X{l - 1}_{d}", p)
                            rw_o.done(nc.gpsimd.tensor_tensor(w["ml"][:], w["mt"][:], level(l), ALU.mult), f"ml{l}_{d}")
                need(pool, rw_p, f"Y{NCH - 1}_1", p)

        def act_rwkv(act):
            with act.Fori(0, PAIRS) as p:
                for d, w in enumerate(dirs):
                    need(act, rw_p, f"zw{d}", p)
                    rw_a.done(nc.scalar.activation(w["th"][:], banks[4 * d][:, 0:T], ACT.Tanh, scale=0.5,
                                                   bias=hw_sb[:, bass.ds(p + PAIRS * d, 1)]), f"thw{d}")
                    need(act, rw_p, f"za{d}", p)
                    rw_a.done(nc.scalar.activation(w["ad"][:], banks[4 * d + 1][:, 0:T], ACT.Tanh, scale=0.5,
                                                   bias=hw_sb[:, bass.ds(p + (2 + d) * PAIRS, 1)]), f"tha{d}")
                for d, w in enumerate(dirs):
                    need(act, rw_v, f"sx{d}", p)
                    rw_a.done(nc.scalar.activation(w["e1"][:], w["s"][:], ACT.Exp, scale=-HALF_DECAY), f"e1{d}")
                    rw_a.done(nc.scalar.activation(w["e2"][:], w["sx"][:], ACT.Exp, scale=-HALF_DECAY), f"e2{d}")
                    rw_a.done(nc.scalar.activation(w["e3"][:], w["s"][:], ACT.Exp, scale=HALF_DECAY), f"e3{d}")
                for d, w in enumerate(dirs):
                    b = 4 * d
                    need(act, rw_p, f"btok{d}", p)
                    rw_a.done(nc.scalar.activation(w["btok"][:], blocks(b + 1), ACT.Copy), f"btok{d}")
                    need(act, rw_p, f"ktok{d}", p)
                    rw_a.done(nc.scalar.activation(w["ktok"][:], blocks(b + 3), ACT.Copy), f"ktok{d}")
                    if d == 0:
                        need(act, rw_p, "vtok0", p)
                        rw_a.done(nc.scalar.activation(v_tok[:], banks[2][:, 0:T].rearrange("p (c i) -> p c i", c=NCH),
                                                       ACT.Copy), "vtok0")
                for l in LV:
                    for d, w in enumerate(dirs):
                        need(act, rw_p, f"X{l}_{d}", p)
                        if l > 1:
                            need(act, rw_p, f"T{l - 1}_{d}", p)
                        rw_a.done(nc.scalar.activation(w["x"][:], blocks(4 * d + 1), ACT.Copy), f"X{l}_{d}")
                for s in ST:
                    for d in D2:
                        need(act, rw_p, f"W{s}_{d}", p)
                        rw_a.done(nc.scalar.activation(ws[d][:], banks[4 * d][:, 0:CH], ACT.Copy, scale=-1.0), f"W{s}_{d}")
                    for d in D2:
                        need(act, rw_p, f"SA{s}_{d}", p)
                        if s > 0:
                            need(act, rw_p, f"Y{s - 1}_{d}", p)
                        rw_a.done(nc.scalar.activation(sas[d][:], banks[4 * d + 1][:, 0:CH], ACT.Copy), f"SA{s}_{d}")
                need(act, rw_p, f"Y{NCH - 1}_1", p)
                need(act, rw_v, f"Y{NCH - 1}_1", p)

        def dve_rwkv(v):
            with v.Fori(0, PAIRS) as p:
                for d, w in enumerate(dirs):
                    run = const("run_up" if d == 0 else "run_lo")
                    turn = (lambda ap: ap) if d == 0 else (lambda ap: ap[:, ::-1])
                    need(v, rw_a, f"tha{d}", p)
                    rw_v.done(nc.vector.tensor_scalar(w["th"][:], w["th"][:], 1.0, None, ALU.add), f"u{d}")
                    need(v, rw_v, f"u{d}", p)
                    rw_v.done(nc.vector.tensor_tensor_scan(turn(w["s"][:]), turn(run), turn(w["th"][:]), 0.0, ALU.mult, ALU.add), f"s{d}")
                    need(v, rw_v, f"s{d}", p)
                    rw_v.done(nc.vector.tensor_tensor(w["sx"][:], w["s"][:], w["th"][:], ALU.subtract), f"sx{d}")
                    rw_v.done(nc.vector.tensor_scalar(w["ad"][:], w["ad"][:], 0.5, 0.5, ALU.mult, ALU.add), f"ad{d}")
                    need(v, rw_v, f"ad{d}", p)
                    rw_v.done(nc.vector.tensor_tensor(w["bb"][:], kkn[:, p], w["ad"][:], ALU.mult), f"bb{d}")
                    rw_v.done(nc.vector.tensor_scalar(w["kd"][:], w["ad"][:], 1.0, col("k_a", p), ALU.subtract, ALU.mult), f"t{d}")
                    need(v, rw_v, f"t{d}", p)
                    rw_v.done(nc.vector.scalar_tensor_tensor(w["kd"][:], w["kd"][:], 1.0, rkv[:, PAIRS + p], ALU.add, ALU.mult), f"kd{d}")
                    need(v, rw_a, f"e3{d}", p)
                    for h in halves():
                        last = nc.vector.tensor_tensor(w["abd"][h, :, h], kkn[h, p].rearrange("p (c t) -> p c t", c=NCH),
                                                       chunks(w["e2"][h]), ALU.mult)
                    rw_v.done(last, f"abd{d}")
                    for h in halves():
                        last = nc.vector.tensor_tensor(w["bbd"][h, :, h], chunks(w["bb"][h]), chunks(w["e3"][h]), ALU.mult)
                    rw_v.done(last, f"bbd{d}")
                    end = CH - 1 if d == 0 else 0
                    rw_v.done(nc.vector.tensor_copy(e_end[d][:], chunks(w["e1"][:])[:, :, end]), f"end{d}")
                need(v, rw_v, "end1", p)
                rw_v.done(nc.vector.tensor_tensor(ks[:], dirs[0]["kd"][:], dirs[1]["kd"][:], ALU.add), "ks")
                need(v, rw_v, "ks", p)
                rw_v.done(nc.vector.tensor_scalar(ks[:], ks[:], col("r_k", p), None, ALU.mult), "ksr")
                need(v, rw_v, "ksr", p)
                need(v, rw_o, "rbd1", p)
                rw_v.done(nc.vector.tensor_tensor(rkv[:, p], rkv[:, p], ks[:], ALU.mult), "q")
                for d, w in enumerate(dirs):
                    b = 4 * d
                    up, lo, incl = (const(n) for n in (("strict_up", "strict_lo", "incl_up") if d == 0 else
                                                       ("strict_lo", "strict_up", "incl_lo")))
                    for n, bank, dst, mask, sign in (("mt", b, w["mt"], up, -1.0), ("kat", b + 1, w["kat"], up, 1.0),
                                                     ("m", b + 2, w["tm"], lo, -1.0), ("brt", b + 3, w["brt"], incl, 1.0)):
                        need(v, rw_p, f"{n}{d}", p)
                        rw_v.done(nc.vector.scalar_tensor_tensor(dst[:], blocks(bank), sign, four(mask), ALU.mult, ALU.mult), f"{n}{d}")
                for d, w in enumerate(dirs):
                    need(v, rw_p, f"krt{d}", p)
                    incl = const("incl_up" if d == 0 else "incl_lo")
                    rw_v.done(nc.vector.tensor_tensor(w["krt"][:], blocks(4 * d), four(incl), ALU.mult), f"krt{d}")
                for l in LV:
                    for d, w in enumerate(dirs):
                        if l < LEVELS - 1:
                            need(v, rw_p, f"T{l}_{d}", p)
                            rw_v.done(nc.vector.tensor_tensor(w["tm"][:], w["tm"][:], blocks(4 * d + 3), ALU.add), f"T{l}_{d}")
                        else:
                            need(v, rw_p, f"U{l}_{d}", p)
                        rw_v.done(nc.vector.tensor_tensor(w["u"][:], w["u"][:], blocks(4 * d + 2), ALU.add), f"U{l}_{d}")
                for s in ST:
                    for d in D2:
                        c = chunk_of(d, s)
                        need(v, rw_p, f"Y{s}_{d}", p)
                        y = yall[:, p, c]
                        if s < NCH // 2:
                            last = nc.vector.tensor_scalar(y, banks[4 * d + 2][:, 0:CH], 1.0, None, ALU.mult)
                        else:
                            last = nc.vector.tensor_tensor(y, y, banks[4 * d + 2][:, 0:CH], ALU.add)
                        rw_v.done(last, f"Y{s}_{d}")
                    if s == NCH - 1:
                        continue
                    for d in D2:
                        if s > 0:
                            c = chunk_of(d, s)
                            rw_v.done(nc.vector.tensor_scalar(sts[d][:], st[d][:], e_end[d][:, c:c + 1], None, ALU.mult), f"G{s}_{d}")
                    for d in D2:
                        c = chunk_of(d, s)
                        new = banks[4 * d + 3][:, 0:CH]
                        if s == 0:
                            last = nc.vector.tensor_scalar(st[d][:], new, e_end[d][:, c:c + 1], None, ALU.mult)
                        else:
                            need(v, rw_v, f"G{s}_{d}", p)
                            last = nc.vector.scalar_tensor_tensor(st[d][:], new, e_end[d][:, c:c + 1], sts[d][:], ALU.mult, ALU.add)
                        rw_v.done(last, f"S{s}_{d}")

        def pe_rwkv(pe):
            need(pe, kk_a, "tanh")
            with pe.Fori(0, PAIRS) as p:
                for d in D2:
                    need(pe, rw_o, "a2t", p)
                    h = halves()[d]
                    rw_p.done(nc.tensor.matmul(banks[4 * d][:, 0:T], w2t[h], rkv[h, 18], start=True, stop=True), f"zw{d}")
                    rw_p.done(nc.tensor.matmul(banks[4 * d + 1][:, 0:T], a2t[h], rkv[h, 19], start=True, stop=True), f"za{d}")

                def each(bank, lhs, rhs, n=P):
                    for c in range(NCH):
                        last = nc.tensor.matmul(banks[bank][:, n * c:n * c + n], lhs[:, c], rhs[:, c], start=True, stop=True)
                    return last

                def turned(bank, src):
                    for c in range(NCH):
                        last = nc.tensor.transpose(banks[bank][:, P * c:P * c + P], src[:, c], const("ident"))
                    return last

                for d, w in enumerate(dirs):
                    b = 4 * d
                    need(pe, rw_v, f"end{d}", p)
                    need(pe, rw_o, f"rbd{d}", p)
                    rw_p.done(each(b, w["bbd"], w["abd"]), f"mt{d}")
                    rw_p.done(each(b + 1, w["kbd"], w["abd"]), f"kat{d}")
                    rw_p.done(each(b + 2, w["abd"], w["bbd"]), f"m{d}")
                    rw_p.done(each(b + 3, w["bbd"], w["rbd"]), f"brt{d}")
                for d, w in enumerate(dirs):
                    b = 4 * d
                    need(pe, rw_v, f"mt{d}", p)
                    rw_p.done(each(b, w["kbd"], w["rbd"]), f"krt{d}")
                    need(pe, rw_v, f"kat{d}", p)
                    rw_p.done(turned(b + 1, w["bbd"]), f"btok{d}")
                    need(pe, rw_v, f"brt{d}", p)
                    rw_p.done(turned(b + 3, w["kbd"]), f"ktok{d}")
                    if d == 0:
                        need(pe, rw_o, "vbd", p)
                        for c in range(NCH):
                            last = nc.tensor.matmul(banks[2][:, CH * c:CH * c + CH], v_bd[:, c], const("istack"), start=True, stop=True)
                        rw_p.done(last, "vtok0")
                for l in LV:
                    for d, w in enumerate(dirs):
                        need(pe, rw_o, f"ml{l}_{d}", p)
                        if l == 1:
                            need(pe, rw_o, f"t1_{d}", p)
                            need(pe, rw_a, f"btok{d}", p)
                        else:
                            need(pe, rw_v, f"T{l - 1}_{d}", p)
                        rw_p.done(each(4 * d + 1, w["ml"], w["tm"]), f"X{l}_{d}")
                    for d, w in enumerate(dirs):
                        need(pe, rw_a, f"X{l}_{d}", p)
                        if l == 1:
                            need(pe, rw_o, f"u1_{d}", p)
                            need(pe, rw_a, "vtok0" if d == 0 else "ktok1", p)
                        else:
                            need(pe, rw_v, f"U{l - 1}_{d}", p)
                        rw_p.done(each(4 * d + 2, w["x"], w["u"]), f"U{l}_{d}")
                        if l < LEVELS - 1:
                            rw_p.done(each(4 * d + 3, w["u"], w["x"]), f"T{l}_{d}")
                for s in ST:
                    for d, w in enumerate(dirs):
                        c = chunk_of(d, s)
                        o = banks[4 * d][:, 0:CH]
                        if s > 0:
                            need(pe, rw_v, f"S{s - 1}_{d}", p)
                            nc.tensor.matmul(o, w["abd"][:, c], st[d][:], start=True, stop=False)
                        else:
                            need(pe, rw_v, f"krt{d}", p)
                        rw_p.done(nc.tensor.matmul(o, w["kat"][:, c], v_tok[:, c], start=s == 0, stop=True), f"W{s}_{d}")
                    for d, w in enumerate(dirs):
                        c = chunk_of(d, s)
                        if s == 0:
                            need(pe, rw_v, f"U{LEVELS - 1}_{d}", p)
                        need(pe, rw_a, f"W{s}_{d}", p)
                        rw_p.done(nc.tensor.matmul(banks[4 * d + 1][:, 0:CH], w["u"][:, c], ws[d][:], start=True, stop=True), f"SA{s}_{d}")
                    for d, w in enumerate(dirs):
                        if s == NCH - 1:
                            continue
                        c = chunk_of(d, s)
                        need(pe, rw_a, f"SA{s}_{d}", p)
                        o = banks[4 * d + 3][:, 0:CH]
                        nc.tensor.matmul(o, w["btok"][:, c], sas[d][:], start=True, stop=False)
                        rw_p.done(nc.tensor.matmul(o, w["ktok"][:, c], v_tok[:, c], start=False, stop=True), f"S{s}_{d}")
                    for d, w in enumerate(dirs):
                        c = chunk_of(d, s)
                        if s == NCH - 1:
                            need(pe, rw_a, f"SA{s}_{d}", p)
                        if s > 0:
                            need(pe, rw_v, f"Y{s - 1}_{d}", p)
                        o = banks[4 * d + 2][:, 0:CH]
                        if s > 0:
                            nc.tensor.matmul(o, w["rbd"][:, c], st[d][:], start=True, stop=False)
                        nc.tensor.matmul(o, w["brt"][:, c], sas[d][:], start=s == 0, stop=False)
                        rw_p.done(nc.tensor.matmul(o, w["krt"][:, c], v_tok[:, c], start=False, stop=True), f"Y{s}_{d}")

        yhl = at("yhl", B + 48 * K, [P, KT, 2, T], R)
        G0 = B + 82 * K
        gsum = at("gsum", G0, [P, 24])
        gmean = at("gmean", G0 + 128, [P, 24])
        gvar = at("gvar", G0 + 256, [P, 24])
        gstd = at("gstd", G0 + 384, [P, 24])
        grs = at("grs", G0 + 512, [P, 24])
        gsq = at("gsq", G0 + K, [P, 24, CH])
        ybd = at("ybd", G0 + 8 * K, [P, 24, P])
        t1 = at("gn_t1", G0 + 20 * K, [P, PAIRS, T])
        t2 = at("gn_t2", G0 + 26 * K, [P, PAIRS, T])
        gn_o = Steps(sem("gn_pool"), ["zero"])
        gn_a = Steps(sem("gn_act"), ["sq", "std", "hi0", "hi1", "hi2", "hi3"])
        gn_v = Steps(sem("gn_dve"), ["sum", "mean", "center", "var", "rstd", "yn"]
                     + [f"{n}{p}" for p in range(PAIRS) for n in ("ln", "bonus", "sum", "y")]
                     + ["lo0", "lo1", "lo2", "lo3"])
        gn_p = Steps(sem("gn_pe"), ["bonus0", "bonus1", "bonus2", "y0", "y1", "y2"])
        y24 = kkn[:].rearrange("p a (c i) -> p (a c) i", c=NCH)

        def wide(ap):
            return ap.unsqueeze(2).broadcast_to([P, 24, CH])

        def pool_gn(pool):
            need(pool, rw_v, f"Y{NCH - 1}_1", PAIRS - 1)
            need(pool, rw_p, f"Y{NCH - 1}_1", PAIRS - 1)
            gn_o.done(nc.gpsimd.memset(ybd[:], 0.0), "zero")
            need(pool, gn_v, "lo3")
            pool.dma_start(x_res[:], xT).then_inc(in_x2, 16)
            pool.wait_ge(units_used, 2 * FIRST["wout1"])
            pool.dma_start(X1[:, :, 0:META], metaT).then_inc(in_meta, 16)

        def act_gn(act):
            need(act, gn_v, "center")
            gn_a.done(nc.scalar.activation(gsq[:], y24, ACT.Square), "sq")
            need(act, gn_v, "var")
            gn_a.done(nc.scalar.activation(gstd[:], gvar[:], ACT.Sqrt, bias=GN_EPS, scale=1.0 / CH), "std")
            need(act, gn_v, f"y{PAIRS - 1}")
            for q in range(4):
                gn_a.done(nc.scalar.activation(yhl[:, 4 * q:4 * q + 4, 0], sg[:, 4 * q:4 * q + 4], ACT.Copy), f"hi{q}")

        def dve_gn(v):
            need(v, rw_v, f"Y{NCH - 1}_1", PAIRS - 1)
            gn_v.done(nc.vector.tensor_reduce(gsum[:], y24, AX.X, ALU.add), "sum")
            need(v, gn_v, "sum")
            gn_v.done(nc.vector.tensor_scalar(gmean[:], gsum[:], 1.0 / CH, None, ALU.mult), "mean")
            need(v, gn_v, "mean")
            gn_v.done(nc.vector.tensor_tensor(y24, y24, wide(gmean[:]), ALU.subtract), "center")
            need(v, gn_a, "sq")
            gn_v.done(nc.vector.tensor_reduce(gvar[:], gsq[:], AX.X, ALU.add), "var")
            need(v, gn_a, "std")
            gn_v.done(nc.vector.reciprocal(grs[:], gstd[:]), "rstd")
            need(v, gn_v, "rstd")
            need(v, gn_o, "zero")
            for h in halves():
                last = nc.vector.tensor_tensor(ybd[h, :, h], y24[h], wide(grs[:])[h], ALU.mult)
            gn_v.done(last, "yn")
            for p in range(PAIRS):
                at_p_ = T * (p % 2)
                need(v, gn_p, f"y{p // 2}")
                gn_v.done(nc.vector.tensor_scalar(t1[:, p], banks[p // 2][:, at_p_:at_p_ + T], col("ln_w", p), col("ln_b", p),
                                                  ALU.mult, ALU.add), f"ln{p}")
                gn_v.done(nc.vector.tensor_tensor(t2[:, p], banks[3 + p // 2][:, at_p_:at_p_ + T], rkv[:, 2 * PAIRS + p],
                                                  ALU.mult), f"bonus{p}")
                need(v, gn_v, f"bonus{p}")
                gn_v.done(nc.vector.tensor_tensor(t1[:, p], t1[:, p], t2[:, p], ALU.add), f"sum{p}")
                need(v, gn_v, f"sum{p}")
                gn_v.done(nc.vector.tensor_tensor(sg[:, A_T + p], sg[:, A_T + p], t1[:, p], ALU.mult), f"y{p}")
            for q in range(4):
                need(v, gn_a, f"hi{q}")
                gn_v.done(nc.vector.tensor_tensor(yhl[:, 4 * q:4 * q + 4, 1], sg[:, 4 * q:4 * q + 4],
                                                  yhl[:, 4 * q:4 * q + 4, 0].bitcast(F), ALU.subtract), f"lo{q}")

        def pe_gn(pe):
            need(pe, rw_v, f"Y{NCH - 1}_1", PAIRS - 1)
            for b in range(3):
                gn_p.done(nc.tensor.matmul(banks[3 + b][:], const("bdones"), rkv[:, 2 * b:2 * b + 2], start=True, stop=True), f"bonus{b}")
            need(pe, gn_v, "yn")
            for b in range(3):
                for n in range(8):
                    last = nc.tensor.matmul(banks[b][:, CH * n:CH * n + CH], ybd[:, 8 * b + n], const("istack"), start=True, stop=True)
                gn_p.done(last, f"y{b}")

        mg = at("mg", B + 90 * K, [P, KT, 2, T], R)
        gt = at("gt", B + 122 * K, [P, N_BRANCH, T])
        mt_ = at("mt_", B + 125 * K, [P, N_BRANCH, T])
        x_res = at("x_res", B + 32 * K, [P, KT, T])
        X1 = at("X1", B, [P, KT, TM])
        SPANS = [(0, A_T), (A_T, A_T + PAIRS), (A_T + PAIRS, KT)]
        gate_out, wo_out, mg_step, mg_hi, mg_lo, wout1_out = (
            sem(n) for n in ("gate_out", "wo_out", "mg_step", "mg_hi", "mg_lo", "wout1_out"))

        def rnd(tile, c, m):
            return tile.loops[-1][0] * m + c if tile.loops else c

        def act_merge(act):
            def body(tile):
                b = tile.t % 4
                split_hi(act, tile.next())
                tile_done(act, tile)
                m = rnd(tile, 0, 1)
                if b < N_BRANCH:
                    if tile.loops and b == 0:
                        act.wait_ge(mg_step, rnd(tile, -2, 5))
                    nc.scalar.activation(gt[:, b], banks[tile.parity][:, 0:T], ACT.Sigmoid,
                                         bias=col("gate_b", rnd(tile, KT * b, 1))).then_inc(gate_out, 1)
                else:
                    act.wait_ge(mg_step, rnd(tile, 5, 5))
                    nc.scalar.activation(mg[:, m, 0], mt_[:, 0], ACT.Copy).then_inc(mg_hi, 1)
            ruN_TILES(act, "merge1", 4, body)

        def dve_merge(v):
            def body(tile):
                split_lo(v, tile.next())
                if tile.t % 4 < N_BRANCH:
                    return
                m = rnd(tile, 0, 1)
                tile_done(v, tile)
                v.wait_ge(gate_out, rnd(tile, 3, 3))
                for b in range(N_BRANCH):
                    ins = nc.vector.tensor_tensor(mt_[:, b], banks[2 + b][:, 0:T], gt[:, b], ALU.mult)
                    ins.then_inc(mg_step, 1)
                v.wait_ge(mg_step, rnd(tile, 3, 5))
                nc.vector.tensor_tensor(mt_[:, 0], mt_[:, 0], mt_[:, 1], ALU.add).then_inc(mg_step, 1)
                v.wait_ge(mg_step, rnd(tile, 4, 5))
                nc.vector.tensor_tensor(mt_[:, 0], mt_[:, 0], mt_[:, 2], ALU.add).then_inc(mg_step, 1)
                v.wait_ge(mg_hi, rnd(tile, 1, 1))
                nc.vector.tensor_tensor(mg[:, m, 1], mt_[:, 0], mg[:, m, 0].bitcast(F), ALU.subtract).then_inc(mg_lo, 1)
            ruN_TILES(v, "merge1", 4, body)

        def pe_merge(pe):
            need(pe, gn_v, "lo3")

            def body(tile):
                b = tile.t % 4
                if b < N_BRANCH:
                    if b == 2 or tile.loops:
                        pe.wait_ge(gate_out, rnd(tile, b - 1 if b == 2 else 0, 3) if b == 2 else rnd(tile, 0, 3))
                    full_tile(pe, tile, hx)
                    return
                if tile.loops:
                    pe.wait_ge(mg_step, rnd(tile, -2, 5))
                for k in range(2):
                    pe.wait_ge(lo_ready, tile.units(k + 1))
                    for j in range(HALF):
                        kt = HALF * k + j
                        n, (a, z) = next((n, s) for n, s in enumerate(SPANS) if s[0] <= kt < s[1])
                        last = product(banks[2 + n][:, 0:T], yhl, (2 * tile.parity + k) % RING, j, kt, kt == a, kt == z - 1)
                    last.then_inc(units_used, 1)
            ruN_TILES(pe, "merge1", 4, body)

        def dve_wout1(v):
            v.wait_ge(in_x2, 16)

            def body(tile):
                split_lo(v, tile.next())
                tile_done(v, tile)
                m = tile.local()
                nc.vector.tensor_tensor(X1[:, m, META:], banks[tile.parity][:, 0:T], x_res[:, m], ALU.add).then_inc(wout1_out, 1)
            ruN_TILES(v, "wout1", 2, body)

        def act_split_phase(act, phase):
            ruN_TILES(act, phase, 2, lambda tile: split_hi(act, tile.next()), peel=False)

        u1 = at("u1", B + 17 * K, [P, KT, 2, TM], R)
        HL = at("HL", B + 51 * K, [P, KT, T])
        PO = at("PO", B + 67 * K, [P, KT, T])
        Z2 = B + 83 * K
        norm1 = Norm("norm1", X1, TM, "norm1_g", u1, B + 51 * K)
        mg2 = at("mg2", Z2, [P, KT, 2, T], R)
        gpool_out, gelu_out = sem("gpool_out"), sem("gelu_out")

        one272 = at("one272", Z2, [P, TM])
        vp = [at(f"vp{b}", Z2 + (2 + 2 * b) * K, [P, TM]) for b in range(2)]
        cs = [at(f"cs{b}", Z2 + (6 + 2 * b) * K, [P, TM]) for b in range(2)]
        df = [at(f"df{b}", Z2 + (10 + b) * K, [P, T]) for b in range(2)]
        dt = [at(f"dt{b}", Z2 + (12 + b) * K, [P, T]) for b in range(2)]
        dhl = at("dhl", Z2 + 14 * K, [P, POOL_T, 2, T], R)
        vp_copied, vp_step, d_hi, d_lo, po_out, ones_set = (
            sem(n) for n in ("vp_copied", "vp_step", "d_hi", "d_lo", "po_out", "ones_set"))
        NG = len(POOL_WINDOWS)

        def group_place(tile):
            j, g = tile.t % 5, tile.t // 5

            def nth(c, m=1):
                return tile.loops[-1][0] * (8 * m) + (m * (4 * g + j) + c) if tile.loops else m * (4 * g + j) + c

            def grp(c, m=1):
                return tile.loops[-1][0] * (2 * m) + (m * g + c) if tile.loops else m * g + c
            return j, g, nth, grp

        def act_pool(act):
            def body(tile):
                split_hi(act, tile.next())
                j, _, nth, _ = group_place(tile)
                if j == 4:
                    return
                tile_done(act, tile)
                if tile.loops or 4 * (tile.t // 5) + j >= 2:
                    act.wait_ge(vp_step, nth(-3, 3))
                b = (4 * (tile.t // 5) + j) % 2
                nc.scalar.activation(vp[b][:], banks[tile.parity][:, 0:TM], ACT.Copy).then_inc(vp_copied, 1)
                act.wait_ge(vp_step, nth(3, 3))
                nc.scalar.activation(dhl[:, j, 0], dt[b][:], ACT.Copy).then_inc(d_hi, 1)
            ruN_TILES(act, "pool", 10, body)

        def dve_pool(v):
            nc.vector.memset(one272[:], 1.0).then_inc(ones_set, 1)
            v.wait_ge(ones_set, 1)
            v.wait_ge(gpool_out, KT)
            for g, window in enumerate(POOL_WINDOWS):
                for j in range(POOL_T):
                    tile = Tile(FIRST["pool"], 5 * g + j)
                    n = POOL_T * g + j
                    b = n % 2
                    split_lo(v, tile.next())
                    v.wait_ge(vp_copied, n + 1)
                    nc.vector.tensor_tensor_scan(cs[b][:], one272[:], vp[b][:], 0.0, ALU.mult, ALU.add).then_inc(vp_step, 1)
                    v.wait_ge(vp_step, 3 * n + 1)
                    nc.vector.tensor_tensor(df[b][:], cs[b][:, META:], cs[b][:, META - window:TM - window], ALU.subtract).then_inc(vp_step, 1)
                    v.wait_ge(vp_step, 3 * n + 2)
                    nc.vector.scalar_tensor_tensor(dt[b][:], df[b][:], 1.0 / window, vp[b][:, META:], ALU.mult, ALU.subtract).then_inc(vp_step, 1)
                    v.wait_ge(d_hi, n + 1)
                    nc.vector.tensor_tensor(dhl[:, j, 1], dt[b][:], dhl[:, j, 0].bitcast(F), ALU.subtract).then_inc(d_lo, 1)
                tile = Tile(FIRST["pool"], 5 * g + POOL_T)
                split_lo(v, tile.next())
                tile_done(v, tile)
                for m in range(POOL_T):
                    c = POOL_T * g + m
                    nc.vector.scalar_tensor_tensor(PO[:, c], banks[2 + m][:, 0:T], col("pool_scale", c), PO[:, c],
                                                   ALU.mult, ALU.mult).then_inc(po_out, 1)

        def pe_pool(pe):
            def body(tile):
                j, g, nth, grp = group_place(tile)
                if j < 4:
                    first = not tile.loops and g == 0
                    if first and j < 2:
                        pe.wait_ge(gelu_out, KT - 1 + j)
                    else:
                        pe.wait_ge(vp_copied, nth(0 if j == 0 else -1))
                    full_tile(pe, tile, u1, TM)
                    return
                if tile.loops or g > 0:
                    pe.wait_ge(po_out, grp(0, 4))
                pe.wait_ge(d_lo, grp(4, 4))
                for k in range(2):
                    pe.wait_ge(lo_ready, tile.units(k + 1))
                    for jj in range(HALF):
                        m, kt = 2 * k + jj // POOL_T, jj % POOL_T
                        last = product(banks[2 + m][:, 0:T], dhl, (2 * tile.parity + k) % RING, jj, kt, kt == 0, kt == POOL_T - 1)
                    last.then_inc(units_used, 1)
            ruN_TILES(pe, "pool", 10, body)

        LP = CONV2 - 1
        L0 = Z2 + 24 * K
        vl = [at(f"vl{b}", Z2 + 1216 * b, [P, TM + LP]) for b in range(2)]
        xa = at("xa", Z2 + 3 * K, [P, TM])
        xc = at("xc", Z2 + 5 * K, [P, 4, TM])
        xchl = at("xchl", Z2 + 10 * K, [P, 4, 2, TM], R)
        gr = at("gr", Z2 + 19 * K, [P, 2, 2, 2, TM])
        av = at("av", Z2 + 28 * K, [P, 2, 2, TM])
        tv = at("tv", Z2 + 33 * K, [P, 2, 2, TM])
        mv = at("mv", Z2 + 38 * K, [P, 2, 2, TM])
        hv = at("hv", Z2 + 43 * K, [P, 4, TM])
        vl_zero, vl_copied, conv_step, xc_hi, xc_lo, lru_gate, hl_done = (
            sem(n) for n in ("vl_zero", "vl_copied", "conv_step", "xc_hi", "xc_lo", "lru_gate", "hl_done"))
        lru_a = Steps(sem("lru_act"), ["tanh", "exp", "sqrt"])
        lru_v = Steps(sem("lru_dve"), ["sq", "one", "ix", "b", "scan", "out"])

        def act_lru(act):
            need_lam(act)

            def body(tile):
                split_hi(act, tile.next())
                j, g, nth, grp = group_place(tile)
                tile_done(act, tile)
                if j < 4:
                    b = (4 * g + j) % 2
                    if tile.loops or 4 * g + j >= 2:
                        act.wait_ge(conv_step, nth(-4, 4))
                    else:
                        act.wait_ge(vl_zero, 2)
                    nc.scalar.activation(vl[b][:, LP:], banks[tile.parity][:, 0:TM], ACT.Copy).then_inc(vl_copied, 1)
                    act.wait_ge(conv_step, nth(4, 4))
                    nc.scalar.activation(xchl[:, j, 0], xc[:, j], ACT.Copy).then_inc(xc_hi, 1)
                    return
                if tile.loops or g > 0:
                    need(act, lru_v, "out", grp(-1))
                for n in range(8):
                    k, ax, m = n // 4, n // 2 % 2, n % 2
                    bias = col("gate_x_b" if ax else "gate_a_b", grp(2 * k + m, 4))
                    nc.scalar.activation(gr[:, k, ax, m], banks[n][:, 0:TM], ACT.Sigmoid, bias=bias).then_inc(lru_gate, 1)
                act.wait_ge(lru_gate, grp(8, 8))
                for func, dst, scale, name in ((ACT.Tanh, tv, 1, "tanh"), (ACT.Exp, av, 2, "exp")):
                    for n in range(4):
                        s = lam_sb[:, scale, bass.ds(grp(n, 4), 1)]
                        last = nc.scalar.activation(dst[:, n // 2, n % 2], gr[:, n // 2, 0, n % 2], func, scale=s)
                    lru_a.done(last, name)
                need(act, lru_v, "one", grp(0))
                lru_a.done(nc.scalar.activation(mv[:], tv[:], ACT.Sqrt), "sqrt")
            ruN_TILES(act, "lru", 10, body)

        def dve_lru(v):
            v.wait_ge(d_lo, KT)
            for b in range(2):
                nc.vector.memset(vl[b][:], 0.0).then_inc(vl_zero, 1)
            v.wait_ge(gelu_out, KT)

            def body(tile):
                split_lo(v, tile.next())
                j, g, nth, grp = group_place(tile)
                if j < 4:
                    b = (4 * g + j) % 2
                    v.wait_ge(vl_copied, nth(1))
                    for k in range(CONV2):
                        tap = vl[b][:, LP - k:LP - k + TM]
                        w = col("conv_w2", nth(KT * (CONV2 - 1 - k)))
                        dst = xc[:, j] if k == CONV2 - 1 else xa[:]
                        if k == 0:
                            ins = nc.vector.tensor_scalar(dst, tap, w, col("conv_b2", nth(0)), ALU.mult, ALU.add)
                        else:
                            v.wait_ge(conv_step, nth(k, 4))
                            ins = nc.vector.scalar_tensor_tensor(dst, tap, w, xa[:], ALU.mult, ALU.add)
                        ins.then_inc(conv_step, 1)
                    v.wait_ge(xc_hi, nth(1))
                    nc.vector.tensor_tensor(xchl[:, j, 1], xc[:, j], xchl[:, j, 0].bitcast(F), ALU.subtract).then_inc(xc_lo, 1)
                    return
                need(v, lru_a, "exp", grp(0))
                lru_v.done(nc.vector.tensor_tensor(mv[:], av[:], av[:], ALU.mult), "sq")
                need(v, lru_v, "sq", grp(0))
                lru_v.done(nc.vector.scalar_tensor_tensor(tv[:].rearrange("p a b t -> p (a b t)"), mv[:].rearrange("p a b t -> p (a b t)"), 1.0,
                                                          tv[:].rearrange("p a b t -> p (a b t)"), ALU.add, ALU.mult), "one")
                i_gate = gr[:, :, 1].rearrange("p k m t -> p k (m t)")
                lru_v.done(nc.vector.tensor_tensor(xc[:].rearrange("p (k m) t -> p k (m t)", k=2), i_gate,
                                                   xc[:].rearrange("p (k m) t -> p k (m t)", k=2), ALU.mult), "ix")
                need(v, lru_a, "sqrt", grp(0))
                need(v, lru_v, "ix", grp(0))
                lru_v.done(nc.vector.tensor_tensor(xc[:].rearrange("p a t -> p (a t)"), mv[:].rearrange("p a b t -> p (a b t)"),
                                                   xc[:].rearrange("p a t -> p (a t)"), ALU.mult), "b")
                need(v, lru_v, "b", grp(0))
                for n in range(4):
                    last = nc.vector.tensor_tensor_scan(hv[:, n], av[:, n // 2, n % 2], xc[:, n], 0.0, ALU.mult, ALU.add)
                lru_v.done(last, "scan")
                need(v, lru_v, "scan", grp(0))
                for n in range(4):
                    c = grp(n, 4)
                    last = nc.vector.tensor_tensor(HL[:, c], hv[:, n, META:], HL[:, c], ALU.mult)
                lru_v.done(last, "out")
            ruN_TILES(v, "lru", 10, body)

        def pe_lru(pe):
            pe.wait_ge(po_out, KT)

            def body(tile):
                j, g, nth, grp = group_place(tile)
                if j < 4:
                    if not tile.loops and g == 0 and j < 2:
                        pe.wait_ge(vp_copied, KT)
                    elif j < 2:
                        pe.wait_ge(lru_gate, grp(tile.parity + 1 - 8, 8))
                    else:
                        pe.wait_ge(vl_copied, nth(-1))
                    full_tile(pe, tile, u1, TM)
                    return
                pe.wait_ge(xc_lo, grp(4, 4))
                if tile.loops or g > 0:
                    pe.wait_ge(lru_gate, grp(0, 8))
                for k in range(2):
                    pe.wait_ge(lo_ready, tile.units(k + 1))
                    for jj in range(HALF):
                        n, kt = 4 * k + jj // 2, jj % 2
                        last = product(banks[n][:, 0:TM], xchl, (2 * tile.parity + k) % RING, jj, 2 * k + kt, kt == 0, kt == 1, TM)
                    last.then_inc(units_used, 1)
            ruN_TILES(pe, "lru", 10, body)

        lam_a = Steps(sem("lam_act"), ["abs", "exp"])
        TERMS = list(range(15, 0, -2))
        lam_v = Steps(sem("lam_dve"), ["two", "inv", "z", "zz", "h15"] + [f"{n}{k}" for k in TERMS[1:] for n in ("m", "h")]
                      + ["log", "neg", "sum", "s8", "n8"])

        def need_lam(eng):
            need(eng, lam_v, "n8")

        def act_lam(act):
            act.wait_ge(in_par, 16)
            lam = par[:, PCOL["lam"]:PCOL["lam"] + KT]
            lam_a.done(nc.scalar.activation(lam_sb[:, 0], lam, ACT.Abs), "abs")
            need(act, lam_a, "abs")
            lam_a.done(nc.scalar.activation(lam_sb[:, 0], lam_sb[:, 0], ACT.Exp, scale=-1.0), "exp")

        def dve_lam(v):
            e, z, zz, h, t = (lam_sb[:, k] for k in (0, 1, 2, 3, 4))

            def then(ins, name):
                lam_v.done(ins, name)
                need(v, lam_v, name)
            need(v, lam_a, "exp")
            then(nc.vector.tensor_scalar(t, e, 2.0, None, ALU.add), "two")
            then(nc.vector.reciprocal(t, t), "inv")
            then(nc.vector.tensor_tensor(z, e, t, ALU.mult), "z")
            then(nc.vector.tensor_tensor(zz, z, z, ALU.mult), "zz")
            then(nc.vector.tensor_scalar(h, zz, 0.0, 1.0 / TERMS[0], ALU.mult, ALU.add), "h15")
            for k in TERMS[1:]:
                then(nc.vector.tensor_tensor(h, h, zz, ALU.mult), f"m{k}")
                then(nc.vector.tensor_scalar(h, h, 1.0 / k, None, ALU.add), f"h{k}")
            then(nc.vector.scalar_tensor_tensor(h, h, 2.0, z, ALU.mult, ALU.mult), "log")
            then(nc.vector.tensor_scalar(t, par[:, PCOL["lam"]:PCOL["lam"] + KT], -1.0, 0.0, ALU.mult, ALU.max), "neg")
            then(nc.vector.tensor_tensor(t, t, h, ALU.add), "sum")
            then(nc.vector.tensor_scalar(lam_sb[:, 1], t, 8.0, None, ALU.mult), "s8")
            then(nc.vector.tensor_scalar(lam_sb[:, 2], t, -8.0, None, ALU.mult), "n8")

        sgt = [at(f"sgt{b}", Z2 + (32 + b) * K, [P, T]) for b in range(2)]
        mt2 = [at(f"mt2{b}", Z2 + (34 + b) * K, [P, T]) for b in range(2)]
        glru_out, glru_step, mg2_hi, mg2_lo = (sem(n) for n in ("glru_out", "glru_step", "mg2_hi", "mg2_lo"))

        def act_glru(act):
            need(act, lru_v, "out", 3)

            def body(tile):
                split_hi(act, tile.next())
                tile_done(act, tile)
                b = tile.t % 2
                if tile.loops or tile.t >= 2:
                    act.wait_ge(glru_step, tile.local(2, -3))
                nc.scalar.activation(sgt[b][:], banks[tile.parity][:, 0:T], ACT.Sigmoid).then_inc(glru_out, 1)
                act.wait_ge(glru_step, tile.local(2, 2))
                nc.scalar.activation(mg2[:, tile.local(), 0], mt2[b][:], ACT.Copy).then_inc(mg2_hi, 1)
            ruN_TILES(act, "glru", 2, body)

        def dve_glru(v):
            def body(tile):
                split_lo(v, tile.next())
                b, m = tile.t % 2, tile.local()
                v.wait_ge(glru_out, tile.local(1, 1))
                nc.vector.tensor_tensor(mt2[b][:], HL[:, m], sgt[b][:], ALU.mult).then_inc(glru_step, 1)
                v.wait_ge(glru_step, tile.local(2, 1))
                nc.vector.tensor_tensor(mt2[b][:], mt2[b][:], PO[:, m], ALU.add).then_inc(glru_step, 1)
                v.wait_ge(mg2_hi, tile.local(1, 1))
                nc.vector.tensor_tensor(mg2[:, m, 1], mt2[b][:], mg2[:, m, 0].bitcast(F), ALU.subtract).then_inc(mg2_lo, 1)
            ruN_TILES(v, "glru", 2, body)

        wout2_out = sem("wout2_out")

        def dve_add_phase(v, phase, dst, scale, out_sem):
            def body(tile):
                split_lo(v, tile.next())
                tile_done(v, tile)
                m = tile.local()
                nc.vector.scalar_tensor_tensor(dst[:, m], dst[:, m], scale, banks[tile.parity][:, 0:T],
                                               ALU.mult, ALU.add).then_inc(out_sem, 1)
            ruN_TILES(v, phase, 2, body)

        class Mlp:
            def __init__(self, phase, x, moving, hidden, tmp, scale):
                self.phase, self.x, self.moving, self.hid, self.scale = phase, x, moving, hidden, scale
                self.r = [at(f"{phase}_r{b}", tmp + K * b, [P, T]) for b in range(2)]
                self.q = [at(f"{phase}_q{b}", tmp + K * (2 + b), [P, T]) for b in range(2)]
                self.relu, self.hi, self.lo, self.out = (sem(f"{phase}_{n}") for n in ("relu", "hi", "lo", "out"))

            def groups(self, eng, up, down):
                def group(loops):
                    first = FIRST[self.phase]
                    ruN_TILES(eng, self.phase, 2, lambda t: up(t, bool(loops)), loops, first, KT)
                    ruN_TILES(eng, self.phase, 2, lambda t: down(t, bool(loops)), loops, first + KT, KT)
                group(())
                with eng.Fori(1, FF_GROUPS) as n:
                    group(((n, 2 * KT),))

            @staticmethod
            def nth(tile, c, m, grouped):
                v = m * tile.t + c
                for k, (reg, per) in enumerate(tile.loops):
                    v = reg * ((KT if grouped and k == 0 else per) * m) + v
                return v

            @staticmethod
            def place(tile, grouped):
                v = tile.t
                for reg, per in tile.loops[1 if grouped else 0:]:
                    v = reg * per + v
                return v

            def act(self, act):
                def up(tile, grouped):
                    split_hi(act, tile.next())
                    tile_done(act, tile)
                    b, m = tile.t % 2, self.place(tile, grouped)
                    if grouped or tile.loops or tile.t >= 2:
                        act.wait_ge(self.lo, self.nth(tile, -1, 1, grouped))
                    nc.scalar.activation(self.r[b][:], banks[tile.parity][:, 0:T], ACT.Relu).then_inc(self.relu, 1)
                    act.wait_ge(self.relu, self.nth(tile, 1, 2, grouped))
                    nc.scalar.activation(self.q[b][:], self.r[b][:], ACT.Square).then_inc(self.relu, 1)
                    act.wait_ge(self.relu, self.nth(tile, 2, 2, grouped))
                    nc.scalar.activation(self.hid[:, m, 0], self.q[b][:], ACT.Copy).then_inc(self.hi, 1)
                self.groups(act, up, lambda tile, grouped: split_hi(act, tile.next()))

            def dve(self, v):
                def up(tile, grouped):
                    split_lo(v, tile.next())
                    b, m = tile.t % 2, self.place(tile, grouped)
                    v.wait_ge(self.hi, self.nth(tile, 1, 1, grouped))
                    nc.vector.tensor_tensor(self.hid[:, m, 1], self.q[b][:], self.hid[:, m, 0].bitcast(F),
                                            ALU.subtract).then_inc(self.lo, 1)

                def down(tile, grouped):
                    split_lo(v, tile.next())
                    tile_done(v, tile)
                    m = self.place(tile, grouped)
                    nc.vector.scalar_tensor_tensor(self.x[:, m], self.x[:, m], 1.0 if grouped else self.scale,
                                                   banks[tile.parity][:, 0:T], ALU.mult, ALU.add).then_inc(self.out, 1)
                self.groups(v, up, down)

            def pe(self, pe, before):
                def up(tile, grouped):
                    place0 = tile.t if not tile.loops[1 if grouped else 0:] else 2
                    if place0 >= 2:
                        pe.wait_ge(self.relu, self.nth(tile, -3, 2, grouped))
                    elif grouped:
                        pe.wait_ge(self.out, self.nth(tile, -1, 1, grouped))
                    full_tile(pe, tile, self.moving, T, before if not tile.loops and tile.t == 0 else None)

                def down(tile, grouped):
                    place0 = tile.t if not tile.loops[1 if grouped else 0:] else 2
                    if place0 >= 2:
                        pe.wait_ge(self.out, self.nth(tile, -1, 1, grouped))
                    else:
                        pe.wait_ge(self.relu, self.nth(tile, 2 * KT - 3, 2, grouped))

                    def hidden_ready(k):
                        pe.wait_ge(self.lo, self.nth(tile, HALF * (k + 1) - tile.t, 1, grouped))
                    full_tile(pe, tile, self.hid, T, hidden_ready if place0 < 2 else None)
                self.groups(pe, up, down)

        x2 = X1[:, :, META:]
        u2 = at("u2", B + 17 * K, [P, KT, 2, T], R)
        hid2 = at("hid2", B + 51 * K, [P, KT, 2, T], R)
        norm2 = Norm("norm2", x2, T, "norm2_g", u2, Z2)
        mlp2 = Mlp("ff2", x2, u2, hid2, Z2 + 20 * K, 1.0)
        X3 = at("X3", B + 83 * K, [P, KT, T])
        xh3 = at("xh3", B + 99 * K, [P, KT, 2, T], R)
        final = Norm("final", x2, T, "final_g", xh3, B + 17 * K, keep=X3)

        mix = at("mix", B + 17 * K, [P, KT, 2, T], R)
        Q = B + 49 * K
        gp = at("gp", Q, [P, 17, T])
        sr = at("sr", Q + 17 * K, [P, GLA_VT, T])
        ym = at("ym", Q + 25 * K, [P, C3_T, T])
        cg = [at(f"cg{b}", B + b * K, [P, T]) for b in range(2)]
        hp = at("hp", B + 2 * K, [P, T + 2])
        ca = at("ca", B + 4 * K, [P, T])
        hp_zero, c_out, ub_out, c3_step, sr_out, gp_out = (
            sem(n) for n in ("hp_zero", "c_out", "ub_out", "c3_step", "sr_out", "gp_out"))

        def conv_place(tile):
            kind, s = tile.t % 3, tile.t // 3

            def nth(c=0, m=1):
                return tile.loops[-1][0] * (2 * m) + (m * s + c) if tile.loops else m * s + c
            return kind, s, nth

        def act_conv3(act):
            def body(tile):
                split_hi(act, tile.next())
                kind, s, nth = conv_place(tile)
                if kind == 0:
                    tile_done(act, tile)
                    if tile.loops:
                        act.wait_ge(ub_out, nth(-3, 2))
                    nc.scalar.activation(cg[s % 2][:], banks[tile.parity][:, 0:T], ACT.Copy).then_inc(c_out, 1)
            ruN_TILES(act, "conv3", 6, body)

        def dve_conv3(v):
            need(v, final.v, "lo3")
            nc.vector.memset(hp[:], 0.0).then_inc(hp_zero, 1)
            v.wait_ge(hp_zero, 1)

            def body(tile):
                split_lo(v, tile.next())
                kind, s, nth = conv_place(tile)
                if kind == 0:
                    return
                tile_done(v, tile)
                if kind == 1:
                    v.wait_ge(c_out, nth(1))
                    nc.vector.tensor_tensor(hp[:, 2:], banks[tile.parity][:, 0:T], cg[s % 2][:], ALU.mult).then_inc(ub_out, 1)
                    v.wait_ge(ub_out, nth(1, 2))
                    for k in range(CONV3):
                        tap, w = hp[:, 2 - k:2 - k + T], col("conv_w3", nth(C3_T * (CONV3 - 1 - k)))
                        if k == 0:
                            ins = nc.vector.tensor_scalar(ca[:], tap, w, None, ALU.mult)
                        else:
                            v.wait_ge(c3_step, nth(k, 3))
                            ins = nc.vector.scalar_tensor_tensor(ca[:], tap, w, ca[:], ALU.mult, ALU.add)
                        ins.then_inc(c3_step, 1)
                else:
                    v.wait_ge(c3_step, nth(3, 3))
                    nc.vector.tensor_tensor(ym[:, nth()], banks[tile.parity][:, 0:T], ca[:], ALU.mult).then_inc(ub_out, 1)
            ruN_TILES(v, "conv3", 6, body)

        def pe_conv3(pe):
            def body(tile):
                kind, s, nth = conv_place(tile)
                first = not tile.loops and s == 0
                if kind == 2:
                    pe.wait_ge(c_out, nth(1))
                elif not first:
                    pe.wait_ge(ub_out, nth(-1 if kind == 0 else 0, 2))
                full_tile(pe, tile, xh3, T, (lambda k: final.ready(pe, k)) if first and kind == 0 else None)
            ruN_TILES(pe, "conv3", 6, body)

        zl, q3, k3 = gp[:, 0], gp[:, 1:5], gp[:, 5:9]
        E3 = B + 99 * K
        qd = at("qd", E3, [P, GLA_H, T])
        ki = at("ki", E3 + 4 * K, [P, GLA_H, T])
        ke = at("ke", E3 + 8 * K, [P, GLA_H, T])
        ss = at("gla_s", E3 + 12 * K, [P, GLA_H, T])
        l1 = at("gla_l1", E3 + 16 * K, [P, GLA_H, T])
        l2 = at("gla_l2", E3 + 20 * K, [P, GLA_H, T])
        ps3 = at("gla_ps", E3 + 24 * K, [P, GLA_H * NB, P])
        dcy = at("gla_dcy", E3 + 28 * K, [P, GLA_H * NCH])
        crs = at("conv_rs", B, [P, C3_T, T])
        csq = at("conv_sq", B + 8 * K, [P, C3_T, T])
        sst = at("gla_state", B, [P, GLA_H, NCH - 1, T])
        k_tok = at("k_tok", B + 12 * K, [P, NB, GLA_H * P])
        v_tok3 = at("v_tok3", Q, [P, NB, GLA_VT * P])
        oo = at("gla_o", E3 + 16 * K, [P, GLA_VT, T])
        osq = at("gla_osq", E3 + 4 * K, [P, GLA_VT, T])
        ors = at("gla_ors", E3 + 12 * K, [P, GLA_H, T])
        H4 = range(GLA_H)
        g_o = Steps(sem("gla_pool"), ["zero"])
        g_a = Steps(sem("gla_act"), ["csq"] + [f"cstd{b}" for b in range(4)] + [f"idn{h}" for h in H4] + ["abs", "exp", "ln"]
                    + ["chi0", "chi1", "eq", "ek", "ee", "kt0", "kt1", "vt0", "vt1", "vt2", "vt3"]
                    + [f"o{h}" for h in H4] + ["osq", "ostd0", "ostd1", "ohi0", "ohi1"])
        g_v = Steps(sem("gla_dve"), [f"crs{b}" for b in range(4)] + ["cy", "min", "la"] + [f"sum{h}" for h in H4] + ["rest"]
                    + ["clo0", "clo1", "dec", "qd", "ki", "ke", "sc0", "sc1"]
                    + [f"st{h}_{c}" for h in H4 for c in range(NCH - 1)] + ["ors0", "ors1", "on", "oy", "olo0", "olo1"])
        g_p = Steps(sem("gla_pe"), [f"cst{b}" for b in range(4)] + [f"z{h}" for h in H4]
                    + ["vt0", "vt1", "vt2", "vt3", "kt0", "kt1", "sc0", "sc1"]
                    + [n for h in H4 for n in (f"dl{h}", f"o{h}")] + ["ost0", "ost1"])

        def two(bank):
            return banks[bank][:].rearrange("p (a t) -> p a t", a=2)

        def by_chunk(ap):
            return ap.rearrange("p h (c t) -> p (h c) t", c=NCH)

        def pool_gla(pool):
            pool.wait_ge(gp_out, COUNT["gla_p"])
            g_o.done(nc.gpsimd.memset(ps3[:], 0.0), "zero")

        def act_gla(act):
            act.wait_ge(ub_out, 2 * C3_T)
            g_a.done(nc.scalar.activation(csq[:], ym[:], ACT.Square), "csq")
            for b in range(4):
                need(act, g_p, f"cst{b}")
                g_a.done(nc.scalar.activation(crs[:, 2 * b:2 * b + 2], two(4 + b), ACT.Sqrt, bias=EPS, scale=1.0 / P), f"cstd{b}")
            for h in H4:
                need(act, g_p, f"z{h | 1}")
                g_a.done(nc.scalar.activation(l1[:, h], two(2 + h // 2)[:, h % 2], ACT.Identity, bias=col("gate_bias3", h)), f"idn{h}")
            need(act, g_a, f"idn{GLA_H - 1}")
            g_a.done(nc.scalar.activation(l2[:], l1[:], ACT.Abs), "abs")
            need(act, g_a, "abs")
            g_a.done(nc.scalar.activation(l2[:], l2[:], ACT.Exp, scale=-1.0), "exp")
            need(act, g_a, "exp")
            g_a.done(nc.scalar.activation(l2[:], l2[:], ACT.Ln, bias=1.0), "ln")
            need(act, g_v, "cy")
            for q in range(2):
                g_a.done(nc.scalar.activation(mix[:, 4 * q:4 * q + 4, 0], ym[:, 4 * q:4 * q + 4], ACT.Copy), f"chi{q}")
            need(act, g_v, f"sum{GLA_H - 1}")
            g_a.done(nc.scalar.activation(qd[:], ss[:], ACT.Exp, scale=1.0 / GATE_TAU), "eq")
            g_a.done(nc.scalar.activation(ki[:], ss[:], ACT.Exp, scale=-1.0 / GATE_TAU), "ek")
            need(act, g_v, "rest")
            g_a.done(nc.scalar.activation(ke[:], ke[:], ACT.Exp, scale=1.0 / GATE_TAU), "ee")
            for b in range(NB):
                need(act, g_p, f"kt{b}")
                g_a.done(nc.scalar.activation(k_tok[:, b], banks[2 + b][:], ACT.Copy), f"kt{b}")
            need(act, g_v, "ke")
            for n in range(4):
                need(act, g_p, f"vt{n}")
                g_a.done(nc.scalar.activation(v_tok3[:, n // 2, 512 * (n % 2):512 * (n % 2) + 512], banks[4 + n][:], ACT.Copy), f"vt{n}")
            for h in H4:
                need(act, g_p, f"o{h}")
                g_a.done(nc.scalar.activation(oo[:, 2 * h:2 * h + 2], two(5 + h % 2), ACT.Copy), f"o{h}")
            need(act, g_a, f"o{GLA_H - 1}")
            g_a.done(nc.scalar.activation(osq[:], oo[:], ACT.Square), "osq")
            for b in range(2):
                need(act, g_p, f"ost{b}")
                g_a.done(nc.scalar.activation(ors[:, 2 * b:2 * b + 2], two(2 + b), ACT.Sqrt, bias=EPS, scale=1.0 / T), f"ostd{b}")
            need(act, g_v, "oy")
            for q in range(2):
                g_a.done(nc.scalar.activation(mix[:, 8 + 4 * q:12 + 4 * q, 0], oo[:, 4 * q:4 * q + 4], ACT.Copy), f"ohi{q}")

        def dve_gla(v):
            for b in range(4):
                need(v, g_a, f"cstd{b}")
                g_v.done(nc.vector.reciprocal(crs[:, 2 * b:2 * b + 2], crs[:, 2 * b:2 * b + 2]), f"crs{b}")
            need(v, g_v, "crs3")
            for c in range(C3_T):
                last = nc.vector.scalar_tensor_tensor(ym[:, c], ym[:, c], col("conv_g3", c), crs[:, c], ALU.mult, ALU.mult)
            g_v.done(last, "cy")
            need(v, g_a, "abs")
            g_v.done(nc.vector.tensor_scalar(l1[:], l1[:], 0.0, None, ALU.min), "min")
            need(v, g_v, "min")
            need(v, g_a, "ln")
            g_v.done(nc.vector.tensor_tensor(l1[:], l1[:], l2[:], ALU.subtract), "la")
            need(v, g_v, "la")
            for h in H4:
                g_v.done(nc.vector.tensor_tensor_scan(ss[:, h], const("run_up"), l1[:, h], 0.0, ALU.mult, ALU.add), f"sum{h}")
            need(v, g_v, f"sum{GLA_H - 1}")
            s_end = by_chunk(ss[:])[:, :, CH - 1].unsqueeze(2).broadcast_to([P, GLA_H * NCH, CH])
            g_v.done(nc.vector.tensor_tensor(by_chunk(ke[:]), s_end, by_chunk(ss[:]), ALU.subtract), "rest")
            for q in range(2):
                need(v, g_a, f"chi{q}")
                g_v.done(nc.vector.tensor_tensor(mix[:, 4 * q:4 * q + 4, 1], ym[:, 4 * q:4 * q + 4],
                                                 mix[:, 4 * q:4 * q + 4, 0].bitcast(F), ALU.subtract), f"clo{q}")
            need(v, g_a, "eq")
            g_v.done(nc.vector.tensor_copy(dcy[:], by_chunk(qd[:])[:, :, CH - 1]), "dec")
            need(v, g_v, "dec")
            def flat(ap):
                return ap.rearrange("p h t -> p (h t)")
            g_v.done(nc.vector.scalar_tensor_tensor(flat(qd[:]), flat(q3), P ** -0.5, flat(qd[:]), ALU.mult, ALU.mult), "qd")
            need(v, g_a, "ek")
            g_v.done(nc.vector.tensor_tensor(ki[:], k3, ki[:], ALU.mult), "ki")
            need(v, g_a, "ee")
            g_v.done(nc.vector.tensor_tensor(ke[:], k3, ke[:], ALU.mult), "ke")
            need(v, g_o, "zero")
            mask = const("incl_up").bitcast(mybir.dt.uint32).unsqueeze(1).broadcast_to([P, 4, P])
            for b in range(2):
                need(v, g_p, f"sc{b}")
                g_v.done(nc.vector.copy_predicated(ps3[:, 4 * b:4 * b + 4], mask, banks[b][:].rearrange("p (n c) -> p n c", n=4)), f"sc{b}")
            for h in H4:
                need(v, g_p, f"dl{h}")
                for c in range(NCH - 1):
                    new = banks[2 + c][:, 0:T]
                    if c == 0:
                        ins = nc.vector.tensor_copy(sst[:, h, c], new)
                    else:
                        need(v, g_v, f"st{h}_{c - 1}")
                        ins = nc.vector.scalar_tensor_tensor(sst[:, h, c], sst[:, h, c - 1], dcy[:, NCH * h + c:NCH * h + c + 1],
                                                             new, ALU.mult, ALU.add)
                    g_v.done(ins, f"st{h}_{c}")
            for b in range(2):
                need(v, g_a, f"ostd{b}")
                g_v.done(nc.vector.reciprocal(ors[:, 2 * b:2 * b + 2], ors[:, 2 * b:2 * b + 2]), f"ors{b}")
            need(v, g_v, "ors1")
            for c in range(GLA_VT):
                last = nc.vector.scalar_tensor_tensor(oo[:, c], oo[:, c], col("gla_g3", c), ors[:, c // 2], ALU.mult, ALU.mult)
            g_v.done(last, "on")
            need(v, g_v, "on")
            g_v.done(nc.vector.tensor_tensor(oo[:], oo[:], sr[:], ALU.mult), "oy")
            for q in range(2):
                need(v, g_a, f"ohi{q}")
                g_v.done(nc.vector.tensor_tensor(mix[:, 8 + 4 * q:12 + 4 * q, 1], oo[:, 4 * q:4 * q + 4],
                                                 mix[:, 8 + 4 * q:12 + 4 * q, 0].bitcast(F), ALU.subtract), f"olo{q}")

        def pe_gla(pe):
            need(pe, g_a, "csq")
            for b in range(4):
                g_p.done(nc.tensor.matmul(banks[4 + b][:], const("ones"), csq[:, 2 * b:2 * b + 2], start=True, stop=True), f"cst{b}")
            pe.wait_ge(gp_out, COUNT["gla_p"])
            for h in H4:
                g_p.done(nc.tensor.matmul(two(2 + h // 2)[:, h % 2], wgu_sb[:, h], zl[0:16], start=True, stop=True), f"z{h}")
            for n in range(4):
                need(pe, g_a, f"cstd{n}")
                for c in range(4):
                    last = nc.tensor.transpose(banks[4 + n][:, P * c:P * c + P],
                                               gp[:, 9 + 4 * (n % 2) + c, P * (n // 2):P * (n // 2) + P], const("ident"))
                g_p.done(last, f"vt{n}")
            need(pe, g_v, "ke")
            need(pe, g_a, f"idn{GLA_H - 1}")
            for b in range(NB):
                for h in H4:
                    last = nc.tensor.transpose(banks[2 + b][:, P * h:P * h + P], ke[:, h, P * b:P * b + P], const("ident"))
                g_p.done(last, f"kt{b}")
            for b in range(2):
                for n in range(4):
                    h, tb = (4 * b + n) // NB, n % NB
                    last = nc.tensor.matmul(banks[b][:, P * n:P * n + P], ki[:, h, P * tb:P * tb + P], qd[:, h, P * tb:P * tb + P],
                                            start=True, stop=True)
                g_p.done(last, f"sc{b}")
            need(pe, g_a, "vt3")
            for h in H4:
                if h > 0:
                    need(pe, g_v, f"st{h - 1}_{NCH - 2}")
                for c in range(NCH - 1):
                    rows = slice(CH * (c % 2), CH * (c % 2) + CH)
                    last = nc.tensor.matmul(banks[2 + c][:, 0:T], k_tok[rows, c // 2, P * h:P * h + P],
                                            v_tok3[rows, c // 2, T * h:T * h + T], start=True, stop=True)
                g_p.done(last, f"dl{h}")
                need(pe, g_v, f"st{h}_{NCH - 2}")
                if h >= 2:
                    need(pe, g_a, f"o{h - 2}")
                for n in range(2):
                    o = two(5 + h % 2)[:, n]
                    c0 = T * h + P * n
                    for tb in range(NB):
                        nc.tensor.matmul(o[:, P * tb:P * tb + P], v_tok3[:, tb, c0:c0 + P], ps3[:, NB * h + tb], start=tb == 0, stop=False)
                    for c in range(1, NCH):
                        last = nc.tensor.matmul(o[:, CH * c:CH * c + CH], sst[:, h, c - 1, P * n:P * n + P], qd[:, h, CH * c:CH * c + CH],
                                                start=False, stop=c == NCH - 1)
                g_p.done(last, f"o{h}")
            need(pe, g_a, "osq")
            for b in range(2):
                for n in range(2):
                    for m in range(2):
                        last = nc.tensor.matmul(two(2 + b)[:, n], const("ones"), osq[:, 4 * b + 2 * n + m], start=m == 0, stop=m == 1)
                g_p.done(last, f"ost{b}")

        wout3_out = sem("wout3_out")

        class LayerNorm:
            def __init__(self, name, x, g, b, dst, scratch):
                self.x, self.g, self.b, self.dst = x, g, b, dst
                self.sq = at(name + "_sq", scratch, [P, 2, 4, T])
                self.mu = at(name + "_mu", scratch + 8 * K, [P, T])
                self.std = at(name + "_std", scratch + 9 * K, [P, T])
                self.rstd = at(name + "_rstd", scratch + 10 * K, [P, T])
                last = [f"{n}{q}" for q in range(4) for n in (("aff", "hi") if dst is not None else ("aff",))]
                self.a = Steps(sem(name + "_act"), ["mu"] + [f"sq{q}" for q in range(4)] + ["std"] + last)
                self.v = Steps(sem(name + "_dve"), [f"cen{q}" for q in range(4)] + ["rstd"] + [f"nrm{q}" for q in range(4)]
                               + ([f"lo{q}" for q in range(4)] if dst is not None else []))
                self.p = Steps(sem(name + "_pe"), ["mean"] + [f"var{q}" for q in range(4)])

            def part(self, q):
                return self.x[:, 4 * q:4 * q + 4]

            @staticmethod
            def over(ap):
                return ap.unsqueeze(1).broadcast_to([P, 4, T])

            def act(self, act):
                need(act, self.p, "mean")
                self.a.done(nc.scalar.activation(self.mu[:], banks[2][:, 0:T], ACT.Copy, scale=1.0 / D), "mu")
                for q in range(4):
                    need(act, self.v, f"cen{q}")
                    if q >= 2:
                        need(act, self.p, f"var{q - 2}")
                    self.a.done(nc.scalar.activation(self.sq[:, q % 2], self.part(q), ACT.Square), f"sq{q}")
                need(act, self.p, "var3")
                self.a.done(nc.scalar.activation(self.std[:], banks[3][:, 0:T], ACT.Sqrt, bias=LN_EPS, scale=1.0 / D), "std")
                for q in range(4):
                    need(act, self.v, f"nrm{q}")
                    for j in range(4):
                        kt = 4 * q + j
                        last = nc.scalar.activation(self.x[:, kt], self.x[:, kt], ACT.Identity, bias=col(self.b, kt), scale=col(self.g, kt))
                    self.a.done(last, f"aff{q}")
                    if self.dst is not None:
                        need(act, self.a, f"aff{q}")
                        self.a.done(nc.scalar.activation(self.dst[:, 4 * q:4 * q + 4, 0], self.part(q), ACT.Copy), f"hi{q}")

            def pe(self, pe):
                for kt in range(KT):
                    last = nc.tensor.matmul(banks[2][:, 0:T], const("ones"), self.x[:, kt], start=kt == 0, stop=kt == KT - 1)
                self.p.done(last, "mean")
                for q in range(4):
                    need(pe, self.a, f"sq{q}")
                    for j in range(4):
                        last = nc.tensor.matmul(banks[3][:, 0:T], const("ones"), self.sq[:, q % 2, j], start=q + j == 0, stop=q + j == 6)
                    self.p.done(last, f"var{q}")

            def dve(self, v):
                need(v, self.a, "mu")
                for q in range(4):
                    self.v.done(nc.vector.tensor_tensor(self.part(q), self.part(q), self.over(self.mu[:]), ALU.subtract), f"cen{q}")
                need(v, self.a, "std")
                self.v.done(nc.vector.reciprocal(self.rstd[:], self.std[:]), "rstd")
                need(v, self.v, "rstd")
                for q in range(4):
                    self.v.done(nc.vector.tensor_tensor(self.part(q), self.part(q), self.over(self.rstd[:]), ALU.mult), f"nrm{q}")
                if self.dst is not None:
                    for q in range(4):
                        need(v, self.a, f"hi{q}")
                        self.v.done(nc.vector.tensor_tensor(self.dst[:, 4 * q:4 * q + 4, 1], self.part(q),
                                                            self.dst[:, 4 * q:4 * q + 4, 0].bitcast(F), ALU.subtract), f"lo{q}")

            def ready(self, pe, k):
                need(pe, self.v, f"lo{2 * k + 1}")

        xh4 = at("xh4", B + 99 * K, [P, KT, 2, T], R)
        hid3 = at("hid3", B + 17 * K, [P, KT, 2, T], R)
        ln1 = LayerNorm("ln1", X3, "ln1_g", "ln1_b", xh4, B)
        mlp3 = Mlp("ff3", X3, xh4, hid3, B + 49 * K, ALPHA3)
        ln2 = LayerNorm("ln2", X3, "ln2_g", "ln2_b", None, B + 17 * K)

        block = ctx.enter_context(nc.Block())

        @block.sync
        def _(sp):
            for k in range(RING):
                sp.dma_start(raw[:, k], stream[k]).then_inc(raw_in[k], 16)
            rounds = 2 * (N_TILES + 1) // RING
            by_round = stream[0:RING * rounds].rearrange("(n k) p j c -> n k p j c", k=RING)
            with sp.Fori(1, rounds) as n:
                for k in range(RING):
                    sp.wait_ge(lo_ready, n * RING + (k + 1 - RING))
                    sp.dma_start(raw[:, k], by_round[n, k]).then_inc(raw_in[k], 16)
            for u in range(RING * rounds, 2 * (N_TILES + 1)):
                sp.wait_ge(lo_ready, u + 1 - RING)
                sp.dma_start(raw[:, u % RING], stream[u]).then_inc(raw_in[u % RING], 16)
            for q in range(4):
                need(sp, ln2.a, f"aff{q}")
                sp.dma_start(out[:, 4 * q:4 * q + 4], X3[:, 4 * q:4 * q + 4]).then_inc(stored, 16)
            sp.wait_ge(stored, 64)

        @block.gpsimd
        def _(pool):
            pool_kk(pool)
            pool_rwkv(pool)
            pool_gn(pool)
            pool_gla(pool)

        @block.scalar
        def _(act):
            act.dma_start(mem_raw[:], memT).then_inc(in_mem, 16)
            act.dma_start(cst[:], consts).then_inc(in_cst, 16)
            act.dma_start(par[:], params).then_inc(in_par, 16)
            act.dma_start(x_raw[:], xT).then_inc(in_x, 16)
            act.dma_start(w2_sb[:], w2).then_inc(in_lora, 16)
            act.dma_start(a2_sb[:], a2).then_inc(in_lora, 16)
            act.dma_start(wgu_sb[:], wgu).then_inc(in_lora, 16)
            split_hi(act, Tile(0, 0))
            act.wait_ge(in_mem, 16)
            mem_norm.act(act)
            act.wait_ge(in_x, 16)
            x_norm.act(act)
            act_lam(act)
            act_copy_phase(act, "mem_kv", mkv, ACT.Copy, mem_out)
            act_shift(act)
            act_copy_phase(act, "silu", sg, ACT.Silu, silu_out)
            act_copy_phase(act, "plain", pl, ACT.Copy, plain_out)
            act_attn(act)
            act_kk(act)
            act_rwkv(act)
            act_gn(act)
            act_merge(act)
            act_split_phase(act, "wout1")
            act.wait_ge(wout1_out, KT)
            act.wait_ge(in_meta, 16)
            norm1.act(act)
            act_copy_phase(act, "gpool", PO, ACT.Sigmoid, gpool_out)
            act_copy_phase(act, "gelu", HL, ACT.Gelu_apprx_tanh, gelu_out)
            act_pool(act)
            act_lru(act)
            act_glru(act)
            act_split_phase(act, "wout2")
            act.wait_ge(wout2_out, KT)
            norm2.act(act)
            mlp2.act(act)
            act.wait_ge(mlp2.out, KT * FF_GROUPS)
            final.act(act)
            act_conv3(act)
            act_copy_phase(act, "gla_r", sr, ACT.Silu, sr_out)
            act_copy_phase(act, "gla_p", gp, ACT.Copy, gp_out)
            act_gla(act)
            act_split_phase(act, "wout3")
            ln1.act(act)
            mlp3.act(act)
            ln2.act(act)

        @block.vector
        def _(v):
            split_lo(v, Tile(0, 0))
            v.wait_ge(in_cst, 16)
            v.wait_ge(in_par, 16)
            mem_norm.dve(v)
            x_norm.dve(v)
            dve_lam(v)
            dve_split_phase(v, "mem_kv")
            dve_shift(v)
            dve_split_phase(v, "silu")
            dve_split_phase(v, "plain")
            dve_attn(v)
            dve_kk(v)
            dve_rwkv(v)
            dve_gn(v)
            dve_merge(v)
            dve_wout1(v)
            norm1.dve(v)
            dve_split_phase(v, "gpool")
            dve_split_phase(v, "gelu")
            dve_pool(v)
            dve_lru(v)
            dve_glru(v)
            dve_add_phase(v, "wout2", x2, 1.0, wout2_out)
            norm2.dve(v)
            mlp2.dve(v)
            final.dve(v)
            dve_conv3(v)
            dve_split_phase(v, "gla_r")
            dve_split_phase(v, "gla_p")
            dve_gla(v)
            dve_add_phase(v, "wout3", X3, ALPHA3, wout3_out)
            ln1.dve(v)
            mlp3.dve(v)
            ln2.dve(v)

        @block.tensor
        def _(pe):
            pe.wait_ge(in_cst, 16)
            mem_norm.pe(pe)
            x_norm.pe(pe)
            plain_phase(pe, "mem_kv", mem_hl, mem_out, before=lambda k: mem_norm.ready(pe, k))
            plain_phase(pe, "shift", hx, shift_copied, before=lambda k: x_norm.ready(pe, k),
                        entry=lambda t: pe.wait_ge(mem_out, COUNT["mem_kv"] - 1 + t))
            plain_phase(pe, "silu", hx, silu_out, entry=lambda t: pe.wait_ge(shift_copied, COUNT["shift"] - 1 + t))
            plain_phase(pe, "plain", hx, plain_out, entry=lambda t: pe.wait_ge(silu_out, COUNT["silu"] - 1 + t))
            pe_attn(pe)
            pe_kk(pe)
            pe_rwkv(pe)
            pe_gn(pe)
            pe_merge(pe)
            pe.wait_ge(mg_lo, KT)
            plain_phase(pe, "wout1", mg, wout1_out)
            norm1.pe(pe)
            plain_phase(pe, "gpool", u1, gpool_out, before=lambda k: norm1.ready(pe, k))
            plain_phase(pe, "gelu", u1, gelu_out, entry=lambda t: pe.wait_ge(gpool_out, KT - 1 + t))
            pe_pool(pe)
            pe_lru(pe)
            plain_phase(pe, "glru", u1, glru_out, entry=lambda t: pe.wait_ge(lru_gate, 3 * 8 + t + 1))
            pe.wait_ge(mg2_lo, KT)
            plain_phase(pe, "wout2", mg2, wout2_out)
            norm2.pe(pe)
            mlp2.pe(pe, lambda k: norm2.ready(pe, k))
            final.pe(pe)
            pe_conv3(pe)
            def conv_out(t):
                pe.wait_ge(ub_out, 2 * C3_T)
            plain_phase(pe, "gla_r", xh3, sr_out, entry=conv_out)
            plain_phase(pe, "gla_p", xh3, gp_out, entry=lambda t: pe.wait_ge(sr_out, GLA_VT - 1 + t))
            pe_gla(pe)
            need(pe, g_v, "olo1")
            plain_phase(pe, "wout3", mix, wout3_out)
            pe.wait_ge(wout3_out, KT)
            ln1.pe(pe)
            mlp3.pe(pe, lambda k: ln1.ready(pe, k))
            pe.wait_ge(mlp3.out, KT * FF_GROUPS)
            ln2.pe(pe)


def full_tiles(w):
    n = w.shape[1] // P
    return w.reshape(2, HALF, P, n, P).transpose(3, 0, 2, 1, 4).reshape(n, 2, P, HALF, P)


def stream_of(a):
    w_in, w_in2, w_in3 = a["w_in"][0], a["w_in_2"][0], a["w_in_3"][0]
    order = [h for pair in Q_PAIRS for h in pair]

    def by_pairs(w):
        return w.reshape(D, A_HEADS, HD)[:, order].reshape(D, A_HEADS * HD)
    aq, ak, av, ag, rs, rg, xq, xg, mg = np.split(w_in, np.cumsum([768, 256, 256, 768, 2560, 768, 512, 512]), axis=1)
    wo = np.concatenate([a["attn_w_o"][0].reshape(A_HEADS, HD, D)[order].reshape(A_HEADS * HD, D),
                         a["rwkv_w_o"][0], a["x_w_o"][0]], 0)
    gates = full_tiles(mg).reshape(N_BRANCH, KT, 2, P, HALF, P)
    merge1 = np.concatenate([gates, full_tiles(wo)[None]], 0).transpose(1, 0, 2, 3, 4, 5)
    v_pool, v_lru, v_gelu, g_pool, g_lru = np.split(w_in2, 5, axis=1)
    pool_w = a["pool_w_2"][0].reshape(4, 4, P, 2, 2, P).transpose(0, 3, 2, 4, 1, 5).reshape(4, 1, 2, P, HALF, P)
    lru_w = np.stack([a["gate_a_w_2"][0], a["gate_x_w_2"][0]], 0).reshape(2, 4, 2, 2, P, 2, P)
    lru_w = lru_w.transpose(1, 2, 4, 0, 5, 3, 6).reshape(4, 1, 2, P, HALF, P)

    def with_own(w, own):
        return np.concatenate([full_tiles(w).reshape(4, 4, 2, P, HALF, P), own], 1)
    b3, c3, u3, q3, k3, v3, r3, z3 = np.split(w_in3, np.cumsum([1024, 1024, 1024, 512, 512, 1024, 1024]), axis=1)
    z3 = np.concatenate([z3, np.zeros((D, P - z3.shape[1]), z3.dtype)], 1)
    conv3 = np.stack([full_tiles(c3), full_tiles(u3), full_tiles(b3)], 0).transpose(1, 0, 2, 3, 4, 5)

    def mlp(w1, w2):
        up = full_tiles(w1).reshape(FF_GROUPS, KT, 2, P, HALF, P)
        down = np.stack([full_tiles(w) for w in w2.reshape(FF_GROUPS, D, D)], 0)
        return np.concatenate([up, down], 1)
    parts = [full_tiles(a["x_w_kv"][0]), full_tiles(rs), full_tiles(np.concatenate([by_pairs(ag), rg, xg], 1)),
             full_tiles(np.concatenate([by_pairs(aq), ak, xq, av], 1)), merge1, full_tiles(a["w_out"][0]),
             full_tiles(g_pool), full_tiles(v_gelu), with_own(v_pool, pool_w), with_own(v_lru, lru_w),
             full_tiles(g_lru), full_tiles(a["w_out_2"][0]), mlp(a["mlp_w1_2"][0], a["mlp_w2_2"][0]),
             conv3, full_tiles(r3), full_tiles(np.concatenate([z3, q3, k3, v3], 1)), full_tiles(a["w_out_3"][0]),
             mlp(a["w_ff_up_3"][0], a["w_ff_down_3"][0]), np.zeros((2, P, HALF, P), w_in.dtype)]
    return np.concatenate([p.reshape(-1, P, HALF, P) for p in parts], 0)


def params_of(a):
    named = {"mu": "rwkv_mu", "k_k": "rwkv_k_k", "k_a": "rwkv_k_a", "r_k": "rwkv_r_k", "w0": "rwkv_w0", "a0": "rwkv_a0",
             "ln_w": "rwkv_ln_w", "ln_b": "rwkv_ln_b", "q_g": "attn_q_norm_g", "k_g": "attn_k_norm_g",
             "xq_g": "x_q_norm_g", "xk_g": "x_k_norm_g", "norm1_g": "norm1_g_2", "pool_scale": "pool_scale_2",
             "conv_w2": "conv_w_2", "conv_b2": "conv_b_2", "gate_a_b": "gate_a_b_2", "gate_x_b": "gate_x_b_2",
             "lam": "lru_lambda_2", "norm2_g": "norm2_g_2", "final_g": "final_g_2", "conv_w3": "conv_w_3",
             "conv_g3": "conv_norm_g_3", "gate_bias3": "gate_bias_3", "gla_g3": "gla_norm_g_3", "ln1_g": "ln1_g_3",
             "ln1_b": "ln1_b_3", "ln2_g": "ln2_g_3", "ln2_b": "ln2_b_3"}
    cols = []
    for name, n in PARAMS:
        if name == "sink":
            pairs = a["attn_sink"][0][np.array(Q_PAIRS)]
            c = np.broadcast_to(np.repeat(pairs.reshape(-1), NB)[None], (P, n))
        else:
            c = a[named.get(name, name)].reshape(-1)
            c = np.concatenate([c, c]) if c.shape[0] == HD else c
            c = c.reshape(n, P).T
        cols.append(c)
    return np.ascontiguousarray(np.concatenate(cols, 1))


def channel_major(x):
    return np.ascontiguousarray(x.T.reshape(KT, P, -1).transpose(1, 0, 2))


def arrays_of(inputs):
    a = {k: np.asarray(v) for k, v in inputs.items()}
    return {
        "stream": stream_of(a), "consts": constants(), "params": params_of(a),
        "w2": np.ascontiguousarray(a["rwkv_w2"][0].reshape(P, PAIRS, P)),
        "a2": np.ascontiguousarray(a["rwkv_a2"][0].reshape(P, PAIRS, P)),
        "wgu": np.ascontiguousarray(a["w_gate_up_3"][0].reshape(16, GLA_H, P)),
        "memT": channel_major(a["mem"][0]), "xT": channel_major(a["x"][0]), "metaT": channel_major(a["meta_tokens_2"]),
    }


def kernel(**inputs):
    import concourse.bacc as bacc
    from concourse.bass_utils import run_bass_kernel_spmd

    nc = bacc.Bacc("TRN2", target_bir_lowering=False, num_devices=1)
    arrays = arrays_of(inputs)
    args = [nc.dram_tensor(n, x.shape, mybir.dt.from_np(x.dtype), kind="ExternalInput").ap() for n, x in arrays.items()]
    out = nc.dram_tensor("out", (P, KT, T), mybir.dt.float32, kind="ExternalOutput").ap()
    build(nc, *args, out)
    got = run_bass_kernel_spmd(nc, [arrays], core_ids=[0]).results[0]["out"]
    return got.transpose(2, 1, 0).reshape(1, T, D)
```

```python
import numpy as np
import concourse.bass as bass
from concourse import mybir
from contextlib import ExitStack

P = 128
D = 2048
KT = D // P
T = 256
META = 16
TM = META + T
NB = T // P
HALF = KT // 2
UNIT = HALF * P
RING = 4

A_HEADS, A_KV, HD = 12, 4, 64
A_T = A_HEADS * HD // P
KV_T = A_KV * HD // P
R_HEADS = 12
PAIRS = R_HEADS * HD // P
CH = 64
NCH = T // CH
LEVELS = 6
X_HEADS = 4
X_T = X_HEADS
N_BRANCH = 3
WINDOW = 128
POOL_WINDOWS = (2, 4, 8, 16)
POOL_T = D // P // len(POOL_WINDOWS)
CONV2 = 4
LRU_HEADS = 8
FF_GROUPS = 4
CONV3 = 3
C3_T = 8
GLA_H = 4
GLA_VT = 8
HALF_DECAY = 0.5 * float(np.exp(-0.5))
ALPHA3 = 2.0 ** 0.25
EPS = 1e-6
GN_EPS = 64e-5
LN_EPS = 1e-5
GATE_TAU = 16.0
NEG = -1e30

Q_PAIRS = [(0, 3), (1, 4), (2, 5), (6, 9), (7, 10), (8, 11)]

STREAM = [("plain", 14), ("mem_kv", 8), ("attn", 30), ("silu", 6), ("merge1", 64), ("wout1", 16),
          ("gpool", 16), ("gelu", 16), ("pool", 20), ("lru", 20), ("glru", 16), ("wout2", 16),
          ("ff2", 128), ("conv3", 24), ("gla_r", 8), ("gla_p", 17), ("wout3", 16), ("ff3", 128)]
FIRST = {}
N_TILES = 0
for _name, _n in STREAM:
    FIRST[_name] = N_TILES
    N_TILES += _n
COUNT = dict(STREAM)
PAD = RING // 2
N_UNITS = 2 * (N_TILES + PAD)

SHIFT_T = 3 * PAIRS + 2
ATTN_BEFORE = 6
ATTN_UNITS = [[("silu", u if u < A_T else A_T + PAIRS + u - A_T), ("shift", ATTN_BEFORE + u)]
              + ([("shift", ATTN_BEFORE + A_T + X_T + u)] if ATTN_BEFORE + A_T + X_T + u < SHIFT_T else []) for u in range(A_T + X_T)]
ATTN_TILES = [("shift", k) for k in range(ATTN_BEFORE)] + [x for unit in ATTN_UNITS for x in unit]

OWN = POOL_T
OWN_ORDER = [(0, j) for j in range(POOL_T)] + [
    x for g in range(1, 4) for x in [(g, 0), (g - 1, OWN), (g, 1), (g, 2), (g, 3)]] + [(3, OWN)]

PARAMS = [("mem_norm_g", 16), ("norm_g", 16), ("mu", 20), ("k_k", 6), ("k_a", 6), ("r_k", 6),
          ("w0", 12), ("a0", 12), ("ln_w", 6), ("ln_b", 6), ("gate_b", 48), ("q_g", 1), ("k_g", 1),
          ("xq_g", 1), ("xk_g", 1), ("sink", 24), ("norm1_g", 16), ("pool_scale", 16),
          ("conv_w2", 64), ("conv_b2", 16), ("gate_a_b", 16), ("gate_x_b", 16), ("lam", 16),
          ("norm2_g", 16), ("final_g", 16), ("conv_w3", 24), ("conv_g3", 8), ("gate_bias3", 4),
          ("gla_g3", 8), ("ln1_g", 16), ("ln1_b", 16), ("ln2_g", 16), ("ln2_b", 16)]
PCOL = {}
N_PARAM = 0
for _name, _n in PARAMS:
    PCOL[_name] = N_PARAM
    N_PARAM += _n

CONSTS = [("ident", 128), ("ones", 128), ("bdones", 128), ("rot", 128), ("istack", 64),
          ("cos", 256), ("sin", 256), ("amask", 512), ("strict_up", 128), ("strict_lo", 128),
          ("incl_up", 128), ("incl_lo", 128), ("levels", 768), ("run_up", 256), ("run_lo", 256)]
CCOL = {}
N_CONST = 0
for _name, _n in CONSTS:
    CCOL[_name] = N_CONST
    N_CONST += _n


def constants():
    f = np.float32
    i = np.arange(P)
    head, s = i // CH, i % CH
    same = head[:, None] == head[None, :]
    rot = np.zeros((P, P), f)
    for m in range(P):
        j = m % HD
        if j < HD // 2:
            rot[m + HD // 2, m] = -1.0
        else:
            rot[m - HD // 2, m] = 1.0
    half = HD // 2
    inv = np.float32(10000.0) ** (-np.arange(half, dtype=f) / np.float32(half))
    ang = np.arange(T, dtype=f)[None, :] * inv.astype(f)[:, None]
    cos, sin = (np.tile(fn(ang).astype(f), (4, 1)) for fn in (np.cos, np.sin))
    key = np.arange(T)
    amask = np.stack([np.where(np.abs(key[None, :] - (i[:, None] + b * P)) <= WINDOW, 0.0, NEG)
                      for b in range(NB)], 1)
    up = same & (s[:, None] < s[None, :])
    incl = same & (s[:, None] <= s[None, :])
    levels = [same & (s[:, None] >> (l + 1) == s[None, :] >> (l + 1))
              & (s[:, None] >> l != s[None, :] >> l) for l in range(LEVELS)]
    t = np.arange(T)
    table = {
        "ident": np.eye(P), "ones": np.ones((P, P)), "bdones": same, "rot": rot,
        "istack": (s[:, None] == np.arange(CH)[None, :]), "cos": cos, "sin": sin,
        "amask": amask.reshape(P, NB * T), "strict_up": up, "strict_lo": up.T, "incl_up": incl,
        "incl_lo": incl.T, "levels": np.concatenate(levels, 1),
        "run_up": np.tile(t % CH != 0, (P, 1)), "run_lo": np.tile(t % CH != CH - 1, (P, 1)),
    }
    return np.ascontiguousarray(np.concatenate([table[n].astype(f) for n, _ in CONSTS], 1))


class Steps:

    def __init__(self, sem, names):
        self.sem, self.names = sem, list(names)
        self.place = {n: k for k, n in enumerate(self.names)}
        assert len(self.place) == len(self.names), "a step's name stands twice"
        self.cursor = 0

    def at(self, name, it=None):
        n = self.place[name] + 1
        return n if it is None else it * len(self.names) + n

    def done(self, ins, name):
        assert self.names[self.cursor % len(self.names)] == name, (name, self.names[self.cursor % len(self.names)])
        self.cursor += 1
        ins.then_inc(self.sem, 1)


def need(eng, steps, name, it=None):
    eng.wait_ge(steps.sem, steps.at(name, it))


class Tile:

    def __init__(self, first, t, loops=()):
        self.first, self.t, self.loops = first, t, tuple(loops)

    def sum(self, c, m):
        for reg, per in self.loops:
            c = reg * (per * m) + c
        return c

    def units(self, c):
        return self.sum(2 * (self.first + self.t) + c, 2)

    def local(self, m=1, c=0):
        return self.sum(m * self.t + c, m)

    def later(self):
        return Tile(self.first, self.t + RING // 2, self.loops)

    @property
    def parity(self):
        return (self.first + self.t) % 2

    @property
    def start(self):
        return not self.loops and self.first + self.t < 2


def run_tiles(eng, phase, per, body, loops=(), first=None, count=None, peel=1):
    first = FIRST[phase] if first is None else first
    count = COUNT[phase] if count is None else count
    rounds = count // per
    for j in range(per * peel):
        body(Tile(first, j, loops))
    with eng.Fori(peel, rounds) as i:
        for j in range(per):
            body(Tile(first, j, tuple(loops) + ((i, per),)))
    for t in range(rounds * per, count):
        body(Tile(first, t, loops))


def build(nc, stream, consts, params, w2, a2, wgu, memT, xT, metaT, out):
    F, R = mybir.dt.float32, mybir.dt.float32r
    ACT, ALU = mybir.ActivationFunctionType, mybir.AluOpType
    AX = mybir.AxisListType
    ctx = ExitStack()
    with ctx:
        def sem(name):
            return ctx.enter_context(nc.semaphore(name))

        K = 1024
        base = -(-nc.sbuf_base // 64) * 64
        slab = 206 * K
        ctx.enter_context(nc.sbuf_tensor("slab", [P, slab // 4], F, align_bytes=64))

        def at(name, offset, shape, dtype=F):
            size = 4 * int(np.prod(shape[1:]))
            assert offset + size <= slab, (name, offset + size - slab)
            return nc.alloc_sbuf_tensor_at(name, list(shape), dtype, offset=base + offset)

        raw = at("raw", 0, [P, RING, HALF, P])
        w_hi = at("w_hi", 16 * K, [P, RING, HALF, P], R)
        w_lo = at("w_lo", 32 * K, [P, RING, HALF, P], R)
        cst = at("cst", 48 * K, [P, N_CONST])
        par = at("par", 62 * K, [P, N_PARAM])
        w2_sb = at("w2_sb", 64 * K, [P, PAIRS, P])
        a2_sb = at("a2_sb", 67 * K, [P, PAIRS, P])
        wgu_sb = at("wgu_sb", 70 * K, [16, GLA_H, P])
        lam_sb = at("lam_sb", 72 * K, [P, 6, 16])
        hw_sb = at("hw_sb", 72 * K + 384, [P, 24])
        RSTD = 72 * K + 512
        B = 74 * K
        banks = [ctx.enter_context(nc.psum_tensor(f"bank{b}", [P, 512], F)) for b in range(8)]

        def const(name):
            return cst[:, CCOL[name]:CCOL[name] + dict(CONSTS)[name]]

        def col(name, k):
            return par[:, PCOL[name]:PCOL[name] + dict(PARAMS)[name]][:, bass.ds(k, 1)]

        raw_in = [sem(f"raw_in{k}") for k in range(RING)]
        hi_ready, lo_ready, units_used = sem("hi_ready"), sem("lo_ready"), sem("units_used")

        def split_hi(act, tile, units=(0, 1)):
            if not tile.loops and tile.first + tile.t >= N_TILES + PAD:
                return
            for k in units:
                slot = (2 * tile.parity + k) % RING
                g = tile.first + tile.t
                act.wait_ge(raw_in[slot], tile.sum(16 * (g // 2 + 1), 8))
                if not tile.start:
                    act.wait_ge(units_used, tile.units(k + 1 - RING))
                nc.scalar.activation(w_hi[:, slot], raw[:, slot], ACT.Copy).then_inc(hi_ready, 1)

        def split_lo(v, tile, units=(0, 1)):
            if not tile.loops and tile.first + tile.t >= N_TILES + PAD:
                return
            for k in units:
                slot = (2 * tile.parity + k) % RING
                v.wait_ge(hi_ready, tile.units(k + 1))
                nc.vector.tensor_tensor(w_lo[:, slot], raw[:, slot], w_hi[:, slot].bitcast(F),
                                        ALU.subtract).then_inc(lo_ready, 1)

        def tile_done(eng, tile):
            eng.wait_ge(units_used, tile.units(2))

        def product(dst, moving, slot, j, kt, first, last, n=T):
            hi, lo = moving[:, kt, 0, TM - n:] if moving.shape[-1] == TM else moving[:, kt, 0], \
                moving[:, kt, 1, TM - n:] if moving.shape[-1] == TM else moving[:, kt, 1]
            nc.tensor.matmul(dst, w_hi[:, slot, j], hi, start=first, stop=False)
            nc.tensor.matmul(dst, w_hi[:, slot, j], lo, start=False, stop=False)
            return nc.tensor.matmul(dst, w_lo[:, slot, j], hi, start=False, stop=last)

        def full_tile(pe, tile, moving, n=T, before=None):
            dst = banks[tile.parity][:, 0:n]
            for k in range(2):
                if before is not None:
                    before(k)
                pe.wait_ge(lo_ready, tile.units(k + 1))
                for j in range(HALF):
                    kt = HALF * k + j
                    last = product(dst, moving, (2 * tile.parity + k) % RING, j, kt,
                                   kt == 0, kt == KT - 1, n)
                last.then_inc(units_used, 1)

        def plain_phase(pe, phase, moving, bank_free, n=T, before=None, entry=None, after=None, after_t=0):
            def body(tile):
                if tile.loops or tile.t >= 2:
                    pe.wait_ge(bank_free, tile.local(1, -1))
                elif entry is not None:
                    entry(tile.t)
                first = not tile.loops and tile.t == 0
                full_tile(pe, tile, moving, n, before if first else None)
                if not tile.loops and tile.t == after_t and after is not None:
                    after()
            run_tiles(pe, phase, 2, body)

        def hooked(tile, hooks):
            if hooks and not tile.loops and tile.t in hooks:
                hooks[tile.t]()

        in_cst, in_par, in_lora, in_res, in_meta, stored = (
            sem(n) for n in ("in_cst", "in_par", "in_lora", "in_res", "in_meta", "stored"))
        in_x, in_mem = ([sem(f"{n}{q}") for q in range(4)] for n in ("in_x", "in_mem"))

        class Norm:
            def __init__(self, name, src, n, g, dst, scratch, rstd=RSTD):
                self.src, self.n, self.g, self.dst = src, n, g, dst
                self.sq, self.acc, self.std = (at(f"{name}_{b}", scratch + 4 * n * k, [P, n])
                                               for k, b in enumerate(("sq", "acc", "std")))
                self.rstd = at(name + "_rstd", rstd, [P, n])
                self.hi, self.lo, self.sums, self.stat, self.rooted, self.known = (
                    sem(f"{name}_{b}") for b in ("hi", "lo", "sums", "stat", "rooted", "known"))

            def act_tile(self, act, kt):
                nc.scalar.activation(self.dst[:, kt, 0], self.src[:, kt], ACT.Identity, scale=col(self.g, kt)).then_inc(self.hi, 1)

            def dve_tile(self, v, kt, count):
                v.wait_ge(self.hi, count)
                nc.vector.scalar_tensor_tensor(self.dst[:, kt, 1], self.src[:, kt], col(self.g, kt),
                                               self.dst[:, kt, 0].bitcast(F), ALU.mult, ALU.subtract).then_inc(self.lo, 1)

            def pool_start(self, pool):
                nc.gpsimd.memset(self.acc[:], 0.0).then_inc(self.sums, 1)

            def pool_tile(self, pool, kt):
                pool.wait_ge(self.sums, kt * 2 + 1)
                nc.gpsimd.tensor_tensor(self.sq[:], self.src[:, kt], self.src[:, kt], ALU.mult).then_inc(self.sums, 1)
                pool.wait_ge(self.sums, kt * 2 + 2)
                nc.gpsimd.tensor_tensor(self.acc[:], self.acc[:], self.sq[:], ALU.add).then_inc(self.sums, 1)

            def pool(self, pool, src_ready, before=0):
                pool.wait_ge(src_ready, before + 1)
                self.pool_start(pool)
                with pool.Fori(0, KT) as kt:
                    pool.wait_ge(src_ready, kt + (before + 1))
                    self.pool_tile(pool, kt)

            def pe(self, pe):
                pe.wait_ge(self.sums, 2 * KT + 1)
                nc.tensor.matmul(banks[2][:, 0:self.n], const("ones"), self.acc[:], start=True, stop=True).then_inc(self.stat, 1)

            def act_root(self, act):
                act.wait_ge(self.stat, 1)
                nc.scalar.activation(self.std[:], banks[2][:, 0:self.n], ACT.Sqrt, bias=EPS, scale=1.0 / D).then_inc(self.rooted, 1)

            def dve_rstd(self, v):
                v.wait_ge(self.rooted, 1)
                nc.vector.reciprocal(self.rstd[:], self.std[:]).then_inc(self.known, 1)
                v.wait_ge(self.known, 1)

            def ready(self, pe, k):
                pe.wait_ge(self.lo, HALF * (k + 1))

        hx = at("hx", B, [P, KT, 2, T], R)
        sg = at("sg", B + 32 * K, [P, KT, T])
        pl = at("pl", B + 48 * K, [P, 14, T])
        rkv = at("rkv", B + 62 * K, [P, 20, T])
        mkv = at("mkv", B + 82 * K, [P, 8, T])
        Z = B + 90 * K
        mem_raw = at("mem_raw", B + 62 * K, [P, KT, T])
        mem_hl = at("mem_hl", Z, [P, KT, 2, T], R)
        x_raw = at("x_raw", B + 32 * K, [P, KT, T])
        x_norm = Norm("x_norm", x_raw, T, "norm_g", hx, B + 122 * K)
        mem_norm = Norm("mem_norm", mem_raw, T, "mem_norm_g", mem_hl, B + 126 * K, B + 129 * K)

        mem_out, plain_out, silu_out, silu_pre = (sem(n) for n in ("mem_out", "plain_out", "silu_out", "silu_pre"))
        sl = at("sl", B + 130 * K, [P, 2, T])

        def dve_scaled_phase(v, phase, norm, dst, out_sem, hooks=None, late=None):
            rstd = norm.rstd[:, norm.n - T:]

            def body(tile):
                hooked(tile, hooks)
                tile_done(v, tile)
                nc.vector.tensor_tensor(dst[:, tile.local()], banks[tile.parity][:, 0:T], rstd, ALU.mult).then_inc(out_sem, 1)
                split_lo(v, tile.later())
                hooked(tile, late)
            run_tiles(v, phase, 2, body)

        def dve_pre_phase(v, phase, norm, tmp, pre_sem, out_sem, hooks=None):
            rstd = norm.rstd[:, norm.n - T:]

            def body(tile):
                hooked(tile, hooks)
                tile_done(v, tile)
                if tile.loops or tile.t >= 2:
                    v.wait_ge(out_sem, tile.local(1, -1))
                nc.vector.tensor_tensor(tmp[:, tile.t % 2], banks[tile.parity][:, 0:T], rstd, ALU.mult).then_inc(pre_sem, 1)
                split_lo(v, tile.later())
            run_tiles(v, phase, 2, body)

        def act_func_phase(act, phase, tmp, pre_sem, dst, func, out_sem, hooks=None):
            def body(tile):
                split_hi(act, tile.later())
                hooked(tile, hooks)
                act.wait_ge(pre_sem, tile.local(1, 1))
                nc.scalar.activation(dst[:, tile.local()], tmp[:, tile.t % 2], func).then_inc(out_sem, 1)
            run_tiles(act, phase, 2, body)

        def act_split_phase(act, phase, hooks=None):
            def body(tile):
                split_hi(act, tile.later())
                hooked(tile, hooks)
            run_tiles(act, phase, 2, body, peel=0 if hooks is None else 1)

        pad = [at(f"pad{b}", Z + K * 26 + b * 1088, [P, T + 2]) for b in range(2)]
        sh = [at(f"sh{b}", Z + K * 26 + 2176 + b * 1024, [P, T]) for b in range(2)]
        sa = at("sa", Z + 38 * K, [P, 2, T])
        pads_zero, shift_copied, shift_step, agate_pre, agate_out = (
            sem(n) for n in ("pads_zero", "shift_copied", "shift_step", "agate_pre", "agate_out"))

        def beside(k):
            kind, m = ATTN_TILES[k]
            return Tile(FIRST["attn"], k), kind, m, sum(x[0] == kind for x in ATTN_TILES[:k])

        def act_beside(act, tiles):
            for k in tiles:
                tile, kind, m, n = beside(k)
                split_hi(act, tile.later(), (0,))
                if kind == "silu":
                    act.wait_ge(agate_pre, n + 1)
                    nc.scalar.activation(sg[:, m], sa[:, n % 2], ACT.Silu).then_inc(agate_out, 1)
                split_hi(act, tile.later(), (1,))

        def dve_beside(v, tiles):
            for k in tiles:
                tile, kind, m, n = beside(k)
                tile_done(v, tile)
                psum = banks[tile.parity][:, 0:T]
                if kind == "silu":
                    if n >= 2:
                        v.wait_ge(agate_out, n - 1)
                    nc.vector.tensor_tensor(sa[:, n % 2], psum, x_norm.rstd[:], ALU.mult).then_inc(agate_pre, 1)
                    split_lo(v, tile.later())
                    continue
                if n == 0:
                    for b in range(2):
                        nc.vector.memset(pad[b][:], 0.0).then_inc(pads_zero, 1)
                    v.wait_ge(pads_zero, 2)
                p, s = pad[n % 2], sh[n % 2]
                nc.vector.tensor_tensor(p[:, 1:T + 1], psum, x_norm.rstd[:], ALU.mult).then_inc(shift_copied, 1)
                v.wait_ge(shift_copied, n + 1)
                nc.vector.tensor_tensor(s[:], p[:, 0:T], p[:, 2:T + 2], ALU.add).then_inc(shift_step, 1)
                v.wait_ge(shift_step, 3 * n + 1)
                nc.vector.scalar_tensor_tensor(s[:], s[:], 0.5, p[:, 1:T + 1], ALU.mult, ALU.subtract).then_inc(shift_step, 1)
                v.wait_ge(shift_step, 3 * n + 2)
                nc.vector.scalar_tensor_tensor(rkv[:, m], s[:], col("mu", m), p[:, 1:T + 1], ALU.mult, ALU.add).then_inc(shift_step, 1)
                split_lo(v, tile.later())

        def pe_beside(pe, tiles):
            for k in tiles:
                tile = beside(k)[0]
                if k < 2:
                    pe.wait_ge(mem_out, COUNT["mem_kv"] - 1 + k)
                else:
                    _, kind, _, n = beside(k - 2)
                    pe.wait_ge(agate_pre if kind == "silu" else shift_copied, n + 1)
                full_tile(pe, tile, hx)

        def unit_tiles(u):
            first = ATTN_BEFORE + sum(len(x) for x in ATTN_UNITS[:u])
            return list(range(first, first + len(ATTN_UNITS[u])))

        sq_at = at("sq_at", Z, [P, 16, T])
        rs_at = sq_at
        tmp_at = at("tmp_at", Z, [P, 8, T])
        vtok = at("vtok", Z + 32 * K, [P, NB, KV_T * P])
        vmtok = at("vmtok", Z + 34 * K, [P, NB, X_T * P])
        U_ALL = range(A_T + X_T)
        sc = [at(f"sc{b}", Z + 4 * K * b, [P, 4, T]) for b in range(2)]
        pr = [at(f"pr{b}", Z + 8 * K + 4 * K * b, [P, 4, T]) for b in range(2)]
        pt = [at(f"pt{b}", Z + 16 * K + 4 * K * b, [P, 4, T]) for b in range(2)]
        mx = at("mx", Z + 24 * K, [P, 10, 4])
        ngm = at("ngm", Z + 24 * K + 160, [P, 10, 4])
        sm = at("sm", Z + 24 * K + 320, [P, 10, 4])
        es = at("es", Z + 24 * K + 480, [P, 10, 4])
        rd = at("rd", Z + 24 * K + 640, [P, 10, 4])
        at_src = [(pl, k) for k in range(12)] + [(mkv, k) for k in range(4)]
        at_g = ["q_g"] * 6 + ["k_g"] * 2 + ["xq_g"] * 4 + ["xk_g"] * 4
        def exp_names(u):
            return [f"ex{u}"] * (u < len(U_ALL)) + [f"sk{u}"] * (u < A_T)
        at_a = Steps(sem("attn_act"), ["sq0", "sq1", "sq2"] + [f"std{b}" for b in range(8)] + ["vt", "vm0", "vm1"]
                     + exp_names(0) + [n for u in U_ALL for n in exp_names(u + 1) + [f"pt{u}"]])

        def attn_dve_names():
            names = [f"rstd{b}" for b in range(8)] + ["norm"]
            names += [f"{s}{b}" for b in range(4) for s in ("sin", "cos", "rope")]
            def soft(u):
                return [f"{s}{u}" for s in (("mask", "max", "msk", "neg", "dsk") if u < A_T else ("max", "neg"))]
            names += soft(0)
            for u in U_ALL:
                names += soft(u + 1) if u + 1 < len(U_ALL) else []
                names += ([f"den{u}"] if u < A_T else []) + [f"rd{u}", f"pr{u}", f"y{u}"]
            return names
        at_v = Steps(sem("attn_dve"), attn_dve_names())
        at_p = Steps(sem("attn_pe"), [f"stat{b}" for b in range(8)] + ["vt", "vm0", "vm1"] + [f"rot{b}" for b in range(4)]
                     + ["sc0"] + [n for u in U_ALL for n in (f"sc{u + 1}", f"tr{u}", f"pv{u}") if n != f"sc{len(U_ALL)}"])

        def heads(u):
            return [(HD * h, HD, b) for h in range(2) for b in range(NB)] if u < A_T else [(0, P, b) for b in range(NB)]

        def sc_bank(u, h):
            return banks[2 + h] if u < A_T else banks[2 + u % 2]

        def pt_bank(u, h):
            return banks[4 + h] if u < A_T else banks[4 + u % 2]

        def pv_bank(u):
            return banks[6 + u % 2]

        STAT_BANK = [2, 3, 4, 5, 6, 7, 2, 3]
        VT_BANK, VM_BANK, ROT_BANK = 4, (5, 6), (2, 3, 7, 4)

        def act_attn(act):
            need_sem = plain_out
            act.wait_ge(need_sem, COUNT["plain"])
            act.wait_ge(mem_out, COUNT["mem_kv"])
            at_a.done(nc.scalar.activation(sq_at[:, 0:8], pl[:, 0:8], ACT.Square), "sq0")
            at_a.done(nc.scalar.activation(sq_at[:, 8:12], pl[:, 8:12], ACT.Square), "sq1")
            at_a.done(nc.scalar.activation(sq_at[:, 12:16], mkv[:, 0:4], ACT.Square), "sq2")
            act_beside(act, (0, 1))
            for b in range(8):
                need(act, at_p, f"stat{b}")
                dim = HD if b < 4 else P
                at_a.done(nc.scalar.activation(rs_at[:, 2 * b:2 * b + 2], banks[STAT_BANK[b]][:].rearrange("p (a t) -> p a t", a=2),
                                               ACT.Sqrt, bias=EPS, scale=1.0 / dim), f"std{b}")
            act_beside(act, [2])
            need(act, at_p, "vt")
            at_a.done(nc.scalar.activation(vtok[:], banks[VT_BANK][:].rearrange("p (b c) -> p b c", b=NB), ACT.Copy), "vt")
            for b in range(NB):
                need(act, at_p, f"vm{b}")
                at_a.done(nc.scalar.activation(vmtok[:, b], banks[VM_BANK[b]][:], ACT.Copy), f"vm{b}")
            act_beside(act, range(3, ATTN_BEFORE))

            def exps(u):
                need(act, at_v, f"neg{u}")
                if u >= 2:
                    need(act, at_p, f"tr{u - 2}")
                for n in range(len(heads(u))):
                    src = sc[u % 2][:, n] if u < A_T else sc_bank(u, 0)[:, T * n:T * n + T]
                    last = nc.scalar.activation(pr[u % 2][:, n], src, ACT.Exp, bias=ngm[:, u, n:n + 1],
                                                scale=1.0 if u < A_T else P ** -0.5, accum_out=sm[:, u, n:n + 1])
                at_a.done(last, f"ex{u}")
                if u < A_T:
                    need(act, at_v, f"dsk{u}")
                    at_a.done(nc.scalar.activation(es[:, u], es[:, u], ACT.Exp), f"sk{u}")
            exps(0)
            for u in U_ALL:
                first, *others = unit_tiles(u)
                if u + 1 < len(U_ALL):
                    exps(u + 1)
                act_beside(act, [first])
                need(act, at_p, f"tr{u}")
                for h in range(2 if u < A_T else 1):
                    last = nc.scalar.activation(pt[u % 2][:, 2 * h:2 * h + 2],
                                                pt_bank(u, h)[:].rearrange("p (b q) -> p b q", b=NB), ACT.Copy)
                at_a.done(last, f"pt{u}")
                act_beside(act, others)

        def pe_attn(pe):
            pe_beside(pe, (0, 1))
            for b in range(8):
                need(pe, at_a, "sq0" if b < 4 else "sq1" if b < 6 else "sq2")
                if b >= 6:
                    need(pe, at_a, f"std{b - 6}")
                at_p.done(nc.tensor.matmul(banks[STAT_BANK[b]][:], const("bdones" if b < 4 else "ones"), sq_at[:, 2 * b:2 * b + 2],
                                           start=True, stop=True), f"stat{b}")
            pe_beside(pe, [2])
            need(pe, at_a, "std4")
            for b in range(NB):
                for c in range(KV_T):
                    o = (b * KV_T + c) * P
                    last = nc.tensor.transpose(banks[VT_BANK][:, o:o + P], pl[:, 12 + c, b * P:b * P + P], const("ident"))
            at_p.done(last, "vt")
            for b in range(NB):
                for c in range(X_T):
                    last = nc.tensor.transpose(banks[VM_BANK[b]][:, c * P:c * P + P], mkv[:, 4 + c, b * P:b * P + P], const("ident"))
                at_p.done(last, f"vm{b}")
            pe_beside(pe, [3])
            need(pe, at_v, "norm")
            need(pe, at_a, "vt")
            for b in range(4):
                at_p.done(nc.tensor.matmul(banks[ROT_BANK[b]][:], const("rot"), pl[:, 2 * b:2 * b + 2], start=True, stop=True), f"rot{b}")
            pe_beside(pe, range(4, ATTN_BEFORE))
            need(pe, at_v, "rope3")

            def scores(u):
                if u >= 2:
                    w = u - 1 if u < A_T or u == A_T else u - 2
                    if w < A_T:
                        need(pe, at_v, f"mask{w}")
                    else:
                        need(pe, at_a, f"ex{w}")
                elif u == 1:
                    need(pe, at_v, "mask0")
                for r, n, b in heads(u):
                    q = pl[r:r + n, u if u < A_T else 8 + u - A_T, b * P:b * P + P]
                    k = pl[r:r + n, A_T + u // 3, :] if u < A_T else mkv[:, u - A_T, :]
                    last = nc.tensor.matmul(sc_bank(u, r // HD)[:, b * T:b * T + T], q, k, start=True, stop=True)
                at_p.done(last, f"sc{u}")

            def values(u):
                first, *others = unit_tiles(u)
                pe_beside(pe, [first])
                need(pe, at_v, f"pr{u}")
                if u >= 1:
                    need(pe, at_a, f"pt{u - 1}")
                for n, (r, _, b) in enumerate(heads(u)):
                    for kb in range(NB):
                        o = kb * T + b * P
                        last = nc.tensor.transpose(pt_bank(u, r // HD)[:, o:o + P], pr[u % 2][:, n, kb * P:kb * P + P], const("ident"))
                at_p.done(last, f"tr{u}")
                pe_beside(pe, others[:1])
                need(pe, at_a, f"pt{u}")
                if u >= 2:
                    need(pe, at_v, f"y{u - 2}")
                for h in range(2 if u < A_T else 1):
                    rows = HD if u < A_T else P
                    for kb in range(NB):
                        c = (2 * (u // 3) + h) * HD if u < A_T else (u - A_T) * P
                        v = (vtok if u < A_T else vmtok)[:, kb, c:c + rows]
                        last = nc.tensor.matmul(pv_bank(u)[h * HD:h * HD + rows, 0:T], v, pt[u % 2][:, 2 * h + kb],
                                                start=kb == 0, stop=kb == NB - 1)
                at_p.done(last, f"pv{u}")
                pe_beside(pe, others[1:])

            scores(0)
            for u in U_ALL:
                if u + 1 < len(U_ALL):
                    scores(u + 1)
                values(u)

        def dve_attn(v):
            dve_beside(v, (0, 1))
            for b in range(8):
                need(v, at_a, f"std{b}")
                at_v.done(nc.vector.reciprocal(rs_at[:, 2 * b:2 * b + 2], rs_at[:, 2 * b:2 * b + 2]), f"rstd{b}")
            dve_beside(v, [2])
            need(v, at_v, "rstd7")
            for k, ((buf, c), g) in enumerate(zip(at_src, at_g)):
                last = nc.vector.scalar_tensor_tensor(buf[:, c], buf[:, c], col(g, 0), rs_at[:, k], ALU.mult, ALU.mult)
            at_v.done(last, "norm")
            dve_beside(v, [3])
            need(v, at_v, "norm")
            for b in range(4):
                need(v, at_p, f"rot{b}")
                cos, sin = (const(n).unsqueeze(1).broadcast_to([P, 2, T]) for n in ("cos", "sin"))
                two = pl[:, 2 * b:2 * b + 2]
                t2 = tmp_at[:, 2 * b:2 * b + 2]
                at_v.done(nc.vector.tensor_tensor(t2, banks[ROT_BANK[b]][:].rearrange("p (a t) -> p a t", a=2), sin, ALU.mult), f"sin{b}")
                at_v.done(nc.vector.tensor_tensor(two, two, cos, ALU.mult), f"cos{b}")
                need(v, at_v, f"cos{b}")
                at_v.done(nc.vector.tensor_tensor(two, two, t2, ALU.add), f"rope{b}")
            dve_beside(v, range(4, ATTN_BEFORE))

            def soft(u):
                nb = len(heads(u))
                if u < A_T:
                    need(v, at_p, f"sc{u}")
                    if u >= 2:
                        need(v, at_a, f"ex{u - 2}")
                    mask = const("amask").rearrange("p (b k) -> p b k", b=NB)
                    for h in range(2):
                        last = nc.vector.scalar_tensor_tensor(
                            sc[u % 2][:, 2 * h:2 * h + 2], sc_bank(u, h)[:].rearrange("p (b k) -> p b k", b=NB),
                            HD ** -0.5, mask, ALU.mult, ALU.add)
                    at_v.done(last, f"mask{u}")
                    need(v, at_v, f"mask{u}")
                    at_v.done(nc.vector.tensor_reduce(mx[:, u], sc[u % 2][:], AX.X, ALU.max), f"max{u}")
                    need(v, at_v, f"max{u}")
                    sink = par[:, PCOL["sink"] + 4 * u:PCOL["sink"] + 4 * u + 4]
                    at_v.done(nc.vector.tensor_tensor(mx[:, u], mx[:, u], sink, ALU.max), f"msk{u}")
                    need(v, at_v, f"msk{u}")
                    at_v.done(nc.vector.tensor_scalar(ngm[:, u], mx[:, u], -1.0, None, ALU.mult), f"neg{u}")
                    need(v, at_v, f"neg{u}")
                    at_v.done(nc.vector.tensor_tensor(es[:, u], sink, ngm[:, u], ALU.add), f"dsk{u}")
                else:
                    need(v, at_p, f"sc{u}")
                    at_v.done(nc.vector.tensor_reduce(mx[:, u, 0:2], sc_bank(u, 0)[:].rearrange("p (b k) -> p b k", b=NB),
                                                      AX.X, ALU.max), f"max{u}")
                    need(v, at_v, f"max{u}")
                    at_v.done(nc.vector.tensor_scalar(ngm[:, u, 0:2], mx[:, u, 0:2], -(P ** -0.5), None, ALU.mult), f"neg{u}")

            def scale(u):
                nb = len(heads(u))
                if u < A_T:
                    need(v, at_a, f"sk{u}")
                    at_v.done(nc.vector.tensor_tensor(sm[:, u], sm[:, u], es[:, u], ALU.add), f"den{u}")
                    need(v, at_v, f"den{u}")
                else:
                    need(v, at_a, f"ex{u}")
                at_v.done(nc.vector.reciprocal(rd[:, u, 0:nb], sm[:, u, 0:nb]), f"rd{u}")
                need(v, at_v, f"rd{u}")
                for n in range(nb):
                    last = nc.vector.tensor_scalar(pr[u % 2][:, n], pr[u % 2][:, n], rd[:, u, n:n + 1], None, ALU.mult)
                at_v.done(last, f"pr{u}")
                first, second, *others = unit_tiles(u)
                dve_beside(v, [first, second])
                need(v, at_p, f"pv{u}")
                v.wait_ge(agate_out, u + 1)
                m = u if u < A_T else 12 + u - A_T
                at_v.done(nc.vector.tensor_tensor(sg[:, m], pv_bank(u)[:, 0:T], sg[:, m], ALU.mult), f"y{u}")
                dve_beside(v, others)

            soft(0)
            for u in U_ALL:
                if u + 1 < len(U_ALL):
                    soft(u + 1)
                scale(u)

        kkn = at("kkn", B + 48 * K, [P, PAIRS, T])
        yall = kkn[:].rearrange("p a (c i) -> p a c i", c=NCH)
        v_bd = at("v_bd", B + 54 * K, [P, NCH, P])
        v_tok = at("v_tok", B + 56 * K, [P, NCH, CH])
        w2t = at("w2t", B + 57 * K, [P, P])
        a2t = at("a2t", B + 57 * K + 512, [P, P])
        small = B + 58 * K
        ws = [at(f"ws{d}", small + 256 * d, [P, CH]) for d in range(2)]
        sas = [at(f"sas{d}", small + 512 + 256 * d, [P, CH]) for d in range(2)]
        st = [at(f"st{d}", small + 1024 + 256 * d, [P, CH]) for d in range(2)]
        sts = [at(f"sts{d}", small + 1536 + 256 * d, [P, CH]) for d in range(2)]
        e_end = [at(f"e_end{d}", small + 2048 + 32 * d, [P, NCH]) for d in range(2)]
        ks = at("ks", B + 61 * K, [P, T])
        dirs = []
        for d in range(2):
            o = B + 82 * K + 24 * K * d
            w = {}
            for k, n in enumerate(("abd", "rbd", "bbd", "kbd", "mt", "kat", "tm", "brt", "krt", "ml", "btok", "ktok")):
                w[n] = at(f"{n}{d}", o + 2 * K * k, [P, NCH, P])
            w["u"], w["x"] = w["kbd"], w["bbd"]
            for k, n in enumerate(("s", "sx", "ad", "bb", "kd", "e1", "e2", "e3", "th")):
                w[n] = at(f"{n}_{d}", o + 8 * K + K * k, [P, T])
            dirs.append(w)
        sq_kk = at("sq_kk", B + 82 * K, [P, PAIRS, T])
        nrm_kk = at("nrm_kk", B + 90 * K, [P, PAIRS, T])
        kk_a = Steps(sem("kk_act"), ["sq", "nrm0", "nrm1", "nrm2", "tanh"])
        kk_v = Steps(sem("kk_dve"), ["raw", "half", "max", "inv", "kk"])
        kk_p = Steps(sem("kk_pe"), ["stat0", "stat1", "stat2"])
        zeroed = sem("rwkv_zeroed")

        def act_kk(act):
            need(act, kk_v, "raw")
            kk_a.done(nc.scalar.activation(sq_kk[:], kkn[:], ACT.Square), "sq")
            for b in range(3):
                need(act, kk_p, f"stat{b}")
                kk_a.done(nc.scalar.activation(nrm_kk[:, 2 * b:2 * b + 2], banks[b][:].rearrange("p (a t) -> p a t", a=2),
                                               ACT.Sqrt), f"nrm{b}")
            kk_a.done(nc.scalar.activation(rkv[:, 18], rkv[:, 18], ACT.Tanh), "tanh")

        def dve_kk(v):
            need(v, at_p, f"pv{A_T + X_T - 1}")
            for p in range(PAIRS):
                last = nc.vector.tensor_scalar(kkn[:, p], rkv[:, PAIRS + p], col("k_k", p), None, ALU.mult)
            kk_v.done(last, "raw")
            kk_v.done(nc.vector.tensor_scalar(hw_sb[:], par[:, PCOL["w0"]:PCOL["w0"] + 24], 0.5, None, ALU.mult), "half")
            need(v, kk_a, "nrm2")
            kk_v.done(nc.vector.tensor_scalar(nrm_kk[:], nrm_kk[:], 1e-12, None, ALU.max), "max")
            need(v, kk_v, "max")
            kk_v.done(nc.vector.reciprocal(nrm_kk[:], nrm_kk[:]), "inv")
            need(v, kk_v, "inv")
            kk_v.done(nc.vector.tensor_tensor(kkn[:], kkn[:], nrm_kk[:], ALU.mult), "kk")

        def pe_kk(pe):
            need(pe, kk_a, "sq")
            need(pe, at_v, f"y{A_T + X_T - 1}")
            for b in range(3):
                kk_p.done(nc.tensor.matmul(banks[b][:], const("bdones"), sq_kk[:, 2 * b:2 * b + 2], start=True, stop=True), f"stat{b}")

        def pool_kk(pool):
            pool.wait_ge(kk_v.sem, kk_v.at("kk"))
            nc.gpsimd.memset(v_bd[:], 0.0).then_inc(zeroed, 1)
            for d in range(2):
                for m in (dirs[d]["abd"], dirs[d]["rbd"], dirs[d]["bbd"], dirs[d]["kbd"]):
                    nc.gpsimd.memset(m[:], 0.0).then_inc(zeroed, 1)

        LV = range(1, LEVELS)
        ST = range(NCH)
        D2 = range(2)
        rw_o = Steps(sem("rwkv_pool"), ["w2t", "a2t", "vbd"] + [f"{n}{d}" for d in D2 for n in ("kbd", "rbd")]
                     + [f"{n}{d}" for d in D2 for n in ("t0_", "t1_", "ml1_", "u0_", "u1_")]
                     + [f"ml{l}_{d}" for l in LV if l > 1 for d in D2])
        rw_v = Steps(sem("rwkv_dve"), [f"{n}{d}" for d in D2 for n in ("u", "s", "sx", "ad", "bb", "t", "kd", "abd", "bbd", "end")]
                     + ["ks", "ksr", "q"] + [f"{n}{d}" for d in D2 for n in ("mt", "kat", "m", "brt")]
                     + [f"krt{d}" for d in D2]
                     + [f"{n}{l}_{d}" for l in LV for d in D2 for n in (("T", "U") if l < LEVELS - 1 else ("U",))]
                     + [f"{n}{s}_{d}" for s in ST for n in ("Y", "G", "S") for d in D2
                        if not (n == "S" and s == NCH - 1) and not (n == "G" and (s == 0 or s == NCH - 1))])
        rw_a = Steps(sem("rwkv_act"), [f"{n}{d}" for d in D2 for n in ("thw", "tha")]
                     + [f"{n}{d}" for d in D2 for n in ("e1", "e2", "e3")]
                     + [f"{n}{d}" for d in D2 for n in (("btok", "ktok", "vtok") if d == 0 else ("btok", "ktok"))]
                     + [f"X{l}_{d}" for l in LV for d in D2] + [f"{n}{s}_{d}" for s in ST for n in ("W", "SA") for d in D2])
        rw_p = Steps(sem("rwkv_pe"), [f"{n}{d}" for d in D2 for n in ("zw", "za")]
                     + [f"{n}{d}" for d in D2 for n in ("mt", "kat", "m", "brt")]
                     + [f"{n}{d}" for d in D2 for n in (("krt", "btok", "ktok", "vtok") if d == 0 else ("krt", "btok", "ktok"))]
                     + [s for l in LV for s in [f"X{l}_{d}" for d in D2]
                        + [f"{n}{l}_{d}" for d in D2 for n in (("U", "T") if l < LEVELS - 1 else ("U",))]]
                     + [f"{n}{s}_{d}" for s in ST for n in ("W", "SA", "S", "Y") for d in D2
                        if not (n == "S" and s == NCH - 1)])

        def chunks(ap):
            return ap.rearrange("p (c t) -> p c t", c=NCH)

        def four(ap):
            return ap.unsqueeze(1).broadcast_to([P, NCH, P])

        def blocks(bank):
            return banks[bank][:].rearrange("p (c t) -> p c t", c=NCH)

        def level(l):
            return four(const("levels")[:, P * l:P * l + P])

        def halves():
            return [slice(CH * h, CH * h + CH) for h in range(2)]

        def chunk_of(d, s):
            return s if d == 0 else NCH - 1 - s

        def pool_rwkv(pool):
            pool.wait_ge(zeroed, 9)
            pool.wait_ge(in_lora, 48)
            need(pool, kk_a, "tanh")
            with pool.Fori(0, PAIRS) as p:
                rw_o.done(nc.gpsimd.tensor_copy(w2t[:], w2_sb[:, p]), "w2t")
                rw_o.done(nc.gpsimd.tensor_copy(a2t[:], a2_sb[:, p]), "a2t")
                need(pool, rw_o, "a2t", p)
                for h in halves():
                    last = nc.gpsimd.tensor_copy(v_bd[h, :, h], rkv[h, 2 * PAIRS + p].rearrange("p (c t) -> p c t", c=NCH))
                rw_o.done(last, "vbd")
                for d, w in enumerate(dirs):
                    need(pool, rw_v, f"kd{d}", p)
                    need(pool, rw_a, f"e3{d}", p)
                    for h in halves():
                        last = nc.gpsimd.tensor_tensor(w["kbd"][h, :, h], chunks(w["kd"][h]), chunks(w["e3"][h]), ALU.mult)
                    rw_o.done(last, f"kbd{d}")
                    for h in halves():
                        last = nc.gpsimd.tensor_tensor(w["rbd"][h, :, h], rkv[h, p].rearrange("p (c t) -> p c t", c=NCH),
                                                       chunks(w["e1"][h]), ALU.mult)
                    rw_o.done(last, f"rbd{d}")
                ident = four(const("ident"))
                need(pool, rw_o, "rbd1", p)
                for d, w in enumerate(dirs):
                    need(pool, rw_v, f"m{d}", p)
                    rw_o.done(nc.gpsimd.tensor_tensor(w["tm"][:], w["tm"][:], level(0), ALU.mult), f"t0_{d}")
                    need(pool, rw_o, f"t0_{d}", p)
                    rw_o.done(nc.gpsimd.tensor_tensor(w["tm"][:], w["tm"][:], ident, ALU.add), f"t1_{d}")
                    rw_o.done(nc.gpsimd.tensor_tensor(w["ml"][:], w["mt"][:], level(1), ALU.mult), f"ml1_{d}")
                    need(pool, rw_p, f"ktok{d}", p)
                    rw_o.done(nc.gpsimd.tensor_tensor(w["u"][:], w["mt"][:], level(0), ALU.mult), f"u0_{d}")
                    need(pool, rw_o, f"u0_{d}", p)
                    rw_o.done(nc.gpsimd.tensor_tensor(w["u"][:], w["u"][:], ident, ALU.add), f"u1_{d}")
                for l in LV:
                    if l > 1:
                        for d, w in enumerate(dirs):
                            need(pool, rw_p, f"X{l - 1}_{d}", p)
                            rw_o.done(nc.gpsimd.tensor_tensor(w["ml"][:], w["mt"][:], level(l), ALU.mult), f"ml{l}_{d}")
                need(pool, rw_p, f"Y{NCH - 1}_1", p)

        def act_rwkv(act):
            with act.Fori(0, PAIRS) as p:
                for d, w in enumerate(dirs):
                    need(act, rw_p, f"zw{d}", p)
                    rw_a.done(nc.scalar.activation(w["th"][:], banks[4 * d][:, 0:T], ACT.Tanh, scale=0.5,
                                                   bias=hw_sb[:, bass.ds(p + PAIRS * d, 1)]), f"thw{d}")
                    need(act, rw_p, f"za{d}", p)
                    rw_a.done(nc.scalar.activation(w["ad"][:], banks[4 * d + 1][:, 0:T], ACT.Tanh, scale=0.5,
                                                   bias=hw_sb[:, bass.ds(p + (2 + d) * PAIRS, 1)]), f"tha{d}")
                for d, w in enumerate(dirs):
                    need(act, rw_v, f"sx{d}", p)
                    rw_a.done(nc.scalar.activation(w["e1"][:], w["s"][:], ACT.Exp, scale=-HALF_DECAY), f"e1{d}")
                    rw_a.done(nc.scalar.activation(w["e2"][:], w["sx"][:], ACT.Exp, scale=-HALF_DECAY), f"e2{d}")
                    rw_a.done(nc.scalar.activation(w["e3"][:], w["s"][:], ACT.Exp, scale=HALF_DECAY), f"e3{d}")
                for d, w in enumerate(dirs):
                    b = 4 * d
                    need(act, rw_p, f"btok{d}", p)
                    rw_a.done(nc.scalar.activation(w["btok"][:], blocks(b + 1), ACT.Copy), f"btok{d}")
                    need(act, rw_p, f"ktok{d}", p)
                    rw_a.done(nc.scalar.activation(w["ktok"][:], blocks(b + 3), ACT.Copy), f"ktok{d}")
                    if d == 0:
                        need(act, rw_p, "vtok0", p)
                        rw_a.done(nc.scalar.activation(v_tok[:], banks[2][:, 0:T].rearrange("p (c i) -> p c i", c=NCH),
                                                       ACT.Copy), "vtok0")
                for l in LV:
                    for d, w in enumerate(dirs):
                        need(act, rw_p, f"X{l}_{d}", p)
                        if l > 1:
                            need(act, rw_p, f"T{l - 1}_{d}", p)
                        rw_a.done(nc.scalar.activation(w["x"][:], blocks(4 * d + 1), ACT.Copy), f"X{l}_{d}")
                for s in ST:
                    for d in D2:
                        need(act, rw_p, f"W{s}_{d}", p)
                        rw_a.done(nc.scalar.activation(ws[d][:], banks[4 * d][:, 0:CH], ACT.Copy, scale=-1.0), f"W{s}_{d}")
                    for d in D2:
                        need(act, rw_p, f"SA{s}_{d}", p)
                        if s > 0:
                            need(act, rw_p, f"Y{s - 1}_{d}", p)
                        rw_a.done(nc.scalar.activation(sas[d][:], banks[4 * d + 1][:, 0:CH], ACT.Copy), f"SA{s}_{d}")
                need(act, rw_p, f"Y{NCH - 1}_1", p)
                need(act, rw_v, f"Y{NCH - 1}_1", p)

        def dve_rwkv(v):
            with v.Fori(0, PAIRS) as p:
                for d, w in enumerate(dirs):
                    run = const("run_up" if d == 0 else "run_lo")
                    turn = (lambda ap: ap) if d == 0 else (lambda ap: ap[:, ::-1])
                    need(v, rw_a, f"tha{d}", p)
                    rw_v.done(nc.vector.tensor_scalar(w["th"][:], w["th"][:], 1.0, None, ALU.add), f"u{d}")
                    need(v, rw_v, f"u{d}", p)
                    rw_v.done(nc.vector.tensor_tensor_scan(turn(w["s"][:]), turn(run), turn(w["th"][:]), 0.0, ALU.mult, ALU.add), f"s{d}")
                    need(v, rw_v, f"s{d}", p)
                    rw_v.done(nc.vector.tensor_tensor(w["sx"][:], w["s"][:], w["th"][:], ALU.subtract), f"sx{d}")
                    rw_v.done(nc.vector.tensor_scalar(w["ad"][:], w["ad"][:], 0.5, 0.5, ALU.mult, ALU.add), f"ad{d}")
                    need(v, rw_v, f"ad{d}", p)
                    rw_v.done(nc.vector.tensor_tensor(w["bb"][:], kkn[:, p], w["ad"][:], ALU.mult), f"bb{d}")
                    rw_v.done(nc.vector.tensor_scalar(w["kd"][:], w["ad"][:], 1.0, col("k_a", p), ALU.subtract, ALU.mult), f"t{d}")
                    need(v, rw_v, f"t{d}", p)
                    rw_v.done(nc.vector.scalar_tensor_tensor(w["kd"][:], w["kd"][:], 1.0, rkv[:, PAIRS + p], ALU.add, ALU.mult), f"kd{d}")
                    need(v, rw_a, f"e3{d}", p)
                    for h in halves():
                        last = nc.vector.tensor_tensor(w["abd"][h, :, h], kkn[h, p].rearrange("p (c t) -> p c t", c=NCH),
                                                       chunks(w["e2"][h]), ALU.mult)
                    rw_v.done(last, f"abd{d}")
                    for h in halves():
                        last = nc.vector.tensor_tensor(w["bbd"][h, :, h], chunks(w["bb"][h]), chunks(w["e3"][h]), ALU.mult)
                    rw_v.done(last, f"bbd{d}")
                    end = CH - 1 if d == 0 else 0
                    rw_v.done(nc.vector.tensor_copy(e_end[d][:], chunks(w["e1"][:])[:, :, end]), f"end{d}")
                need(v, rw_v, "end1", p)
                rw_v.done(nc.vector.tensor_tensor(ks[:], dirs[0]["kd"][:], dirs[1]["kd"][:], ALU.add), "ks")
                need(v, rw_v, "ks", p)
                rw_v.done(nc.vector.tensor_scalar(ks[:], ks[:], col("r_k", p), None, ALU.mult), "ksr")
                need(v, rw_v, "ksr", p)
                need(v, rw_o, "rbd1", p)
                rw_v.done(nc.vector.tensor_tensor(rkv[:, p], rkv[:, p], ks[:], ALU.mult), "q")
                for d, w in enumerate(dirs):
                    b = 4 * d
                    up, lo, incl = (const(n) for n in (("strict_up", "strict_lo", "incl_up") if d == 0 else
                                                       ("strict_lo", "strict_up", "incl_lo")))
                    for n, bank, dst, mask, sign in (("mt", b, w["mt"], up, -1.0), ("kat", b + 1, w["kat"], up, 1.0),
                                                     ("m", b + 2, w["tm"], lo, -1.0), ("brt", b + 3, w["brt"], incl, 1.0)):
                        need(v, rw_p, f"{n}{d}", p)
                        rw_v.done(nc.vector.scalar_tensor_tensor(dst[:], blocks(bank), sign, four(mask), ALU.mult, ALU.mult), f"{n}{d}")
                for d, w in enumerate(dirs):
                    need(v, rw_p, f"krt{d}", p)
                    incl = const("incl_up" if d == 0 else "incl_lo")
                    rw_v.done(nc.vector.tensor_tensor(w["krt"][:], blocks(4 * d), four(incl), ALU.mult), f"krt{d}")
                for l in LV:
                    for d, w in enumerate(dirs):
                        if l < LEVELS - 1:
                            need(v, rw_p, f"T{l}_{d}", p)
                            rw_v.done(nc.vector.tensor_tensor(w["tm"][:], w["tm"][:], blocks(4 * d + 3), ALU.add), f"T{l}_{d}")
                        else:
                            need(v, rw_p, f"U{l}_{d}", p)
                        rw_v.done(nc.vector.tensor_tensor(w["u"][:], w["u"][:], blocks(4 * d + 2), ALU.add), f"U{l}_{d}")
                for s in ST:
                    for d in D2:
                        c = chunk_of(d, s)
                        need(v, rw_p, f"Y{s}_{d}", p)
                        y = yall[:, p, c]
                        if s < NCH // 2:
                            last = nc.vector.tensor_scalar(y, banks[4 * d + 2][:, 0:CH], 1.0, None, ALU.mult)
                        else:
                            last = nc.vector.tensor_tensor(y, y, banks[4 * d + 2][:, 0:CH], ALU.add)
                        rw_v.done(last, f"Y{s}_{d}")
                    if s == NCH - 1:
                        continue
                    for d in D2:
                        if s > 0:
                            c = chunk_of(d, s)
                            rw_v.done(nc.vector.tensor_scalar(sts[d][:], st[d][:], e_end[d][:, c:c + 1], None, ALU.mult), f"G{s}_{d}")
                    for d in D2:
                        c = chunk_of(d, s)
                        new = banks[4 * d + 3][:, 0:CH]
                        if s == 0:
                            last = nc.vector.tensor_scalar(st[d][:], new, e_end[d][:, c:c + 1], None, ALU.mult)
                        else:
                            need(v, rw_v, f"G{s}_{d}", p)
                            last = nc.vector.scalar_tensor_tensor(st[d][:], new, e_end[d][:, c:c + 1], sts[d][:], ALU.mult, ALU.add)
                        rw_v.done(last, f"S{s}_{d}")

        def pe_rwkv(pe):
            need(pe, kk_a, "tanh")
            with pe.Fori(0, PAIRS) as p:
                for d in D2:
                    need(pe, rw_o, "a2t", p)
                    h = halves()[d]
                    rw_p.done(nc.tensor.matmul(banks[4 * d][:, 0:T], w2t[h], rkv[h, 18], start=True, stop=True), f"zw{d}")
                    rw_p.done(nc.tensor.matmul(banks[4 * d + 1][:, 0:T], a2t[h], rkv[h, 19], start=True, stop=True), f"za{d}")

                def each(bank, lhs, rhs, n=P):
                    for c in range(NCH):
                        last = nc.tensor.matmul(banks[bank][:, n * c:n * c + n], lhs[:, c], rhs[:, c], start=True, stop=True)
                    return last

                def turned(bank, src):
                    for c in range(NCH):
                        last = nc.tensor.transpose(banks[bank][:, P * c:P * c + P], src[:, c], const("ident"))
                    return last

                for d, w in enumerate(dirs):
                    b = 4 * d
                    need(pe, rw_v, f"end{d}", p)
                    need(pe, rw_o, f"rbd{d}", p)
                    rw_p.done(each(b, w["bbd"], w["abd"]), f"mt{d}")
                    rw_p.done(each(b + 1, w["kbd"], w["abd"]), f"kat{d}")
                    rw_p.done(each(b + 2, w["abd"], w["bbd"]), f"m{d}")
                    rw_p.done(each(b + 3, w["bbd"], w["rbd"]), f"brt{d}")
                for d, w in enumerate(dirs):
                    b = 4 * d
                    need(pe, rw_v, f"mt{d}", p)
                    rw_p.done(each(b, w["kbd"], w["rbd"]), f"krt{d}")
                    need(pe, rw_v, f"kat{d}", p)
                    rw_p.done(turned(b + 1, w["bbd"]), f"btok{d}")
                    need(pe, rw_v, f"brt{d}", p)
                    rw_p.done(turned(b + 3, w["kbd"]), f"ktok{d}")
                    if d == 0:
                        need(pe, rw_o, "vbd", p)
                        for c in range(NCH):
                            last = nc.tensor.matmul(banks[2][:, CH * c:CH * c + CH], v_bd[:, c], const("istack"), start=True, stop=True)
                        rw_p.done(last, "vtok0")
                for l in LV:
                    for d, w in enumerate(dirs):
                        need(pe, rw_o, f"ml{l}_{d}", p)
                        if l == 1:
                            need(pe, rw_o, f"t1_{d}", p)
                            need(pe, rw_a, f"btok{d}", p)
                        else:
                            need(pe, rw_v, f"T{l - 1}_{d}", p)
                        rw_p.done(each(4 * d + 1, w["ml"], w["tm"]), f"X{l}_{d}")
                    for d, w in enumerate(dirs):
                        need(pe, rw_a, f"X{l}_{d}", p)
                        if l == 1:
                            need(pe, rw_o, f"u1_{d}", p)
                            need(pe, rw_a, "vtok0" if d == 0 else "ktok1", p)
                        else:
                            need(pe, rw_v, f"U{l - 1}_{d}", p)
                        rw_p.done(each(4 * d + 2, w["x"], w["u"]), f"U{l}_{d}")
                        if l < LEVELS - 1:
                            rw_p.done(each(4 * d + 3, w["u"], w["x"]), f"T{l}_{d}")
                for s in ST:
                    for d, w in enumerate(dirs):
                        c = chunk_of(d, s)
                        o = banks[4 * d][:, 0:CH]
                        if s > 0:
                            need(pe, rw_v, f"S{s - 1}_{d}", p)
                            nc.tensor.matmul(o, w["abd"][:, c], st[d][:], start=True, stop=False)
                        else:
                            need(pe, rw_v, f"krt{d}", p)
                        rw_p.done(nc.tensor.matmul(o, w["kat"][:, c], v_tok[:, c], start=s == 0, stop=True), f"W{s}_{d}")
                    for d, w in enumerate(dirs):
                        c = chunk_of(d, s)
                        if s == 0:
                            need(pe, rw_v, f"U{LEVELS - 1}_{d}", p)
                        need(pe, rw_a, f"W{s}_{d}", p)
                        rw_p.done(nc.tensor.matmul(banks[4 * d + 1][:, 0:CH], w["u"][:, c], ws[d][:], start=True, stop=True), f"SA{s}_{d}")
                    for d, w in enumerate(dirs):
                        if s == NCH - 1:
                            continue
                        c = chunk_of(d, s)
                        need(pe, rw_a, f"SA{s}_{d}", p)
                        o = banks[4 * d + 3][:, 0:CH]
                        nc.tensor.matmul(o, w["btok"][:, c], sas[d][:], start=True, stop=False)
                        rw_p.done(nc.tensor.matmul(o, w["ktok"][:, c], v_tok[:, c], start=False, stop=True), f"S{s}_{d}")
                    for d, w in enumerate(dirs):
                        c = chunk_of(d, s)
                        if s == NCH - 1:
                            need(pe, rw_a, f"SA{s}_{d}", p)
                        if s > 0:
                            need(pe, rw_v, f"Y{s - 1}_{d}", p)
                        o = banks[4 * d + 2][:, 0:CH]
                        if s > 0:
                            nc.tensor.matmul(o, w["rbd"][:, c], st[d][:], start=True, stop=False)
                        nc.tensor.matmul(o, w["brt"][:, c], sas[d][:], start=s == 0, stop=False)
                        rw_p.done(nc.tensor.matmul(o, w["krt"][:, c], v_tok[:, c], start=False, stop=True), f"Y{s}_{d}")

        yhl = at("yhl", B + 48 * K, [P, KT, 2, T], R)
        G0 = B + 82 * K
        gsum = at("gsum", G0, [P, 24])
        gmean = at("gmean", G0 + 128, [P, 24])
        gvar = at("gvar", G0 + 256, [P, 24])
        gstd = at("gstd", G0 + 384, [P, 24])
        grs = at("grs", G0 + 512, [P, 24])
        gsq = at("gsq", G0 + K, [P, 24, CH])
        ybd = at("ybd", G0 + 8 * K, [P, 24, P])
        t1 = at("gn_t1", G0 + 20 * K, [P, PAIRS, T])
        t2 = at("gn_t2", G0 + 26 * K, [P, PAIRS, T])
        gn_o = Steps(sem("gn_pool"), ["zero"])
        gn_a = Steps(sem("gn_act"), ["sq", "std", "hi0", "hi1", "hi2", "hi3"])
        gn_v = Steps(sem("gn_dve"), ["sum", "mean", "center", "var", "rstd", "yn"]
                     + [f"{n}{p}" for p in range(PAIRS) for n in ("ln", "bonus", "sum", "y")]
                     + ["lo0", "lo1", "lo2", "lo3"])
        gn_p = Steps(sem("gn_pe"), ["bonus0", "bonus1", "bonus2", "y0", "y1", "y2"])
        y24 = kkn[:].rearrange("p a (c i) -> p (a c) i", c=NCH)

        def wide(ap):
            return ap.unsqueeze(2).broadcast_to([P, 24, CH])

        def pool_gn(pool):
            need(pool, rw_v, f"Y{NCH - 1}_1", PAIRS - 1)
            need(pool, rw_p, f"Y{NCH - 1}_1", PAIRS - 1)
            gn_o.done(nc.gpsimd.memset(ybd[:], 0.0), "zero")
            need(pool, gn_v, "lo3")
            pool.dma_start(x_res[:], xT).then_inc(in_res, 16)
            pool.wait_ge(units_used, 2 * FIRST["wout1"])
            pool.dma_start(X1[:, :, 0:META], metaT).then_inc(in_meta, 16)

        def act_gn(act):
            need(act, gn_v, "center")
            gn_a.done(nc.scalar.activation(gsq[:], y24, ACT.Square), "sq")
            need(act, gn_v, "var")
            gn_a.done(nc.scalar.activation(gstd[:], gvar[:], ACT.Sqrt, bias=GN_EPS, scale=1.0 / CH), "std")
            need(act, gn_v, f"y{PAIRS - 1}")
            for q in range(4):
                gn_a.done(nc.scalar.activation(yhl[:, 4 * q:4 * q + 4, 0], sg[:, 4 * q:4 * q + 4], ACT.Copy), f"hi{q}")

        def dve_gn(v):
            need(v, rw_v, f"Y{NCH - 1}_1", PAIRS - 1)
            gn_v.done(nc.vector.tensor_reduce(gsum[:], y24, AX.X, ALU.add), "sum")
            need(v, gn_v, "sum")
            gn_v.done(nc.vector.tensor_scalar(gmean[:], gsum[:], 1.0 / CH, None, ALU.mult), "mean")
            need(v, gn_v, "mean")
            gn_v.done(nc.vector.tensor_tensor(y24, y24, wide(gmean[:]), ALU.subtract), "center")
            need(v, gn_a, "sq")
            gn_v.done(nc.vector.tensor_reduce(gvar[:], gsq[:], AX.X, ALU.add), "var")
            need(v, gn_a, "std")
            gn_v.done(nc.vector.reciprocal(grs[:], gstd[:]), "rstd")
            need(v, gn_v, "rstd")
            need(v, gn_o, "zero")
            for h in halves():
                last = nc.vector.tensor_tensor(ybd[h, :, h], y24[h], wide(grs[:])[h], ALU.mult)
            gn_v.done(last, "yn")
            for p in range(PAIRS):
                at_p_ = T * (p % 2)
                need(v, gn_p, f"y{p // 2}")
                gn_v.done(nc.vector.tensor_scalar(t1[:, p], banks[p // 2][:, at_p_:at_p_ + T], col("ln_w", p), col("ln_b", p),
                                                  ALU.mult, ALU.add), f"ln{p}")
                gn_v.done(nc.vector.tensor_tensor(t2[:, p], banks[3 + p // 2][:, at_p_:at_p_ + T], rkv[:, 2 * PAIRS + p],
                                                  ALU.mult), f"bonus{p}")
                need(v, gn_v, f"bonus{p}")
                gn_v.done(nc.vector.tensor_tensor(t1[:, p], t1[:, p], t2[:, p], ALU.add), f"sum{p}")
                need(v, gn_v, f"sum{p}")
                gn_v.done(nc.vector.tensor_tensor(sg[:, A_T + p], sg[:, A_T + p], t1[:, p], ALU.mult), f"y{p}")
            for q in range(4):
                need(v, gn_a, f"hi{q}")
                gn_v.done(nc.vector.tensor_tensor(yhl[:, 4 * q:4 * q + 4, 1], sg[:, 4 * q:4 * q + 4],
                                                  yhl[:, 4 * q:4 * q + 4, 0].bitcast(F), ALU.subtract), f"lo{q}")

        def pe_gn(pe):
            need(pe, rw_v, f"Y{NCH - 1}_1", PAIRS - 1)
            for b in range(3):
                gn_p.done(nc.tensor.matmul(banks[3 + b][:], const("bdones"), rkv[:, 2 * b:2 * b + 2], start=True, stop=True), f"bonus{b}")
            need(pe, gn_v, "yn")
            for b in range(3):
                for n in range(8):
                    last = nc.tensor.matmul(banks[b][:, CH * n:CH * n + CH], ybd[:, 8 * b + n], const("istack"), start=True, stop=True)
                gn_p.done(last, f"y{b}")

        mg = at("mg", B + 90 * K, [P, KT, 2, T], R)
        gt = at("gt", B + 122 * K, [P, N_BRANCH, T])
        gpre = at("gpre", B + 128 * K, [P, N_BRANCH, T])
        gate_pre = sem("gate_pre")
        mt_ = at("mt_", B + 125 * K, [P, N_BRANCH, T])
        x_res = at("x_res", B + 32 * K, [P, KT, T])
        X1 = at("X1", B, [P, KT, TM])
        SPANS = [(0, A_T), (A_T, A_T + PAIRS), (A_T + PAIRS, KT)]
        gate_out, wo_out, mg_step, mg_hi, mg_lo, wout1_out = (
            sem(n) for n in ("gate_out", "wo_out", "mg_step", "mg_hi", "mg_lo", "wout1_out"))

        def rnd(tile, c, m):
            return tile.loops[-1][0] * m + c if tile.loops else c

        def act_merge(act):
            def body(tile):
                b = tile.t % 4
                m = rnd(tile, 0, 1)
                if b < N_BRANCH:
                    split_hi(act, tile.later())
                    act.wait_ge(gate_pre, rnd(tile, b + 1, 3))
                    if tile.loops and b == 0:
                        act.wait_ge(mg_step, rnd(tile, -2, 5))
                    nc.scalar.activation(gt[:, b], gpre[:, b], ACT.Sigmoid,
                                         bias=col("gate_b", rnd(tile, KT * b, 1))).then_inc(gate_out, 1)
                else:
                    act.wait_ge(mg_step, rnd(tile, 5, 5))
                    nc.scalar.activation(mg[:, m, 0], mt_[:, 0], ACT.Copy).then_inc(mg_hi, 1)
                    split_hi(act, tile.later())
            run_tiles(act, "merge1", 4, body)

        def dve_merge(v):
            def body(tile):
                m, b = rnd(tile, 0, 1), tile.t % 4
                tile_done(v, tile)
                if b < N_BRANCH:
                    nc.vector.tensor_tensor(gpre[:, b], banks[tile.parity][:, 0:T], x_norm.rstd[:], ALU.mult).then_inc(gate_pre, 1)
                    split_lo(v, tile.later())
                    return
                v.wait_ge(gate_out, rnd(tile, 3, 3))
                for b in range(N_BRANCH):
                    ins = nc.vector.tensor_tensor(mt_[:, b], banks[2 + b][:, 0:T], gt[:, b], ALU.mult)
                    ins.then_inc(mg_step, 1)
                v.wait_ge(mg_step, rnd(tile, 3, 5))
                nc.vector.tensor_tensor(mt_[:, 0], mt_[:, 0], mt_[:, 1], ALU.add).then_inc(mg_step, 1)
                v.wait_ge(mg_step, rnd(tile, 4, 5))
                nc.vector.tensor_tensor(mt_[:, 0], mt_[:, 0], mt_[:, 2], ALU.add).then_inc(mg_step, 1)
                v.wait_ge(mg_hi, rnd(tile, 1, 1))
                nc.vector.tensor_tensor(mg[:, m, 1], mt_[:, 0], mg[:, m, 0].bitcast(F), ALU.subtract).then_inc(mg_lo, 1)
                split_lo(v, tile.later())
            run_tiles(v, "merge1", 4, body)

        def pe_merge(pe):
            need(pe, gn_v, "lo3")

            def body(tile):
                b = tile.t % 4
                if b < N_BRANCH:
                    if b == 2 or tile.loops:
                        pe.wait_ge(gate_pre, rnd(tile, 1 if b == 2 else 0, 3))
                    full_tile(pe, tile, hx)
                    return
                if tile.loops:
                    pe.wait_ge(mg_step, rnd(tile, -2, 5))
                for k in range(2):
                    pe.wait_ge(lo_ready, tile.units(k + 1))
                    for j in range(HALF):
                        kt = HALF * k + j
                        n, (a, z) = next((n, s) for n, s in enumerate(SPANS) if s[0] <= kt < s[1])
                        last = product(banks[2 + n][:, 0:T], yhl, (2 * tile.parity + k) % RING, j, kt, kt == a, kt == z - 1)
                    last.then_inc(units_used, 1)
            run_tiles(pe, "merge1", 4, body)

        def dve_wout1(v):
            v.wait_ge(in_res, 16)
            v.wait_ge(in_meta, 16)

            def body(tile):
                tile_done(v, tile)
                m = tile.local()
                nc.vector.tensor_tensor(X1[:, m, META:], banks[tile.parity][:, 0:T], x_res[:, m], ALU.add).then_inc(wout1_out, 1)
                norm1.dve_tile(v, m, tile.local(1, 1))
                split_lo(v, tile.later())
            run_tiles(v, "wout1", 2, body)

        def act_norm_phase(act, phase, norm, x_out):
            def body(tile):
                act.wait_ge(x_out, tile.local(1, 1))
                norm.act_tile(act, tile.local())
                split_hi(act, tile.later())
            run_tiles(act, phase, 2, body)

        u1 = at("u1", B + 49 * K, [P, KT, 2, TM], R)
        HP = at("HP", B + 17 * K, [P, KT, 2, T])
        HL, PO = HP[:, :, 0], HP[:, :, 1]
        mg2 = at("mg2", B + 17 * K, [P, KT, 2, T], R)
        Z2 = B + 83 * K
        norm1 = Norm("norm1", X1, TM, "norm1_g", u1, B + 128 * K)
        gpool_out, gelu_out, gpool_pre, gelu_pre = (sem(n) for n in ("gpool_out", "gelu_out", "gpool_pre", "gelu_pre"))
        gpl = at("gpl", Z2 + 30 * K, [P, 2, T])
        gel = at("gel", Z2 + 32 * K, [P, 2, T])

        one272 = at("one272", Z2, [P, TM])
        vp = [at(f"vp{b}", Z2 + (2 + 2 * b) * K, [P, TM]) for b in range(2)]
        cs = [at(f"cs{b}", Z2 + (6 + 2 * b) * K, [P, TM]) for b in range(2)]
        df = [at(f"df{b}", Z2 + (10 + b) * K, [P, T]) for b in range(2)]
        dt = [at(f"dt{b}", Z2 + (12 + b) * K, [P, T]) for b in range(2)]
        dhl = at("dhl", Z2 + 14 * K, [P, POOL_T + 1, 2, T], R)
        vp_copied, vp_step, d_hi, d_lo, po_out, ones_set = (
            sem(n) for n in ("vp_copied", "vp_step", "d_hi", "d_lo", "po_out", "ones_set"))
        NG = len(POOL_WINDOWS)

        def own_tiles(phase):
            return [(Tile(FIRST[phase], t), g, j, POOL_T * g + j) for t, (g, j) in enumerate(OWN_ORDER)]

        def bank_user(t):
            while t >= 2:
                t -= 2
                if OWN_ORDER[t][1] != OWN:
                    return POOL_T * OWN_ORDER[t][0] + OWN_ORDER[t][1]
            return None

        def act_pool(act):
            for tile, g, j, n in own_tiles("pool"):
                split_hi(act, tile.later(), (0,))
                if j != OWN:
                    act.wait_ge(vp_step, 3 * n + 3)
                    nc.scalar.activation(dhl[:, n % 5, 0], dt[n % 2][:], ACT.Copy).then_inc(d_hi, 1)
                split_hi(act, tile.later(), (1,))

        def dve_pool(v):
            nc.vector.memset(one272[:], 1.0).then_inc(ones_set, 1)
            v.wait_ge(ones_set, 1)
            v.wait_ge(gpool_out, KT)
            for tile, g, j, n in own_tiles("pool"):
                b, window = n % 2, POOL_WINDOWS[g]
                tile_done(v, tile)
                if j == OWN:
                    for m in range(POOL_T):
                        c = POOL_T * g + m
                        nc.vector.scalar_tensor_tensor(PO[:, c], banks[2 + m][:, 0:T], col("pool_scale", c), PO[:, c],
                                                       ALU.mult, ALU.mult).then_inc(po_out, 1)
                    split_lo(v, tile.later())
                    continue
                nc.vector.tensor_tensor(vp[b][:], banks[tile.parity][:, 0:TM], norm1.rstd[:], ALU.mult).then_inc(vp_copied, 1)
                v.wait_ge(vp_copied, n + 1)
                nc.vector.tensor_tensor_scan(cs[b][:], one272[:], vp[b][:], 0.0, ALU.mult, ALU.add).then_inc(vp_step, 1)
                v.wait_ge(vp_step, 3 * n + 1)
                nc.vector.tensor_tensor(df[b][:], cs[b][:, META:], cs[b][:, META - window:TM - window], ALU.subtract).then_inc(vp_step, 1)
                v.wait_ge(vp_step, 3 * n + 2)
                nc.vector.scalar_tensor_tensor(dt[b][:], df[b][:], 1.0 / window, vp[b][:, META:], ALU.mult, ALU.subtract).then_inc(vp_step, 1)
                v.wait_ge(d_hi, n + 1)
                nc.vector.tensor_tensor(dhl[:, n % 5, 1], dt[b][:], dhl[:, n % 5, 0].bitcast(F), ALU.subtract).then_inc(d_lo, 1)
                split_lo(v, tile.later())

        def pe_pool(pe):
            for tile, g, j, n in own_tiles("pool"):
                if j != OWN:
                    user = bank_user(tile.t)
                    if user is None:
                        pe.wait_ge(gelu_pre, KT - 1 + tile.t)
                    else:
                        pe.wait_ge(vp_copied, user + 1)
                    full_tile(pe, tile, u1, TM)
                    continue
                if g > 0:
                    pe.wait_ge(po_out, POOL_T * g)
                pe.wait_ge(d_lo, POOL_T * (g + 1))
                for k in range(2):
                    pe.wait_ge(lo_ready, tile.units(k + 1))
                    for jj in range(HALF):
                        m, kt = 2 * k + jj // POOL_T, jj % POOL_T
                        last = product(banks[2 + m][:, 0:T], dhl, (2 * tile.parity + k) % RING, jj, (POOL_T * g + kt) % 5,
                                       kt == 0, kt == POOL_T - 1)
                    last.then_inc(units_used, 1)

        LP = CONV2 - 1
        vl = [at(f"vl{b}", Z2 + 1216 * b, [P, TM + LP]) for b in range(2)]
        xa = at("xa", Z2 + 2432, [P, TM])
        xc = at("xc", Z2 + 2432 + 1088, [P, 5, TM])
        xchl = at("xchl", Z2 + 2432 + 1088 * 6, [P, 5, 2, TM], R)
        ga = at("ga", Z2 + 2432 + 1088 * 16, [P, 2, 2, TM])
        gx = [at(f"gx{b}", Z2 + 2432 + 1088 * (20 + 4 * b), [P, 2, 2, TM]) for b in range(2)]
        av, tv, mv = (at(f"lru_{n}", Z2 + 2432 + 1088 * (28 + 4 * k), [P, 2, 2, TM]) for k, n in enumerate(("a", "t", "m")))
        hv = mv[:].rearrange("p k m t -> p (k m) t")
        vl_zero, vl_copied, conv_step, xc_hi, xc_lo, own_out, lru_gate = (
            sem(n) for n in ("vl_zero", "vl_copied", "conv_step", "xc_hi", "xc_lo", "own_out", "lru_gate"))
        lru_a = Steps(sem("lru_act"), ["tanh", "exp", "sqrt"])
        lru_v = Steps(sem("lru_dve"), ["one", "scan"])
        lru_o = Steps(sem("lru_pool"), ["ix", "sq", "b", "out"])

        def flat4(ap):
            return ap.rearrange("p a b t -> p (a b t)")

        def act_lru_decay(act, g, func, dst, scale, name):
            for n in range(4):
                s = lam_sb[:, scale, 4 * g + n:4 * g + n + 1]
                last = nc.scalar.activation(dst[:, n // 2, n % 2], ga[:, n // 2, n % 2], func, scale=s)
            lru_a.done(last, name)

        def act_lru_tanh(act, g):
            act.wait_ge(lru_gate, 8 * (g + 1))
            act_lru_decay(act, g, ACT.Tanh, tv, 1, "tanh")

        def act_lru_exp(act, g):
            if g > 0:
                need(act, lru_v, "scan", g - 1)
            act_lru_decay(act, g, ACT.Exp, av, 2, "exp")

        def act_lru_root(act, g):
            need(act, lru_v, "one", g)
            lru_a.done(nc.scalar.activation(mv[:], tv[:], ACT.Sqrt), "sqrt")

        def dve_lru_one(v, g):
            need(v, lru_a, "tanh", g)
            need(v, lru_o, "sq", g)
            lru_v.done(nc.vector.scalar_tensor_tensor(flat4(tv[:]), flat4(mv[:]), 1.0, flat4(tv[:]), ALU.add, ALU.mult), "one")

        def dve_lru_scan(v, g):
            need(v, lru_o, "b", g)
            for n in range(4):
                last = nc.vector.tensor_tensor_scan(hv[:, n], av[:, n // 2, n % 2], gx[g % 2][:, n // 2, n % 2], 0.0, ALU.mult, ALU.add)
            lru_v.done(last, "scan")

        def pool_lru(pool):
            for g in range(4):
                x = gx[g % 2]
                pool.wait_ge(lru_gate, 8 * (g + 1))
                for n in range(4):
                    row = x[:, n // 2, n % 2]
                    last = nc.gpsimd.tensor_tensor(row, row, xc[:, (4 * g + n) % 5], ALU.mult)
                lru_o.done(last, "ix")
                need(pool, lru_a, "exp", g)
                if g > 0:
                    need(pool, lru_o, "out", g - 1)
                lru_o.done(nc.gpsimd.tensor_tensor(mv[:], av[:], av[:], ALU.mult), "sq")
                need(pool, lru_a, "sqrt", g)
                lru_o.done(nc.gpsimd.tensor_tensor(flat4(x[:]), flat4(mv[:]), flat4(x[:]), ALU.mult), "b")
                need(pool, lru_v, "scan", g)
                h = HL[:, 4 * g:4 * g + 4]
                lru_o.done(nc.gpsimd.tensor_tensor(h, hv[:, :, META:], h, ALU.mult), "out")

        def act_lru(act):
            need_lam(act)
            for tile, g, j, n in own_tiles("lru"):
                if j != OWN:
                    split_hi(act, tile.later(), (0,))
                    act.wait_ge(conv_step, 4 * n + 4)
                    nc.scalar.activation(xchl[:, n % 5, 0], xc[:, n % 5], ACT.Copy).then_inc(xc_hi, 1)
                    split_hi(act, tile.later(), (1,))
                    if g > 0 and j > 0:
                        (act_lru_tanh, act_lru_exp, act_lru_root)[j - 1](act, g - 1)
                    continue
                if g > 1:
                    need(act, lru_v, "scan", g - 2)
                for o in range(8):
                    k, ax, m = o // 4, o // 2 % 2, o % 2
                    c = 4 * g + 2 * k + m
                    if o % 4 == 3:
                        act.wait_ge(units_used, tile.units(k + 1))
                    else:
                        act.wait_ge(own_out, 6 * g + 3 * k + o % 4 + 1)
                    nc.scalar.activation((gx[g % 2] if ax else ga)[:, k, m], banks[2 + o % 6][:, 0:TM], ACT.Sigmoid,
                                         bias=col("gate_x_b" if ax else "gate_a_b", c)).then_inc(lru_gate, 1)
                split_hi(act, tile.later())

        def dve_lru(v):
            v.wait_ge(d_lo, KT)
            for b in range(2):
                nc.vector.memset(vl[b][:], 0.0).then_inc(vl_zero, 1)
            v.wait_ge(vl_zero, 2)
            v.wait_ge(gelu_out, KT)
            for tile, g, j, n in own_tiles("lru"):
                if j == OWN:
                    split_lo(v, tile.later())
                    continue
                row = vl[n % 2]
                tile_done(v, tile)
                nc.vector.tensor_tensor(row[:, LP:], banks[tile.parity][:, 0:TM], norm1.rstd[:], ALU.mult).then_inc(vl_copied, 1)
                v.wait_ge(vl_copied, n + 1)
                for k in range(CONV2):
                    tap = row[:, LP - k:LP - k + TM]
                    w = col("conv_w2", n + KT * (CONV2 - 1 - k))
                    if k == 0:
                        ins = nc.vector.tensor_scalar(xa[:], tap, w, col("conv_b2", n), ALU.mult, ALU.add)
                    else:
                        v.wait_ge(conv_step, 4 * n + k)
                        dst = xc[:, n % 5] if k == CONV2 - 1 else xa[:]
                        if k == CONV2 - 1 and n >= 5:
                            need(v, lru_o, "ix", (n - 5) // 4)
                        ins = nc.vector.scalar_tensor_tensor(dst, tap, w, xa[:], ALU.mult, ALU.add)
                    ins.then_inc(conv_step, 1)
                v.wait_ge(xc_hi, n + 1)
                nc.vector.tensor_tensor(xchl[:, n % 5, 1], xc[:, n % 5], xchl[:, n % 5, 0].bitcast(F), ALU.subtract).then_inc(xc_lo, 1)
                split_lo(v, tile.later())
                if g > 0 and j == 3:
                    dve_lru_one(v, g - 1)
                if g > 1 and j == 0:
                    dve_lru_scan(v, g - 2)

        def pe_lru(pe):
            pe.wait_ge(po_out, KT)
            for tile, g, j, n in own_tiles("lru"):
                if j != OWN:
                    user = bank_user(tile.t)
                    if user is None:
                        pe.wait_ge(vp_copied, KT)
                    else:
                        pe.wait_ge(vl_copied, user + 1)
                    full_tile(pe, tile, u1, TM)
                    continue
                pe.wait_ge(xc_lo, POOL_T * (g + 1))
                if g > 0:
                    pe.wait_ge(lru_gate, 8 * g)
                for k in range(2):
                    pe.wait_ge(lo_ready, tile.units(k + 1))
                    for jj in range(HALF):
                        o, kt = 4 * k + jj // 2, jj % 2
                        if o >= 6 and kt == 0:
                            pe.wait_ge(lru_gate, 8 * g + o - 5)
                        last = product(banks[2 + o % 6][:, 0:TM], xchl, (2 * tile.parity + k) % RING, jj, (4 * g + 2 * k + kt) % 5,
                                       kt == 0, kt == 1, TM)
                        if kt == 1 and jj < HALF - 1:
                            last.then_inc(own_out, 1)
                    last.then_inc(units_used, 1)

        lam_a = Steps(sem("lam_act"), ["abs", "exp"])
        TERMS = list(range(15, 0, -2))
        lam_v = Steps(sem("lam_dve"), ["two", "inv", "z", "zz", "h15"] + [f"{n}{k}" for k in TERMS[1:] for n in ("m", "h")]
                      + ["log", "neg", "sum", "s8", "n8"])

        def need_lam(eng):
            need(eng, lam_v, "n8")

        def act_lam(act):
            act.wait_ge(in_par, 16)
            lam = par[:, PCOL["lam"]:PCOL["lam"] + KT]
            lam_a.done(nc.scalar.activation(lam_sb[:, 0], lam, ACT.Abs), "abs")
            need(act, lam_a, "abs")
            lam_a.done(nc.scalar.activation(lam_sb[:, 0], lam_sb[:, 0], ACT.Exp, scale=-1.0), "exp")

        def dve_lam(v):
            e, z, zz, h, t = (lam_sb[:, k] for k in (0, 1, 2, 3, 4))

            def then(ins, name):
                lam_v.done(ins, name)
                need(v, lam_v, name)
            need(v, lam_a, "exp")
            then(nc.vector.tensor_scalar(t, e, 2.0, None, ALU.add), "two")
            then(nc.vector.reciprocal(t, t), "inv")
            then(nc.vector.tensor_tensor(z, e, t, ALU.mult), "z")
            then(nc.vector.tensor_tensor(zz, z, z, ALU.mult), "zz")
            then(nc.vector.tensor_scalar(h, zz, 0.0, 1.0 / TERMS[0], ALU.mult, ALU.add), "h15")
            for k in TERMS[1:]:
                then(nc.vector.tensor_tensor(h, h, zz, ALU.mult), f"m{k}")
                then(nc.vector.tensor_scalar(h, h, 1.0 / k, None, ALU.add), f"h{k}")
            then(nc.vector.scalar_tensor_tensor(h, h, 2.0, z, ALU.mult, ALU.mult), "log")
            then(nc.vector.tensor_scalar(t, par[:, PCOL["lam"]:PCOL["lam"] + KT], -1.0, 0.0, ALU.mult, ALU.max), "neg")
            then(nc.vector.tensor_tensor(t, t, h, ALU.add), "sum")
            then(nc.vector.tensor_scalar(lam_sb[:, 1], t, 8.0, None, ALU.mult), "s8")
            then(nc.vector.tensor_scalar(lam_sb[:, 2], t, -8.0, None, ALU.mult), "n8")

        ZG = Z2 + 2432 + 1088 * 40
        glp = at("glp", ZG, [P, 2, T])
        sgt = [at(f"sgt{b}", ZG + (2 + b) * K, [P, T]) for b in range(2)]
        mt2 = [at(f"mt2{b}", Z2 + b * K, [P, T]) for b in range(2)]
        glru_pre, glru_out, glru_step, mg2_hi, mg2_lo = (sem(n) for n in ("glru_pre", "glru_out", "glru_step", "mg2_hi", "mg2_lo"))

        def act_glru(act):
            def body(tile):
                b = tile.t % 2
                act.wait_ge(glru_pre, tile.local(1, 1))
                if tile.loops or tile.t >= 2:
                    act.wait_ge(glru_step, tile.local(2, -3))
                nc.scalar.activation(sgt[b][:], glp[:, b], ACT.Sigmoid).then_inc(glru_out, 1)
                act.wait_ge(glru_step, tile.local(2, 2))
                nc.scalar.activation(mg2[:, tile.local(), 0], mt2[b][:], ACT.Copy).then_inc(mg2_hi, 1)
                split_hi(act, tile.later())
                if not tile.loops and tile.t < 3:
                    (act_lru_tanh, act_lru_exp, act_lru_root)[tile.t](act, 3)
            run_tiles(act, "glru", 2, body, peel=2)

        def dve_glru(v):
            def body(tile):
                b, m = tile.t % 2, tile.local()
                tile_done(v, tile)
                if tile.loops or tile.t >= 2:
                    v.wait_ge(glru_out, tile.local(1, -1))
                nc.vector.tensor_tensor(glp[:, b], banks[tile.parity][:, 0:T], norm1.rstd[:, META:], ALU.mult).then_inc(glru_pre, 1)
                v.wait_ge(glru_out, tile.local(1, 1))
                nc.vector.tensor_tensor(mt2[b][:], HL[:, m], sgt[b][:], ALU.mult).then_inc(glru_step, 1)
                v.wait_ge(glru_step, tile.local(2, 1))
                nc.vector.tensor_tensor(mt2[b][:], mt2[b][:], PO[:, m], ALU.add).then_inc(glru_step, 1)
                v.wait_ge(mg2_hi, tile.local(1, 1))
                nc.vector.tensor_tensor(mg2[:, m, 1], mt2[b][:], mg2[:, m, 0].bitcast(F), ALU.subtract).then_inc(mg2_lo, 1)
                split_lo(v, tile.later())
                if not tile.loops and tile.t == 0:
                    dve_lru_scan(v, 2)
                if not tile.loops and tile.t == 2:
                    dve_lru_one(v, 3)
                if not tile.loops and tile.t == 3:
                    dve_lru_scan(v, 3)
                    need(v, lru_o, "out", 3)
            run_tiles(v, "glru", 2, body, peel=2)

        wout2_out = sem("wout2_out")

        def dve_add_phase(v, phase, dst, scale, out_sem, norm=None):
            def body(tile):
                tile_done(v, tile)
                m = tile.local()
                nc.vector.scalar_tensor_tensor(dst[:, m], dst[:, m], scale, banks[tile.parity][:, 0:T],
                                               ALU.mult, ALU.add).then_inc(out_sem, 1)
                if norm is not None:
                    norm.dve_tile(v, m, tile.local(1, 1))
                split_lo(v, tile.later())
            run_tiles(v, phase, 2, body)

        class Mlp:
            def __init__(self, phase, x, moving, hidden, tmp, scale, norm=None, norm_out=None):
                self.phase, self.x, self.moving, self.hid, self.scale = phase, x, moving, hidden, scale
                self.norm, self.norm_out = norm, norm_out
                self.r = [at(f"{phase}_r{b}", tmp + K * b, [P, T]) for b in range(2)]
                self.q = [at(f"{phase}_q{b}", tmp + K * (2 + b), [P, T]) for b in range(2)]
                self.relu, self.sq, self.hi, self.lo, self.out = (sem(f"{phase}_{n}") for n in ("relu", "sq", "hi", "lo", "out"))

            def groups(self, eng, up, down):
                def group(loops, g):
                    first = FIRST[self.phase] + (0 if loops else 2 * KT * g)
                    run_tiles(eng, self.phase, 2, lambda t: up(t, g), loops, first, KT)
                    run_tiles(eng, self.phase, 2, lambda t: down(t, g), loops, first + KT, KT)
                group((), 0)
                with eng.Fori(1, FF_GROUPS - 1) as n:
                    group(((n, 2 * KT),), n)
                group((), FF_GROUPS - 1)

            @staticmethod
            def inner(tile, g):
                return tile.loops if isinstance(g, int) else tile.loops[1:]

            def nth(self, tile, c, g, m=1):
                v = m * tile.t + c
                v = v + m * KT * g if isinstance(g, int) else g * (KT * m) + v
                for reg, per in self.inner(tile, g):
                    v = reg * (per * m) + v
                return v

            def place(self, tile, g):
                v = tile.t
                for reg, per in self.inner(tile, g):
                    v = reg * per + v
                return v

            def early(self, tile, g):
                return not self.inner(tile, g) and tile.t < 2

            @staticmethod
            def is_group(g, n):
                return isinstance(g, int) and g == n

            def act(self, act, hooks=None):
                def up(tile, g):
                    if self.is_group(g, 0):
                        hooked(tile, hooks)
                    b, m = tile.t % 2, self.place(tile, g)
                    act.wait_ge(self.relu, self.nth(tile, 1, g))
                    if not (self.is_group(g, 0) and self.early(tile, g)):
                        act.wait_ge(self.lo, self.nth(tile, -1, g))
                    nc.scalar.activation(self.q[b][:], self.r[b][:], ACT.Square).then_inc(self.sq, 1)
                    act.wait_ge(self.sq, self.nth(tile, 1, g))
                    nc.scalar.activation(self.hid[:, m, 0], self.q[b][:], ACT.Copy).then_inc(self.hi, 1)
                    split_hi(act, tile.later())

                def down(tile, g):
                    if self.norm_out is not None and self.is_group(g, FF_GROUPS - 1):
                        act.wait_ge(self.out, self.nth(tile, 1, g))
                        self.norm_out.act_tile(act, self.place(tile, g))
                    split_hi(act, tile.later())
                self.groups(act, up, down)

            def dve(self, v, hooks=None):
                def up(tile, g):
                    if self.is_group(g, 0):
                        hooked(tile, hooks)
                    b, m = tile.t % 2, self.place(tile, g)
                    tile_done(v, tile)
                    if not (self.is_group(g, 0) and self.early(tile, g)):
                        v.wait_ge(self.sq, self.nth(tile, -1, g))
                    if self.norm is None:
                        ins = nc.vector.tensor_scalar(self.r[b][:], banks[tile.parity][:, 0:T], 0.0, None, ALU.max)
                    else:
                        ins = nc.vector.scalar_tensor_tensor(self.r[b][:], banks[tile.parity][:, 0:T], 0.0, self.norm.rstd[:],
                                                             ALU.max, ALU.mult)
                    ins.then_inc(self.relu, 1)
                    v.wait_ge(self.hi, self.nth(tile, 1, g))
                    nc.vector.tensor_tensor(self.hid[:, m, 1], self.q[b][:], self.hid[:, m, 0].bitcast(F),
                                            ALU.subtract).then_inc(self.lo, 1)
                    split_lo(v, tile.later())

                def down(tile, g):
                    tile_done(v, tile)
                    m = self.place(tile, g)
                    nc.vector.scalar_tensor_tensor(self.x[:, m], self.x[:, m], self.scale if self.is_group(g, 0) else 1.0,
                                                   banks[tile.parity][:, 0:T], ALU.mult, ALU.add).then_inc(self.out, 1)
                    if self.norm_out is not None and self.is_group(g, FF_GROUPS - 1):
                        self.norm_out.dve_tile(v, m, self.place(tile, g) + 1)
                    split_lo(v, tile.later())
                self.groups(v, up, down)

            def pe(self, pe, before, after=None, entry=None):
                def up(tile, g):
                    if self.is_group(g, 0) and self.early(tile, g) and entry is not None:
                        entry(tile.t)
                    if not self.early(tile, g):
                        pe.wait_ge(self.relu, self.nth(tile, -1, g))
                    elif not self.is_group(g, 0):
                        pe.wait_ge(self.out, self.nth(tile, -1, g))
                    first = self.is_group(g, 0) and not tile.loops and tile.t == 0
                    full_tile(pe, tile, self.moving, T, before if first else None)
                    if first and after is not None:
                        after()

                def down(tile, g):
                    if self.early(tile, g):
                        pe.wait_ge(self.relu, self.nth(tile, KT - 1, g))
                    else:
                        pe.wait_ge(self.out, self.nth(tile, -1, g))

                    def hidden_ready(k):
                        pe.wait_ge(self.lo, self.nth(tile, HALF * (k + 1) - tile.t, g))
                    full_tile(pe, tile, self.hid, T, hidden_ready if self.early(tile, g) else None)
                self.groups(pe, up, down)

        x2 = X1[:, :, META:]
        u2 = at("u2", B + 49 * K, [P, KT, 2, T], R)
        hid2 = at("hid2", B + 17 * K, [P, KT, 2, T], R)
        X3 = at("X3", B + 83 * K, [P, KT, T])
        xh3 = at("xh3", B + 99 * K, [P, KT, 2, T], R)
        norm2 = Norm("norm2", x2, T, "norm2_g", u2, Z2)
        final = Norm("final", x2, T, "final_g", xh3, B + 49 * K)
        mlp2 = Mlp("ff2", x2, u2, hid2, Z2 + 4 * K, 1.0, norm2, final)

        mix = at("mix", B + 17 * K, [P, KT, 2, T], R)
        Q = B + 49 * K
        gp = at("gp", Q, [P, 17, T])
        sr = at("sr", Q + 17 * K, [P, GLA_VT, T])
        ym = at("ym", Q + 25 * K, [P, C3_T, T])
        cg = [at(f"cg{b}", B + (17 + b) * K, [P, T]) for b in range(2)]
        hp = at("hp", B + 19 * K, [P, T + 2])
        ca = at("ca", B + 21 * K, [P, T])
        rstd_sq = at("rstd_sq", B + 22 * K, [P, T])
        srp = at("srp", B + 23 * K, [P, 2, T])
        rstd_squared, x3_out, sr_pre = (sem(n) for n in ("rstd_squared", "x3_out", "sr_pre"))
        hp_zero, c_out, ub_out, c3_step, sr_out, gp_out = (
            sem(n) for n in ("hp_zero", "c_out", "ub_out", "c3_step", "sr_out", "gp_out"))

        def conv_place(tile):
            kind, s = tile.t % 3, tile.t // 3

            def nth(c=0, m=1):
                return tile.loops[-1][0] * (2 * m) + (m * s + c) if tile.loops else m * s + c
            return kind, s, nth

        def dve_conv3(v):
            nc.vector.memset(hp[:], 0.0).then_inc(hp_zero, 1)
            v.wait_ge(hp_zero, 1)

            def body(tile):
                kind, s, nth = conv_place(tile)
                if not tile.loops and tile.t == 0:
                    final.dve_rstd(v)
                    nc.vector.tensor_tensor(rstd_sq[:], final.rstd[:], final.rstd[:], ALU.mult).then_inc(rstd_squared, 1)
                    v.wait_ge(rstd_squared, 1)
                tile_done(v, tile)
                if kind == 0:
                    nc.vector.tensor_tensor(cg[s % 2][:], banks[tile.parity][:, 0:T], rstd_sq[:], ALU.mult).then_inc(c_out, 1)
                    split_lo(v, tile.later())
                    for k in range(2):
                        kt = nth(k, 2)
                        nc.vector.scalar_tensor_tensor(X3[:, kt], x2[:, kt], col("final_g", kt), final.rstd[:],
                                                       ALU.mult, ALU.mult).then_inc(x3_out, 1)
                elif kind == 1:
                    v.wait_ge(c_out, nth(1))
                    nc.vector.tensor_tensor(hp[:, 2:], banks[tile.parity][:, 0:T], cg[s % 2][:], ALU.mult).then_inc(ub_out, 1)
                    v.wait_ge(ub_out, nth(1, 2))
                    for k in range(CONV3):
                        tap, w = hp[:, 2 - k:2 - k + T], col("conv_w3", nth(C3_T * (CONV3 - 1 - k)))
                        if k == 0:
                            ins = nc.vector.tensor_scalar(ca[:], tap, w, None, ALU.mult)
                        else:
                            v.wait_ge(c3_step, nth(k, 4))
                            ins = nc.vector.scalar_tensor_tensor(ca[:], tap, w, ca[:], ALU.mult, ALU.add)
                        ins.then_inc(c3_step, 1)
                    v.wait_ge(c3_step, nth(3, 4))
                    nc.vector.tensor_tensor(ca[:], ca[:], final.rstd[:], ALU.mult).then_inc(c3_step, 1)
                    split_lo(v, tile.later())
                else:
                    v.wait_ge(c3_step, nth(4, 4))
                    nc.vector.tensor_tensor(ym[:, nth()], banks[tile.parity][:, 0:T], ca[:], ALU.mult).then_inc(ub_out, 1)
                    split_lo(v, tile.later())
            run_tiles(v, "conv3", 6, body)

        def pe_conv3(pe):
            def body(tile):
                kind, s, nth = conv_place(tile)
                first = not tile.loops and s == 0
                if kind == 2:
                    pe.wait_ge(c_out, nth(1))
                elif first:
                    pe.wait_ge(mlp2.out, KT * FF_GROUPS - 1 + kind)
                elif not first:
                    pe.wait_ge(ub_out, nth(-1 if kind == 0 else 0, 2))
                full_tile(pe, tile, xh3, T, (lambda k: final.ready(pe, k)) if first and kind == 0 else None)
                if first and kind == 0:
                    final.pe(pe)
            run_tiles(pe, "conv3", 6, body)

        zl, q3, k3 = gp[:, 0], gp[:, 1:5], gp[:, 5:9]
        E3 = B + 99 * K
        qd = at("qd", E3, [P, GLA_H, T])
        ki = at("ki", E3 + 4 * K, [P, GLA_H, T])
        ke = at("ke", E3 + 8 * K, [P, GLA_H, T])
        ss = at("gla_s", E3 + 12 * K, [P, GLA_H, T])
        l1 = at("gla_l1", E3 + 16 * K, [P, GLA_H, T])
        l2 = at("gla_l2", E3 + 20 * K, [P, GLA_H, T])
        ps3 = at("gla_ps", E3 + 24 * K, [P, GLA_H * NB, P])
        dcy = at("gla_dcy", E3 + 28 * K, [P, GLA_H * NCH])
        crs = at("conv_rs", B, [P, C3_T, T])
        csq = at("conv_sq", B + 8 * K, [P, C3_T, T])
        sst = at("gla_state", B, [P, GLA_H, NCH - 1, T])
        k_tok = at("k_tok", B + 12 * K, [P, NB, GLA_H * P])
        v_tok3 = at("v_tok3", Q, [P, NB, GLA_VT * P])
        oo = at("gla_o", E3 + 16 * K, [P, GLA_VT, T])
        osq = at("gla_osq", E3 + 4 * K, [P, GLA_VT, T])
        ors = at("gla_ors", E3 + 12 * K, [P, GLA_H, T])
        H4 = range(GLA_H)
        g_o = Steps(sem("gla_pool"), ["zero"])
        g_a = Steps(sem("gla_act"), ["csq"] + [f"cstd{b}" for b in range(4)] + [f"idn{h}" for h in H4] + ["abs", "exp", "ln"]
                    + ["chi0", "chi1", "eq", "ek", "ee", "kt0", "kt1", "vt0", "vt1", "vt2", "vt3"]
                    + [f"o{h}" for h in H4] + ["osq", "ostd0", "ostd1", "ohi0", "ohi1"])
        g_v = Steps(sem("gla_dve"), [f"crs{b}" for b in range(4)] + ["cy", "min", "la"] + [f"sum{h}" for h in H4] + ["rest"]
                    + ["clo0", "clo1", "dec", "qd", "ki", "ke", "sc0", "sc1"]
                    + [f"st{h}_{c}" for h in H4 for c in range(NCH - 1)] + ["ors0", "ors1", "on", "oy", "olo0", "olo1"])
        g_p = Steps(sem("gla_pe"), [f"cst{b}" for b in range(4)] + [f"z{h}" for h in H4]
                    + ["vt0", "vt1", "vt2", "vt3", "kt0", "kt1", "sc0", "sc1"]
                    + [n for h in H4 for n in (f"dl{h}", f"o{h}")] + ["ost0", "ost1"])

        def two(bank):
            return banks[bank][:].rearrange("p (a t) -> p a t", a=2)

        def by_chunk(ap):
            return ap.rearrange("p h (c t) -> p (h c) t", c=NCH)

        def pool_gla(pool):
            pool.wait_ge(gp_out, COUNT["gla_p"])
            g_o.done(nc.gpsimd.memset(ps3[:], 0.0), "zero")

        def act_gla(act):
            act.wait_ge(ub_out, 2 * C3_T)
            g_a.done(nc.scalar.activation(csq[:], ym[:], ACT.Square), "csq")
            for b in range(4):
                need(act, g_p, f"cst{b}")
                g_a.done(nc.scalar.activation(crs[:, 2 * b:2 * b + 2], two(4 + b), ACT.Sqrt, bias=EPS, scale=1.0 / P), f"cstd{b}")
            for h in H4:
                need(act, g_p, f"z{h | 1}")
                g_a.done(nc.scalar.activation(l1[:, h], two(2 + h // 2)[:, h % 2], ACT.Identity, bias=col("gate_bias3", h)), f"idn{h}")
            need(act, g_a, f"idn{GLA_H - 1}")
            g_a.done(nc.scalar.activation(l2[:], l1[:], ACT.Abs), "abs")
            need(act, g_a, "abs")
            g_a.done(nc.scalar.activation(l2[:], l2[:], ACT.Exp, scale=-1.0), "exp")
            need(act, g_a, "exp")
            g_a.done(nc.scalar.activation(l2[:], l2[:], ACT.Ln, bias=1.0), "ln")
            need(act, g_v, "cy")
            for q in range(2):
                g_a.done(nc.scalar.activation(mix[:, 4 * q:4 * q + 4, 0], ym[:, 4 * q:4 * q + 4], ACT.Copy), f"chi{q}")
            need(act, g_v, f"sum{GLA_H - 1}")
            g_a.done(nc.scalar.activation(qd[:], ss[:], ACT.Exp, scale=1.0 / GATE_TAU), "eq")
            g_a.done(nc.scalar.activation(ki[:], ss[:], ACT.Exp, scale=-1.0 / GATE_TAU), "ek")
            need(act, g_v, "rest")
            g_a.done(nc.scalar.activation(ke[:], ke[:], ACT.Exp, scale=1.0 / GATE_TAU), "ee")
            for b in range(NB):
                need(act, g_p, f"kt{b}")
                g_a.done(nc.scalar.activation(k_tok[:, b], banks[2 + b][:], ACT.Copy), f"kt{b}")
            need(act, g_v, "ke")
            for n in range(4):
                need(act, g_p, f"vt{n}")
                g_a.done(nc.scalar.activation(v_tok3[:, n // 2, 512 * (n % 2):512 * (n % 2) + 512], banks[4 + n][:], ACT.Copy), f"vt{n}")
            for h in H4:
                need(act, g_p, f"o{h}")
                g_a.done(nc.scalar.activation(oo[:, 2 * h:2 * h + 2], two(5 + h % 2), ACT.Copy), f"o{h}")
            need(act, g_a, f"o{GLA_H - 1}")
            g_a.done(nc.scalar.activation(osq[:], oo[:], ACT.Square), "osq")
            for b in range(2):
                need(act, g_p, f"ost{b}")
                g_a.done(nc.scalar.activation(ors[:, 2 * b:2 * b + 2], two(2 + b), ACT.Sqrt, bias=EPS, scale=1.0 / T), f"ostd{b}")
            need(act, g_v, "oy")
            for q in range(2):
                g_a.done(nc.scalar.activation(mix[:, 8 + 4 * q:12 + 4 * q, 0], oo[:, 4 * q:4 * q + 4], ACT.Copy), f"ohi{q}")

        def dve_gla(v):
            for b in range(4):
                need(v, g_a, f"cstd{b}")
                g_v.done(nc.vector.reciprocal(crs[:, 2 * b:2 * b + 2], crs[:, 2 * b:2 * b + 2]), f"crs{b}")
            need(v, g_v, "crs3")
            for c in range(C3_T):
                last = nc.vector.scalar_tensor_tensor(ym[:, c], ym[:, c], col("conv_g3", c), crs[:, c], ALU.mult, ALU.mult)
            g_v.done(last, "cy")
            need(v, g_a, "abs")
            g_v.done(nc.vector.tensor_scalar(l1[:], l1[:], 0.0, None, ALU.min), "min")
            need(v, g_v, "min")
            need(v, g_a, "ln")
            g_v.done(nc.vector.tensor_tensor(l1[:], l1[:], l2[:], ALU.subtract), "la")
            need(v, g_v, "la")
            for h in H4:
                g_v.done(nc.vector.tensor_tensor_scan(ss[:, h], const("run_up"), l1[:, h], 0.0, ALU.mult, ALU.add), f"sum{h}")
            need(v, g_v, f"sum{GLA_H - 1}")
            s_end = by_chunk(ss[:])[:, :, CH - 1].unsqueeze(2).broadcast_to([P, GLA_H * NCH, CH])
            g_v.done(nc.vector.tensor_tensor(by_chunk(ke[:]), s_end, by_chunk(ss[:]), ALU.subtract), "rest")
            for q in range(2):
                need(v, g_a, f"chi{q}")
                g_v.done(nc.vector.tensor_tensor(mix[:, 4 * q:4 * q + 4, 1], ym[:, 4 * q:4 * q + 4],
                                                 mix[:, 4 * q:4 * q + 4, 0].bitcast(F), ALU.subtract), f"clo{q}")
            need(v, g_a, "eq")
            g_v.done(nc.vector.tensor_copy(dcy[:], by_chunk(qd[:])[:, :, CH - 1]), "dec")
            need(v, g_v, "dec")
            def flat(ap):
                return ap.rearrange("p h t -> p (h t)")
            g_v.done(nc.vector.scalar_tensor_tensor(flat(qd[:]), flat(q3), P ** -0.5, flat(qd[:]), ALU.mult, ALU.mult), "qd")
            need(v, g_a, "ek")
            g_v.done(nc.vector.tensor_tensor(ki[:], k3, ki[:], ALU.mult), "ki")
            need(v, g_a, "ee")
            g_v.done(nc.vector.tensor_tensor(ke[:], k3, ke[:], ALU.mult), "ke")
            need(v, g_o, "zero")
            mask = const("incl_up").bitcast(mybir.dt.uint32).unsqueeze(1).broadcast_to([P, 4, P])
            for b in range(2):
                need(v, g_p, f"sc{b}")
                g_v.done(nc.vector.copy_predicated(ps3[:, 4 * b:4 * b + 4], mask, banks[b][:].rearrange("p (n c) -> p n c", n=4)), f"sc{b}")
            for h in H4:
                need(v, g_p, f"dl{h}")
                for c in range(NCH - 1):
                    new = banks[2 + c][:, 0:T]
                    if c == 0:
                        ins = nc.vector.tensor_copy(sst[:, h, c], new)
                    else:
                        need(v, g_v, f"st{h}_{c - 1}")
                        ins = nc.vector.scalar_tensor_tensor(sst[:, h, c], sst[:, h, c - 1], dcy[:, NCH * h + c:NCH * h + c + 1],
                                                             new, ALU.mult, ALU.add)
                    g_v.done(ins, f"st{h}_{c}")
            for b in range(2):
                need(v, g_a, f"ostd{b}")
                g_v.done(nc.vector.reciprocal(ors[:, 2 * b:2 * b + 2], ors[:, 2 * b:2 * b + 2]), f"ors{b}")
            need(v, g_v, "ors1")
            for c in range(GLA_VT):
                last = nc.vector.scalar_tensor_tensor(oo[:, c], oo[:, c], col("gla_g3", c), ors[:, c // 2], ALU.mult, ALU.mult)
            g_v.done(last, "on")
            need(v, g_v, "on")
            g_v.done(nc.vector.tensor_tensor(oo[:], oo[:], sr[:], ALU.mult), "oy")
            for q in range(2):
                need(v, g_a, f"ohi{q}")
                g_v.done(nc.vector.tensor_tensor(mix[:, 8 + 4 * q:12 + 4 * q, 1], oo[:, 4 * q:4 * q + 4],
                                                 mix[:, 8 + 4 * q:12 + 4 * q, 0].bitcast(F), ALU.subtract), f"olo{q}")

        def pe_gla(pe):
            need(pe, g_a, "csq")
            for b in range(4):
                g_p.done(nc.tensor.matmul(banks[4 + b][:], const("ones"), csq[:, 2 * b:2 * b + 2], start=True, stop=True), f"cst{b}")
            pe.wait_ge(gp_out, COUNT["gla_p"])
            for h in H4:
                g_p.done(nc.tensor.matmul(two(2 + h // 2)[:, h % 2], wgu_sb[:, h], zl[0:16], start=True, stop=True), f"z{h}")
            for n in range(4):
                need(pe, g_a, f"cstd{n}")
                for c in range(4):
                    last = nc.tensor.transpose(banks[4 + n][:, P * c:P * c + P],
                                               gp[:, 9 + 4 * (n % 2) + c, P * (n // 2):P * (n // 2) + P], const("ident"))
                g_p.done(last, f"vt{n}")
            need(pe, g_v, "ke")
            need(pe, g_a, f"idn{GLA_H - 1}")
            for b in range(NB):
                for h in H4:
                    last = nc.tensor.transpose(banks[2 + b][:, P * h:P * h + P], ke[:, h, P * b:P * b + P], const("ident"))
                g_p.done(last, f"kt{b}")
            for b in range(2):
                for n in range(4):
                    h, tb = (4 * b + n) // NB, n % NB
                    last = nc.tensor.matmul(banks[b][:, P * n:P * n + P], ki[:, h, P * tb:P * tb + P], qd[:, h, P * tb:P * tb + P],
                                            start=True, stop=True)
                g_p.done(last, f"sc{b}")
            need(pe, g_a, "vt3")
            for h in H4:
                if h > 0:
                    need(pe, g_v, f"st{h - 1}_{NCH - 2}")
                for c in range(NCH - 1):
                    rows = slice(CH * (c % 2), CH * (c % 2) + CH)
                    last = nc.tensor.matmul(banks[2 + c][:, 0:T], k_tok[rows, c // 2, P * h:P * h + P],
                                            v_tok3[rows, c // 2, T * h:T * h + T], start=True, stop=True)
                g_p.done(last, f"dl{h}")
                need(pe, g_v, f"st{h}_{NCH - 2}")
                if h >= 2:
                    need(pe, g_a, f"o{h - 2}")
                for n in range(2):
                    o = two(5 + h % 2)[:, n]
                    c0 = T * h + P * n
                    for tb in range(NB):
                        nc.tensor.matmul(o[:, P * tb:P * tb + P], v_tok3[:, tb, c0:c0 + P], ps3[:, NB * h + tb], start=tb == 0, stop=False)
                    for c in range(1, NCH):
                        last = nc.tensor.matmul(o[:, CH * c:CH * c + CH], sst[:, h, c - 1, P * n:P * n + P], qd[:, h, CH * c:CH * c + CH],
                                                start=False, stop=c == NCH - 1)
                g_p.done(last, f"o{h}")
            need(pe, g_a, "osq")
            for b in range(2):
                for n in range(2):
                    for m in range(2):
                        last = nc.tensor.matmul(two(2 + b)[:, n], const("ones"), osq[:, 4 * b + 2 * n + m], start=m == 0, stop=m == 1)
                g_p.done(last, f"ost{b}")

        wout3_out = sem("wout3_out")

        class LayerNorm:
            def __init__(self, name, x, g, b, dst, scratch):
                self.x, self.g, self.b, self.dst = x, g, b, dst
                self.sq = at(name + "_sq", scratch, [P, 2, 4, T])
                self.mu = at(name + "_mu", scratch + 8 * K, [P, T])
                self.std = at(name + "_std", scratch + 9 * K, [P, T])
                self.rstd = at(name + "_rstd", scratch + 10 * K, [P, T])
                last = [f"{n}{q}" for q in range(4) for n in (("aff", "hi") if dst is not None else ("aff",))]
                self.a = Steps(sem(name + "_act"), ["mu"] + [f"sq{q}" for q in range(4)] + ["std"] + last)
                self.v = Steps(sem(name + "_dve"), [f"cen{q}" for q in range(4)] + ["rstd"] + [f"nrm{q}" for q in range(4)]
                               + ([f"lo{q}" for q in range(4)] if dst is not None else []))
                self.p = Steps(sem(name + "_pe"), ["mean"] + [f"var{q}" for q in range(4)])

            def part(self, q):
                return self.x[:, 4 * q:4 * q + 4]

            @staticmethod
            def over(ap):
                return ap.unsqueeze(1).broadcast_to([P, 4, T])

            def act(self, act):
                need(act, self.p, "mean")
                self.a.done(nc.scalar.activation(self.mu[:], banks[2][:, 0:T], ACT.Copy, scale=1.0 / D), "mu")
                for q in range(4):
                    need(act, self.v, f"cen{q}")
                    if q >= 2:
                        need(act, self.p, f"var{q - 2}")
                    self.a.done(nc.scalar.activation(self.sq[:, q % 2], self.part(q), ACT.Square), f"sq{q}")
                need(act, self.p, "var3")
                self.a.done(nc.scalar.activation(self.std[:], banks[3][:, 0:T], ACT.Sqrt, bias=LN_EPS, scale=1.0 / D), "std")
                for q in range(4):
                    need(act, self.v, f"nrm{q}")
                    for j in range(4):
                        kt = 4 * q + j
                        last = nc.scalar.activation(self.x[:, kt], self.x[:, kt], ACT.Identity, bias=col(self.b, kt), scale=col(self.g, kt))
                    self.a.done(last, f"aff{q}")
                    if self.dst is not None:
                        need(act, self.a, f"aff{q}")
                        self.a.done(nc.scalar.activation(self.dst[:, 4 * q:4 * q + 4, 0], self.part(q), ACT.Copy), f"hi{q}")

            def pe(self, pe):
                for kt in range(KT):
                    last = nc.tensor.matmul(banks[2][:, 0:T], const("ones"), self.x[:, kt], start=kt == 0, stop=kt == KT - 1)
                self.p.done(last, "mean")
                for q in range(4):
                    need(pe, self.a, f"sq{q}")
                    for j in range(4):
                        last = nc.tensor.matmul(banks[3][:, 0:T], const("ones"), self.sq[:, q % 2, j], start=q + j == 0, stop=q + j == 6)
                    self.p.done(last, f"var{q}")

            def dve(self, v):
                need(v, self.a, "mu")
                for q in range(4):
                    self.v.done(nc.vector.tensor_tensor(self.part(q), self.part(q), self.over(self.mu[:]), ALU.subtract), f"cen{q}")
                need(v, self.a, "std")
                self.v.done(nc.vector.reciprocal(self.rstd[:], self.std[:]), "rstd")
                need(v, self.v, "rstd")
                for q in range(4):
                    self.v.done(nc.vector.tensor_tensor(self.part(q), self.part(q), self.over(self.rstd[:]), ALU.mult), f"nrm{q}")
                if self.dst is not None:
                    for q in range(4):
                        need(v, self.a, f"hi{q}")
                        self.v.done(nc.vector.tensor_tensor(self.dst[:, 4 * q:4 * q + 4, 1], self.part(q),
                                                            self.dst[:, 4 * q:4 * q + 4, 0].bitcast(F), ALU.subtract), f"lo{q}")

            def ready(self, pe, k):
                need(pe, self.v, f"lo{2 * k + 1}")

        xh4 = at("xh4", B + 99 * K, [P, KT, 2, T], R)
        hid3 = at("hid3", B + 17 * K, [P, KT, 2, T], R)
        ln1 = LayerNorm("ln1", X3, "ln1_g", "ln1_b", xh4, B)
        mlp3 = Mlp("ff3", X3, xh4, hid3, B + 49 * K, ALPHA3)
        ln2 = LayerNorm("ln2", X3, "ln2_g", "ln2_b", None, B + 17 * K)

        block = ctx.enter_context(nc.Block())

        @block.sync
        def _(sp):
            for k in range(RING):
                sp.dma_start(raw[:, k], stream[k]).then_inc(raw_in[k], 16)
            rounds = N_UNITS // RING
            by_round = stream[0:RING * rounds].rearrange("(n k) p j c -> n k p j c", k=RING)
            with sp.Fori(1, rounds) as n:
                for k in range(RING):
                    sp.wait_ge(lo_ready, n * RING + (k + 1 - RING))
                    sp.dma_start(raw[:, k], by_round[n, k]).then_inc(raw_in[k], 16)
            for u in range(RING * rounds, N_UNITS):
                sp.wait_ge(lo_ready, u + 1 - RING)
                sp.dma_start(raw[:, u % RING], stream[u]).then_inc(raw_in[u % RING], 16)
            for q in range(4):
                need(sp, ln2.a, f"aff{q}")
                sp.dma_start(out[:, 4 * q:4 * q + 4], X3[:, 4 * q:4 * q + 4]).then_inc(stored, 16)
            sp.wait_ge(stored, 64)

        @block.gpsimd
        def _(pool):
            for norm, parts in ((x_norm, in_x), (mem_norm, in_mem)):
                norm.pool_start(pool)
                for q in range(4):
                    pool.wait_ge(parts[q], 16)
                    for j in range(4):
                        norm.pool_tile(pool, 4 * q + j)
            pool_kk(pool)
            pool_rwkv(pool)
            pool_gn(pool)
            pool.wait_ge(in_meta, 16)
            norm1.pool(pool, wout1_out)
            pool_lru(pool)
            norm2.pool(pool, wout2_out)
            final.pool(pool, mlp2.out, KT * (FF_GROUPS - 1))
            pool_gla(pool)

        @block.scalar
        def _(act):
            act.dma_start(par[:], params).then_inc(in_par, 16)
            for q in range(4):
                act.dma_start(x_raw[:, 4 * q:4 * q + 4], xT[:, 4 * q:4 * q + 4]).then_inc(in_x[q], 16)
            act.dma_start(cst[:], consts).then_inc(in_cst, 16)
            for q in range(4):
                act.dma_start(mem_raw[:, 4 * q:4 * q + 4], memT[:, 4 * q:4 * q + 4]).then_inc(in_mem[q], 16)
            act.dma_start(w2_sb[:], w2).then_inc(in_lora, 16)
            act.dma_start(a2_sb[:], a2).then_inc(in_lora, 16)
            act.dma_start(wgu_sb[:], wgu).then_inc(in_lora, 16)

            def split_all(norm, parts, half=(0, 1)):
                for kt in range(HALF * half[0], HALF * (half[-1] + 1)):
                    if kt % 4 == 0:
                        act.wait_ge(parts[kt // 4], 16)
                    norm.act_tile(act, kt)
            for t in range(RING // 2):
                split_hi(act, Tile(0, t))
            act.wait_ge(in_par, 16)
            split_all(x_norm, in_x)

            def after_plain0():
                x_norm.act_root(act)
                act_lam(act)
                split_all(mem_norm, in_mem, (0,))
            act_split_phase(act, "plain", {0: after_plain0, 1: lambda: split_all(mem_norm, in_mem, (1,))})
            act_split_phase(act, "mem_kv", {0: lambda: mem_norm.act_root(act)})
            act_attn(act)
            act_func_phase(act, "silu", sl, silu_pre, sg[:, A_T:A_T + PAIRS], ACT.Silu, silu_out)
            act_kk(act)
            act_rwkv(act)
            act_gn(act)
            act_merge(act)
            act.wait_ge(in_meta, 16)
            act_norm_phase(act, "wout1", norm1, wout1_out)
            act_func_phase(act, "gpool", gpl, gpool_pre, PO, ACT.Sigmoid, gpool_out, {0: lambda: norm1.act_root(act)})
            act_func_phase(act, "gelu", gel, gelu_pre, HL, ACT.Gelu_apprx_tanh, gelu_out)
            act_pool(act)
            act_lru(act)
            act_glru(act)
            act_norm_phase(act, "wout2", norm2, wout2_out)
            mlp2.act(act, {0: lambda: norm2.act_root(act)})
            act_split_phase(act, "conv3", {0: lambda: final.act_root(act)})
            act_func_phase(act, "gla_r", srp, sr_pre, sr, ACT.Silu, sr_out)
            act_split_phase(act, "gla_p")
            act_gla(act)
            act_split_phase(act, "wout3")
            ln1.act(act)
            mlp3.act(act)
            ln2.act(act)

        @block.vector
        def _(v):
            def split_all(norm, half=(0, 1)):
                for kt in range(HALF * half[0], HALF * (half[-1] + 1)):
                    norm.dve_tile(v, kt, kt + 1)
            for t in range(RING // 2):
                split_lo(v, Tile(0, t))
            v.wait_ge(in_par, 16)
            split_all(x_norm)

            dve_scaled_phase(v, "plain", x_norm, pl, plain_out, {0: lambda: x_norm.dve_rstd(v)},
                             {0: lambda: split_all(mem_norm, (0,)), 1: lambda: split_all(mem_norm, (1,))})
            dve_scaled_phase(v, "mem_kv", mem_norm, mkv, mem_out, {0: lambda: mem_norm.dve_rstd(v)}, {1: lambda: dve_lam(v)})
            dve_attn(v)
            dve_pre_phase(v, "silu", x_norm, sl, silu_pre, silu_out)
            dve_kk(v)
            dve_rwkv(v)
            dve_gn(v)
            dve_merge(v)
            dve_wout1(v)
            dve_pre_phase(v, "gpool", norm1, gpl, gpool_pre, gpool_out, {0: lambda: norm1.dve_rstd(v)})
            dve_pre_phase(v, "gelu", norm1, gel, gelu_pre, gelu_out)
            dve_pool(v)
            dve_lru(v)
            dve_glru(v)
            dve_add_phase(v, "wout2", x2, 1.0, wout2_out, norm2)
            mlp2.dve(v, {0: lambda: norm2.dve_rstd(v)})
            dve_conv3(v)
            dve_pre_phase(v, "gla_r", final, srp, sr_pre, sr_out)
            dve_scaled_phase(v, "gla_p", final, gp, gp_out)
            dve_gla(v)
            dve_add_phase(v, "wout3", X3, ALPHA3, wout3_out)
            ln1.dve(v)
            mlp3.dve(v)
            ln2.dve(v)

        @block.tensor
        def _(pe):
            def x_stat():
                pe.wait_ge(in_cst, 16)
                x_norm.pe(pe)
            plain_phase(pe, "plain", hx, plain_out, before=lambda k: x_norm.ready(pe, k), after=x_stat, after_t=1)
            plain_phase(pe, "mem_kv", mem_hl, mem_out, before=lambda k: mem_norm.ready(pe, k), after=lambda: mem_norm.pe(pe),
                        entry=lambda t: pe.wait_ge(plain_out, COUNT["plain"] - 1 + t))
            pe_attn(pe)
            plain_phase(pe, "silu", hx, silu_pre, entry=lambda t: pe.wait_ge(shift_copied, SHIFT_T))
            pe_kk(pe)
            pe_rwkv(pe)
            pe_gn(pe)
            pe_merge(pe)
            plain_phase(pe, "wout1", mg, wout1_out, before=lambda k: pe.wait_ge(mg_lo, HALF * (k + 1)),
                        entry=lambda t: pe.wait_ge(gate_pre, N_BRANCH * KT))
            plain_phase(pe, "gpool", u1, gpool_pre, before=lambda k: norm1.ready(pe, k), after=lambda: norm1.pe(pe),
                        entry=lambda t: pe.wait_ge(wout1_out, KT - 1 + t))
            plain_phase(pe, "gelu", u1, gelu_pre, entry=lambda t: pe.wait_ge(gpool_pre, KT - 1 + t))
            pe_pool(pe)
            pe_lru(pe)
            plain_phase(pe, "glru", u1, glru_pre, entry=lambda t: pe.wait_ge(vl_copied, KT))
            plain_phase(pe, "wout2", mg2, wout2_out, before=lambda k: pe.wait_ge(mg2_lo, HALF * (k + 1)),
                        entry=lambda t: pe.wait_ge(glru_pre, KT - 1 + t))
            mlp2.pe(pe, lambda k: norm2.ready(pe, k), lambda: norm2.pe(pe), lambda t: pe.wait_ge(wout2_out, KT - 1 + t))
            pe_conv3(pe)

            def conv_out(t):
                pe.wait_ge(ub_out, 2 * C3_T)
            plain_phase(pe, "gla_r", xh3, sr_pre, entry=conv_out)
            plain_phase(pe, "gla_p", xh3, gp_out, entry=lambda t: pe.wait_ge(sr_pre, GLA_VT - 1 + t))
            pe_gla(pe)
            plain_phase(pe, "wout3", mix, wout3_out, before=lambda k: need(pe, g_v, ("clo1", "olo1")[k]))
            pe.wait_ge(wout3_out, KT)
            ln1.pe(pe)
            mlp3.pe(pe, lambda k: ln1.ready(pe, k))
            pe.wait_ge(mlp3.out, KT * FF_GROUPS)
            ln2.pe(pe)


def full_tiles(w):
    n = w.shape[1] // P
    return w.reshape(2, HALF, P, n, P).transpose(3, 0, 2, 1, 4).reshape(n, 2, P, HALF, P)


def stream_of(a):
    w_in, w_in2, w_in3 = a["w_in"][0], a["w_in_2"][0], a["w_in_3"][0]
    order = [h for pair in Q_PAIRS for h in pair]

    def by_pairs(w):
        return w.reshape(D, A_HEADS, HD)[:, order].reshape(D, A_HEADS * HD)
    aq, ak, av, ag, rs, rg, xq, xg, mg = np.split(w_in, np.cumsum([768, 256, 256, 768, 2560, 768, 512, 512]), axis=1)
    tiles = {"shift": full_tiles(rs), "silu": full_tiles(np.concatenate([by_pairs(ag), rg, xg], 1))}
    beside = np.stack([tiles[kind][m] for kind, m in ATTN_TILES], 0)
    wo = np.concatenate([a["attn_w_o"][0].reshape(A_HEADS, HD, D)[order].reshape(A_HEADS * HD, D),
                         a["rwkv_w_o"][0], a["x_w_o"][0]], 0)
    gates = full_tiles(mg).reshape(N_BRANCH, KT, 2, P, HALF, P)
    merge1 = np.concatenate([gates, full_tiles(wo)[None]], 0).transpose(1, 0, 2, 3, 4, 5)
    v_pool, v_lru, v_gelu, g_pool, g_lru = np.split(w_in2, 5, axis=1)
    pool_w = a["pool_w_2"][0].reshape(4, 4, P, 2, 2, P).transpose(0, 3, 2, 4, 1, 5).reshape(4, 1, 2, P, HALF, P)
    lru_w = np.stack([a["gate_a_w_2"][0], a["gate_x_w_2"][0]], 0).reshape(2, 4, 2, 2, P, 2, P)
    lru_w = lru_w.transpose(1, 2, 4, 0, 5, 3, 6).reshape(4, 1, 2, P, HALF, P)

    def with_own(w, own):
        four = np.concatenate([full_tiles(w).reshape(4, 4, 2, P, HALF, P), own], 1)
        return np.stack([four[g, j] for g, j in OWN_ORDER], 0)
    b3, c3, u3, q3, k3, v3, r3, z3 = np.split(w_in3, np.cumsum([1024, 1024, 1024, 512, 512, 1024, 1024]), axis=1)
    z3 = np.concatenate([z3, np.zeros((D, P - z3.shape[1]), z3.dtype)], 1)
    conv3 = np.stack([full_tiles(c3), full_tiles(u3), full_tiles(b3)], 0).transpose(1, 0, 2, 3, 4, 5)

    def mlp(w1, w2):
        up = full_tiles(w1).reshape(FF_GROUPS, KT, 2, P, HALF, P)
        down = np.stack([full_tiles(w) for w in w2.reshape(FF_GROUPS, D, D)], 0)
        return np.concatenate([up, down], 1)
    parts = [full_tiles(np.concatenate([by_pairs(aq), ak, xq, av], 1)), full_tiles(a["x_w_kv"][0]), beside, full_tiles(rg), merge1, full_tiles(a["w_out"][0]),
             full_tiles(g_pool), full_tiles(v_gelu), with_own(v_pool, pool_w), with_own(v_lru, lru_w),
             full_tiles(g_lru), full_tiles(a["w_out_2"][0]), mlp(a["mlp_w1_2"][0], a["mlp_w2_2"][0]),
             conv3, full_tiles(r3), full_tiles(np.concatenate([z3, q3, k3, v3], 1)), full_tiles(a["w_out_3"][0]),
             mlp(a["w_ff_up_3"][0], a["w_ff_down_3"][0]), np.zeros((2 * PAD, P, HALF, P), w_in.dtype)]
    return np.concatenate([p.reshape(-1, P, HALF, P) for p in parts], 0)


def params_of(a):
    named = {"mu": "rwkv_mu", "k_k": "rwkv_k_k", "k_a": "rwkv_k_a", "r_k": "rwkv_r_k", "w0": "rwkv_w0", "a0": "rwkv_a0",
             "ln_w": "rwkv_ln_w", "ln_b": "rwkv_ln_b", "q_g": "attn_q_norm_g", "k_g": "attn_k_norm_g",
             "xq_g": "x_q_norm_g", "xk_g": "x_k_norm_g", "norm1_g": "norm1_g_2", "pool_scale": "pool_scale_2",
             "conv_w2": "conv_w_2", "conv_b2": "conv_b_2", "gate_a_b": "gate_a_b_2", "gate_x_b": "gate_x_b_2",
             "lam": "lru_lambda_2", "norm2_g": "norm2_g_2", "final_g": "final_g_2", "conv_w3": "conv_w_3",
             "conv_g3": "conv_norm_g_3", "gate_bias3": "gate_bias_3", "gla_g3": "gla_norm_g_3", "ln1_g": "ln1_g_3",
             "ln1_b": "ln1_b_3", "ln2_g": "ln2_g_3", "ln2_b": "ln2_b_3"}
    cols = []
    for name, n in PARAMS:
        if name == "sink":
            pairs = a["attn_sink"][0][np.array(Q_PAIRS)]
            c = np.broadcast_to(np.repeat(pairs.reshape(-1), NB)[None], (P, n))
        else:
            c = a[named.get(name, name)].reshape(-1)
            c = np.concatenate([c, c]) if c.shape[0] == HD else c
            c = c.reshape(n, P).T
        cols.append(c)
    return np.ascontiguousarray(np.concatenate(cols, 1))


def channel_major(x):
    return np.ascontiguousarray(x.T.reshape(KT, P, -1).transpose(1, 0, 2))


def arrays_of(inputs):
    a = {k: np.asarray(v) for k, v in inputs.items()}
    return {
        "stream": stream_of(a), "consts": constants(), "params": params_of(a),
        "w2": np.ascontiguousarray(a["rwkv_w2"][0].reshape(P, PAIRS, P)),
        "a2": np.ascontiguousarray(a["rwkv_a2"][0].reshape(P, PAIRS, P)),
        "wgu": np.ascontiguousarray(a["w_gate_up_3"][0].reshape(16, GLA_H, P)),
        "memT": channel_major(a["mem"][0]), "xT": channel_major(a["x"][0]), "metaT": channel_major(a["meta_tokens_2"]),
    }


def kernel(**inputs):
    import concourse.bacc as bacc
    from concourse.bass_utils import run_bass_kernel_spmd

    nc = bacc.Bacc("TRN2", target_bir_lowering=False, num_devices=1)
    arrays = arrays_of(inputs)
    args = [nc.dram_tensor(n, x.shape, mybir.dt.from_np(x.dtype), kind="ExternalInput").ap() for n, x in arrays.items()]
    out = nc.dram_tensor("out", (P, KT, T), mybir.dt.float32, kind="ExternalOutput").ap()
    build(nc, *args, out)
    got = run_bass_kernel_spmd(nc, [arrays], core_ids=[0]).results[0]["out"]
    return got.transpose(2, 1, 0).reshape(1, T, D)
```

```python
import numpy as np
import concourse.bass as bass
from concourse import mybir
from contextlib import ExitStack

P = 128
D = 2048
KT = D // P
T = 256
META = 16
TM = META + T
NB = T // P
HALF = KT // 2
UNIT = HALF * P
RING = 4

A_HEADS, A_KV, HD = 12, 4, 64
A_T = A_HEADS * HD // P
KV_T = A_KV * HD // P
R_HEADS = 12
PAIRS = R_HEADS * HD // P
CH = 64
NCH = T // CH
LEVELS = 6
X_HEADS = 4
X_T = X_HEADS
N_BRANCH = 3
WINDOW = 128
POOL_WINDOWS = (2, 4, 8, 16)
POOL_T = D // P // len(POOL_WINDOWS)
CONV2 = 4
LRU_HEADS = 8
FF_GROUPS = 4
CONV3 = 3
C3_T = 8
GLA_H = 4
GLA_VT = 8
HALF_DECAY = 0.5 * float(np.exp(-0.5))
ALPHA3 = 2.0 ** 0.25
EPS = 1e-6
GN_EPS = 64e-5
LN_EPS = 1e-5
GATE_TAU = 16.0
NEG = -1e30

Q_PAIRS = [(0, 3), (1, 4), (2, 5), (6, 9), (7, 10), (8, 11)]

STREAM = [("plain", 14), ("mem_kv", 8), ("attn", 30), ("rwkv", 24), ("merge_a", 40), ("merge_b", 6), ("wout1", 16),
          ("gpool", 16), ("gelu", 16), ("pool", 20), ("lru", 20), ("glru", 16), ("wout2", 16),
          ("ff2", 128), ("conv3", 24), ("gla", 25), ("wout3", 16), ("ff3", 128)]
FIRST = {}
N_TILES = 0
for _name, _n in STREAM:
    FIRST[_name] = N_TILES
    N_TILES += _n
COUNT = dict(STREAM)
PAD = RING // 2
N_UNITS = 2 * (N_TILES + PAD)

SHIFT_T = 3 * PAIRS + 2
ATTN_FIRST = 4
ATTN_BEFORE = 6
ATTN_UNITS = [[("silu", u if u < A_T else A_T + PAIRS + u - A_T), ("shift", ATTN_BEFORE + u)]
              + ([("shift", ATTN_BEFORE + A_T + X_T + u)] if ATTN_BEFORE + A_T + X_T + u < SHIFT_T else []) for u in range(A_T + X_T)]
ATTN_TILES = [("shift", k) for k in range(ATTN_BEFORE)] + [x for unit in ATTN_UNITS for x in unit]

BESIDE = 1 + 3
MERGE_A = 10

GO_START, GO_PREP, GO_GRAM, GO_LEVEL, GO_STEP = 8, 24, 4, 1, 1

SHIFT_TILE = 5

OWN = POOL_T
OWN_ORDER = [(0, j) for j in range(POOL_T)] + [
    x for g in range(1, 4) for x in [(g, 0), (g - 1, OWN), (g, 1), (g, 2), (g, 3)]] + [(3, OWN)]

PARAMS = [("mem_norm_g", 16), ("norm_g", 16), ("mu", 20), ("k_k", 6), ("k_a", 6), ("r_k", 6),
          ("w0", 12), ("a0", 12), ("ln_w", 6), ("ln_b", 6), ("gate_b", 48), ("q_g", 1), ("k_g", 1),
          ("xq_g", 1), ("xk_g", 1), ("sink", 24), ("norm1_g", 16), ("pool_scale", 16),
          ("conv_w2", 64), ("conv_b2", 16), ("gate_a_b", 16), ("gate_x_b", 16), ("lam", 16),
          ("norm2_g", 16), ("final_g", 16), ("conv_w3", 24), ("conv_g3", 8), ("gate_bias3", 4),
          ("gla_g3", 8), ("ln1_g", 16), ("ln1_b", 16), ("ln2_g", 16), ("ln2_b", 16)]
PCOL = {}
N_PARAM = 0
for _name, _n in PARAMS:
    PCOL[_name] = N_PARAM
    N_PARAM += _n

CONSTS = [("ident", 128), ("ones", 128), ("bdones", 128), ("rot", 128), ("istack", 64),
          ("cos", 256), ("sin", 256), ("amask", 512), ("strict_up", 128), ("strict_lo", 128),
          ("incl_up", 128), ("incl_lo", 128), ("levels", 768), ("run_up", 256), ("run_lo", 256)]
CCOL = {}
N_CONST = 0
for _name, _n in CONSTS:
    CCOL[_name] = N_CONST
    N_CONST += _n


def constants():
    f = np.float32
    i = np.arange(P)
    head, s = i // CH, i % CH
    same = head[:, None] == head[None, :]
    rot = np.zeros((P, P), f)
    for m in range(P):
        j = m % HD
        if j < HD // 2:
            rot[m + HD // 2, m] = -1.0
        else:
            rot[m - HD // 2, m] = 1.0
    half = HD // 2
    inv = np.float32(10000.0) ** (-np.arange(half, dtype=f) / np.float32(half))
    ang = np.arange(T, dtype=f)[None, :] * inv.astype(f)[:, None]
    cos, sin = (np.tile(fn(ang).astype(f), (4, 1)) for fn in (np.cos, np.sin))
    key = np.arange(T)
    amask = np.stack([np.where(np.abs(key[None, :] - (i[:, None] + b * P)) <= WINDOW, 0.0, NEG)
                      for b in range(NB)], 1)
    up = same & (s[:, None] < s[None, :])
    incl = same & (s[:, None] <= s[None, :])
    levels = [same & (s[:, None] >> (l + 1) == s[None, :] >> (l + 1))
              & (s[:, None] >> l != s[None, :] >> l) for l in range(LEVELS)]
    t = np.arange(T)
    table = {
        "ident": np.eye(P), "ones": np.ones((P, P)), "bdones": same, "rot": rot,
        "istack": (s[:, None] == np.arange(CH)[None, :]), "cos": cos, "sin": sin,
        "amask": amask.reshape(P, NB * T), "strict_up": up, "strict_lo": up.T, "incl_up": incl,
        "incl_lo": incl.T, "levels": np.concatenate(levels, 1),
        "run_up": np.tile(t % CH != 0, (P, 1)), "run_lo": np.tile(t % CH != CH - 1, (P, 1)),
    }
    return np.ascontiguousarray(np.concatenate([table[n].astype(f) for n, _ in CONSTS], 1))


class Steps:

    def __init__(self, sem, names):
        self.sem, self.names = sem, list(names)
        self.place = {n: k for k, n in enumerate(self.names)}
        assert len(self.place) == len(self.names), "a step's name stands twice"
        self.cursor = 0

    def at(self, name, it=None):
        n = self.place[name] + 1
        return n if it is None else it * len(self.names) + n

    def done(self, ins, name):
        assert self.names[self.cursor % len(self.names)] == name, (name, self.names[self.cursor % len(self.names)])
        self.cursor += 1
        ins.then_inc(self.sem, 1)


def need(eng, steps, name, it=None):
    eng.wait_ge(steps.sem, steps.at(name, it))


class Tile:

    def __init__(self, first, t, loops=()):
        self.first, self.t, self.loops = first, t, tuple(loops)

    def sum(self, c, m):
        for reg, per in self.loops:
            c = reg * (per * m) + c
        return c

    def units(self, c):
        return self.sum(2 * (self.first + self.t) + c, 2)

    def local(self, m=1, c=0):
        return self.sum(m * self.t + c, m)

    def later(self):
        return Tile(self.first, self.t + RING // 2, self.loops)

    @property
    def parity(self):
        return (self.first + self.t) % 2

    @property
    def start(self):
        return not self.loops and self.first + self.t < 2


def run_tiles(eng, phase, per, body, loops=(), first=None, count=None, peel=1):
    first = FIRST[phase] if first is None else first
    count = COUNT[phase] if count is None else count
    rounds = count // per
    for j in range(per * peel):
        body(Tile(first, j, loops))
    if peel < rounds:
        with eng.Fori(peel, rounds) as i:
            for j in range(per):
                body(Tile(first, j, tuple(loops) + ((i, per),)))
    for t in range(rounds * per, count):
        body(Tile(first, t, loops))


def build(nc, stream, consts, params, w2, a2, wgu, memT, xT, metaT, out):
    F, R = mybir.dt.float32, mybir.dt.float32r
    ACT, ALU = mybir.ActivationFunctionType, mybir.AluOpType
    AX = mybir.AxisListType
    ctx = ExitStack()
    with ctx:
        def sem(name):
            return ctx.enter_context(nc.semaphore(name))

        K = 1024
        base = -(-nc.sbuf_base // 64) * 64
        slab = 206 * K
        ctx.enter_context(nc.sbuf_tensor("slab", [P, slab // 4], F, align_bytes=64))

        def at(name, offset, shape, dtype=F):
            size = 4 * int(np.prod(shape[1:]))
            assert offset + size <= slab, (name, offset + size - slab)
            return nc.alloc_sbuf_tensor_at(name, list(shape), dtype, offset=base + offset)

        raw = at("raw", 0, [P, RING, HALF, P])
        w_hi = at("w_hi", 16 * K, [P, RING, HALF, P], R)
        w_lo = at("w_lo", 32 * K, [P, RING, HALF, P], R)
        cst = at("cst", 48 * K, [P, N_CONST])
        par = at("par", 62 * K, [P, N_PARAM])
        w2_sb = at("w2_sb", 64 * K, [P, PAIRS, P])
        a2_sb = at("a2_sb", 67 * K, [P, PAIRS, P])
        wgu_sb = at("wgu_sb", 70 * K, [16, GLA_H, P])
        lam_sb = at("lam_sb", 72 * K, [P, 6, 16])
        hw_sb = at("hw_sb", 72 * K + 384, [P, 24])
        RSTD = 72 * K + 512
        B = 74 * K
        banks = [ctx.enter_context(nc.psum_tensor(f"bank{b}", [P, 512], F)) for b in range(8)]

        def const(name):
            return cst[:, CCOL[name]:CCOL[name] + dict(CONSTS)[name]]

        def col(name, k):
            return par[:, PCOL[name]:PCOL[name] + dict(PARAMS)[name]][:, bass.ds(k, 1)]

        raw_in = [sem(f"raw_in{k}") for k in range(RING)]
        hi_ready, lo_ready, units_used = sem("hi_ready"), sem("lo_ready"), sem("units_used")

        def split_hi(act, tile, units=(0, 1)):
            if not tile.loops and tile.first + tile.t >= N_TILES + PAD:
                return
            for k in units:
                slot = (2 * tile.parity + k) % RING
                g = tile.first + tile.t
                act.wait_ge(raw_in[slot], tile.sum(16 * (g // 2 + 1), 8))
                if not tile.start:
                    act.wait_ge(units_used, tile.units(k + 1 - RING))
                nc.scalar.activation(w_hi[:, slot], raw[:, slot], ACT.Copy).then_inc(hi_ready, 1)

        def split_lo(v, tile, units=(0, 1)):
            if not tile.loops and tile.first + tile.t >= N_TILES + PAD:
                return
            for k in units:
                slot = (2 * tile.parity + k) % RING
                v.wait_ge(hi_ready, tile.units(k + 1))
                nc.vector.tensor_tensor(w_lo[:, slot], raw[:, slot], w_hi[:, slot].bitcast(F),
                                        ALU.subtract).then_inc(lo_ready, 1)

        def tile_done(eng, tile):
            eng.wait_ge(units_used, tile.units(2))

        def product(dst, moving, slot, j, kt, first, last, n=T):
            hi, lo = moving[:, kt, 0, TM - n:] if moving.shape[-1] == TM else moving[:, kt, 0], \
                moving[:, kt, 1, TM - n:] if moving.shape[-1] == TM else moving[:, kt, 1]
            nc.tensor.matmul(dst, w_hi[:, slot, j], hi, start=first, stop=False)
            nc.tensor.matmul(dst, w_hi[:, slot, j], lo, start=False, stop=False)
            return nc.tensor.matmul(dst, w_lo[:, slot, j], hi, start=False, stop=last)

        def full_tile(pe, tile, moving, n=T, before=None):
            dst = banks[tile.parity][:, 0:n]
            for k in range(2):
                if before is not None:
                    before(k)
                pe.wait_ge(lo_ready, tile.units(k + 1))
                for j in range(HALF):
                    kt = HALF * k + j
                    last = product(dst, moving, (2 * tile.parity + k) % RING, j, kt,
                                   kt == 0, kt == KT - 1, n)
                last.then_inc(units_used, 1)

        def plain_phase(pe, phase, moving, bank_free, n=T, before=None, entry=None, after=None, peel=1):
            def body(tile):
                if tile.loops or tile.t >= 2:
                    pe.wait_ge(bank_free, tile.local(1, -1))
                elif entry is not None:
                    entry(tile.t)
                first = not tile.loops and tile.t == 0
                full_tile(pe, tile, moving, n, before if first else None)
                hooked(tile, after)
            run_tiles(pe, phase, 2, body, peel=peel)

        def hooked(tile, hooks):
            if hooks and not tile.loops and tile.t in hooks:
                hooks[tile.t]()

        in_cst, in_par, in_lora, in_res, in_meta, stored = (
            sem(n) for n in ("in_cst", "in_par", "in_lora", "in_res", "in_meta", "stored"))
        in_x, in_mem = ([sem(f"{n}{q}") for q in range(4)] for n in ("in_x", "in_mem"))

        class Norm:
            def __init__(self, name, src, n, g, dst, scratch, rstd=RSTD):
                self.src, self.n, self.g, self.dst = src, n, g, dst
                self.sq, self.acc, self.std = (at(f"{name}_{b}", scratch + 4 * n * k, [P, n])
                                               for k, b in enumerate(("sq", "acc", "std")))
                self.rstd = at(name + "_rstd", rstd, [P, n])
                self.hi, self.lo, self.sums, self.stat, self.rooted, self.known = (
                    sem(f"{name}_{b}") for b in ("hi", "lo", "sums", "stat", "rooted", "known"))

            def act_tile(self, act, kt):
                nc.scalar.activation(self.dst[:, kt, 0], self.src[:, kt], ACT.Identity, scale=col(self.g, kt)).then_inc(self.hi, 1)

            def dve_tile(self, v, kt, count):
                v.wait_ge(self.hi, count)
                nc.vector.scalar_tensor_tensor(self.dst[:, kt, 1], self.src[:, kt], col(self.g, kt),
                                               self.dst[:, kt, 0].bitcast(F), ALU.mult, ALU.subtract).then_inc(self.lo, 1)

            def pool_start(self, pool):
                nc.gpsimd.memset(self.acc[:], 0.0).then_inc(self.sums, 1)

            def pool_tile(self, pool, kt):
                pool.wait_ge(self.sums, kt * 2 + 1)
                nc.gpsimd.tensor_tensor(self.sq[:], self.src[:, kt], self.src[:, kt], ALU.mult).then_inc(self.sums, 1)
                pool.wait_ge(self.sums, kt * 2 + 2)
                nc.gpsimd.tensor_tensor(self.acc[:], self.acc[:], self.sq[:], ALU.add).then_inc(self.sums, 1)

            def pool(self, pool, src_ready, before=0):
                pool.wait_ge(src_ready, before + 1)
                self.pool_start(pool)
                with pool.Fori(0, KT) as kt:
                    pool.wait_ge(src_ready, kt + (before + 1))
                    self.pool_tile(pool, kt)

            def pe(self, pe):
                pe.wait_ge(self.sums, 2 * KT + 1)
                nc.tensor.matmul(banks[2][:, 0:self.n], const("ones"), self.acc[:], start=True, stop=True).then_inc(self.stat, 1)

            def act_root(self, act):
                act.wait_ge(self.stat, 1)
                nc.scalar.activation(self.std[:], banks[2][:, 0:self.n], ACT.Sqrt, bias=EPS, scale=1.0 / D).then_inc(self.rooted, 1)

            def dve_rstd(self, v):
                v.wait_ge(self.rooted, 1)
                nc.vector.reciprocal(self.rstd[:], self.std[:]).then_inc(self.known, 1)
                v.wait_ge(self.known, 1)

            def ready(self, pe, k):
                pe.wait_ge(self.lo, HALF * (k + 1))

        hx = at("hx", B, [P, KT, 2, T], R)
        sg = at("sg", B + 32 * K, [P, KT, T])
        pl = at("pl", B + 48 * K, [P, 14, T])
        rkv = at("rkv", B + 62 * K, [P, 20, T])
        mkv = at("mkv", B + 82 * K, [P, 8, T])
        Z = B + 90 * K
        mem_raw = at("mem_raw", B + 62 * K, [P, KT, T])
        mem_hl = at("mem_hl", Z, [P, KT, 2, T], R)
        x_raw = at("x_raw", B + 32 * K, [P, KT, T])
        x_norm = Norm("x_norm", x_raw, T, "norm_g", hx, B + 122 * K)
        mem_norm = Norm("mem_norm", mem_raw, T, "mem_norm_g", mem_hl, B + 126 * K, B + 129 * K)

        mem_out, plain_out = (sem(n) for n in ("mem_out", "plain_out"))

        def dve_scaled_phase(v, phase, norm, dst, out_sem, hooks=None, late=None, peel=1):
            rstd = norm.rstd[:, norm.n - T:]

            def body(tile):
                hooked(tile, hooks)
                tile_done(v, tile)
                nc.vector.tensor_tensor(dst[:, tile.local()], banks[tile.parity][:, 0:T], rstd, ALU.mult).then_inc(out_sem, 1)
                split_lo(v, tile.later())
                hooked(tile, late)
            run_tiles(v, phase, 2, body, peel=peel)

        def dve_pre_phase(v, phase, norm, tmp, pre_sem, out_sem, hooks=None):
            rstd = norm.rstd[:, norm.n - T:]

            def body(tile):
                hooked(tile, hooks)
                tile_done(v, tile)
                if tile.loops or tile.t >= 2:
                    v.wait_ge(out_sem, tile.local(1, -1))
                nc.vector.tensor_tensor(tmp[:, tile.t % 2], banks[tile.parity][:, 0:T], rstd, ALU.mult).then_inc(pre_sem, 1)
                split_lo(v, tile.later())
            run_tiles(v, phase, 2, body)

        def act_func_phase(act, phase, tmp, pre_sem, dst, func, out_sem, hooks=None):
            def body(tile):
                split_hi(act, tile.later())
                hooked(tile, hooks)
                act.wait_ge(pre_sem, tile.local(1, 1))
                nc.scalar.activation(dst[:, tile.local()], tmp[:, tile.t % 2], func).then_inc(out_sem, 1)
            run_tiles(act, phase, 2, body)

        def act_split_phase(act, phase, hooks=None, peel=1):
            def body(tile):
                split_hi(act, tile.later())
                hooked(tile, hooks)
            run_tiles(act, phase, 2, body, peel=0 if hooks is None else peel)

        pad = [at(f"pad{b}", Z + K * 26 + b * 1088, [P, T + 2]) for b in range(2)]
        sh = [at(f"sh{b}", Z + K * 26 + 2176 + b * 1024, [P, T]) for b in range(2)]
        sa = at("sa", Z + 38 * K, [P, 2, T])
        pads_zero, shift_copied, shift_step, agate_pre, agate_out = (
            sem(n) for n in ("pads_zero", "shift_copied", "shift_step", "agate_pre", "agate_out"))

        def beside(k):
            kind, m = ATTN_TILES[k]
            return Tile(FIRST["attn"], k), kind, m, sum(x[0] == kind for x in ATTN_TILES[:k])

        def act_beside(act, tiles):
            for k in tiles:
                tile, kind, m, n = beside(k)
                split_hi(act, tile.later(), (0,))
                if kind == "silu":
                    act.wait_ge(agate_pre, n + 1)
                    nc.scalar.activation(sg[:, m], sa[:, n % 2], ACT.Silu).then_inc(agate_out, 1)
                split_hi(act, tile.later(), (1,))

        def dve_beside(v, tiles):
            for k in tiles:
                tile, kind, m, n = beside(k)
                tile_done(v, tile)
                psum = banks[tile.parity][:, 0:T]
                if kind == "silu":
                    if n >= 2:
                        v.wait_ge(agate_out, n - 1)
                    nc.vector.tensor_tensor(sa[:, n % 2], psum, x_norm.rstd[:], ALU.mult).then_inc(agate_pre, 1)
                    split_lo(v, tile.later())
                    continue
                if n == 0:
                    for b in range(2):
                        nc.vector.memset(pad[b][:], 0.0).then_inc(pads_zero, 1)
                    v.wait_ge(pads_zero, 2)
                p, s = pad[n % 2], sh[n % 2]
                nc.vector.tensor_tensor(p[:, 1:T + 1], psum, x_norm.rstd[:], ALU.mult).then_inc(shift_copied, 1)
                v.wait_ge(shift_copied, n + 1)
                nc.vector.tensor_tensor(s[:], p[:, 0:T], p[:, 2:T + 2], ALU.add).then_inc(shift_step, 1)
                v.wait_ge(shift_step, 3 * n + 1)
                nc.vector.scalar_tensor_tensor(s[:], s[:], 0.5, p[:, 1:T + 1], ALU.mult, ALU.subtract).then_inc(shift_step, 1)
                v.wait_ge(shift_step, 3 * n + 2)
                nc.vector.scalar_tensor_tensor(rkv[:, m], s[:], col("mu", m), p[:, 1:T + 1], ALU.mult, ALU.add).then_inc(shift_step, 1)
                split_lo(v, tile.later())

        def pe_beside(pe, tiles):
            for k in tiles:
                tile = beside(k)[0]
                if k < 2:
                    pe.wait_ge(mem_out, COUNT["mem_kv"] - 1 + k)
                else:
                    _, kind, _, n = beside(k - 2)
                    pe.wait_ge(agate_pre if kind == "silu" else shift_copied, n + 1)
                full_tile(pe, tile, hx)

        def unit_tiles(u):
            first = ATTN_BEFORE + sum(len(x) for x in ATTN_UNITS[:u])
            return list(range(first, first + len(ATTN_UNITS[u])))

        sq_at = at("sq_at", B + 32 * K, [P, 16, T])
        rs_at = sq_at
        rope_tmp = [at(f"rope_tmp{b}", B + (122, 130)[b] * K, [P, 2, T]) for b in range(2)]
        vtok = at("vtok", Z + 32 * K, [P, NB, KV_T * P])
        vmtok = at("vmtok", Z + 34 * K, [P, NB, X_T * P])
        U_ALL = range(A_T + X_T)
        sc = [at(f"sc{b}", Z + 4 * K * b, [P, 4, T]) for b in range(2)]
        pr = [at(f"pr{b}", Z + 8 * K + 4 * K * b, [P, 4, T]) for b in range(2)]
        pt = [at(f"pt{b}", Z + 16 * K + 4 * K * b, [P, 4, T]) for b in range(2)]
        mx = at("mx", Z + 24 * K, [P, 10, 4])
        ngm = at("ngm", Z + 24 * K + 160, [P, 10, 4])
        sm = at("sm", Z + 24 * K + 320, [P, 10, 4])
        es = at("es", Z + 24 * K + 480, [P, 10, 4])
        rd = at("rd", Z + 24 * K + 640, [P, 10, 4])
        at_src = [(pl, k) for k in range(12)] + [(mkv, k) for k in range(4)]
        at_g = ["q_g"] * 6 + ["k_g"] * 2 + ["xq_g"] * 4 + ["xk_g"] * 4
        def exp_names(u):
            return [f"ex{u}"] * (u < len(U_ALL)) + [f"sk{u}"] * (u < A_T)
        at_a = Steps(sem("attn_act"), ["sq0"] + [f"std{b}" for b in range(4)] + ["sq1", "std4", "std5", "sq2", "std6", "std7", "vt", "vm0", "vm1"]
                     + exp_names(0) + [n for u in U_ALL for n in [f"pt{u}"] + exp_names(u + 1)])

        def attn_dve_names():
            names = [f"rstd{b}" for b in range(6)] + ["norm"]
            names += [f"{s}{b}" for b in range(4) for s in ("sin", "cos", "rope")] + ["rstd6", "rstd7", "xnorm"]
            def soft(u):
                return [f"{s}{u}" for s in (("mask", "max", "msk", "neg", "dsk") if u < A_T else ("max", "neg"))]
            names += soft(0)
            for u in U_ALL:
                names += ([f"den{u}"] if u < A_T else []) + [f"rd{u}", f"pr{u}"]
                names += (soft(u + 1) if u + 1 < len(U_ALL) else []) + [f"y{u}"]
            return names
        at_v = Steps(sem("attn_dve"), attn_dve_names())
        at_p = Steps(sem("attn_pe"), [f"stat{b}" for b in range(8)] + [f"rot{b}" for b in range(4)] + ["vt", "vm0", "vm1"]
                     + ["sc0"] + [n for u in U_ALL for n in (f"sc{u + 1}", f"tr{u}", f"pv{u}") if n != f"sc{len(U_ALL)}"])

        def heads(u):
            return [(HD * h, HD, b) for h in range(2) for b in range(NB)] if u < A_T else [(0, P, b) for b in range(NB)]

        def sc_bank(u, h):
            return banks[2 + h] if u < A_T else banks[2 + u % 2]

        def pt_bank(u, h):
            return banks[4 + h] if u < A_T else banks[4 + u % 2]

        def pv_bank(u):
            return banks[6 + u % 2]

        STAT_BANK = [3, 4, 5, 6, 7, 3, 4, 5]
        VT_BANK, VM_BANK, ROT_BANK = 5, (6, 5), (2, 3, 7, 6)

        def act_squares(act, k):
            if k < 2:
                act.wait_ge(plain_out, (8, 12)[k])
                tiles = pl[:, 0:8] if k == 0 else pl[:, 8:12]
            else:
                act.wait_ge(mem_out, X_T)
                tiles = mkv[:, 0:X_T]
            at_a.done(nc.scalar.activation(sq_at[:, (0, 8, 12)[k]:(8, 12, 16)[k]], tiles, ACT.Square), f"sq{k}")

        def pe_stats(pe, which):
            for b in which:
                need(pe, at_a, "sq0" if b < 4 else "sq1" if b < 6 else "sq2")
                if b >= 5:
                    need(pe, at_a, f"std{b - 5}")
                at_p.done(nc.tensor.matmul(banks[STAT_BANK[b]][:], const("bdones" if b < 4 else "ones"), sq_at[:, 2 * b:2 * b + 2],
                                           start=True, stop=True), f"stat{b}")

        def act_roots(act, which):
            for b in which:
                need(act, at_p, f"stat{b}")
                dim = HD if b < 4 else P
                at_a.done(nc.scalar.activation(rs_at[:, 2 * b:2 * b + 2], banks[STAT_BANK[b]][:].rearrange("p (a t) -> p a t", a=2),
                                               ACT.Sqrt, bias=EPS, scale=1.0 / dim), f"std{b}")

        def dve_factors(v, which):
            for b in which:
                need(v, at_a, f"std{b}")
                at_v.done(nc.vector.reciprocal(rs_at[:, 2 * b:2 * b + 2], rs_at[:, 2 * b:2 * b + 2]), f"rstd{b}")

        def dve_normed(v, first, last, name):
            need(v, at_v, f"rstd{last // 2 - 1}")
            for k, ((buf, c), g) in list(enumerate(zip(at_src, at_g)))[first:last]:
                ins = nc.vector.scalar_tensor_tensor(buf[:, c], buf[:, c], col(g, 0), rs_at[:, k], ALU.mult, ALU.mult)
            at_v.done(ins, name)

        def act_attn(act):
            act.wait_ge(mem_out, COUNT["mem_kv"])
            act_beside(act, [0])
            need(act, at_p, "vt")
            at_a.done(nc.scalar.activation(vtok[:], banks[VT_BANK][:].rearrange("p (b c) -> p b c", b=NB), ACT.Copy), "vt")
            for b in range(NB):
                need(act, at_p, f"vm{b}")
                at_a.done(nc.scalar.activation(vmtok[:, b], banks[VM_BANK[b]][:], ACT.Copy), f"vm{b}")
                act_beside(act, [1 + b])
            act_beside(act, range(3, ATTN_FIRST))

            def exps(u):
                need(act, at_v, f"neg{u}")
                if u >= 2:
                    need(act, at_p, f"tr{u - 2}")
                for n in range(len(heads(u))):
                    src = sc[u % 2][:, n] if u < A_T else sc_bank(u, 0)[:, T * n:T * n + T]
                    last = nc.scalar.activation(pr[u % 2][:, n], src, ACT.Exp, bias=ngm[:, u, n:n + 1],
                                                scale=1.0 if u < A_T else P ** -0.5, accum_out=sm[:, u, n:n + 1])
                at_a.done(last, f"ex{u}")
                if u < A_T:
                    need(act, at_v, f"dsk{u}")
                    at_a.done(nc.scalar.activation(es[:, u], es[:, u], ACT.Exp), f"sk{u}")
            exps(0)
            act_beside(act, range(ATTN_FIRST, ATTN_BEFORE))
            for u in U_ALL:
                first, *others = unit_tiles(u)
                act_beside(act, [first])
                act_kk_root(act, u)
                need(act, at_p, f"tr{u}")
                for h in range(2 if u < A_T else 1):
                    last = nc.scalar.activation(pt[u % 2][:, 2 * h:2 * h + 2],
                                                pt_bank(u, h)[:].rearrange("p (b q) -> p b q", b=NB), ACT.Copy)
                at_a.done(last, f"pt{u}")
                if u + 1 < len(U_ALL):
                    exps(u + 1)
                act_beside(act, others)
                if u == A_T - 1:
                    act_kk_squares(act)

        def pe_rotated(pe):
            need(pe, at_v, "norm")
            for b in range(4):
                at_p.done(nc.tensor.matmul(banks[ROT_BANK[b]][:], const("rot"), pl[:, 2 * b:2 * b + 2], start=True, stop=True), f"rot{b}")

        def pe_attn(pe):
            pe_beside(pe, [0])
            need(pe, at_a, "std7")
            need(pe, at_v, "rope3")
            pe.wait_ge(mem_out, COUNT["mem_kv"])
            for b in range(NB):
                for c in range(KV_T):
                    o = (b * KV_T + c) * P
                    last = nc.tensor.transpose(banks[VT_BANK][:, o:o + P], pl[:, 12 + c, b * P:b * P + P], const("ident"))
            at_p.done(last, "vt")
            for b in range(NB):
                if b == 1:
                    pe_beside(pe, [1])
                    need(pe, at_a, "vt")
                for c in range(X_T):
                    last = nc.tensor.transpose(banks[VM_BANK[b]][:, c * P:c * P + P], mkv[:, 4 + c, b * P:b * P + P], const("ident"))
                at_p.done(last, f"vm{b}")
            pe_beside(pe, range(2, ATTN_FIRST))

            def scores(u):
                if u == A_T:
                    need(pe, at_v, "xnorm")
                if u >= 2:
                    w = u - 1 if u < A_T or u == A_T else u - 2
                    if w < A_T:
                        need(pe, at_v, f"mask{w}")
                    else:
                        need(pe, at_a, f"ex{w}")
                elif u == 1:
                    need(pe, at_v, "mask0")
                for r, n, b in heads(u):
                    q = pl[r:r + n, u if u < A_T else 8 + u - A_T, b * P:b * P + P]
                    k = pl[r:r + n, A_T + u // 3, :] if u < A_T else mkv[:, u - A_T, :]
                    last = nc.tensor.matmul(sc_bank(u, r // HD)[:, b * T:b * T + T], q, k, start=True, stop=True)
                at_p.done(last, f"sc{u}")

            def values(u):
                first, *others = unit_tiles(u)
                pe_kk(pe, u)
                pe_beside(pe, [first])
                need(pe, at_v, f"pr{u}")
                if u >= 1:
                    need(pe, at_a, f"pt{u - 1}")
                for n, (r, _, b) in enumerate(heads(u)):
                    for kb in range(NB):
                        o = kb * T + b * P
                        last = nc.tensor.transpose(pt_bank(u, r // HD)[:, o:o + P], pr[u % 2][:, n, kb * P:kb * P + P], const("ident"))
                at_p.done(last, f"tr{u}")
                pe_beside(pe, others[:1])
                need(pe, at_a, f"pt{u}")
                if u >= 2:
                    need(pe, at_v, f"y{u - 2}")
                if u in KK_UNITS:
                    need(pe, kk_a, f"root{KK_UNITS.index(u)}")
                for h in range(2 if u < A_T else 1):
                    rows = HD if u < A_T else P
                    for kb in range(NB):
                        c = (2 * (u // 3) + h) * HD if u < A_T else (u - A_T) * P
                        v = (vtok if u < A_T else vmtok)[:, kb, c:c + rows]
                        last = nc.tensor.matmul(pv_bank(u)[h * HD:h * HD + rows, 0:T], v, pt[u % 2][:, 2 * h + kb],
                                                start=kb == 0, stop=kb == NB - 1)
                at_p.done(last, f"pv{u}")
                pe_beside(pe, others[1:])

            scores(0)
            pe_beside(pe, range(ATTN_FIRST, ATTN_BEFORE))
            for u in U_ALL:
                if u + 1 < len(U_ALL):
                    scores(u + 1)
                values(u)

        def dve_rope(v, which):
            need(v, at_v, "norm")
            for b in which:
                need(v, at_p, f"rot{b}")
                cos, sin = (const(n).unsqueeze(1).broadcast_to([P, 2, T]) for n in ("cos", "sin"))
                two = pl[:, 2 * b:2 * b + 2]
                t2 = rope_tmp[b % 2][:]
                if b >= 2:
                    need(v, at_v, f"rope{b - 2}")
                at_v.done(nc.vector.tensor_tensor(t2, banks[ROT_BANK[b]][:].rearrange("p (a t) -> p a t", a=2), sin, ALU.mult), f"sin{b}")
                at_v.done(nc.vector.tensor_tensor(two, two, cos, ALU.mult), f"cos{b}")
                need(v, at_v, f"cos{b}")
                at_v.done(nc.vector.tensor_tensor(two, two, t2, ALU.add), f"rope{b}")

        def dve_attn(v):
            dve_beside(v, [0])
            dve_factors(v, [6])
            dve_beside(v, [1])
            dve_factors(v, [7])
            dve_beside(v, range(2, ATTN_FIRST))
            dve_normed(v, 8, 16, "xnorm")

            def soft(u):
                nb = len(heads(u))
                if u < A_T:
                    need(v, at_p, f"sc{u}")
                    if u >= 2:
                        need(v, at_a, f"ex{u - 2}")
                    mask = const("amask").rearrange("p (b k) -> p b k", b=NB)
                    for h in range(2):
                        last = nc.vector.scalar_tensor_tensor(
                            sc[u % 2][:, 2 * h:2 * h + 2], sc_bank(u, h)[:].rearrange("p (b k) -> p b k", b=NB),
                            HD ** -0.5, mask, ALU.mult, ALU.add)
                    at_v.done(last, f"mask{u}")
                    need(v, at_v, f"mask{u}")
                    at_v.done(nc.vector.tensor_reduce(mx[:, u], sc[u % 2][:], AX.X, ALU.max), f"max{u}")
                    need(v, at_v, f"max{u}")
                    sink = par[:, PCOL["sink"] + 4 * u:PCOL["sink"] + 4 * u + 4]
                    at_v.done(nc.vector.tensor_tensor(mx[:, u], mx[:, u], sink, ALU.max), f"msk{u}")
                    need(v, at_v, f"msk{u}")
                    at_v.done(nc.vector.tensor_scalar(ngm[:, u], mx[:, u], -1.0, None, ALU.mult), f"neg{u}")
                    need(v, at_v, f"neg{u}")
                    at_v.done(nc.vector.tensor_tensor(es[:, u], sink, ngm[:, u], ALU.add), f"dsk{u}")
                else:
                    need(v, at_p, f"sc{u}")
                    at_v.done(nc.vector.tensor_reduce(mx[:, u, 0:2], sc_bank(u, 0)[:].rearrange("p (b k) -> p b k", b=NB),
                                                      AX.X, ALU.max), f"max{u}")
                    need(v, at_v, f"max{u}")
                    at_v.done(nc.vector.tensor_scalar(ngm[:, u, 0:2], mx[:, u, 0:2], -(P ** -0.5), None, ALU.mult), f"neg{u}")

            def scale(u):
                nb = len(heads(u))
                if u < A_T:
                    need(v, at_a, f"sk{u}")
                    at_v.done(nc.vector.tensor_tensor(sm[:, u], sm[:, u], es[:, u], ALU.add), f"den{u}")
                    need(v, at_v, f"den{u}")
                else:
                    need(v, at_a, f"ex{u}")
                at_v.done(nc.vector.reciprocal(rd[:, u, 0:nb], sm[:, u, 0:nb]), f"rd{u}")
                need(v, at_v, f"rd{u}")
                for n in range(nb):
                    last = nc.vector.tensor_scalar(pr[u % 2][:, n], pr[u % 2][:, n], rd[:, u, n:n + 1], None, ALU.mult)
                at_v.done(last, f"pr{u}")

            def finish(u):
                first, second, *others = unit_tiles(u)
                dve_beside(v, [first, second])
                need(v, at_p, f"pv{u}")
                v.wait_ge(agate_out, u + 1)
                m = u if u < A_T else 12 + u - A_T
                at_v.done(nc.vector.tensor_tensor(sg[:, m], pv_bank(u)[:, 0:T], sg[:, m], ALU.mult), f"y{u}")
                dve_beside(v, others)
                dve_kk(v, u)

            soft(0)
            dve_beside(v, range(ATTN_FIRST, ATTN_BEFORE))
            for u in U_ALL:
                scale(u)
                if u + 1 < len(U_ALL):
                    soft(u + 1)
                finish(u)

        kkn = at("kkn", B + 54 * K, [P, PAIRS, T])
        yall = kkn[:].rearrange("p a (c i) -> p a c i", c=NCH)
        v_bd = at("v_bd", B + 128 * K, [P, NCH, P])
        v_tok = at("v_tok", B + 130 * K, [P, NCH, CH])
        w2t = at("w2t", B + 131 * K, [P, P])
        a2t = at("a2t", B + 131 * K + 512, [P, P])
        small = B + 60 * K
        ws = [at(f"ws{d}", small + 256 * d, [P, CH]) for d in range(2)]
        sas = [at(f"sas{d}", small + 512 + 256 * d, [P, CH]) for d in range(2)]
        st = [at(f"st{d}", small + 1024 + 512 * d, [P, 2, CH]) for d in range(2)]
        e_end = [at(f"e_end{d}", 72 * K + 480 + 1120 * d, [P, NCH]) for d in range(2)]
        dirs = []
        for d in range(2):
            o = B + 82 * K + 19 * K * d
            w = {}
            for k, n in enumerate(("abd", "rbd", "bbd", "kbd", "mt", "tm", "brt", "btok", "ktok")):
                w[n] = at(f"{n}{d}", o + 2 * K * k, [P, NCH, P])
            w["nkatv"] = at(f"nkatv{d}", o + 18 * K, [P, NCH, CH])
            w["u"], w["x"], w["kat"], w["krt"] = w["kbd"], w["bbd"], w["btok"], w["ktok"]
            w["ml"] = v_bd if d == 0 else at("ml1", o + 19 * K, [P, NCH, P])
            for k, n in enumerate(("s", "sx", "ad", "bb", "kd", "e1", "e2", "e3", "th")):
                w[n] = at(f"{n}_{d}", o + 8 * K + K * k, [P, T])
            dirs.append(w)
        ks = at("ks", B + 82 * K + 17 * K, [P, T])
        keep = [at("gate0", B + 122 * K, [P, PAIRS, T]), at("gate1", B + 48 * K, [P, PAIRS, T]), rkv[:, PAIRS:2 * PAIRS]]
        gate_kept = sem("gate_kept")
        nrm_kk = at("nrm_kk", B + 48 * K, [P, PAIRS, T])
        THIRDS = range(3)
        KK_UNITS = [A_T + b for b in THIRDS]
        kk_a = Steps(sem("kk_act"), [f"sq{b}" for b in THIRDS] + ["tanh"] + [f"root{b}" for b in THIRDS])
        kk_v = Steps(sem("kk_dve"), [f"{n}{b}" for b in THIRDS for n in ("max", "inv")] + ["half"] + [f"kk{b}" for b in THIRDS])
        kk_p = Steps(sem("kk_pe"), [f"stat{b}" for b in THIRDS])
        zeroed = sem("rwkv_zeroed")

        def third(ap, b):
            return ap[:, 2 * b:2 * b + 2]

        def act_kk_squares(act):
            need(act, at_p, f"sc{A_T - 1}")
            act.wait_ge(shift_step, 3 * sum(x[0] == "shift" for x in ATTN_TILES[:unit_tiles(A_T)[0]]))
            for b in THIRDS:
                for p in (2 * b, 2 * b + 1):
                    last = nc.scalar.activation(nrm_kk[:, p], rkv[:, PAIRS + p], ACT.Square, scale=col("k_k", p))
                kk_a.done(last, f"sq{b}")
            kk_a.done(nc.scalar.activation(rkv[:, 18], rkv[:, 18], ACT.Tanh), "tanh")

        def pe_kk(pe, u):
            if u in KK_UNITS:
                b = KK_UNITS.index(u)
                need(pe, at_v, f"y{u - 2}")
                need(pe, kk_a, f"sq{b}")
                kk_p.done(nc.tensor.matmul(pv_bank(u)[:], const("bdones"), third(nrm_kk, b), start=True, stop=True), f"stat{b}")

        def act_kk_root(act, u):
            if u in KK_UNITS:
                b = KK_UNITS.index(u)
                need(act, kk_p, f"stat{b}")
                kk_a.done(nc.scalar.activation(third(nrm_kk, b), pv_bank(u)[:].rearrange("p (a t) -> p a t", a=2), ACT.Sqrt), f"root{b}")

        def dve_kk(v, u):
            if u in KK_UNITS:
                b = KK_UNITS.index(u)
                need(v, kk_a, f"root{b}")
                kk_v.done(nc.vector.tensor_scalar(third(nrm_kk, b), third(nrm_kk, b), 1e-12, None, ALU.max), f"max{b}")
                need(v, kk_v, f"max{b}")
                kk_v.done(nc.vector.reciprocal(third(nrm_kk, b), third(nrm_kk, b)), f"inv{b}")
            elif u == A_T + X_T - 1:
                kk_v.done(nc.vector.tensor_scalar(hw_sb[:], par[:, PCOL["w0"]:PCOL["w0"] + 24], 0.5, None, ALU.mult), "half")
                need(v, kk_v, "inv2")
                for b in THIRDS:
                    for p in (2 * b, 2 * b + 1):
                        last = nc.vector.scalar_tensor_tensor(kkn[:, p], rkv[:, PAIRS + p], col("k_k", p), nrm_kk[:, p], ALU.mult, ALU.mult)
                    kk_v.done(last, f"kk{b}")

        def pool_kk(pool):
            need(pool, at_p, f"sc{A_T + X_T - 1}")
            for d in range(2):
                if d == 1:
                    need(pool, at_p, f"pv{A_T + X_T - 1}")
                    pool.wait_ge(agate_out, A_T + X_T)
                    nc.gpsimd.memset(v_bd[:], 0.0).then_inc(zeroed, 1)
                for m in (dirs[d]["abd"], dirs[d]["rbd"], dirs[d]["bbd"], dirs[d]["kbd"]):
                    nc.gpsimd.memset(m[:], 0.0).then_inc(zeroed, 1)

        LV = range(1, LEVELS)
        ST = range(NCH)
        D2 = range(2)
        rw_o = Steps(sem("rwkv_pool"), ["w2t", "a2t", "vbd"] + [f"{n}{d}" for d in D2 for n in ("kbd", "rbd")]
                     + [f"{n}{d}" for d in D2 for n in ("t0_", "t1_", "ml1_")] + [f"{n}{d}" for d in D2 for n in ("u0_", "u1_")]
                     + [f"ml{l}_{d}" for l in LV if l > 1 for d in D2])
        rw_v = Steps(sem("rwkv_dve"), [f"{n}{d}" for d in D2 for n in ("u", "s", "sx")] + [f"{n}{d}" for d in D2 for n in ("ad", "bb", "t", "kd")]
                     + [f"{n}{d}" for d in D2 for n in ("abd", "bbd", "end")] + ["ks", "ksr", "q"]
                     + [f"{n}{d}" for d in D2 for n in ("mt", "kat", "m")] + [f"{n}{d}" for d in D2 for n in ("brt", "krt")]
                     + [f"{n}{d}" for d in D2 for n in ("nkatv", "krtv")]
                     + [f"{n}{l}_{d}" for l in LV for d in D2 for n in (("T", "U") if l < LEVELS - 1 else ("U",))]
                     + [f"{n}{s}_{d}" for s in ST for n in ("W", "G", "S", "Y") for d in D2
                        if not (n == "S" and s == NCH - 1) and not (n == "W" and s == 0)
                        and not (n == "G" and (s == 0 or s == NCH - 1))])
        rw_a = Steps(sem("rwkv_act"), [f"{n}{d}" for d in D2 for n in ("thw", "tha")] + ["vtok0"]
                     + [f"{n}{d}" for d in D2 for n in ("e1", "e2", "e3")] + [f"btok{d}" for d in D2] + [f"ktok{d}" for d in D2]
                     + [f"X{l}_{d}" for l in LV for d in D2] + [f"SA{s}_{d}" for s in ST for d in D2])
        rw_p = Steps(sem("rwkv_pe"), [f"{n}{d}" for d in D2 for n in ("zw", "za")] + ["vtok0"]
                     + [f"{n}{d}" for d in D2 for n in ("mt", "kat", "m")] + [f"{n}{d}" for d in D2 for n in ("brt", "krt", "btok")]
                     + [f"{n}{d}" for d in D2 for n in ("katv", "krtv", "ktok")]
                     + [s for l in LV for s in [f"X{l}_{d}" for d in D2]
                        + [f"{n}{l}_{d}" for d in D2 for n in (("U", "T") if l < LEVELS - 1 else ("U",))]]
                     + [f"{n}{s}_{d}" for s in ST for n in ("W", "SA", "S", "Y") for d in D2
                        if not (n == "S" and s == NCH - 1) and not (n == "W" and s == 0)])

        def bank_of(d, k):
            return banks[2 + 3 * d + k]

        def pair_tile(p, j):
            return Tile(FIRST["rwkv"], j, ((p, BESIDE),))

        def dve_pair_tile(v, p, j):
            tile = pair_tile(p, j)
            tile_done(v, tile)
            dst = sg[:, p + A_T] if j == 0 else keep[j - 1][:, p]
            nc.vector.tensor_tensor(dst, banks[tile.parity][:, 0:T], x_norm.rstd[:], ALU.mult).then_inc(gate_kept, 1)
            split_lo(v, tile.later())

        def pe_pair_tiles(pe, p):
            taken = [0]

            def go(n):
                for k in range(taken[0], taken[0] + n):
                    tile, kt = pair_tile(p, k // KT), k % KT
                    if kt == 0:
                        pe.wait_ge(gate_kept, p * BESIDE + max(k // KT - 1, 0))
                    if kt % HALF == 0:
                        pe.wait_ge(lo_ready, tile.units(kt // HALF + 1))
                    last = product(banks[tile.parity][:, 0:T], hx, (2 * tile.parity + kt // HALF) % RING, kt % HALF, kt, kt == 0, kt == KT - 1)
                    if kt % HALF == HALF - 1:
                        last.then_inc(units_used, 1)
                taken[0] += n
                assert taken[0] <= BESIDE * KT
            return go

        def chunks(ap):
            return ap.rearrange("p (c t) -> p c t", c=NCH)

        def four(ap):
            return ap.unsqueeze(1).broadcast_to([P, NCH, P])

        def blocks(bank):
            return bank[:].rearrange("p (c t) -> p c t", c=NCH)

        def value_part(bank, k):
            return bank[:, T * k:T * k + T].rearrange("p (c i) -> p c i", c=NCH)

        def level(l):
            return four(const("levels")[:, P * l:P * l + P])

        def halves():
            return [slice(CH * h, CH * h + CH) for h in range(2)]

        def chunk_of(d, s):
            return s if d == 0 else NCH - 1 - s

        def pool_rwkv(pool):
            pool.wait_ge(zeroed, 9)
            pool.wait_ge(in_lora, 48)
            with pool.Fori(0, PAIRS) as p:
                rw_o.done(nc.gpsimd.tensor_copy(w2t[:], w2_sb[:, p]), "w2t")
                rw_o.done(nc.gpsimd.tensor_copy(a2t[:], a2_sb[:, p]), "a2t")
                need(pool, rw_o, "a2t", p)
                for h in halves():
                    last = nc.gpsimd.tensor_copy(v_bd[h, :, h], rkv[h, 2 * PAIRS + p].rearrange("p (c t) -> p c t", c=NCH))
                rw_o.done(last, "vbd")
                for d, w in enumerate(dirs):
                    need(pool, rw_v, f"kd{d}", p)
                    need(pool, rw_a, f"e3{d}", p)
                    for h in halves():
                        last = nc.gpsimd.tensor_tensor(w["kbd"][h, :, h], chunks(w["kd"][h]), chunks(w["e3"][h]), ALU.mult)
                    rw_o.done(last, f"kbd{d}")
                    for h in halves():
                        last = nc.gpsimd.tensor_tensor(w["rbd"][h, :, h], rkv[h, p].rearrange("p (c t) -> p c t", c=NCH),
                                                       chunks(w["e1"][h]), ALU.mult)
                    rw_o.done(last, f"rbd{d}")
                ident = four(const("ident"))
                need(pool, rw_o, "rbd1", p)
                for d, w in enumerate(dirs):
                    need(pool, rw_v, f"m{d}", p)
                    rw_o.done(nc.gpsimd.tensor_tensor(w["tm"][:], w["tm"][:], level(0), ALU.mult), f"t0_{d}")
                    need(pool, rw_o, f"t0_{d}", p)
                    rw_o.done(nc.gpsimd.tensor_tensor(w["tm"][:], w["tm"][:], ident, ALU.add), f"t1_{d}")
                    rw_o.done(nc.gpsimd.tensor_tensor(w["ml"][:], w["mt"][:], level(1), ALU.mult), f"ml1_{d}")
                for d, w in enumerate(dirs):
                    need(pool, rw_p, f"ktok{d}", p)
                    rw_o.done(nc.gpsimd.tensor_tensor(w["u"][:], w["mt"][:], level(0), ALU.mult), f"u0_{d}")
                    need(pool, rw_o, f"u0_{d}", p)
                    rw_o.done(nc.gpsimd.tensor_tensor(w["u"][:], w["u"][:], ident, ALU.add), f"u1_{d}")
                for l in LV:
                    if l > 1:
                        for d, w in enumerate(dirs):
                            need(pool, rw_p, f"X{l - 1}_{d}", p)
                            rw_o.done(nc.gpsimd.tensor_tensor(w["ml"][:], w["mt"][:], level(l), ALU.mult), f"ml{l}_{d}")
                need(pool, rw_p, f"X{LEVELS - 1}_1", p)

        def act_rwkv(act):
            need(act, kk_v, "kk2")
            with act.Fori(0, PAIRS) as p:
                for d, w in enumerate(dirs):
                    need(act, rw_p, f"zw{d}", p)
                    rw_a.done(nc.scalar.activation(w["th"][:], bank_of(d, 0)[:, 0:T], ACT.Tanh, scale=0.5,
                                                   bias=hw_sb[:, bass.ds(p + PAIRS * d, 1)]), f"thw{d}")
                    need(act, rw_p, f"za{d}", p)
                    rw_a.done(nc.scalar.activation(w["ad"][:], bank_of(d, 1)[:, 0:T], ACT.Tanh, scale=0.5,
                                                   bias=hw_sb[:, bass.ds(p + (2 + d) * PAIRS, 1)]), f"tha{d}")
                need(act, rw_p, "vtok0", p)
                rw_a.done(nc.scalar.activation(v_tok[:], value_part(bank_of(0, 2), 0), ACT.Copy), "vtok0")
                for d, w in enumerate(dirs):
                    need(act, rw_v, f"sx{d}", p)
                    rw_a.done(nc.scalar.activation(w["e1"][:], w["s"][:], ACT.Exp, scale=-HALF_DECAY), f"e1{d}")
                    rw_a.done(nc.scalar.activation(w["e2"][:], w["sx"][:], ACT.Exp, scale=-HALF_DECAY), f"e2{d}")
                    rw_a.done(nc.scalar.activation(w["e3"][:], w["s"][:], ACT.Exp, scale=HALF_DECAY), f"e3{d}")
                split_hi(act, pair_tile(p, 0).later())
                split_hi(act, pair_tile(p, 1).later())
                for d, w in enumerate(dirs):
                    need(act, rw_p, f"katv{d}", p)
                    rw_a.done(nc.scalar.activation(w["btok"][:], blocks(bank_of(d, 2)), ACT.Copy), f"btok{d}")
                for d, w in enumerate(dirs):
                    need(act, rw_p, f"ktok{d}", p)
                    rw_a.done(nc.scalar.activation(w["ktok"][:], blocks(bank_of(d, 1)), ACT.Copy), f"ktok{d}")
                for l in LV:
                    if l == LEVELS - 1:
                        split_hi(act, pair_tile(p, 2).later())
                    for d, w in enumerate(dirs):
                        need(act, rw_p, f"X{l}_{d}", p)
                        if l > 1:
                            need(act, rw_p, f"T{l - 1}_{d}", p)
                        rw_a.done(nc.scalar.activation(w["x"][:], blocks(bank_of(d, 1)), ACT.Copy), f"X{l}_{d}")
                for s in ST:
                    for d in D2:
                        need(act, rw_p, f"SA{s}_{d}", p)
                        if s > 0:
                            need(act, rw_p, f"Y{s - 1}_{d}", p)
                        rw_a.done(nc.scalar.activation(sas[d][:], bank_of(d, 1)[:, 0:CH], ACT.Copy), f"SA{s}_{d}")
                split_hi(act, pair_tile(p, 3).later())
                need(act, rw_p, f"Y{NCH - 1}_1", p)
                need(act, rw_v, f"Y{NCH - 1}_1", p)

        def dve_rwkv(v):
            with v.Fori(0, PAIRS) as p:
                for d, w in enumerate(dirs):
                    run = const("run_up" if d == 0 else "run_lo")
                    turn = (lambda ap: ap) if d == 0 else (lambda ap: ap[:, ::-1])
                    need(v, rw_a, f"thw{d}", p)
                    rw_v.done(nc.vector.tensor_scalar(w["th"][:], w["th"][:], 1.0, None, ALU.add), f"u{d}")
                    need(v, rw_v, f"u{d}", p)
                    rw_v.done(nc.vector.tensor_tensor_scan(turn(w["s"][:]), turn(run), turn(w["th"][:]), 0.0, ALU.mult, ALU.add), f"s{d}")
                    need(v, rw_v, f"s{d}", p)
                    rw_v.done(nc.vector.tensor_tensor(w["sx"][:], w["s"][:], w["th"][:], ALU.subtract), f"sx{d}")
                for d, w in enumerate(dirs):
                    need(v, rw_a, f"tha{d}", p)
                    rw_v.done(nc.vector.tensor_scalar(w["ad"][:], w["ad"][:], 0.5, 0.5, ALU.mult, ALU.add), f"ad{d}")
                    need(v, rw_v, f"ad{d}", p)
                    rw_v.done(nc.vector.tensor_tensor(w["bb"][:], kkn[:, p], w["ad"][:], ALU.mult), f"bb{d}")
                    rw_v.done(nc.vector.tensor_scalar(w["kd"][:], w["ad"][:], 1.0, col("k_a", p), ALU.subtract, ALU.mult), f"t{d}")
                    need(v, rw_v, f"t{d}", p)
                    rw_v.done(nc.vector.scalar_tensor_tensor(w["kd"][:], w["kd"][:], 1.0, rkv[:, PAIRS + p], ALU.add, ALU.mult), f"kd{d}")
                for d, w in enumerate(dirs):
                    need(v, rw_a, f"e3{d}", p)
                    for h in halves():
                        last = nc.vector.tensor_tensor(w["abd"][h, :, h], kkn[h, p].rearrange("p (c t) -> p c t", c=NCH),
                                                       chunks(w["e2"][h]), ALU.mult)
                    rw_v.done(last, f"abd{d}")
                    for h in halves():
                        last = nc.vector.tensor_tensor(w["bbd"][h, :, h], chunks(w["bb"][h]), chunks(w["e3"][h]), ALU.mult)
                    rw_v.done(last, f"bbd{d}")
                    end = CH - 1 if d == 0 else 0
                    rw_v.done(nc.vector.tensor_copy(e_end[d][:], chunks(w["e1"][:])[:, :, end]), f"end{d}")
                need(v, rw_v, "end1", p)
                rw_v.done(nc.vector.tensor_tensor(ks[:], dirs[0]["kd"][:], dirs[1]["kd"][:], ALU.add), "ks")
                need(v, rw_v, "ks", p)
                rw_v.done(nc.vector.tensor_scalar(ks[:], ks[:], col("r_k", p), None, ALU.mult), "ksr")
                need(v, rw_v, "ksr", p)
                need(v, rw_o, "rbd1", p)
                rw_v.done(nc.vector.tensor_tensor(rkv[:, p], rkv[:, p], ks[:], ALU.mult), "q")
                dve_pair_tile(v, p, 0)
                up, lo, incl = ([const(n) for n in names] for names in (("strict_up", "strict_lo"), ("strict_lo", "strict_up"),
                                                                        ("incl_up", "incl_lo")))
                for d, w in enumerate(dirs):
                    for n, k, dst, mask, sign in (("mt", 0, w["mt"], up[d], -1.0), ("kat", 1, w["kat"], up[d], 1.0),
                                                  ("m", 2, w["tm"], lo[d], -1.0)):
                        need(v, rw_p, f"{n}{d}", p)
                        rw_v.done(nc.vector.scalar_tensor_tensor(dst[:], blocks(bank_of(d, k)), sign, four(mask), ALU.mult, ALU.mult), f"{n}{d}")
                for d, w in enumerate(dirs):
                    for k, n in enumerate(("brt", "krt")):
                        need(v, rw_p, f"{n}{d}", p)
                        rw_v.done(nc.vector.tensor_tensor(w[n][:], blocks(bank_of(d, k)), four(incl[d]), ALU.mult), f"{n}{d}")
                dve_pair_tile(v, p, 1)
                for d, w in enumerate(dirs):
                    need(v, rw_p, f"krtv{d}", p)
                    rw_v.done(nc.vector.tensor_scalar(w["nkatv"][:], value_part(bank_of(d, 0), 0), -1.0, None, ALU.mult), f"nkatv{d}")
                    part = value_part(bank_of(d, 0), 1)
                    if d == 0:
                        last = nc.vector.tensor_scalar(yall[:, p], part, 1.0, None, ALU.mult)
                    else:
                        need(v, rw_v, "krtv0", p)
                        last = nc.vector.tensor_tensor(yall[:, p], yall[:, p], part, ALU.add)
                    rw_v.done(last, f"krtv{d}")
                for l in LV:
                    if l == LEVELS - 1:
                        dve_pair_tile(v, p, 2)
                    for d, w in enumerate(dirs):
                        if l < LEVELS - 1:
                            need(v, rw_p, f"T{l}_{d}", p)
                            rw_v.done(nc.vector.tensor_tensor(w["tm"][:], w["tm"][:], blocks(bank_of(d, 0)), ALU.add), f"T{l}_{d}")
                        else:
                            need(v, rw_p, f"U{l}_{d}", p)
                        rw_v.done(nc.vector.tensor_tensor(w["u"][:], w["u"][:], blocks(bank_of(d, 2)), ALU.add), f"U{l}_{d}")
                for s in ST:
                    now, old = s % 2, (s - 1) % 2
                    for d in D2:
                        if s > 0:
                            need(v, rw_p, f"W{s}_{d}", p)
                            rw_v.done(nc.vector.tensor_tensor(ws[d][:], dirs[d]["nkatv"][:, chunk_of(d, s)], bank_of(d, 0)[:, 0:CH],
                                                              ALU.subtract), f"W{s}_{d}")
                    for d in D2:
                        if 0 < s < NCH - 1:
                            c = chunk_of(d, s)
                            rw_v.done(nc.vector.tensor_scalar(st[d][:, now], st[d][:, old], e_end[d][:, c:c + 1], None, ALU.mult), f"G{s}_{d}")
                    for d in D2:
                        if s == NCH - 1:
                            continue
                        c = chunk_of(d, s)
                        need(v, rw_p, f"S{s}_{d}", p)
                        new = bank_of(d, 2)[:, 0:CH]
                        if s == 0:
                            last = nc.vector.tensor_scalar(st[d][:, now], new, e_end[d][:, c:c + 1], None, ALU.mult)
                        else:
                            need(v, rw_v, f"G{s}_{d}", p)
                            last = nc.vector.scalar_tensor_tensor(st[d][:, now], new, e_end[d][:, c:c + 1], st[d][:, now], ALU.mult, ALU.add)
                        rw_v.done(last, f"S{s}_{d}")
                    for d in D2:
                        need(v, rw_p, f"Y{s}_{d}", p)
                        y = yall[:, p, chunk_of(d, s)]
                        rw_v.done(nc.vector.tensor_tensor(y, y, bank_of(d, 1)[:, 0:CH], ALU.add), f"Y{s}_{d}")
                dve_pair_tile(v, p, 3)

        def pe_rwkv(pe):
            pe.wait_ge(shift_copied, SHIFT_T)
            pe.wait_ge(agate_pre, A_T + X_T)
            with pe.Fori(0, PAIRS) as p:
                go = pe_pair_tiles(pe, p)

                def each(bank, lhs, rhs, n=P, o=0):
                    for c in range(NCH):
                        last = nc.tensor.matmul(bank[:, o + n * c:o + n * c + n], lhs[:, c], rhs[:, c], start=True, stop=True)
                    return last

                def turned(bank, src):
                    for c in range(NCH):
                        last = nc.tensor.transpose(bank[:, P * c:P * c + P], src[:, c], const("ident"))
                    return last

                go(GO_START)
                pe.wait_ge(rw_v.sem, p * len(rw_v.names))
                need(pe, kk_a, "tanh")
                need(pe, at_v, f"y{A_T + X_T - 1}")
                for d in D2:
                    need(pe, rw_o, "a2t", p)
                    h = halves()[d]
                    rw_p.done(nc.tensor.matmul(bank_of(d, 0)[:, 0:T], w2t[h], rkv[h, 18], start=True, stop=True), f"zw{d}")
                    rw_p.done(nc.tensor.matmul(bank_of(d, 1)[:, 0:T], a2t[h], rkv[h, 19], start=True, stop=True), f"za{d}")
                need(pe, rw_o, "vbd", p)
                for c in range(NCH):
                    last = nc.tensor.matmul(bank_of(0, 2)[:, CH * c:CH * c + CH], v_bd[:, c], const("istack"), start=True, stop=True)
                rw_p.done(last, "vtok0")
                go(GO_PREP)
                for d, w in enumerate(dirs):
                    need(pe, rw_v, f"end{d}", p)
                    need(pe, rw_o, f"rbd{d}", p)
                    rw_p.done(each(bank_of(d, 0), w["bbd"], w["abd"]), f"mt{d}")
                    rw_p.done(each(bank_of(d, 1), w["kbd"], w["abd"]), f"kat{d}")
                    if d == 0:
                        need(pe, rw_a, "vtok0", p)
                    rw_p.done(each(bank_of(d, 2), w["abd"], w["bbd"]), f"m{d}")
                go(GO_GRAM)
                for d, w in enumerate(dirs):
                    need(pe, rw_v, f"mt{d}", p)
                    rw_p.done(each(bank_of(d, 0), w["bbd"], w["rbd"]), f"brt{d}")
                    need(pe, rw_v, f"kat{d}", p)
                    rw_p.done(each(bank_of(d, 1), w["kbd"], w["rbd"]), f"krt{d}")
                    need(pe, rw_v, f"m{d}", p)
                    rw_p.done(turned(bank_of(d, 2), w["bbd"]), f"btok{d}")
                go(GO_GRAM)
                for d, w in enumerate(dirs):
                    need(pe, rw_v, f"krt{d}", p)
                    rw_p.done(each(bank_of(d, 0), w["kat"], v_tok, CH), f"katv{d}")
                    rw_p.done(each(bank_of(d, 0), w["krt"], v_tok, CH, T), f"krtv{d}")
                    rw_p.done(turned(bank_of(d, 1), w["kbd"]), f"ktok{d}")
                go(GO_GRAM)
                for l in LV:
                    for d, w in enumerate(dirs):
                        need(pe, rw_o, f"ml{l}_{d}", p)
                        if l == 1:
                            need(pe, rw_o, f"t1_{d}", p)
                            need(pe, rw_a, f"ktok{d}", p)
                        else:
                            need(pe, rw_v, f"T{l - 1}_{d}", p)
                        rw_p.done(each(bank_of(d, 1), w["ml"], w["tm"]), f"X{l}_{d}")
                    go(GO_LEVEL)
                    for d, w in enumerate(dirs):
                        need(pe, rw_a, f"X{l}_{d}", p)
                        if l == 1:
                            need(pe, rw_o, f"u1_{d}", p)
                            need(pe, rw_a, f"btok{d}", p)
                            need(pe, rw_v, f"krtv{d}", p)
                        else:
                            need(pe, rw_v, f"U{l - 1}_{d}", p)
                        rw_p.done(each(bank_of(d, 2), w["x"], w["u"]), f"U{l}_{d}")
                        if l < LEVELS - 1:
                            rw_p.done(each(bank_of(d, 0), w["u"], w["x"]), f"T{l}_{d}")
                    go(GO_LEVEL)
                for s in ST:
                    old = (s - 1) % 2
                    for d, w in enumerate(dirs):
                        if s > 0:
                            need(pe, rw_v, f"S{s - 1}_{d}", p)
                            rw_p.done(nc.tensor.matmul(bank_of(d, 0)[:, 0:CH], w["abd"][:, chunk_of(d, s)], st[d][:, old],
                                                       start=True, stop=True), f"W{s}_{d}")
                    if s > 0:
                        go(GO_STEP)
                    for d, w in enumerate(dirs):
                        c = chunk_of(d, s)
                        if s == 0:
                            need(pe, rw_v, f"U{LEVELS - 1}_{d}", p)
                        else:
                            need(pe, rw_v, f"Y{s - 1}_{d}", p)
                            need(pe, rw_v, f"W{s}_{d}", p)
                        rhs = w["nkatv"][:, c] if s == 0 else ws[d][:]
                        rw_p.done(nc.tensor.matmul(bank_of(d, 1)[:, 0:CH], w["u"][:, c], rhs, start=True, stop=True), f"SA{s}_{d}")
                    go(GO_STEP)
                    for d, w in enumerate(dirs):
                        if s == NCH - 1:
                            continue
                        c = chunk_of(d, s)
                        need(pe, rw_a, f"SA{s}_{d}", p)
                        o = bank_of(d, 2)[:, 0:CH]
                        nc.tensor.matmul(o, w["btok"][:, c], sas[d][:], start=True, stop=False)
                        rw_p.done(nc.tensor.matmul(o, w["ktok"][:, c], v_tok[:, c], start=False, stop=True), f"S{s}_{d}")
                    for d, w in enumerate(dirs):
                        c = chunk_of(d, s)
                        if s == NCH - 1:
                            need(pe, rw_a, f"SA{s}_{d}", p)
                        o = bank_of(d, 1)[:, 0:CH]
                        if s > 0:
                            nc.tensor.matmul(o, w["rbd"][:, c], st[d][:, old], start=True, stop=False)
                        rw_p.done(nc.tensor.matmul(o, w["brt"][:, c], sas[d][:], start=s == 0, stop=True), f"Y{s}_{d}")
                    go(GO_STEP if s < NCH - 1 else BESIDE * KT - GO_START - GO_PREP - 3 * GO_GRAM - 2 * (LEVELS - 1) * GO_LEVEL
                       - (3 * NCH - 2) * GO_STEP)

        yhl = [at(f"yhl{k}", B + o * K, [P, n, 2, T], R) for k, (o, n) in enumerate(((74, 8), (54, 6), (128, 2)))]
        Y_PIECES = [(0, 0, 0, 4), (0, 4, 4, 4), (1, 0, 8, 4), (1, 4, 12, 2), (2, 0, 14, 2)]
        G0 = B + 82 * K
        gsum = at("gsum", G0, [P, 24])
        gmean = at("gmean", G0 + 128, [P, 24])
        gvar = at("gvar", G0 + 256, [P, 24])
        gstd = at("gstd", G0 + 384, [P, 24])
        grs = at("grs", G0 + 512, [P, 24])
        gsq = at("gsq", G0 + K, [P, 24, CH])
        ybd = at("ybd", G0 + 8 * K, [P, 24, P])
        t1 = at("gn_t1", G0 + 20 * K, [P, PAIRS, T])
        t2 = at("gn_t2", G0 + 26 * K, [P, PAIRS, T])
        gn_o = Steps(sem("gn_pool"), ["zero"])
        gn_a = Steps(sem("gn_act"), ["gate", "sq", "std"] + [f"hi{q}" for q in range(5)])
        gn_v = Steps(sem("gn_dve"), ["sum", "mean", "center", "var", "rstd", "yn"]
                     + [f"{n}{p}" for p in range(PAIRS) for n in ("ln", "bonus", "sum", "y")]
                     + [f"lo{q}" for q in range(5)])
        gn_p = Steps(sem("gn_pe"), ["bonus0", "bonus1", "bonus2", "y0", "y1", "y2"])
        y24 = kkn[:].rearrange("p a (c i) -> p (a c) i", c=NCH)

        def wide(ap):
            return ap.unsqueeze(2).broadcast_to([P, 24, CH])

        def pool_gn(pool):
            need(pool, rw_v, f"Y{NCH - 1}_1", PAIRS - 1)
            need(pool, rw_p, f"Y{NCH - 1}_1", PAIRS - 1)
            gn_o.done(nc.gpsimd.memset(ybd[:], 0.0), "zero")
            pool.wait_ge(units_used, 2 * FIRST["merge_b"])
            pool.dma_start(x_res[:], xT).then_inc(in_res, 16)
            pool.dma_start(X1[:, :, 0:META], metaT).then_inc(in_meta, 16)

        def act_gn(act):
            need(act, rw_v, f"Y{NCH - 1}_1", PAIRS - 1)
            act.wait_ge(gate_kept, BESIDE * PAIRS)
            gn_a.done(nc.scalar.activation(sg[:, A_T:A_T + PAIRS], sg[:, A_T:A_T + PAIRS], ACT.Silu), "gate")
            need(act, gn_v, "center")
            gn_a.done(nc.scalar.activation(gsq[:], y24, ACT.Square), "sq")
            need(act, gn_v, "var")
            gn_a.done(nc.scalar.activation(gstd[:], gvar[:], ACT.Sqrt, bias=GN_EPS, scale=1.0 / CH), "std")

        def act_gn_hi(act):
            need(act, gn_v, f"y{PAIRS - 1}")
            for q, (part, o, kt, n) in enumerate(Y_PIECES):
                gn_a.done(nc.scalar.activation(yhl[part][:, o:o + n, 0], sg[:, kt:kt + n], ACT.Copy), f"hi{q}")

        def dve_gn(v):
            need(v, rw_v, f"Y{NCH - 1}_1", PAIRS - 1)
            gn_v.done(nc.vector.tensor_reduce(gsum[:], y24, AX.X, ALU.add), "sum")
            need(v, gn_v, "sum")
            gn_v.done(nc.vector.tensor_scalar(gmean[:], gsum[:], 1.0 / CH, None, ALU.mult), "mean")
            need(v, gn_v, "mean")
            gn_v.done(nc.vector.tensor_tensor(y24, y24, wide(gmean[:]), ALU.subtract), "center")
            need(v, gn_a, "sq")
            gn_v.done(nc.vector.tensor_reduce(gvar[:], gsq[:], AX.X, ALU.add), "var")
            need(v, gn_a, "std")
            gn_v.done(nc.vector.reciprocal(grs[:], gstd[:]), "rstd")
            need(v, gn_v, "rstd")
            need(v, gn_o, "zero")
            for h in halves():
                last = nc.vector.tensor_tensor(ybd[h, :, h], y24[h], wide(grs[:])[h], ALU.mult)
            gn_v.done(last, "yn")

        GN_BANKS = (2, 6, 7)

        def dve_gn_out(v):
            for p in range(PAIRS):
                at_p_ = T * (p % 2)
                need(v, gn_p, f"y{p // 2}")
                gn_v.done(nc.vector.tensor_scalar(t1[:, p], banks[GN_BANKS[p // 2]][:, at_p_:at_p_ + T], col("ln_w", p), col("ln_b", p),
                                                  ALU.mult, ALU.add), f"ln{p}")
                gn_v.done(nc.vector.tensor_tensor(t2[:, p], banks[3 + p // 2][:, at_p_:at_p_ + T], rkv[:, 2 * PAIRS + p],
                                                  ALU.mult), f"bonus{p}")
                need(v, gn_v, f"bonus{p}")
                gn_v.done(nc.vector.tensor_tensor(t1[:, p], t1[:, p], t2[:, p], ALU.add), f"sum{p}")
                need(v, gn_v, f"sum{p}")
                gn_v.done(nc.vector.tensor_tensor(sg[:, A_T + p], sg[:, A_T + p], t1[:, p], ALU.mult), f"y{p}")

        def dve_gn_lo(v):
            for q, (part, o, kt, n) in enumerate(Y_PIECES):
                need(v, gn_a, f"hi{q}")
                gn_v.done(nc.vector.tensor_tensor(yhl[part][:, o:o + n, 1], sg[:, kt:kt + n],
                                                  yhl[part][:, o:o + n, 0].bitcast(F), ALU.subtract), f"lo{q}")

        def pe_gn(pe):
            need(pe, rw_v, f"Y{NCH - 1}_1", PAIRS - 1)
            for b in range(3):
                gn_p.done(nc.tensor.matmul(banks[3 + b][:], const("bdones"), rkv[:, 2 * b:2 * b + 2], start=True, stop=True), f"bonus{b}")

        def pe_gn_out(pe):
            need(pe, gn_v, "yn")
            for b in range(3):
                for n in range(8):
                    last = nc.tensor.matmul(banks[GN_BANKS[b]][:, CH * n:CH * n + CH], ybd[:, 8 * b + n], const("istack"), start=True, stop=True)
                gn_p.done(last, f"y{b}")

        mg = at("mg", B + 90 * K, [P, KT, 2, T], R)
        gt = at("gt", B + 117 * K, [P, N_BRANCH, T])
        gpre = at("gpre", B + 114 * K, [P, N_BRANCH, T])
        gate_pre = sem("gate_pre")
        mt_ = at("mt_", B + 39 * K, [P, N_BRANCH, T])
        x_res = at("x_res", B + 17 * K, [P, KT, T])
        X1 = at("X1", B, [P, KT, TM])
        SPANS = [(0, A_T), (A_T, A_T + PAIRS), (A_T + PAIRS, KT)]
        gate_out, wo_out, mg_step, mg_hi, mg_lo, wout1_out = (
            sem(n) for n in ("gate_out", "wo_out", "mg_step", "mg_hi", "mg_lo", "wout1_out"))

        def rnd(tile, c, m):
            return tile.loops[-1][0] * m + c if tile.loops else c

        def act_merge(act):
            def body(tile):
                b = tile.t % 4
                m = rnd(tile, 0, 1)
                if b == 2 and not tile.loops:
                    act_gn_hi(act)
                if b < N_BRANCH:
                    split_hi(act, tile.later())
                    act.wait_ge(gate_pre, rnd(tile, b + 1, 3))
                    if tile.loops and b == 0:
                        act.wait_ge(mg_step, rnd(tile, -2, 5))
                    nc.scalar.activation(gt[:, b], gpre[:, b], ACT.Sigmoid,
                                         bias=col("gate_b", rnd(tile, KT * b, 1))).then_inc(gate_out, 1)
                else:
                    act.wait_ge(mg_step, rnd(tile, 5, 5))
                    nc.scalar.activation(mg[:, m, 0], mt_[:, 0], ACT.Copy).then_inc(mg_hi, 1)
                    split_hi(act, tile.later())
            run_tiles(act, "merge_a", 4, body)

        def dve_merged(v, tile, m, bank, gates, count):
            v.wait_ge(gate_out, count(3, 3))
            for b in range(N_BRANCH):
                ins = nc.vector.tensor_tensor(mt_[:, b], banks[bank + b][:, 0:T], gates[:, b], ALU.mult)
                ins.then_inc(mg_step, 1)
            v.wait_ge(mg_step, count(3, 5))
            nc.vector.tensor_tensor(mt_[:, 0], mt_[:, 0], mt_[:, 1], ALU.add).then_inc(mg_step, 1)
            v.wait_ge(mg_step, count(4, 5))
            nc.vector.tensor_tensor(mt_[:, 0], mt_[:, 0], mt_[:, 2], ALU.add).then_inc(mg_step, 1)
            v.wait_ge(mg_hi, count(1, 1))
            nc.vector.tensor_tensor(mg[:, m, 1], mt_[:, 0], mg[:, m, 0].bitcast(F), ALU.subtract).then_inc(mg_lo, 1)
            split_lo(v, tile.later())

        def dve_merge(v):
            def body(tile):
                m, b = rnd(tile, 0, 1), tile.t % 4
                if not tile.loops and b in (1, 2):
                    (dve_gn_out if b == 1 else dve_gn_lo)(v)
                tile_done(v, tile)
                if b < N_BRANCH:
                    nc.vector.tensor_tensor(gpre[:, b], banks[tile.parity][:, 0:T], x_norm.rstd[:], ALU.mult).then_inc(gate_pre, 1)
                    split_lo(v, tile.later())
                    return
                dve_merged(v, tile, m, 2, gt, lambda c, per: rnd(tile, c, per))
            run_tiles(v, "merge_a", 4, body)

        def branches(pe, tile, bank):
            for k in range(2):
                pe.wait_ge(lo_ready, tile.units(k + 1))
                for j in range(HALF):
                    kt = HALF * k + j
                    n, (a, z) = next((n, s) for n, s in enumerate(SPANS) if s[0] <= kt < s[1])
                    part, o = next((part, o + kt - c) for part, o, c, m in Y_PIECES if c <= kt < c + m)
                    slot = (2 * tile.parity + k) % RING
                    last = product(banks[bank + n][:, 0:T], yhl[part], slot, j, o, kt == a, kt == z - 1)
                last.then_inc(units_used, 1)

        def pe_merge(pe):
            def body(tile):
                b = tile.t % 4
                if not tile.loops and b == 1:
                    pe_gn(pe)
                    pe_gn_out(pe)
                if b < N_BRANCH:
                    if b < 2 and not tile.loops:
                        pe.wait_ge(gate_kept, BESIDE * PAIRS - 1 + b)
                    else:
                        pe.wait_ge(gate_pre, rnd(tile, 1 if b == 2 else 0, 3))
                    full_tile(pe, tile, hx)
                    return
                if tile.loops:
                    pe.wait_ge(mg_step, rnd(tile, -2, 5))
                else:
                    need(pe, gn_v, "lo4")
                branches(pe, tile, 2)
            run_tiles(pe, "merge_a", 4, body)

        gt_b = at("gt_b", B + 33 * K, [P, N_BRANCH, T])

        def wo_bank(tile):
            return 5 if tile.t % 2 == 0 else 2

        def act_merge_b(act):
            def body(tile):
                act.wait_ge(mg_step, tile.local(5, 5 * MERGE_A - 2))
                for b in range(N_BRANCH):
                    nc.scalar.activation(gt_b[:, b], keep[b][:, tile.local()], ACT.Sigmoid,
                                         bias=col("gate_b", tile.local(1, KT * b + MERGE_A))).then_inc(gate_out, 1)
                act.wait_ge(mg_step, tile.local(5, 5 * MERGE_A + 5))
                nc.scalar.activation(mg[:, tile.local(1, MERGE_A), 0], mt_[:, 0], ACT.Copy).then_inc(mg_hi, 1)
                split_hi(act, tile.later())
            run_tiles(act, "merge_b", 2, body)

        def dve_merge_b(v):
            def body(tile):
                tile_done(v, tile)
                v.wait_ge(mg_lo, tile.local(1, MERGE_A))
                dve_merged(v, tile, tile.local(1, MERGE_A), wo_bank(tile), gt_b, lambda c, per: tile.local(per, per * MERGE_A + c))
            run_tiles(v, "merge_b", 2, body)

        def pe_merge_b(pe):
            def body(tile):
                pe.wait_ge(mg_step, tile.local(5, 5 * MERGE_A - 7))
                branches(pe, tile, wo_bank(tile))
            run_tiles(pe, "merge_b", 2, body)

        def dve_wout1(v):
            v.wait_ge(in_res, 16)
            v.wait_ge(in_meta, 16)

            def body(tile):
                tile_done(v, tile)
                m = tile.local()
                nc.vector.tensor_tensor(X1[:, m, META:], banks[tile.parity][:, 0:T], x_res[:, m], ALU.add).then_inc(wout1_out, 1)
                norm1.dve_tile(v, m, tile.local(1, 1))
                split_lo(v, tile.later())
            run_tiles(v, "wout1", 2, body)

        def act_norm_phase(act, phase, norm, x_out):
            def body(tile):
                act.wait_ge(x_out, tile.local(1, 1))
                norm.act_tile(act, tile.local())
                split_hi(act, tile.later())
            run_tiles(act, phase, 2, body)

        u1 = at("u1", B + 49 * K, [P, KT, 2, TM], R)
        HP = at("HP", B + 17 * K, [P, KT, 2, T])
        HL, PO = HP[:, :, 0], HP[:, :, 1]
        mg2 = at("mg2", B + 17 * K, [P, KT, 2, T], R)
        Z2 = B + 83 * K
        norm1 = Norm("norm1", X1, TM, "norm1_g", u1, B + 128 * K)
        gpool_out, gelu_out, gpool_pre, gelu_pre = (sem(n) for n in ("gpool_out", "gelu_out", "gpool_pre", "gelu_pre"))
        gpl = at("gpl", Z2 + 30 * K, [P, 2, T])
        gel = at("gel", Z2 + 32 * K, [P, 2, T])

        one272 = at("one272", Z2, [P, TM])
        vp = [at(f"vp{b}", Z2 + (2 + 2 * b) * K, [P, TM]) for b in range(2)]
        cs = [at(f"cs{b}", Z2 + (6 + 2 * b) * K, [P, TM]) for b in range(2)]
        df = [at(f"df{b}", Z2 + (10 + b) * K, [P, T]) for b in range(2)]
        dt = [at(f"dt{b}", Z2 + (12 + b) * K, [P, T]) for b in range(2)]
        dhl = at("dhl", Z2 + 14 * K, [P, POOL_T + 1, 2, T], R)
        vp_copied, vp_step, d_hi, d_lo, po_out, ones_set = (
            sem(n) for n in ("vp_copied", "vp_step", "d_hi", "d_lo", "po_out", "ones_set"))
        NG = len(POOL_WINDOWS)

        def own_tiles(phase):
            return [(Tile(FIRST[phase], t), g, j, POOL_T * g + j) for t, (g, j) in enumerate(OWN_ORDER)]

        def bank_user(t):
            while t >= 2:
                t -= 2
                if OWN_ORDER[t][1] != OWN:
                    return POOL_T * OWN_ORDER[t][0] + OWN_ORDER[t][1]
            return None

        def act_pool(act):
            for tile, g, j, n in own_tiles("pool"):
                split_hi(act, tile.later(), (0,))
                if j != OWN:
                    act.wait_ge(vp_step, 3 * n + 3)
                    nc.scalar.activation(dhl[:, n % 5, 0], dt[n % 2][:], ACT.Copy).then_inc(d_hi, 1)
                split_hi(act, tile.later(), (1,))

        def dve_pool(v):
            nc.vector.memset(one272[:], 1.0).then_inc(ones_set, 1)
            v.wait_ge(ones_set, 1)
            v.wait_ge(gpool_out, KT)
            for tile, g, j, n in own_tiles("pool"):
                b, window = n % 2, POOL_WINDOWS[g]
                tile_done(v, tile)
                if j == OWN:
                    for m in range(POOL_T):
                        c = POOL_T * g + m
                        nc.vector.scalar_tensor_tensor(PO[:, c], banks[2 + m][:, 0:T], col("pool_scale", c), PO[:, c],
                                                       ALU.mult, ALU.mult).then_inc(po_out, 1)
                    split_lo(v, tile.later())
                    continue
                nc.vector.tensor_tensor(vp[b][:], banks[tile.parity][:, 0:TM], norm1.rstd[:], ALU.mult).then_inc(vp_copied, 1)
                v.wait_ge(vp_copied, n + 1)
                nc.vector.tensor_tensor_scan(cs[b][:], one272[:], vp[b][:], 0.0, ALU.mult, ALU.add).then_inc(vp_step, 1)
                v.wait_ge(vp_step, 3 * n + 1)
                nc.vector.tensor_tensor(df[b][:], cs[b][:, META:], cs[b][:, META - window:TM - window], ALU.subtract).then_inc(vp_step, 1)
                v.wait_ge(vp_step, 3 * n + 2)
                nc.vector.scalar_tensor_tensor(dt[b][:], df[b][:], 1.0 / window, vp[b][:, META:], ALU.mult, ALU.subtract).then_inc(vp_step, 1)
                v.wait_ge(d_hi, n + 1)
                nc.vector.tensor_tensor(dhl[:, n % 5, 1], dt[b][:], dhl[:, n % 5, 0].bitcast(F), ALU.subtract).then_inc(d_lo, 1)
                split_lo(v, tile.later())

        def pe_pool(pe):
            for tile, g, j, n in own_tiles("pool"):
                if j != OWN:
                    user = bank_user(tile.t)
                    if user is None:
                        pe.wait_ge(gelu_pre, KT - 1 + tile.t)
                    else:
                        pe.wait_ge(vp_copied, user + 1)
                    full_tile(pe, tile, u1, TM)
                    continue
                if g > 0:
                    pe.wait_ge(po_out, POOL_T * g)
                pe.wait_ge(d_lo, POOL_T * (g + 1))
                for k in range(2):
                    pe.wait_ge(lo_ready, tile.units(k + 1))
                    for jj in range(HALF):
                        m, kt = 2 * k + jj // POOL_T, jj % POOL_T
                        last = product(banks[2 + m][:, 0:T], dhl, (2 * tile.parity + k) % RING, jj, (POOL_T * g + kt) % 5,
                                       kt == 0, kt == POOL_T - 1)
                    last.then_inc(units_used, 1)

        LP = CONV2 - 1
        vl = [at(f"vl{b}", Z2 + 1216 * b, [P, TM + LP]) for b in range(2)]
        xa = at("xa", Z2 + 2432, [P, TM])
        xc = at("xc", Z2 + 2432 + 1088, [P, 5, TM])
        xchl = at("xchl", Z2 + 2432 + 1088 * 6, [P, 5, 2, TM], R)
        ga = at("ga", Z2 + 2432 + 1088 * 16, [P, 2, 2, TM])
        gx = [at(f"gx{b}", Z2 + 2432 + 1088 * (20 + 4 * b), [P, 2, 2, TM]) for b in range(2)]
        av, tv, mv = (at(f"lru_{n}", Z2 + 2432 + 1088 * (28 + 4 * k), [P, 2, 2, TM]) for k, n in enumerate(("a", "t", "m")))
        hv = mv[:].rearrange("p k m t -> p (k m) t")
        vl_zero, vl_copied, conv_step, xc_hi, xc_lo, own_out, lru_gate = (
            sem(n) for n in ("vl_zero", "vl_copied", "conv_step", "xc_hi", "xc_lo", "own_out", "lru_gate"))
        lru_a = Steps(sem("lru_act"), ["tanh", "exp", "sqrt"])
        lru_v = Steps(sem("lru_dve"), ["one", "scan"])
        lru_o = Steps(sem("lru_pool"), ["ix", "sq", "b", "out"])

        def flat4(ap):
            return ap.rearrange("p a b t -> p (a b t)")

        def act_lru_decay(act, g, func, dst, scale, name):
            for n in range(4):
                s = lam_sb[:, scale, 4 * g + n:4 * g + n + 1]
                last = nc.scalar.activation(dst[:, n // 2, n % 2], ga[:, n // 2, n % 2], func, scale=s)
            lru_a.done(last, name)

        def act_lru_tanh(act, g):
            act.wait_ge(lru_gate, 8 * (g + 1))
            act_lru_decay(act, g, ACT.Tanh, tv, 1, "tanh")

        def act_lru_exp(act, g):
            if g > 0:
                need(act, lru_v, "scan", g - 1)
            act_lru_decay(act, g, ACT.Exp, av, 2, "exp")

        def act_lru_root(act, g):
            need(act, lru_v, "one", g)
            lru_a.done(nc.scalar.activation(mv[:], tv[:], ACT.Sqrt), "sqrt")

        def dve_lru_one(v, g):
            need(v, lru_a, "tanh", g)
            need(v, lru_o, "sq", g)
            lru_v.done(nc.vector.scalar_tensor_tensor(flat4(tv[:]), flat4(mv[:]), 1.0, flat4(tv[:]), ALU.add, ALU.mult), "one")

        def dve_lru_scan(v, g):
            need(v, lru_o, "b", g)
            for n in range(4):
                last = nc.vector.tensor_tensor_scan(hv[:, n], av[:, n // 2, n % 2], gx[g % 2][:, n // 2, n % 2], 0.0, ALU.mult, ALU.add)
            lru_v.done(last, "scan")

        def own_bank(tile, o):
            return banks[tile.parity] if o == 6 else banks[2 + o % 7]

        def pool_lru(pool):
            for g in range(4):
                x = gx[g % 2]
                pool.wait_ge(lru_gate, 8 * (g + 1))
                for n in range(4):
                    row = x[:, n // 2, n % 2]
                    last = nc.gpsimd.tensor_tensor(row, row, xc[:, (4 * g + n) % 5], ALU.mult)
                lru_o.done(last, "ix")
                need(pool, lru_a, "exp", g)
                if g > 0:
                    need(pool, lru_o, "out", g - 1)
                lru_o.done(nc.gpsimd.tensor_tensor(mv[:], av[:], av[:], ALU.mult), "sq")
                need(pool, lru_a, "sqrt", g)
                lru_o.done(nc.gpsimd.tensor_tensor(flat4(x[:]), flat4(mv[:]), flat4(x[:]), ALU.mult), "b")
                need(pool, lru_v, "scan", g)
                h = HL[:, 4 * g:4 * g + 4]
                lru_o.done(nc.gpsimd.tensor_tensor(h, hv[:, :, META:], h, ALU.mult), "out")

        def act_lru(act):
            need_lam(act)
            for tile, g, j, n in own_tiles("lru"):
                if j != OWN:
                    split_hi(act, tile.later())
                    act.wait_ge(conv_step, 4 * n + 4)
                    nc.scalar.activation(xchl[:, n % 5, 0], xc[:, n % 5], ACT.Copy).then_inc(xc_hi, 1)
                    if g > 0 and j > 0:
                        (act_lru_tanh, act_lru_exp, act_lru_root)[j - 1](act, g - 1)
                    continue
                if g > 1:
                    need(act, lru_v, "scan", g - 2)
                for o in range(8):
                    k, ax, m = o // 4, o // 2 % 2, o % 2
                    c = 4 * g + 2 * k + m
                    if o % 4 == 3:
                        act.wait_ge(units_used, tile.units(k + 1))
                    else:
                        act.wait_ge(own_out, 6 * g + 3 * k + o % 4 + 1)
                    nc.scalar.activation((gx[g % 2] if ax else ga)[:, k, m], own_bank(tile, o)[:, 0:TM], ACT.Sigmoid,
                                         bias=col("gate_x_b" if ax else "gate_a_b", c)).then_inc(lru_gate, 1)
                split_hi(act, tile.later())

        def dve_lru(v):
            v.wait_ge(d_lo, KT)
            for b in range(2):
                nc.vector.memset(vl[b][:], 0.0).then_inc(vl_zero, 1)
            v.wait_ge(vl_zero, 2)
            v.wait_ge(gelu_out, KT)
            for tile, g, j, n in own_tiles("lru"):
                if j == OWN:
                    split_lo(v, tile.later())
                    continue
                row = vl[n % 2]
                tile_done(v, tile)
                nc.vector.tensor_tensor(row[:, LP:], banks[tile.parity][:, 0:TM], norm1.rstd[:], ALU.mult).then_inc(vl_copied, 1)
                v.wait_ge(vl_copied, n + 1)
                for k in range(CONV2):
                    tap = row[:, LP - k:LP - k + TM]
                    w = col("conv_w2", n + KT * (CONV2 - 1 - k))
                    if k == 0:
                        ins = nc.vector.tensor_scalar(xa[:], tap, w, col("conv_b2", n), ALU.mult, ALU.add)
                    else:
                        v.wait_ge(conv_step, 4 * n + k)
                        dst = xc[:, n % 5] if k == CONV2 - 1 else xa[:]
                        if k == CONV2 - 1 and n >= 5:
                            need(v, lru_o, "ix", (n - 5) // 4)
                        ins = nc.vector.scalar_tensor_tensor(dst, tap, w, xa[:], ALU.mult, ALU.add)
                    ins.then_inc(conv_step, 1)
                v.wait_ge(xc_hi, n + 1)
                nc.vector.tensor_tensor(xchl[:, n % 5, 1], xc[:, n % 5], xchl[:, n % 5, 0].bitcast(F), ALU.subtract).then_inc(xc_lo, 1)
                split_lo(v, tile.later())
                if g > 0 and j == 3:
                    dve_lru_one(v, g - 1)
                if g > 1 and j == 0:
                    dve_lru_scan(v, g - 2)

        def pe_lru(pe):
            for tile, g, j, n in own_tiles("lru"):
                if j != OWN:
                    user = bank_user(tile.t)
                    if tile.t >= 2 and OWN_ORDER[tile.t - 2][1] == OWN:
                        pe.wait_ge(lru_gate, 8 * OWN_ORDER[tile.t - 2][0] + 7)
                    elif user is None:
                        pe.wait_ge(vp_copied, KT)
                    else:
                        pe.wait_ge(vl_copied, user + 1)
                    full_tile(pe, tile, u1, TM)
                    continue
                pe.wait_ge(xc_lo, POOL_T * (g + 1))
                if g > 0:
                    pe.wait_ge(lru_gate, 8 * g)
                else:
                    pe.wait_ge(po_out, KT)
                pe.wait_ge(vl_copied, bank_user(tile.t) + 1)
                for k in range(2):
                    pe.wait_ge(lo_ready, tile.units(k + 1))
                    for jj in range(HALF):
                        o, kt = 4 * k + jj // 2, jj % 2
                        if o == 7 and kt == 0:
                            pe.wait_ge(lru_gate, 8 * g + 1)
                        last = product(own_bank(tile, o)[:, 0:TM], xchl, (2 * tile.parity + k) % RING, jj, (4 * g + 2 * k + kt) % 5,
                                       kt == 0, kt == 1, TM)
                        if kt == 1 and jj < HALF - 1:
                            last.then_inc(own_out, 1)
                    last.then_inc(units_used, 1)

        lam_a = Steps(sem("lam_act"), ["abs", "exp"])
        TERMS = list(range(15, 0, -2))
        lam_v = Steps(sem("lam_dve"), ["two", "inv", "z", "zz", "h15"] + [f"{n}{k}" for k in TERMS[1:] for n in ("m", "h")]
                      + ["log", "neg", "sum", "s8", "n8"])

        def need_lam(eng):
            need(eng, lam_v, "n8")

        def act_lam(act):
            act.wait_ge(in_par, 16)
            lam = par[:, PCOL["lam"]:PCOL["lam"] + KT]
            lam_a.done(nc.scalar.activation(lam_sb[:, 0], lam, ACT.Abs), "abs")
            need(act, lam_a, "abs")
            lam_a.done(nc.scalar.activation(lam_sb[:, 0], lam_sb[:, 0], ACT.Exp, scale=-1.0), "exp")

        def dve_lam(v):
            e, z, zz, h, t = (lam_sb[:, k] for k in (0, 1, 2, 3, 4))

            def then(ins, name):
                lam_v.done(ins, name)
                need(v, lam_v, name)
            need(v, lam_a, "exp")
            then(nc.vector.tensor_scalar(t, e, 2.0, None, ALU.add), "two")
            then(nc.vector.reciprocal(t, t), "inv")
            then(nc.vector.tensor_tensor(z, e, t, ALU.mult), "z")
            then(nc.vector.tensor_tensor(zz, z, z, ALU.mult), "zz")
            then(nc.vector.tensor_scalar(h, zz, 0.0, 1.0 / TERMS[0], ALU.mult, ALU.add), "h15")
            for k in TERMS[1:]:
                then(nc.vector.tensor_tensor(h, h, zz, ALU.mult), f"m{k}")
                then(nc.vector.tensor_scalar(h, h, 1.0 / k, None, ALU.add), f"h{k}")
            then(nc.vector.scalar_tensor_tensor(h, h, 2.0, z, ALU.mult, ALU.mult), "log")
            then(nc.vector.tensor_scalar(t, par[:, PCOL["lam"]:PCOL["lam"] + KT], -1.0, 0.0, ALU.mult, ALU.max), "neg")
            then(nc.vector.tensor_tensor(t, t, h, ALU.add), "sum")
            then(nc.vector.tensor_scalar(lam_sb[:, 1], t, 8.0, None, ALU.mult), "s8")
            then(nc.vector.tensor_scalar(lam_sb[:, 2], t, -8.0, None, ALU.mult), "n8")

        ZG = Z2 + 2432 + 1088 * 40
        glp = at("glp", ZG, [P, 2, T])
        sgt = [at(f"sgt{b}", ZG + (2 + b) * K, [P, T]) for b in range(2)]
        mt2 = [at(f"mt2{b}", Z2 + b * K, [P, T]) for b in range(2)]
        glru_pre, glru_out, glru_step, mg2_hi, mg2_lo = (sem(n) for n in ("glru_pre", "glru_out", "glru_step", "mg2_hi", "mg2_lo"))

        def act_glru(act):
            def body(tile):
                b = tile.t % 2
                split_hi(act, tile.later(), (0,))
                act.wait_ge(glru_pre, tile.local(1, 1))
                if tile.loops or tile.t >= 2:
                    act.wait_ge(glru_step, tile.local(2, -3))
                nc.scalar.activation(sgt[b][:], glp[:, b], ACT.Sigmoid).then_inc(glru_out, 1)
                act.wait_ge(glru_step, tile.local(2, 2))
                nc.scalar.activation(mg2[:, tile.local(), 0], mt2[b][:], ACT.Copy).then_inc(mg2_hi, 1)
                split_hi(act, tile.later(), (1,))
                if not tile.loops and tile.t < 3:
                    (act_lru_tanh, act_lru_exp, act_lru_root)[tile.t](act, 3)
            run_tiles(act, "glru", 2, body, peel=2)

        def dve_glru(v):
            def body(tile):
                b, m = tile.t % 2, tile.local()
                tile_done(v, tile)
                if tile.loops or tile.t >= 2:
                    v.wait_ge(glru_out, tile.local(1, -1))
                nc.vector.tensor_tensor(glp[:, b], banks[tile.parity][:, 0:T], norm1.rstd[:, META:], ALU.mult).then_inc(glru_pre, 1)
                split_lo(v, tile.later(), (0,))
                v.wait_ge(glru_out, tile.local(1, 1))
                nc.vector.tensor_tensor(mt2[b][:], HL[:, m], sgt[b][:], ALU.mult).then_inc(glru_step, 1)
                v.wait_ge(glru_step, tile.local(2, 1))
                nc.vector.tensor_tensor(mt2[b][:], mt2[b][:], PO[:, m], ALU.add).then_inc(glru_step, 1)
                v.wait_ge(mg2_hi, tile.local(1, 1))
                nc.vector.tensor_tensor(mg2[:, m, 1], mt2[b][:], mg2[:, m, 0].bitcast(F), ALU.subtract).then_inc(mg2_lo, 1)
                split_lo(v, tile.later(), (1,))
                if not tile.loops and tile.t == 0:
                    dve_lru_scan(v, 2)
                if not tile.loops and tile.t == 2:
                    dve_lru_one(v, 3)
                if not tile.loops and tile.t == 3:
                    dve_lru_scan(v, 3)
                    need(v, lru_o, "out", 3)
            run_tiles(v, "glru", 2, body, peel=2)

        wout2_out = sem("wout2_out")

        def dve_add_phase(v, phase, dst, scale, out_sem, norm=None):
            def body(tile):
                tile_done(v, tile)
                m = tile.local()
                nc.vector.scalar_tensor_tensor(dst[:, m], dst[:, m], scale, banks[tile.parity][:, 0:T],
                                               ALU.mult, ALU.add).then_inc(out_sem, 1)
                if norm is not None:
                    norm.dve_tile(v, m, tile.local(1, 1))
                split_lo(v, tile.later())
            run_tiles(v, phase, 2, body)

        class Mlp:
            def __init__(self, phase, x, moving, hidden, tmp, scale, norm=None, norm_out=None):
                self.phase, self.x, self.moving, self.hid, self.scale = phase, x, moving, hidden, scale
                self.norm, self.norm_out = norm, norm_out
                self.r = [at(f"{phase}_r{b}", tmp + K * b, [P, T]) for b in range(2)]
                self.q = [at(f"{phase}_q{b}", tmp + K * (2 + b), [P, T]) for b in range(2)]
                self.relu, self.sq, self.hi, self.lo, self.out = (sem(f"{phase}_{n}") for n in ("relu", "sq", "hi", "lo", "out"))

            def groups(self, eng, up, down, peel=1):
                def group(loops, g):
                    first = FIRST[self.phase] + (0 if loops else 2 * KT * g)
                    run_tiles(eng, self.phase, 2, lambda t: up(t, g), loops, first, KT)
                    run_tiles(eng, self.phase, 2, lambda t: down(t, g), loops, first + KT, KT,
                              peel if self.is_group(g, FF_GROUPS - 1) else 1)
                group((), 0)
                with eng.Fori(1, FF_GROUPS - 1) as n:
                    group(((n, 2 * KT),), n)
                group((), FF_GROUPS - 1)

            @staticmethod
            def inner(tile, g):
                return tile.loops if isinstance(g, int) else tile.loops[1:]

            def nth(self, tile, c, g, m=1):
                v = m * tile.t + c
                v = v + m * KT * g if isinstance(g, int) else g * (KT * m) + v
                for reg, per in self.inner(tile, g):
                    v = reg * (per * m) + v
                return v

            def place(self, tile, g):
                v = tile.t
                for reg, per in self.inner(tile, g):
                    v = reg * per + v
                return v

            def early(self, tile, g):
                return not self.inner(tile, g) and tile.t < 2

            @staticmethod
            def is_group(g, n):
                return isinstance(g, int) and g == n

            def last_hooked(self, tile, g, last):
                if last and self.is_group(g, FF_GROUPS - 1):
                    hooked(tile, last)

            def act(self, act, hooks=None, last=None):
                def up(tile, g):
                    if self.is_group(g, 0):
                        hooked(tile, hooks)
                    b, m = tile.t % 2, self.place(tile, g)
                    act.wait_ge(self.relu, self.nth(tile, 1, g))
                    if not (self.is_group(g, 0) and self.early(tile, g)):
                        act.wait_ge(self.lo, self.nth(tile, -1, g))
                    nc.scalar.activation(self.q[b][:], self.r[b][:], ACT.Square).then_inc(self.sq, 1)
                    act.wait_ge(self.sq, self.nth(tile, 1, g))
                    nc.scalar.activation(self.hid[:, m, 0], self.q[b][:], ACT.Copy).then_inc(self.hi, 1)
                    split_hi(act, tile.later())

                def down(tile, g):
                    if self.norm_out is not None and self.is_group(g, FF_GROUPS - 1):
                        act.wait_ge(self.out, self.nth(tile, 1, g))
                        self.norm_out.act_tile(act, self.place(tile, g))
                    split_hi(act, tile.later())
                    self.last_hooked(tile, g, last)
                self.groups(act, up, down, SHIFT_TILE // 2 + 2 if last else 1)

            def dve(self, v, hooks=None):
                def up(tile, g):
                    if self.is_group(g, 0):
                        hooked(tile, hooks)
                    b, m = tile.t % 2, self.place(tile, g)
                    tile_done(v, tile)
                    if not (self.is_group(g, 0) and self.early(tile, g)):
                        v.wait_ge(self.sq, self.nth(tile, -1, g))
                    if self.norm is None:
                        ins = nc.vector.tensor_scalar(self.r[b][:], banks[tile.parity][:, 0:T], 0.0, None, ALU.max)
                    else:
                        ins = nc.vector.scalar_tensor_tensor(self.r[b][:], banks[tile.parity][:, 0:T], 0.0, self.norm.rstd[:],
                                                             ALU.max, ALU.mult)
                    ins.then_inc(self.relu, 1)
                    v.wait_ge(self.hi, self.nth(tile, 1, g))
                    nc.vector.tensor_tensor(self.hid[:, m, 1], self.q[b][:], self.hid[:, m, 0].bitcast(F),
                                            ALU.subtract).then_inc(self.lo, 1)
                    split_lo(v, tile.later())

                def down(tile, g):
                    tile_done(v, tile)
                    m = self.place(tile, g)
                    nc.vector.scalar_tensor_tensor(self.x[:, m], self.x[:, m], self.scale if self.is_group(g, 0) else 1.0,
                                                   banks[tile.parity][:, 0:T], ALU.mult, ALU.add).then_inc(self.out, 1)
                    if self.norm_out is not None and self.is_group(g, FF_GROUPS - 1):
                        self.norm_out.dve_tile(v, m, self.place(tile, g) + 1)
                    split_lo(v, tile.later())
                self.groups(v, up, down)

            def pe(self, pe, before, after=None, entry=None, last=None):
                def up(tile, g):
                    if self.is_group(g, 0) and self.early(tile, g) and entry is not None:
                        entry(tile.t)
                    if not self.early(tile, g):
                        pe.wait_ge(self.relu, self.nth(tile, -1, g))
                    elif not self.is_group(g, 0):
                        pe.wait_ge(self.out, self.nth(tile, -1, g))
                    first = self.is_group(g, 0) and not tile.loops and tile.t == 0
                    full_tile(pe, tile, self.moving, T, before if first else None)
                    if first and after is not None:
                        after()

                def down(tile, g):
                    if self.early(tile, g):
                        pe.wait_ge(self.relu, self.nth(tile, KT - 1, g))
                    else:
                        pe.wait_ge(self.out, self.nth(tile, -1, g))

                    def hidden_ready(k):
                        pe.wait_ge(self.lo, self.nth(tile, HALF * (k + 1) - tile.t, g))
                    full_tile(pe, tile, self.hid, T, hidden_ready if self.early(tile, g) else None)
                    self.last_hooked(tile, g, last)
                self.groups(pe, up, down, SHIFT_TILE // 2 + 2 if last else 1)

        x2 = X1[:, :, META:]
        u2 = at("u2", B + 49 * K, [P, KT, 2, T], R)
        hid2 = at("hid2", B + 17 * K, [P, KT, 2, T], R)
        X3 = at("X3", B + 83 * K, [P, KT, T])
        xh3 = at("xh3", B + 99 * K, [P, KT, 2, T], R)
        norm2 = Norm("norm2", x2, T, "norm2_g", u2, Z2)
        final = Norm("final", x2, T, "final_g", xh3, B + 49 * K)
        mlp2 = Mlp("ff2", x2, u2, hid2, Z2 + 4 * K, 1.0, norm2, final)

        mix = at("mix", B + 17 * K, [P, KT, 2, T], R)
        Q = B + 49 * K
        gp = at("gp", Q, [P, 17, T])
        sr = at("sr", Q + 17 * K, [P, GLA_VT, T])
        ym = at("ym", Q + 25 * K, [P, C3_T, T])
        cg = [at(f"cg{b}", B + (17 + b) * K, [P, T]) for b in range(2)]
        hp = at("hp", B + 19 * K, [P, T + 2])
        ca = at("ca", B + 21 * K, [P, T])
        rstd_sq = at("rstd_sq", B + 22 * K, [P, T])
        rstd_squared, x3_out = (sem(n) for n in ("rstd_squared", "x3_out"))
        hp_zero, c_out, ub_out, c3_step, gp_out = (
            sem(n) for n in ("hp_zero", "c_out", "ub_out", "c3_step", "gp_out"))

        def conv_place(tile):
            kind, s = tile.t % 3, tile.t // 3

            def nth(c=0, m=1):
                return tile.loops[-1][0] * (2 * m) + (m * s + c) if tile.loops else m * s + c
            return kind, s, nth

        def dve_conv3(v):
            nc.vector.memset(hp[:], 0.0).then_inc(hp_zero, 1)
            v.wait_ge(hp_zero, 1)

            def body(tile):
                kind, s, nth = conv_place(tile)
                if not tile.loops and tile.t == 0:
                    final.dve_rstd(v)
                    nc.vector.tensor_tensor(rstd_sq[:], final.rstd[:], final.rstd[:], ALU.mult).then_inc(rstd_squared, 1)
                    v.wait_ge(rstd_squared, 1)
                tile_done(v, tile)
                if kind == 0:
                    nc.vector.tensor_tensor(cg[s % 2][:], banks[tile.parity][:, 0:T], rstd_sq[:], ALU.mult).then_inc(c_out, 1)
                    split_lo(v, tile.later())
                    for k in range(2):
                        kt = nth(k, 2)
                        nc.vector.scalar_tensor_tensor(X3[:, kt], x2[:, kt], col("final_g", kt), final.rstd[:],
                                                       ALU.mult, ALU.mult).then_inc(x3_out, 1)
                elif kind == 1:
                    v.wait_ge(c_out, nth(1))
                    nc.vector.tensor_tensor(hp[:, 2:], banks[tile.parity][:, 0:T], cg[s % 2][:], ALU.mult).then_inc(ub_out, 1)
                    v.wait_ge(ub_out, nth(1, 2))
                    for k in range(CONV3):
                        tap, w = hp[:, 2 - k:2 - k + T], col("conv_w3", nth(C3_T * (CONV3 - 1 - k)))
                        if k == 0:
                            ins = nc.vector.tensor_scalar(ca[:], tap, w, None, ALU.mult)
                        else:
                            v.wait_ge(c3_step, nth(k, 4))
                            ins = nc.vector.scalar_tensor_tensor(ca[:], tap, w, ca[:], ALU.mult, ALU.add)
                        ins.then_inc(c3_step, 1)
                    v.wait_ge(c3_step, nth(3, 4))
                    nc.vector.tensor_tensor(ca[:], ca[:], final.rstd[:], ALU.mult).then_inc(c3_step, 1)
                    split_lo(v, tile.later())
                else:
                    v.wait_ge(c3_step, nth(4, 4))
                    nc.vector.tensor_tensor(ym[:, nth()], banks[tile.parity][:, 0:T], ca[:], ALU.mult).then_inc(ub_out, 1)
                    split_lo(v, tile.later())
            run_tiles(v, "conv3", 6, body)

        def pe_conv3(pe):
            def body(tile):
                kind, s, nth = conv_place(tile)
                first = not tile.loops and s == 0
                if kind == 2:
                    pe.wait_ge(c_out, nth(1))
                elif first:
                    pe.wait_ge(mlp2.out, KT * FF_GROUPS - 1 + kind)
                elif not first:
                    pe.wait_ge(ub_out, nth(-1 if kind == 0 else 0, 2))
                full_tile(pe, tile, xh3, T, (lambda k: final.ready(pe, k)) if first and kind == 0 else None)
                if first and kind == 0:
                    final.pe(pe)
            run_tiles(pe, "conv3", 6, body)

        zl, q3, k3 = gp[:, 0], gp[:, 1:5], gp[:, 5:9]
        GATE_0 = 1 + 2 * GLA_H + GLA_VT
        csq = at("conv_sq", B, [P, C3_T, T])
        crs = csq
        l1 = at("gla_l1", B + 8 * K, [P, GLA_H, T])
        l2 = at("gla_l2", B + 12 * K, [P, GLA_H, T])
        dcy = at("gla_dcy", B + 16 * K, [P, GLA_H * NCH])
        ss = at("gla_s", B + 33 * K, [P, GLA_H, T])
        ki = at("ki", B + 37 * K, [P, GLA_H, T])
        ke = at("ke", B + 41 * K, [P, GLA_H, T])
        qd = at("qd", B + 45 * K, [P, GLA_H, T])
        ps3 = at("gla_ps", B + 8 * K, [P, GLA_H * NB, P])
        k_tok = at("k_tok", B + 12 * K, [P, NB, GLA_H * P])
        v_tok3 = at("v_tok3", Q, [P, NB, GLA_VT * P])
        sst = at("gla_state", B, [P, 2, NCH - 1, T])
        osq = at("gla_osq", B + 6 * K, [P, 2, T])
        ors = [at("gla_ors0", Q + 8 * K, [P, T]), at("gla_ors1", B + 131 * K, [P, T])]
        oo = at("gla_o", Q + 9 * K, [P, GLA_VT, T])
        H4 = range(GLA_H)
        g_o = Steps(sem("gla_pool"), ["zero"])
        g_a = Steps(sem("gla_act"), ["csq"] + [f"cstd{b}" for b in range(4)] + [f"idn{h}" for h in H4] + ["abs", "exp", "ln"]
                    + ["eq", "ek", "ee", "chi0", "chi1", "kt0", "kt1", "vt0", "vt2", "o0", "osq0", "o1", "osq1", "vt1", "vt3",
                       "ostd0", "ostd1", "o2", "osq2", "o3", "osq3", "silu0", "ostd2", "ostd3", "ohi0", "ohi1", "silu1",
                       "ohi2", "silu2", "ohi3"])

        def state_names(h):
            return [f"st{h}_{c}" for c in range(NCH - 1)]
        g_v = Steps(sem("gla_dve"), ["crs0", "crs1", "min", "la"] + [f"sum{h}" for h in H4] + ["rest", "crs2", "crs3", "cy", "dec", "qd"]
                    + ["ke", "ki", "clo0", "clo1", "sc0", "sc1"] + state_names(0) + state_names(1) + ["ors0"] + state_names(2) + ["on0", "ors1"]
                    + state_names(3) + ["on1", "oy0", "oy1", "ors2", "on2", "ors3", "olo0", "olo1", "on3", "oy2", "olo2", "oy3", "olo3"])
        g_p = Steps(sem("gla_pe"), [f"cst{b}" for b in range(4)] + [f"z{h}" for h in H4]
                    + ["kt0", "kt1", "sc0", "sc1", "vt0", "vt2", "dl0", "o0", "dl1", "ost0", "o1", "vt1", "vt3", "ost1", "dl2",
                       "o2", "dl3", "ost2", "o3", "ost3"])

        Z_BANK, KT_BANK, SC_BANK, CST_BANK, VT3_BANK, DL_BANK, O_BANK, OST_BANK = (
            (2, 3), (2, 3), (4, 5), (4, 5, 6, 7), (6, 2, 7, 3), (2, 3, 4), (5, 6), (7, 4))

        def two(bank):
            return banks[bank][:].rearrange("p (a t) -> p a t", a=2)

        def by_chunk(ap):
            return ap.rearrange("p h (c t) -> p (h c) t", c=NCH)

        def flat(ap):
            return ap.rearrange("p h t -> p (h t)")

        def gla_tile(t):
            return Tile(FIRST["gla"], t)

        def pool_gla(pool):
            need(pool, g_v, f"sum{GLA_H - 1}")
            g_o.done(nc.gpsimd.memset(ps3[:], 0.0), "zero")

        def act_gla(act):
            act.wait_ge(ub_out, 2 * C3_T)
            g_a.done(nc.scalar.activation(csq[:], ym[:], ACT.Square), "csq")

            def conv_roots():
                for b in range(4):
                    need(act, g_p, f"cst{b}")
                    g_a.done(nc.scalar.activation(crs[:, 2 * b:2 * b + 2], two(CST_BANK[b]), ACT.Sqrt, bias=EPS, scale=1.0 / P), f"cstd{b}")

            def log_sigmoid():
                for h in H4:
                    need(act, g_p, f"z{h | 1}")
                    g_a.done(nc.scalar.activation(l1[:, h], two(Z_BANK[h // 2])[:, h % 2], ACT.Identity, bias=col("gate_bias3", h)), f"idn{h}")
                need(act, g_a, f"idn{GLA_H - 1}")
                g_a.done(nc.scalar.activation(l2[:], l1[:], ACT.Abs), "abs")
                need(act, g_a, "abs")
                g_a.done(nc.scalar.activation(l2[:], l2[:], ACT.Exp, scale=-1.0), "exp")
                need(act, g_a, "exp")
                g_a.done(nc.scalar.activation(l2[:], l2[:], ACT.Ln, bias=1.0), "ln")

            def decays():
                need(act, g_v, "rest")
                g_a.done(nc.scalar.activation(qd[:], ss[:], ACT.Exp, scale=1.0 / GATE_TAU), "eq")
                g_a.done(nc.scalar.activation(ki[:], ss[:], ACT.Exp, scale=-1.0 / GATE_TAU), "ek")
                g_a.done(nc.scalar.activation(ke[:], ke[:], ACT.Exp, scale=1.0 / GATE_TAU), "ee")

            def conv_hi():
                need(act, g_v, "cy")
                for q in range(2):
                    g_a.done(nc.scalar.activation(mix[:, 4 * q:4 * q + 4, 0], ym[:, 4 * q:4 * q + 4], ACT.Copy), f"chi{q}")

            def keys_by_token():
                for b in range(NB):
                    need(act, g_p, f"kt{b}")
                    g_a.done(nc.scalar.activation(k_tok[:, b], banks[KT_BANK[b]][:], ACT.Copy), f"kt{b}")

            def values_by_token(which):
                need(act, g_v, "ki")
                for n in which:
                    need(act, g_p, f"vt{n}")
                    g_a.done(nc.scalar.activation(v_tok3[:, n // 2, 512 * (n % 2):512 * (n % 2) + 512], banks[VT3_BANK[n]][:], ACT.Copy), f"vt{n}")

            def output(h):
                need(act, g_p, f"o{h}")
                g_a.done(nc.scalar.activation(oo[:, 2 * h:2 * h + 2], two(O_BANK[h % 2]), ACT.Copy), f"o{h}")
                need(act, g_a, f"o{h}")
                if h > 0:
                    need(act, g_p, f"ost{h - 1}")
                g_a.done(nc.scalar.activation(osq[:], oo[:, 2 * h:2 * h + 2], ACT.Square), f"osq{h}")

            def out_roots(which):
                for h in which:
                    need(act, g_p, f"ost{h}")
                    if h >= 2:
                        need(act, g_v, f"on{h - 2}")
                    g_a.done(nc.scalar.activation(ors[h % 2][:], banks[OST_BANK[h % 2]][:, 0:T], ACT.Sqrt, bias=EPS, scale=1.0 / T), f"ostd{h}")

            def gate(n, a, z):
                act.wait_ge(gp_out, GATE_0 + z)
                g_a.done(nc.scalar.activation(sr[:, a:z], sr[:, a:z], ACT.Silu), f"silu{n}")

            def out_hi(which):
                for h in which:
                    need(act, g_v, f"oy{h}")
                    g_a.done(nc.scalar.activation(mix[:, 8 + 2 * h:10 + 2 * h, 0], oo[:, 2 * h:2 * h + 2], ACT.Copy), f"ohi{h}")
            after = {1: [conv_roots], 2: [log_sigmoid], 5: [decays], 7: [conv_hi], 9: [keys_by_token],
                     13: [lambda: values_by_token((0, 2))], 15: [lambda: output(0)], 16: [lambda: output(1)],
                     17: [lambda: values_by_token((1, 3)), lambda: out_roots((0, 1))], 19: [lambda: output(2)],
                     20: [lambda: output(3), lambda: gate(0, 0, 4)], 21: [lambda: out_roots((2, 3))],
                     22: [lambda: out_hi((0, 1)), lambda: gate(1, 4, 6)], 23: [lambda: out_hi([2])]}
            last = COUNT["gla"] - 1
            for t in range(last):
                split_hi(act, gla_tile(t).later())
                for step in after.get(t, ()):
                    step()
            gate(2, 6, 8)
            out_hi([3])
            split_hi(act, gla_tile(last).later())

        def dve_gla(v):
            def conv_factors(which):
                for b in which:
                    need(v, g_a, f"cstd{b}")
                    g_v.done(nc.vector.reciprocal(crs[:, 2 * b:2 * b + 2], crs[:, 2 * b:2 * b + 2]), f"crs{b}")

            def log_sums():
                need(v, g_a, "ln")
                g_v.done(nc.vector.tensor_scalar(l1[:], l1[:], 0.0, None, ALU.min), "min")
                need(v, g_v, "min")
                g_v.done(nc.vector.tensor_tensor(l1[:], l1[:], l2[:], ALU.subtract), "la")
                need(v, g_v, "la")
                for h in H4:
                    g_v.done(nc.vector.tensor_tensor_scan(ss[:, h], const("run_up"), l1[:, h], 0.0, ALU.mult, ALU.add), f"sum{h}")
                need(v, g_v, f"sum{GLA_H - 1}")
                s_end = by_chunk(ss[:])[:, :, CH - 1].unsqueeze(2).broadcast_to([P, GLA_H * NCH, CH])
                g_v.done(nc.vector.tensor_tensor(by_chunk(ke[:]), s_end, by_chunk(ss[:]), ALU.subtract), "rest")

            def conv_norm():
                need(v, g_v, "crs3")
                for c in range(C3_T):
                    last = nc.vector.scalar_tensor_tensor(ym[:, c], ym[:, c], col("conv_g3", c), crs[:, c], ALU.mult, ALU.mult)
                g_v.done(last, "cy")

            def queries():
                need(v, g_a, "eq")
                g_v.done(nc.vector.tensor_copy(dcy[:], by_chunk(qd[:])[:, :, CH - 1]), "dec")
                need(v, g_v, "dec")
                v.wait_ge(gp_out, 1 + GLA_H)
                g_v.done(nc.vector.scalar_tensor_tensor(flat(qd[:]), flat(q3), P ** -0.5, flat(qd[:]), ALU.mult, ALU.mult), "qd")

            def keys():
                need(v, g_a, "ee")
                v.wait_ge(gp_out, 1 + 2 * GLA_H)
                g_v.done(nc.vector.tensor_tensor(ke[:], k3, ke[:], ALU.mult), "ke")
                g_v.done(nc.vector.tensor_tensor(ki[:], k3, ki[:], ALU.mult), "ki")

            def conv_lo():
                for q in range(2):
                    need(v, g_a, f"chi{q}")
                    g_v.done(nc.vector.tensor_tensor(mix[:, 4 * q:4 * q + 4, 1], ym[:, 4 * q:4 * q + 4],
                                                     mix[:, 4 * q:4 * q + 4, 0].bitcast(F), ALU.subtract), f"clo{q}")

            def scores():
                need(v, g_o, "zero")
                mask = const("incl_up").bitcast(mybir.dt.uint32).unsqueeze(1).broadcast_to([P, 4, P])
                for b in range(2):
                    need(v, g_p, f"sc{b}")
                    g_v.done(nc.vector.copy_predicated(ps3[:, 4 * b:4 * b + 4], mask, banks[SC_BANK[b]][:].rearrange("p (n c) -> p n c", n=4)), f"sc{b}")

            def states(h):
                need(v, g_p, f"dl{h}")
                if h >= 2:
                    need(v, g_p, f"o{h - 2}")
                row = sst[:, h % 2]
                for c in range(NCH - 1):
                    new = banks[DL_BANK[c]][:, 0:T]
                    if c == 0:
                        ins = nc.vector.tensor_copy(row[:, c], new)
                    else:
                        need(v, g_v, f"st{h}_{c - 1}")
                        ins = nc.vector.scalar_tensor_tensor(row[:, c], row[:, c - 1], dcy[:, NCH * h + c:NCH * h + c + 1],
                                                             new, ALU.mult, ALU.add)
                    g_v.done(ins, f"st{h}_{c}")

            def out_factor(h):
                need(v, g_a, f"ostd{h}")
                g_v.done(nc.vector.reciprocal(ors[h % 2][:], ors[h % 2][:]), f"ors{h}")

            def out_norm(h):
                need(v, g_v, f"ors{h}")
                for c in (2 * h, 2 * h + 1):
                    last = nc.vector.scalar_tensor_tensor(oo[:, c], oo[:, c], col("gla_g3", c), ors[h % 2][:], ALU.mult, ALU.mult)
                g_v.done(last, f"on{h}")

            def out_gate(h):
                need(v, g_v, f"on{h}")
                need(v, g_a, "silu0" if h < 2 else f"silu{h - 1}")
                g_v.done(nc.vector.tensor_tensor(oo[:, 2 * h:2 * h + 2], oo[:, 2 * h:2 * h + 2], sr[:, 2 * h:2 * h + 2], ALU.mult), f"oy{h}")

            def out_lo(h):
                need(v, g_a, f"ohi{h}")
                g_v.done(nc.vector.tensor_tensor(mix[:, 8 + 2 * h:10 + 2 * h, 1], oo[:, 2 * h:2 * h + 2],
                                                 mix[:, 8 + 2 * h:10 + 2 * h, 0].bitcast(F), ALU.subtract), f"olo{h}")
            after = {1: [lambda: conv_factors([0])], 2: [lambda: conv_factors([1])], 3: [log_sums], 4: [lambda: conv_factors([2])],
                     5: [lambda: conv_factors([3])], 6: [conv_norm], 7: [queries], 8: [keys], 9: [conv_lo], 11: [scores],
                     14: [lambda: states(0)], 15: [lambda: states(1)], 17: [lambda: out_factor(0)],
                     18: [lambda: states(2), lambda: out_norm(0), lambda: out_factor(1)], 19: [lambda: states(3), lambda: out_norm(1)],
                     21: [lambda: out_gate(0), lambda: out_gate(1), lambda: out_factor(2)],
                     22: [lambda: out_norm(2), lambda: out_factor(3), lambda: out_lo(0), lambda: out_lo(1)],
                     23: [lambda: out_norm(3), lambda: out_gate(2), lambda: out_lo(2)]}
            last = COUNT["gla"] - 1
            for t in range(last + 1):
                tile = gla_tile(t)
                tile_done(v, tile)
                dst = gp[:, t] if t < GATE_0 else sr[:, t - GATE_0]
                nc.vector.tensor_tensor(dst, banks[tile.parity][:, 0:T], final.rstd[:], ALU.mult).then_inc(gp_out, 1)
                if t == last:
                    out_gate(3)
                    out_lo(3)
                split_lo(v, tile.later())
                for step in after.get(t, ()):
                    step()

        def pe_gla(pe):
            def conv_sums():
                need(pe, g_a, "csq")
                for b in range(4):
                    g_p.done(nc.tensor.matmul(banks[CST_BANK[b]][:], const("ones"), csq[:, 2 * b:2 * b + 2], start=True, stop=True), f"cst{b}")

            def decay_gates():
                pe.wait_ge(gp_out, 1)
                for h in H4:
                    g_p.done(nc.tensor.matmul(two(Z_BANK[h // 2])[:, h % 2], wgu_sb[:, h], zl[0:16], start=True, stop=True), f"z{h}")

            def keys_by_token():
                need(pe, g_v, "ke")
                need(pe, g_a, f"idn{GLA_H - 1}")
                for b in range(NB):
                    for h in H4:
                        last = nc.tensor.transpose(banks[KT_BANK[b]][:, P * h:P * h + P], ke[:, h, P * b:P * b + P], const("ident"))
                    g_p.done(last, f"kt{b}")

            def scores():
                need(pe, g_v, "ki")
                need(pe, g_a, "cstd3")
                for b in range(2):
                    for n in range(4):
                        h, tb = (4 * b + n) // NB, n % NB
                        last = nc.tensor.matmul(banks[SC_BANK[b]][:, P * n:P * n + P], ki[:, h, P * tb:P * tb + P], qd[:, h, P * tb:P * tb + P],
                                                start=True, stop=True)
                    g_p.done(last, f"sc{b}")

            def values_by_token(which):
                pe.wait_ge(gp_out, 1 + 2 * GLA_H + (4 if which[0] == 0 else GLA_VT))
                for n in which:
                    for c in range(4):
                        last = nc.tensor.transpose(banks[VT3_BANK[n]][:, P * c:P * c + P],
                                                   gp[:, 9 + 4 * (n % 2) + c, P * (n // 2):P * (n // 2) + P], const("ident"))
                    g_p.done(last, f"vt{n}")

            def additions(h):
                need(pe, g_a, "vt2" if h < 2 else "vt3")
                need(pe, g_v, "sc1" if h == 0 else f"st{h - 1}_{NCH - 2}")
                if h == 2:
                    need(pe, g_a, "ostd1")
                for c in range(NCH - 1):
                    rows = slice(CH * (c % 2), CH * (c % 2) + CH)
                    last = nc.tensor.matmul(banks[DL_BANK[c]][:, 0:T], k_tok[rows, c // 2, P * h:P * h + P],
                                            v_tok3[rows, c // 2, T * h:T * h + T], start=True, stop=True)
                g_p.done(last, f"dl{h}")

            def output(h):
                need(pe, g_v, f"st{h}_{NCH - 2}")
                if h >= 2:
                    need(pe, g_a, f"o{h - 2}")
                for n in range(2):
                    o = two(O_BANK[h % 2])[:, n]
                    c0 = T * h + P * n
                    for tb in range(NB):
                        nc.tensor.matmul(o[:, P * tb:P * tb + P], v_tok3[:, tb, c0:c0 + P], ps3[:, NB * h + tb], start=tb == 0, stop=False)
                    for c in range(1, NCH):
                        last = nc.tensor.matmul(o[:, CH * c:CH * c + CH], sst[:, h % 2, c - 1, P * n:P * n + P], qd[:, h, CH * c:CH * c + CH],
                                                start=False, stop=c == NCH - 1)
                g_p.done(last, f"o{h}")

            def out_sums(h):
                need(pe, g_a, f"osq{h}")
                if h == 1:
                    need(pe, g_v, f"st1_{NCH - 2}")
                elif h == 3:
                    need(pe, g_v, f"st3_{NCH - 2}")
                elif h == 2:
                    need(pe, g_a, "ostd0")
                for m in range(2):
                    last = nc.tensor.matmul(banks[OST_BANK[h % 2]][:, 0:T], const("ones"), osq[:, m], start=m == 0, stop=m == 1)
                g_p.done(last, f"ost{h}")
            after = {1: [conv_sums, decay_gates], 9: [keys_by_token], 10: [scores], 13: [lambda: values_by_token((0, 2))],
                     14: [lambda: additions(0)], 15: [lambda: output(0), lambda: additions(1)],
                     16: [lambda: out_sums(0), lambda: output(1)], 17: [lambda: values_by_token((1, 3)), lambda: out_sums(1)],
                     18: [lambda: additions(2)], 19: [lambda: output(2), lambda: additions(3)],
                     20: [lambda: out_sums(2), lambda: output(3)], 21: [lambda: out_sums(3)]}
            for t in range(COUNT["gla"]):
                if t < 2:
                    pe.wait_ge(ub_out, 2 * C3_T)
                else:
                    pe.wait_ge(gp_out, t - 1)
                full_tile(pe, gla_tile(t), xh3)
                for step in after.get(t, ()):
                    step()

        wout3_out = sem("wout3_out")

        class LayerNorm:
            def __init__(self, name, x, g, b, dst, scratch):
                self.x, self.g, self.b, self.dst = x, g, b, dst
                self.acc, self.acc2, self.d, self.sq, self.shift, self.mu, self.var, self.std, self.rstd = (
                    at(f"{name}_{n}", scratch + K * k, [P, T])
                    for k, n in enumerate(("acc", "acc2", "d", "sq", "shift", "mu", "var", "std", "rstd")))
                last = [f"{n}{q}" for q in range(4) for n in (("aff", "hi") if dst is not None else ("aff",))]
                self.quarter = sem(name + "_quarter")
                self.o = Steps(sem(name + "_pool"), ["shifted", "sum", "square", "squares"])
                self.a = Steps(sem(name + "_act"), ["shift", "mu", "std"] + last)
                order = ["musq", "var", "mean", "rstd", "cen0", "nrm0", "cen1", "nrm1", "lo0", "nrm2", "lo1", "nrm3", "lo2", "lo3"]
                self.end = Steps(sem(name + "_end"), ["shifted", "square", "cen2", "cen3"])
                self.v = Steps(sem(name + "_dve"), [n for n in order if dst is not None or not n.startswith("lo")])
                self.p = Steps(sem(name + "_pe"), ["shift", "mean", "var"])

            def part(self, q):
                return self.x[:, 4 * q:4 * q + 4]

            @staticmethod
            def over(ap):
                return ap.unsqueeze(1).broadcast_to([P, 4, T])

            def pool(self, pool, src_ready, before=0):
                pool.wait_ge(src_ready, before + 1)
                for acc in (self.acc, self.acc2):
                    nc.gpsimd.memset(acc[:], 0.0).then_inc(self.quarter, 1)
                with pool.Fori(0, KT // 4) as kt:
                    pool.wait_ge(src_ready, kt + (before + 1))
                    pool.wait_ge(self.quarter, kt + 2)
                    nc.gpsimd.tensor_tensor(self.acc[:], self.acc[:], self.x[:, kt], ALU.add).then_inc(self.quarter, 1)
                need(pool, self.a, "shift")
                nc.gpsimd.memset(self.acc[:], 0.0).then_inc(self.quarter, 1)
                pool.wait_ge(self.quarter, 2 + KT // 4 + 1)
                with pool.Fori(0, KT - 1) as kt:
                    pool.wait_ge(src_ready, kt + (before + 1))
                    pool.wait_ge(self.o.sem, kt * len(self.o.names))
                    self.o.done(nc.gpsimd.tensor_tensor(self.d[:], self.x[:, kt], self.shift[:], ALU.subtract), "shifted")
                    need(pool, self.o, "shifted", kt)
                    self.o.done(nc.gpsimd.tensor_tensor(self.acc[:], self.acc[:], self.d[:], ALU.add), "sum")
                    self.o.done(nc.gpsimd.tensor_tensor(self.sq[:], self.d[:], self.d[:], ALU.mult), "square")
                    need(pool, self.o, "square", kt)
                    self.o.done(nc.gpsimd.tensor_tensor(self.acc2[:], self.acc2[:], self.sq[:], ALU.add), "squares")
                pool.wait_ge(src_ready, before + KT)
                need(pool, self.o, "squares", KT - 2)
                self.end.done(nc.gpsimd.tensor_tensor(self.d[:], self.x[:, KT - 1], self.shift[:], ALU.subtract), "shifted")
                need(pool, self.end, "shifted")
                self.end.done(nc.gpsimd.tensor_tensor(self.sq[:], self.d[:], self.d[:], ALU.mult), "square")
                need(pool, self.v, "mean")
                for q in (2, 3):
                    self.end.done(nc.gpsimd.tensor_tensor(self.part(q), self.part(q), self.over(self.mu[:]), ALU.subtract), f"cen{q}")

            def pe_shift(self, pe):
                pe.wait_ge(self.quarter, 2 + KT // 4)
                self.p.done(nc.tensor.matmul(banks[2][:, 0:T], const("ones"), self.acc[:], start=True, stop=True), "shift")

            def act_shift(self, act):
                need(act, self.p, "shift")
                self.a.done(nc.scalar.activation(self.shift[:], banks[2][:, 0:T], ACT.Copy, scale=4.0 / D), "shift")

            def pe(self, pe):
                need(pe, self.o, "squares", KT - 2)
                for bank, acc, tail, name, step in ((2, self.acc, self.d, "mean", "shifted"), (3, self.acc2, self.sq, "var", "square")):
                    nc.tensor.matmul(banks[bank][:, 0:T], const("ones"), acc[:], start=True, stop=False)
                    need(pe, self.end, step)
                    self.p.done(nc.tensor.matmul(banks[bank][:, 0:T], const("ones"), tail[:], start=False, stop=True), name)

            def act(self, act):
                need(act, self.p, "mean")
                self.a.done(nc.scalar.activation(self.mu[:], banks[2][:, 0:T], ACT.Copy, scale=1.0 / D), "mu")
                need(act, self.v, "var")
                self.a.done(nc.scalar.activation(self.std[:], self.var[:], ACT.Sqrt, bias=LN_EPS), "std")
                for q in range(4):
                    need(act, self.v, f"nrm{q}")
                    for j in range(4):
                        kt = 4 * q + j
                        last = nc.scalar.activation(self.x[:, kt], self.x[:, kt], ACT.Identity, bias=col(self.b, kt), scale=col(self.g, kt))
                    self.a.done(last, f"aff{q}")
                    if self.dst is not None:
                        need(act, self.a, f"aff{q}")
                        self.a.done(nc.scalar.activation(self.dst[:, 4 * q:4 * q + 4, 0], self.part(q), ACT.Copy), f"hi{q}")

            def dve(self, v):
                need(v, self.a, "mu")
                self.v.done(nc.vector.tensor_tensor(self.var[:], self.mu[:], self.mu[:], ALU.mult), "musq")
                need(v, self.v, "musq")
                need(v, self.p, "var")
                self.v.done(nc.vector.scalar_tensor_tensor(self.var[:], banks[3][:, 0:T], 1.0 / D, self.var[:], ALU.mult, ALU.subtract), "var")
                self.v.done(nc.vector.tensor_tensor(self.mu[:], self.mu[:], self.shift[:], ALU.add), "mean")
                need(v, self.v, "mean")

                def centered(q):
                    self.v.done(nc.vector.tensor_tensor(self.part(q), self.part(q), self.over(self.mu[:]), ALU.subtract), f"cen{q}")

                def normed(q):
                    need(v, self.v if q < 2 else self.end, f"cen{q}")
                    self.v.done(nc.vector.tensor_tensor(self.part(q), self.part(q), self.over(self.rstd[:]), ALU.mult), f"nrm{q}")

                def rest(q):
                    if self.dst is not None:
                        need(v, self.a, f"hi{q}")
                        self.v.done(nc.vector.tensor_tensor(self.dst[:, 4 * q:4 * q + 4, 1], self.part(q),
                                                            self.dst[:, 4 * q:4 * q + 4, 0].bitcast(F), ALU.subtract), f"lo{q}")
                need(v, self.a, "std")
                self.v.done(nc.vector.reciprocal(self.rstd[:], self.std[:]), "rstd")
                for q in range(2):
                    centered(q)
                    normed(q)
                rest(0)
                normed(2)
                rest(1)
                normed(3)
                rest(2)
                rest(3)

            def ready(self, pe, k):
                need(pe, self.v, f"lo{2 * k + 1}")

        xh4 = at("xh4", B + 99 * K, [P, KT, 2, T], R)
        hid3 = at("hid3", B + 17 * K, [P, KT, 2, T], R)
        ln1 = LayerNorm("ln1", X3, "ln1_g", "ln1_b", xh4, B)
        mlp3 = Mlp("ff3", X3, xh4, hid3, B + 49 * K, ALPHA3)
        ln2 = LayerNorm("ln2", X3, "ln2_g", "ln2_b", None, B)

        block = ctx.enter_context(nc.Block())

        @block.sync
        def _(sp):
            for k in range(RING):
                sp.dma_start(raw[:, k], stream[k]).then_inc(raw_in[k], 16)
            rounds = N_UNITS // RING
            by_round = stream[0:RING * rounds].rearrange("(n k) p j c -> n k p j c", k=RING)
            with sp.Fori(1, rounds) as n:
                for k in range(RING):
                    sp.wait_ge(lo_ready, n * RING + (k + 1 - RING))
                    sp.dma_start(raw[:, k], by_round[n, k]).then_inc(raw_in[k], 16)
            for u in range(RING * rounds, N_UNITS):
                sp.wait_ge(lo_ready, u + 1 - RING)
                sp.dma_start(raw[:, u % RING], stream[u]).then_inc(raw_in[u % RING], 16)
            for q in range(4):
                need(sp, ln2.a, f"aff{q}")
                sp.dma_start(out[:, 4 * q:4 * q + 4], X3[:, 4 * q:4 * q + 4]).then_inc(stored, 16)
            sp.wait_ge(stored, 64)

        @block.gpsimd
        def _(pool):
            for norm, parts in ((x_norm, in_x), (mem_norm, in_mem)):
                norm.pool_start(pool)
                for q in range(4):
                    pool.wait_ge(parts[q], 16)
                    for j in range(4):
                        norm.pool_tile(pool, 4 * q + j)
            pool_kk(pool)
            pool_rwkv(pool)
            pool_gn(pool)
            pool.wait_ge(in_meta, 16)
            norm1.pool(pool, wout1_out)
            pool_lru(pool)
            norm2.pool(pool, wout2_out)
            final.pool(pool, mlp2.out, KT * (FF_GROUPS - 1))
            pool_gla(pool)
            ln1.pool(pool, wout3_out)
            ln2.pool(pool, mlp3.out, KT * (FF_GROUPS - 1))

        @block.scalar
        def _(act):
            act.dma_start(par[:], params).then_inc(in_par, 16)
            for q in range(4):
                act.dma_start(x_raw[:, 4 * q:4 * q + 4], xT[:, 4 * q:4 * q + 4]).then_inc(in_x[q], 16)
            act.dma_start(cst[:], consts).then_inc(in_cst, 16)
            for q in range(4):
                act.dma_start(mem_raw[:, 4 * q:4 * q + 4], memT[:, 4 * q:4 * q + 4]).then_inc(in_mem[q], 16)
            act.dma_start(w2_sb[:], w2).then_inc(in_lora, 16)
            act.dma_start(a2_sb[:], a2).then_inc(in_lora, 16)
            act.dma_start(wgu_sb[:], wgu).then_inc(in_lora, 16)

            def split_all(norm, parts, half=(0, 1)):
                for kt in range(HALF * half[0], HALF * (half[-1] + 1)):
                    if kt % 4 == 0:
                        act.wait_ge(parts[kt // 4], 16)
                    norm.act_tile(act, kt)
            split_hi(act, Tile(0, 0), (0,))
            act.wait_ge(in_par, 16)
            split_all(x_norm, in_x, (0,))
            split_hi(act, Tile(0, 0), (1,))
            split_all(x_norm, in_x, (1,))
            split_hi(act, Tile(0, 1))

            def after_plain0():
                x_norm.act_root(act)
                act_lam(act)
                split_all(mem_norm, in_mem, (0,))
            act_split_phase(act, "plain", {0: after_plain0, 1: lambda: split_all(mem_norm, in_mem, (1,)), 8: lambda: act_squares(act, 0),
                                           10: lambda: act_roots(act, range(4)), 12: lambda: act_squares(act, 1)}, peel=COUNT["plain"] // 2)
            act_split_phase(act, "mem_kv", {0: lambda: (act_roots(act, (4, 5)), mem_norm.act_root(act)), 4: lambda: act_squares(act, 2),
                                            6: lambda: act_roots(act, (6, 7))}, peel=COUNT["mem_kv"] // 2)
            act_attn(act)
            act_rwkv(act)
            act_gn(act)
            act_merge(act)
            act_merge_b(act)
            act.wait_ge(in_meta, 16)
            act_norm_phase(act, "wout1", norm1, wout1_out)
            act_func_phase(act, "gpool", gpl, gpool_pre, PO, ACT.Sigmoid, gpool_out, {0: lambda: norm1.act_root(act)})
            act_func_phase(act, "gelu", gel, gelu_pre, HL, ACT.Gelu_apprx_tanh, gelu_out)
            act_pool(act)
            act_lru(act)
            act_glru(act)
            act_norm_phase(act, "wout2", norm2, wout2_out)
            mlp2.act(act, {0: lambda: norm2.act_root(act)})
            act_split_phase(act, "conv3", {0: lambda: final.act_root(act)})
            act_gla(act)
            act_split_phase(act, "wout3", {SHIFT_TILE + 1: lambda: ln1.act_shift(act)}, peel=SHIFT_TILE // 2 + 2)
            ln1.act(act)
            mlp3.act(act, last={SHIFT_TILE + 1: lambda: ln2.act_shift(act)})
            ln2.act(act)

        @block.vector
        def _(v):
            def split_all(norm, half=(0, 1)):
                for kt in range(HALF * half[0], HALF * (half[-1] + 1)):
                    norm.dve_tile(v, kt, kt + 1)
            split_lo(v, Tile(0, 0), (0,))
            v.wait_ge(in_par, 16)
            split_all(x_norm, (0,))
            split_lo(v, Tile(0, 0), (1,))
            split_all(x_norm, (1,))
            split_lo(v, Tile(0, 1))

            dve_scaled_phase(v, "plain", x_norm, pl, plain_out, {0: lambda: x_norm.dve_rstd(v)},
                             {0: lambda: split_all(mem_norm, (0,)), 1: lambda: split_all(mem_norm, (1,)),
                              **{11 + b: lambda b=b: dve_factors(v, [b]) for b in range(3)}}, peel=COUNT["plain"] // 2)
            dve_scaled_phase(v, "mem_kv", mem_norm, mkv, mem_out, {0: lambda: mem_norm.dve_rstd(v)}, {0: lambda: dve_factors(v, [3]), 1: lambda: dve_factors(v, [4]), 2: lambda: dve_factors(v, [5]),
                              3: lambda: dve_normed(v, 0, 8, "norm"), 6: lambda: dve_rope(v, (0, 1)), 7: lambda: dve_rope(v, (2, 3)),
                              4: lambda: dve_lam(v)},
                             peel=COUNT["mem_kv"] // 2)
            dve_attn(v)
            dve_rwkv(v)
            dve_gn(v)
            dve_merge(v)
            dve_merge_b(v)
            dve_wout1(v)
            dve_pre_phase(v, "gpool", norm1, gpl, gpool_pre, gpool_out, {0: lambda: norm1.dve_rstd(v)})
            dve_pre_phase(v, "gelu", norm1, gel, gelu_pre, gelu_out)
            dve_pool(v)
            dve_lru(v)
            dve_glru(v)
            dve_add_phase(v, "wout2", x2, 1.0, wout2_out, norm2)
            mlp2.dve(v, {0: lambda: norm2.dve_rstd(v)})
            dve_conv3(v)
            dve_gla(v)
            dve_add_phase(v, "wout3", X3, ALPHA3, wout3_out)
            ln1.dve(v)
            mlp3.dve(v)
            ln2.dve(v)

        @block.tensor
        def _(pe):
            def x_stat():
                pe.wait_ge(in_cst, 16)
                x_norm.pe(pe)
            plain_phase(pe, "plain", hx, plain_out, before=lambda k: x_norm.ready(pe, k), after={1: x_stat, 9: lambda: pe_stats(pe, range(4)), 13: lambda: pe_stats(pe, (4, 5))}, peel=COUNT["plain"] // 2)
            STATS = {0: lambda: mem_norm.pe(pe), 5: lambda: pe_stats(pe, (6, 7)), 6: lambda: pe_rotated(pe)}
            plain_phase(pe, "mem_kv", mem_hl, mem_out, before=lambda k: mem_norm.ready(pe, k), after=STATS, peel=COUNT["mem_kv"] // 2,
                        entry=lambda t: pe.wait_ge(plain_out, COUNT["plain"] - 1 + t))
            pe_attn(pe)
            pe_rwkv(pe)
            pe_merge(pe)
            pe_merge_b(pe)
            plain_phase(pe, "wout1", mg, wout1_out, before=lambda k: pe.wait_ge(mg_lo, HALF * (k + 1)),
                        entry=lambda t: pe.wait_ge(gate_pre, N_BRANCH * MERGE_A))
            plain_phase(pe, "gpool", u1, gpool_pre, before=lambda k: norm1.ready(pe, k), after={0: lambda: norm1.pe(pe)},
                        entry=lambda t: pe.wait_ge(wout1_out, KT - 1 + t))
            plain_phase(pe, "gelu", u1, gelu_pre, entry=lambda t: pe.wait_ge(gpool_pre, KT - 1 + t))
            pe_pool(pe)
            pe_lru(pe)
            plain_phase(pe, "glru", u1, glru_pre, entry=lambda t: pe.wait_ge(vl_copied, KT))
            plain_phase(pe, "wout2", mg2, wout2_out, before=lambda k: pe.wait_ge(mg2_lo, HALF * (k + 1)),
                        entry=lambda t: pe.wait_ge(glru_pre, KT - 1 + t))
            mlp2.pe(pe, lambda k: norm2.ready(pe, k), lambda: norm2.pe(pe), lambda t: pe.wait_ge(wout2_out, KT - 1 + t))
            pe_conv3(pe)

            pe_gla(pe)
            plain_phase(pe, "wout3", mix, wout3_out, before=lambda k: need(pe, g_v, ("clo1", "olo3")[k]),
                        entry=lambda t: pe.wait_ge(gp_out, COUNT["gla"] - 1 + t),
                        after={SHIFT_TILE: lambda: ln1.pe_shift(pe)}, peel=SHIFT_TILE // 2 + 2)
            ln1.pe(pe)
            mlp3.pe(pe, lambda k: ln1.ready(pe, k), entry=lambda t: pe.wait_ge(wout3_out, KT - 1 + t),
                    last={SHIFT_TILE: lambda: ln2.pe_shift(pe)})
            ln2.pe(pe)


def full_tiles(w):
    n = w.shape[1] // P
    return w.reshape(2, HALF, P, n, P).transpose(3, 0, 2, 1, 4).reshape(n, 2, P, HALF, P)


def stream_of(a):
    w_in, w_in2, w_in3 = a["w_in"][0], a["w_in_2"][0], a["w_in_3"][0]
    order = [h for pair in Q_PAIRS for h in pair]

    def by_pairs(w):
        return w.reshape(D, A_HEADS, HD)[:, order].reshape(D, A_HEADS * HD)
    aq, ak, av, ag, rs, rg, xq, xg, mg = np.split(w_in, np.cumsum([768, 256, 256, 768, 2560, 768, 512, 512]), axis=1)
    tiles = {"shift": full_tiles(rs), "silu": full_tiles(np.concatenate([by_pairs(ag), rg, xg], 1))}
    beside = np.stack([tiles[kind][m] for kind, m in ATTN_TILES], 0)
    wo = np.concatenate([a["attn_w_o"][0].reshape(A_HEADS, HD, D)[order].reshape(A_HEADS * HD, D),
                         a["rwkv_w_o"][0], a["x_w_o"][0]], 0)
    gates = full_tiles(mg).reshape(N_BRANCH, KT, 2, P, HALF, P)
    wo = full_tiles(wo)
    rwkv = np.concatenate([full_tiles(rg)[None], gates[:, MERGE_A:]], 0).transpose(1, 0, 2, 3, 4, 5)
    merge_a = np.concatenate([gates[:, :MERGE_A], wo[None, :MERGE_A]], 0).transpose(1, 0, 2, 3, 4, 5)
    merge_b = wo[MERGE_A:]
    v_pool, v_lru, v_gelu, g_pool, g_lru = np.split(w_in2, 5, axis=1)
    pool_w = a["pool_w_2"][0].reshape(4, 4, P, 2, 2, P).transpose(0, 3, 2, 4, 1, 5).reshape(4, 1, 2, P, HALF, P)
    lru_w = np.stack([a["gate_a_w_2"][0], a["gate_x_w_2"][0]], 0).reshape(2, 4, 2, 2, P, 2, P)
    lru_w = lru_w.transpose(1, 2, 4, 0, 5, 3, 6).reshape(4, 1, 2, P, HALF, P)

    def with_own(w, own):
        four = np.concatenate([full_tiles(w).reshape(4, 4, 2, P, HALF, P), own], 1)
        return np.stack([four[g, j] for g, j in OWN_ORDER], 0)
    b3, c3, u3, q3, k3, v3, r3, z3 = np.split(w_in3, np.cumsum([1024, 1024, 1024, 512, 512, 1024, 1024]), axis=1)
    z3 = np.concatenate([z3, np.zeros((D, P - z3.shape[1]), z3.dtype)], 1)
    conv3 = np.stack([full_tiles(c3), full_tiles(u3), full_tiles(b3)], 0).transpose(1, 0, 2, 3, 4, 5)

    def mlp(w1, w2):
        up = full_tiles(w1).reshape(FF_GROUPS, KT, 2, P, HALF, P)
        down = np.stack([full_tiles(w) for w in w2.reshape(FF_GROUPS, D, D)], 0)
        return np.concatenate([up, down], 1)
    parts = [full_tiles(np.concatenate([by_pairs(aq), ak, xq, av], 1)), full_tiles(a["x_w_kv"][0]), beside, rwkv, merge_a, merge_b, full_tiles(a["w_out"][0]),
             full_tiles(g_pool), full_tiles(v_gelu), with_own(v_pool, pool_w), with_own(v_lru, lru_w),
             full_tiles(g_lru), full_tiles(a["w_out_2"][0]), mlp(a["mlp_w1_2"][0], a["mlp_w2_2"][0]),
             conv3, full_tiles(np.concatenate([z3, q3, k3, v3, r3], 1)), full_tiles(a["w_out_3"][0]),
             mlp(a["w_ff_up_3"][0], a["w_ff_down_3"][0]), np.zeros((2 * PAD, P, HALF, P), w_in.dtype)]
    return np.concatenate([p.reshape(-1, P, HALF, P) for p in parts], 0)


def params_of(a):
    named = {"mu": "rwkv_mu", "k_k": "rwkv_k_k", "k_a": "rwkv_k_a", "r_k": "rwkv_r_k", "w0": "rwkv_w0", "a0": "rwkv_a0",
             "ln_w": "rwkv_ln_w", "ln_b": "rwkv_ln_b", "q_g": "attn_q_norm_g", "k_g": "attn_k_norm_g",
             "xq_g": "x_q_norm_g", "xk_g": "x_k_norm_g", "norm1_g": "norm1_g_2", "pool_scale": "pool_scale_2",
             "conv_w2": "conv_w_2", "conv_b2": "conv_b_2", "gate_a_b": "gate_a_b_2", "gate_x_b": "gate_x_b_2",
             "lam": "lru_lambda_2", "norm2_g": "norm2_g_2", "final_g": "final_g_2", "conv_w3": "conv_w_3",
             "conv_g3": "conv_norm_g_3", "gate_bias3": "gate_bias_3", "gla_g3": "gla_norm_g_3", "ln1_g": "ln1_g_3",
             "ln1_b": "ln1_b_3", "ln2_g": "ln2_g_3", "ln2_b": "ln2_b_3"}
    cols = []
    for name, n in PARAMS:
        if name == "sink":
            pairs = a["attn_sink"][0][np.array(Q_PAIRS)]
            c = np.broadcast_to(np.repeat(pairs.reshape(-1), NB)[None], (P, n))
        else:
            c = a[named.get(name, name)].reshape(-1)
            c = np.concatenate([c, c]) if c.shape[0] == HD else c
            c = c.reshape(n, P).T
        cols.append(c)
    return np.ascontiguousarray(np.concatenate(cols, 1))


def channel_major(x):
    return np.ascontiguousarray(x.T.reshape(KT, P, -1).transpose(1, 0, 2))


def arrays_of(inputs):
    a = {k: np.asarray(v) for k, v in inputs.items()}
    return {
        "stream": stream_of(a), "consts": constants(), "params": params_of(a),
        "w2": np.ascontiguousarray(a["rwkv_w2"][0].reshape(P, PAIRS, P)),
        "a2": np.ascontiguousarray(a["rwkv_a2"][0].reshape(P, PAIRS, P)),
        "wgu": np.ascontiguousarray(a["w_gate_up_3"][0].reshape(16, GLA_H, P)),
        "memT": channel_major(a["mem"][0]), "xT": channel_major(a["x"][0]), "metaT": channel_major(a["meta_tokens_2"]),
    }


def kernel(**inputs):
    import concourse.bacc as bacc
    from concourse.bass_utils import run_bass_kernel_spmd

    nc = bacc.Bacc("TRN2", target_bir_lowering=False, num_devices=1)
    arrays = arrays_of(inputs)
    args = [nc.dram_tensor(n, x.shape, mybir.dt.from_np(x.dtype), kind="ExternalInput").ap() for n, x in arrays.items()]
    out = nc.dram_tensor("out", (P, KT, T), mybir.dt.float32, kind="ExternalOutput").ap()
    build(nc, *args, out)
    got = run_bass_kernel_spmd(nc, [arrays], core_ids=[0]).results[0]["out"]
    return got.transpose(2, 1, 0).reshape(1, T, D)
```
